# Optimizing a Trainium2 kernel written in Bass

```python
import math
import jax
import jax.numpy as jnp
from jax import lax
import numpy as np

D_MODEL = 1024
BATCH = 1
SEQ = 256
DEPTH = 2
DEC_BATCH = 8
DEC_SEQ = 1
PAST_LEN = 1024
PAGE_SIZE = 128

MLA_HEADS = 8
MLA_NOPE = 64
MLA_ROPE = 32
MLA_V = 64
Q_LORA = 256
KV_LORA = 256
ROPE_THETA = 10000.0
MLA_SCALE = (MLA_NOPE + MLA_ROPE) ** -0.5
Q_BLOCK = 128
MLA_IN = Q_LORA + KV_LORA + MLA_ROPE
RWKV_HEADS = 8
RWKV_HEAD = 64
RWKV_DIM = RWKV_HEADS * RWKV_HEAD
DECAY_LORA = 64
AAA_LORA = 64
GATE_LORA = 128
RWKV_IN = 3 * RWKV_DIM + DECAY_LORA + AAA_LORA + GATE_LORA
RWKV_LN_EPS = 64e-5
SSM_HEADS = 8
SSM_HEAD = 64
SSM_DIM = SSM_HEADS * SSM_HEAD
SSM_GROUPS = 2
SSM_STATE = 128
SSM_CONV = 4
SSM_CHUNK = 128
SSM_CONV_DIM = SSM_DIM + 2 * SSM_GROUPS * SSM_STATE
SSM_IN = SSM_DIM + SSM_CONV_DIM + SSM_HEADS
N_BRANCH = 3
BRANCH_DIM = 512
IN_DIM = MLA_IN + RWKV_IN + SSM_IN + N_BRANCH * D_MODEL
D_FF = 2816
N_EXPERTS = 8
TOP_K = 2
D_FF_EXPERT = 3584
EPS = 1e-6

kernel_name = 'hybrid_mla_rwkv7_mamba2_adaln_decode_step'

def _split(x, sizes):
    return jnp.split(x, list(np.cumsum(sizes)[:-1]), axis=-1)

def rmsnorm(x, w):
    x32 = x.astype(jnp.float32)
    y = x32 * lax.rsqrt(jnp.mean(x32 * x32, axis=-1, keepdims=True) + EPS)
    return (y * w.astype(jnp.float32)).astype(x.dtype)

def rope(x, pos):
    half = x.shape[-1] // 2
    freq = ROPE_THETA ** (-jnp.arange(half, dtype=jnp.float32) / half)
    ang = pos.astype(jnp.float32)[:, None] * freq[None, :]
    ang = ang.reshape((1, pos.shape[0]) + (1,) * (x.ndim - 3) + (half,))
    cos, sin = jnp.cos(ang), jnp.sin(ang)
    x32 = x.astype(jnp.float32)
    x1, x2 = x32[..., :half], x32[..., half:]
    return jnp.concatenate([x1 * cos - x2 * sin, x2 * cos + x1 * sin], axis=-1).astype(x.dtype)

def mla_attend_causal(q_abs, q_pe, ckv, kpe):
    b, s, h, c = q_abs.shape
    nb = s // Q_BLOCK
    qa = jnp.moveaxis(q_abs.reshape(b, nb, Q_BLOCK, h, c), 1, 0)
    qp = jnp.moveaxis(q_pe.reshape(b, nb, Q_BLOCK, h, MLA_ROPE), 1, 0)
    kpos = jnp.arange(s)

    def block(args):
        qa_i, qp_i, i = args
        sc = (jnp.einsum('bqhc,bkc->bhqk', qa_i, ckv) + jnp.einsum('bqhr,bkr->bhqk', qp_i, kpe)).astype(jnp.float32) * MLA_SCALE
        qpos = i * Q_BLOCK + jnp.arange(Q_BLOCK)
        sc = jnp.where(kpos[None, :] <= qpos[:, None], sc, -jnp.inf)
        pr = jax.nn.softmax(sc, axis=-1).astype(ckv.dtype)
        return jnp.einsum('bhqk,bkc->bqhc', pr, ckv)

    o = lax.map(block, (qa, qp, jnp.arange(nb)))
    return jnp.moveaxis(o, 0, 1).reshape(b, s, h, c)

def paged_attend(ckv_past, kpe_past):
    def attend(q_abs, q_pe, ckv, kpe):
        s = q_abs.shape[1]
        n_past = ckv_past.shape[1]
        sc_past = jnp.einsum('bqhc,bkc->bhqk', q_abs, ckv_past) + jnp.einsum('bqhr,bkr->bhqk', q_pe, kpe_past)
        sc_new = jnp.einsum('bqhc,bkc->bhqk', q_abs, ckv) + jnp.einsum('bqhr,bkr->bhqk', q_pe, kpe)
        causal = jnp.arange(s)[None, :] <= jnp.arange(s)[:, None]
        sc_new = jnp.where(causal, sc_new.astype(jnp.float32), -jnp.inf)
        sc = jnp.concatenate([sc_past.astype(jnp.float32), sc_new], axis=-1) * MLA_SCALE
        pr = jax.nn.softmax(sc, axis=-1).astype(ckv.dtype)
        return (jnp.einsum('bhqk,bkc->bqhc', pr[..., :n_past], ckv_past)
                + jnp.einsum('bhqk,bkc->bqhc', pr[..., n_past:], ckv))
    return attend

def mla_branch(q_c, kv_c, kr, pos, p, attend):
    b, s, _ = q_c.shape
    q = (rmsnorm(q_c, p['q_norm']) @ p['w_uq']).reshape(b, s, MLA_HEADS, MLA_NOPE + MLA_ROPE)
    q_nope, q_pe = q[..., :MLA_NOPE], rope(q[..., MLA_NOPE:], pos)
    ckv = rmsnorm(kv_c, p['kv_norm'])
    kpe = rope(kr, pos)
    q_abs = jnp.einsum('bshd,chd->bshc', q_nope, p['w_uk'])
    o_lat = attend(q_abs, q_pe, ckv, kpe)
    out = jnp.einsum('bshc,chv->bshv', o_lat, p['w_uv']).reshape(b, s, MLA_HEADS * MLA_V)
    return out, ckv, kpe

def rwkv_branch(rw, shift0, wkv0, p):
    b, s, _ = rw.shape
    f32 = jnp.float32
    prev = jnp.concatenate([shift0[:, None, :], rw[:, :-1]], axis=1)
    xs = rw + (prev - rw) * p['rwkv_mu']
    r, k, v, wl, al, gl = _split(xs, [RWKV_DIM, RWKV_DIM, RWKV_DIM, DECAY_LORA, AAA_LORA, GATE_LORA])
    w = -jax.nn.softplus(-(p['rwkv_w0'] + jnp.tanh(wl) @ p['rwkv_w2']).astype(f32)) - 0.5
    decay = jnp.exp(-jnp.exp(w))
    a = jax.nn.sigmoid((p['rwkv_a0'] + al @ p['rwkv_a2']).astype(f32))
    g = jax.nn.sigmoid(gl) @ p['rwkv_g2']

    def heads(t):
        return t.astype(f32).reshape(b, s, RWKV_HEADS, RWKV_HEAD)

    r_h, v_h, a_h, w_h = heads(r), heads(v), heads(a), heads(decay)
    kk = heads(k * p['rwkv_k_k'])
    kk = kk * lax.rsqrt(jnp.maximum(jnp.sum(kk * kk, axis=-1, keepdims=True), 1e-24))
    k_a = p['rwkv_k_a'].astype(f32).reshape(RWKV_HEADS, RWKV_HEAD)
    k_h = heads(k) * (1.0 + (a_h - 1.0) * k_a)

    def step(S, inp):
        r_t, w_t, k_t, v_t, kk_t, a_t = inp
        sa = jnp.einsum('bhij,bhj->bhi', S, -kk_t)
        S = S * w_t[:, :, None, :] + sa[..., None] * (kk_t * a_t)[:, :, None, :] + v_t[..., None] * k_t[:, :, None, :]
        return S, jnp.einsum('bhij,bhj->bhi', S, r_t)

    seq = tuple(jnp.moveaxis(t, 1, 0) for t in (r_h, w_h, k_h, v_h, kk, a_h))
    S1, y = lax.scan(step, wkv0.astype(f32), seq)
    y = jnp.moveaxis(y, 0, 1)
    mu = jnp.mean(y, axis=-1, keepdims=True)
    var = jnp.mean(jnp.square(y - mu), axis=-1, keepdims=True)
    y = (y - mu) * lax.rsqrt(var + RWKV_LN_EPS)
    y = (y * p['rwkv_ln_w'].astype(f32).reshape(RWKV_HEADS, RWKV_HEAD)
         + p['rwkv_ln_b'].astype(f32).reshape(RWKV_HEADS, RWKV_HEAD))
    y = y + jnp.sum(r_h * k_h * p['rwkv_r_k'].astype(f32), axis=-1, keepdims=True) * v_h
    out = y.reshape(b, s, RWKV_DIM).astype(rw.dtype) * g
    return out, rw[:, -1], S1.astype(rw.dtype)

def ssd(x, dt, a, bm, cm, h0):
    b, l, h, pdim = x.shape
    cl = min(SSM_CHUNK, l)
    pad = (-l) % cl
    if pad:
        x = jnp.pad(x, ((0, 0), (0, pad), (0, 0), (0, 0)))
        dt = jnp.pad(dt, ((0, 0), (0, pad), (0, 0)))
        bm = jnp.pad(bm, ((0, 0), (0, pad), (0, 0), (0, 0)))
        cm = jnp.pad(cm, ((0, 0), (0, pad), (0, 0), (0, 0)))
    nc = (l + pad) // cl
    rep = h // SSM_GROUPS
    Bh = jnp.repeat(bm, rep, axis=2).reshape(b, nc, cl, h, SSM_STATE)
    Ch = jnp.repeat(cm, rep, axis=2).reshape(b, nc, cl, h, SSM_STATE)
    X = (x * dt[..., None]).reshape(b, nc, cl, h, pdim)
    adt = jnp.transpose((dt * a).reshape(b, nc, cl, h), (0, 3, 1, 2))
    cs = jnp.cumsum(adt, axis=-1)
    seg = cs[..., :, None] - cs[..., None, :]
    causal = jnp.tril(jnp.ones((cl, cl), dtype=bool))
    Lmat = jnp.where(causal, jnp.exp(jnp.where(causal, seg, 0.0)), 0.0)
    y_diag = jnp.einsum('bclhn,bcshn,bhcls,bcshp->bclhp', Ch, Bh, Lmat, X)
    decay_states = jnp.exp(cs[..., -1:] - cs)
    states = jnp.einsum('bclhn,bhcl,bclhp->bchpn', Bh, decay_states, X)
    chunk_decay = jnp.exp(cs[..., -1])

    def step(hc, inp):
        st, dec = inp
        return hc * dec[:, :, None, None] + st, hc

    hT, h_prev = lax.scan(step, h0, (jnp.moveaxis(states, 1, 0), jnp.moveaxis(chunk_decay, 2, 0)))
    h_prev = jnp.moveaxis(h_prev, 0, 1)
    y_off = jnp.einsum('bclhn,bchpn,bhcl->bclhp', Ch, h_prev, jnp.exp(cs))
    y = (y_diag + y_off).reshape(b, nc * cl, h, pdim)[:, :l]
    return y, hT

def ssm_branch(z, xbc, dt_raw, conv0, ssm0, p):
    b, s, _ = xbc.shape
    f32 = jnp.float32
    full = jnp.concatenate([conv0, xbc], axis=1)
    conv = p['conv_b'] + sum(full[:, i:i + s] * p['conv_w'][i] for i in range(SSM_CONV))
    conv1 = full[:, -(SSM_CONV - 1):]
    xa, bm, cm = _split(jax.nn.silu(conv), [SSM_DIM, SSM_GROUPS * SSM_STATE, SSM_GROUPS * SSM_STATE])
    x = xa.astype(f32).reshape(b, s, SSM_HEADS, SSM_HEAD)
    dt = jax.nn.softplus((dt_raw + p['dt_bias']).astype(f32))
    a = -jnp.exp(p['a_log'].astype(f32))
    y, ssm1 = ssd(x, dt, a, bm.astype(f32).reshape(b, s, SSM_GROUPS, SSM_STATE),
                  cm.astype(f32).reshape(b, s, SSM_GROUPS, SSM_STATE), ssm0.astype(f32))
    y = y + p['d_skip'].astype(f32)[:, None] * x
    y = y.reshape(b, s, SSM_DIM) * jax.nn.silu(z.astype(f32))
    yg = y.reshape(b, s, SSM_GROUPS, SSM_DIM // SSM_GROUPS)
    yg = yg * lax.rsqrt(jnp.mean(yg * yg, axis=-1, keepdims=True) + EPS)
    out = (yg.reshape(b, s, SSM_DIM) * p['ssm_norm'].astype(f32)).astype(xbc.dtype)
    return out, conv1, ssm1.astype(xbc.dtype)

def token_mixers(h, pos, p, attend, shift0, wkv0, conv0, ssm0):
    b, s, _ = h.shape
    proj = h @ p['w_in']
    q_c, kv_c, kr, rw, z, xbc, dt_raw, gate_raw = _split(
        proj, [Q_LORA, KV_LORA, MLA_ROPE, RWKV_IN, SSM_DIM, SSM_CONV_DIM, SSM_HEADS, N_BRANCH * D_MODEL])
    a_out, ckv, kpe = mla_branch(q_c, kv_c, kr, pos, p, attend)
    r_out, shift1, wkv1 = rwkv_branch(rw, shift0, wkv0, p)
    s_out, conv1, ssm1 = ssm_branch(z, xbc, dt_raw, conv0, ssm0, p)
    branches = jnp.stack([a_out, r_out, s_out], axis=2)
    per_branch = jnp.einsum('bsrw,rwd->bsrd', branches, p['w_branch'])
    gates = jax.nn.sigmoid(gate_raw.reshape(b, s, N_BRANCH, D_MODEL))
    mix = jnp.sum(gates * per_branch, axis=2) @ p['w_out']
    return mix, ckv, kpe, shift1, wkv1, conv1, ssm1

def swiglu(h, w1, w3, w2):
    return (jax.nn.silu(h @ w1) * (h @ w3)) @ w2

def moe_ffn(h, router, router_b, w1, w3, w2):
    logits = (h @ router + router_b).astype(jnp.float32)
    top_v, top_i = lax.top_k(logits, TOP_K)
    top_w = jax.nn.softmax(top_v, axis=-1)
    gate = jnp.sum(jax.nn.one_hot(top_i, N_EXPERTS, dtype=jnp.float32) * top_w[..., None], axis=-2).astype(h.dtype)
    out = jnp.zeros_like(h)
    for e in range(N_EXPERTS):
        out = out + gate[..., e:e + 1] * swiglu(h, w1[e], w3[e], w2[e])
    return out

def setup_inputs(seed: int = 0) -> dict:
    key = jax.random.key(seed)
    ks = jax.random.split(key, 64)
    cnt = [0]

    def nk():
        cnt[0] += 1
        return ks[cnt[0] - 1]

    def nrm(shape, scale):
        return jax.random.normal(nk(), shape, jnp.float32) * scale

    def unif(shape, lo, hi):
        return jax.random.uniform(nk(), shape, jnp.float32, lo, hi)

    n_pages = PAST_LEN // PAGE_SIZE
    n_phys = (DEC_BATCH * n_pages * 5) // 4
    n_dense, n_moe = (DEPTH + 1) // 2, DEPTH // 2
    page_table = jax.random.permutation(nk(), n_phys)[:DEC_BATCH * n_pages].reshape(DEC_BATCH, n_pages).astype(jnp.int32)
    dt0 = jnp.exp(unif((DEPTH, SSM_HEADS), math.log(1e-3), math.log(1e-1)))
    return {
        'x_prompt': nrm((BATCH, SEQ, D_MODEL), 1.0),
        'x_sample': nrm((DEC_BATCH, DEC_SEQ, D_MODEL), 1.0),
        'cache_ckv': nrm((DEPTH, n_phys, PAGE_SIZE, KV_LORA), 1.0),
        'cache_kpe': nrm((DEPTH, n_phys, PAGE_SIZE, MLA_ROPE), 1.0),
        'state_rwkv_shift': nrm((DEPTH, DEC_BATCH, RWKV_IN), 1.0),
        'state_rwkv_wkv': nrm((DEPTH, DEC_BATCH, RWKV_HEADS, RWKV_HEAD, RWKV_HEAD), 0.3),
        'state_ssm_conv': nrm((DEPTH, DEC_BATCH, SSM_CONV - 1, SSM_CONV_DIM), 1.0),
        'state_ssm': nrm((DEPTH, DEC_BATCH, SSM_HEADS, SSM_HEAD, SSM_STATE), 0.3),
        'page_table': page_table,
        'c_prompt': nrm((BATCH, D_MODEL), 1.0),
        'c_sample': nrm((DEC_BATCH, D_MODEL), 1.0),
        'w_ada': nrm((DEPTH, D_MODEL, 6 * D_MODEL), 0.5 * D_MODEL ** -0.5),
        'b_ada': nrm((DEPTH, 6 * D_MODEL), 0.02),
        'norm_attn': 1.0 + nrm((DEPTH, D_MODEL), 0.05),
        'norm_ffn': 1.0 + nrm((DEPTH, D_MODEL), 0.05),
        'norm_final': 1.0 + nrm((D_MODEL,), 0.05),
        'w_in': nrm((DEPTH, D_MODEL, IN_DIM), D_MODEL ** -0.5),
        'mla_q_norm': 1.0 + nrm((DEPTH, Q_LORA), 0.05),
        'mla_w_uq': nrm((DEPTH, Q_LORA, MLA_HEADS * (MLA_NOPE + MLA_ROPE)), Q_LORA ** -0.5),
        'mla_kv_norm': 1.0 + nrm((DEPTH, KV_LORA), 0.05),
        'mla_w_uk': nrm((DEPTH, KV_LORA, MLA_HEADS, MLA_NOPE), KV_LORA ** -0.5),
        'mla_w_uv': nrm((DEPTH, KV_LORA, MLA_HEADS, MLA_V), KV_LORA ** -0.5),
        'rwkv_mu': unif((DEPTH, RWKV_IN), 0.0, 1.0),
        'rwkv_w0': nrm((DEPTH, RWKV_DIM), 0.5),
        'rwkv_w2': nrm((DEPTH, DECAY_LORA, RWKV_DIM), 0.1),
        'rwkv_a0': nrm((DEPTH, RWKV_DIM), 0.1),
        'rwkv_a2': nrm((DEPTH, AAA_LORA, RWKV_DIM), 0.1),
        'rwkv_g2': nrm((DEPTH, GATE_LORA, RWKV_DIM), GATE_LORA ** -0.5),
        'rwkv_k_k': 0.85 + nrm((DEPTH, RWKV_DIM), 0.05),
        'rwkv_k_a': 1.0 + nrm((DEPTH, RWKV_DIM), 0.05),
        'rwkv_r_k': nrm((DEPTH, RWKV_HEADS, RWKV_HEAD), 0.1),
        'rwkv_ln_w': 1.0 + nrm((DEPTH, RWKV_DIM), 0.05),
        'rwkv_ln_b': nrm((DEPTH, RWKV_DIM), 0.02),
        'ssm_conv_w': nrm((DEPTH, SSM_CONV, SSM_CONV_DIM), SSM_CONV ** -0.5),
        'ssm_conv_b': nrm((DEPTH, SSM_CONV_DIM), 0.02),
        'ssm_dt_bias': dt0 + jnp.log(-jnp.expm1(-dt0)),
        'ssm_a_log': jnp.log(unif((DEPTH, SSM_HEADS), 1.0, 16.0)),
        'ssm_d': 1.0 + nrm((DEPTH, SSM_HEADS), 0.1),
        'ssm_norm': 1.0 + nrm((DEPTH, SSM_DIM), 0.05),
        'w_branch': nrm((DEPTH, N_BRANCH, BRANCH_DIM, D_MODEL), BRANCH_DIM ** -0.5),
        'w_out': nrm((DEPTH, D_MODEL, D_MODEL), D_MODEL ** -0.5),
        'ffn_w1': nrm((n_dense, D_MODEL, D_FF), D_MODEL ** -0.5),
        'ffn_w3': nrm((n_dense, D_MODEL, D_FF), D_MODEL ** -0.5),
        'ffn_w2': nrm((n_dense, D_FF, D_MODEL), D_FF ** -0.5),
        'moe_router': nrm((n_moe, D_MODEL, N_EXPERTS), D_MODEL ** -0.5),
        'moe_router_b': nrm((n_moe, N_EXPERTS), 0.01),
        'moe_w1': nrm((n_moe, N_EXPERTS, D_MODEL, D_FF_EXPERT), D_MODEL ** -0.5),
        'moe_w3': nrm((n_moe, N_EXPERTS, D_MODEL, D_FF_EXPERT), D_MODEL ** -0.5),
        'moe_w2': nrm((n_moe, N_EXPERTS, D_FF_EXPERT, D_MODEL), D_FF_EXPERT ** -0.5),
    }

def reference(x_prompt, x_sample, cache_ckv, cache_kpe, state_rwkv_shift, state_rwkv_wkv, state_ssm_conv, state_ssm,
              page_table, c_prompt, c_sample, w_ada, b_ada, norm_attn, norm_ffn, norm_final, w_in,
              mla_q_norm, mla_w_uq, mla_kv_norm, mla_w_uk, mla_w_uv,
              rwkv_mu, rwkv_w0, rwkv_w2, rwkv_a0, rwkv_a2, rwkv_g2, rwkv_k_k, rwkv_k_a, rwkv_r_k, rwkv_ln_w, rwkv_ln_b,
              ssm_conv_w, ssm_conv_b, ssm_dt_bias, ssm_a_log, ssm_d, ssm_norm, w_branch, w_out,
              ffn_w1, ffn_w3, ffn_w2, moe_router, moe_router_b, moe_w1, moe_w3, moe_w2):

    def trunk(x, c, pos, paged, shift0, wkv0, conv0, ssm0):
        outs = [[] for _ in range(6)]
        for l in range(DEPTH):
            ada = (jax.nn.silu(c) @ w_ada[l] + b_ada[l])[:, None, :]
            sh_a, sc_a, g_a, sh_f, sc_f, g_f = jnp.split(ada, 6, axis=-1)
            h = rmsnorm(x, norm_attn[l]) * (1.0 + sc_a) + sh_a
            if paged is None:
                attend = mla_attend_causal
            else:
                ck, kp, pt = paged
                attend = paged_attend(ck[l][pt].reshape(pt.shape[0], -1, KV_LORA),
                                      kp[l][pt].reshape(pt.shape[0], -1, MLA_ROPE))
            p = dict(w_in=w_in[l], q_norm=mla_q_norm[l], w_uq=mla_w_uq[l], kv_norm=mla_kv_norm[l],
                     w_uk=mla_w_uk[l], w_uv=mla_w_uv[l], rwkv_mu=rwkv_mu[l], rwkv_w0=rwkv_w0[l],
                     rwkv_w2=rwkv_w2[l], rwkv_a0=rwkv_a0[l], rwkv_a2=rwkv_a2[l], rwkv_g2=rwkv_g2[l],
                     rwkv_k_k=rwkv_k_k[l], rwkv_k_a=rwkv_k_a[l], rwkv_r_k=rwkv_r_k[l], rwkv_ln_w=rwkv_ln_w[l],
                     rwkv_ln_b=rwkv_ln_b[l], conv_w=ssm_conv_w[l], conv_b=ssm_conv_b[l], dt_bias=ssm_dt_bias[l],
                     a_log=ssm_a_log[l], d_skip=ssm_d[l], ssm_norm=ssm_norm[l], w_branch=w_branch[l], w_out=w_out[l])
            mix, *st = token_mixers(h, pos, p, attend, shift0[l], wkv0[l], conv0[l], ssm0[l])
            x = x + g_a * mix
            h = rmsnorm(x, norm_ffn[l]) * (1.0 + sc_f) + sh_f
            if l % 2 == 0:
                f = swiglu(h, ffn_w1[l // 2], ffn_w3[l // 2], ffn_w2[l // 2])
            else:
                f = moe_ffn(h, moe_router[l // 2], moe_router_b[l // 2], moe_w1[l // 2], moe_w3[l // 2], moe_w2[l // 2])
            x = x + g_f * f
            for lst, v in zip(outs, st):
                lst.append(v)
        return rmsnorm(x, norm_final), [jnp.stack(v) for v in outs]

    bp, sp = x_prompt.shape[0], x_prompt.shape[1]
    dt = x_prompt.dtype
    pos_p = jnp.arange(sp, dtype=jnp.int32)
    y_prompt, (p_ckv, p_kpe, p_shift, p_wkv, p_conv, p_ssm) = trunk(
        x_prompt, c_prompt, pos_p, None,
        jnp.zeros((DEPTH, bp, RWKV_IN), dt),
        jnp.zeros((DEPTH, bp, RWKV_HEADS, RWKV_HEAD, RWKV_HEAD), dt),
        jnp.zeros((DEPTH, bp, SSM_CONV - 1, SSM_CONV_DIM), dt),
        jnp.zeros((DEPTH, bp, SSM_HEADS, SSM_HEAD, SSM_STATE), dt))
    p_ckv = p_ckv.reshape(DEPTH, bp * sp // PAGE_SIZE, PAGE_SIZE, KV_LORA)
    p_kpe = p_kpe.reshape(DEPTH, bp * sp // PAGE_SIZE, PAGE_SIZE, MLA_ROPE)

    past_len = page_table.shape[1] * PAGE_SIZE
    pos_s = past_len + jnp.arange(x_sample.shape[1], dtype=jnp.int32)
    y_sample, (s_ckv, s_kpe, s_shift, s_wkv, s_conv, s_ssm) = trunk(
        x_sample, c_sample, pos_s, (cache_ckv, cache_kpe, page_table),
        state_rwkv_shift, state_rwkv_wkv, state_ssm_conv, state_ssm)
    return (y_prompt, y_sample, p_ckv, p_kpe, p_shift, p_wkv, p_conv, p_ssm,
            s_ckv, s_kpe, s_shift, s_wkv, s_conv, s_ssm)


_drawn_inputs = setup_inputs


def setup_inputs(seed=0):
    import zlib

    import numpy as np

    out = dict(_drawn_inputs(seed))
    spreads = {}
    factors = {'cache_ckv': 4.865,
     'cache_kpe': 8.0,
     'mla_q_norm': 8.0,
     'rwkv_k_k': 9.01,
     'rwkv_ln_w': 6.036,
     'rwkv_ln_b': 8.0,
     'ssm_d': 4.037,
     'ssm_norm': 4.262,
     'moe_router_b': 15.812}
    for name, (base, spread) in spreads.items():
        noise = np.random.default_rng([zlib.crc32(name.encode()), seed]).standard_normal(out[name].shape)
        drawn = base * np.exp(spread * noise) if base else spread * noise
        out[name] = jnp.asarray(drawn.astype(out[name].dtype))
    for name, factor in factors.items():
        out[name] = (out[name] * factor).astype(out[name].dtype)
    return out
```

```python
import concourse.bass as bass
import numpy as np
from concourse import mybir

F32 = mybir.dt.float32
I32 = mybir.dt.int32
U32 = mybir.dt.uint32
ALU = mybir.AluOpType
ACT = mybir.ActivationFunctionType
X = mybir.AxisListType.X

P = 128
D = 1024
KC = D // P
SEQ = 256
NB = 8
T = SEQ + NB
NT = SEQ // P
DEPTH = 2
PAGE = 128
NPAGE = 8
HEADS = 8
ROPE = 32
LORA = 256
CACHE = LORA + ROPE
MLA_SCALE = 96 ** -0.5
RW_CH = 14
FF = 2816
NE = 8
FE = 3584
SLOT = KC * 512
RING_KEPT = 2
RING = 6
NSEQ = 1 + NB
EPS = 1e-6
LN_EPS = 64e-5
DECAY = -float(np.exp(-0.5))
LEVELS = (1, 2, 4, 8, 16, 32, 64)


def columns(widths):
    at, out = 0, {}
    for name, n in widths:
        out[name] = (at, at + n)
        at += n
    return out, at


VEC, NVEC = columns([("norm_attn", 8), ("norm_ffn", 8), ("norm_final", 8), ("b_ada", 48), ("q_norm", 2),
                     ("kv_norm", 2), ("mu", 14), ("a0", 4), ("k_k", 4), ("k_a", 4), ("r_k", 4), ("ln_w", 4),
                     ("ln_b", 4), ("conv_w", 32), ("conv_b", 8), ("d", 4), ("ssm_norm", 4), ("dt_bias", 1),
                     ("a_log", 1), ("router_b", 8)])
SMALL, NSMALL = columns([("w_kr", 1024), ("w_dt", 64), ("router", 64)])
MLA_W, NMLA = columns([("w_uq", 1536), ("w_uk", 1024), ("w_uv", 1024), ("w_ukT", 2048)])
RWKV_W, NRWKV = columns([("w2", 512), ("a2", 512), ("g2", 512)])
CONST, NCONST = columns([("ident", 128), ("ones", 128), ("block_ones", 128), ("decay_tri", 129), ("decay_id", 8),
                         ("levels", 7 * 128), ("strict", 128), ("upto", 128), ("causal", 128), ("fold", 64),
                         ("rotate", 128), ("cos", T), ("sin", T), ("spread", 512), ("eps", 1), ("ln_eps", 1), ("expert_ids", 8)])


class Steps:

    def __init__(self, nc, name, book):
        self.sem, self.name, self.book, self.count = nc.alloc_semaphore(name), name, book, 0

    def did(self, *step, by=1):
        self.count += by
        self.book.setdefault((self.name, step), self.count)
        return self.sem, by

    def at(self, *step):
        return self.sem, self.book.get((self.name, step), 1)


class Arena:

    def __init__(self, tensor, at, size):
        self.tensor, self.next, self.end = tensor, at, at + size

    def take(self, *shape):
        n = int(np.prod(shape))
        assert self.next + n <= self.end, (self.next, n, self.end)
        ap = self.tensor[:, self.next:self.next + n]
        self.next += n
        if len(shape) == 2:
            ap = ap.rearrange("p (a b) -> p a b", a=shape[0])
        elif len(shape) == 3:
            ap = ap.rearrange("p (a b c) -> p a b c", a=shape[0], b=shape[1])
        elif len(shape) == 4:
            ap = ap.rearrange("p (a b c d) -> p a b c d", a=shape[0], b=shape[1], c=shape[2])
        return ap


def bc(ap, axis, n):
    v = ap.unsqueeze(axis)
    shape = list(v.shape)
    shape[axis] = n
    return v.broadcast_to(shape)


class StageSteps:

    def __init__(self, steps, layer):
        self.steps, self.layer = steps, layer

    def did(self, *step):
        return self.steps.did(self.layer, *(step or ("step", self.steps.count)))

    def at(self, *step):
        return self.steps.at(self.layer, *step)

    def serial(self, eng):
        def do(ins, *step):
            ins.then_inc(*self.did(*step))
            eng.wait_ge(self.steps.sem, self.steps.count)
        return do


class Stage:

    def __init__(self, k, kind, layer):
        self.k, self.kind, self.l = k, kind, layer
        k.stages.append(self)
        self.before = k.stages[-2] if len(k.stages) > 1 else None
        self.t, self.v, self.a, self.g = (StageSteps(k.steps(kind, e), layer) for e in ("tensor", "vector", "scalar", "pool"))

    def by(self, who):
        return {"tensor": self.t, "vector": self.v, "scalar": self.a, "pool": self.g}[who]

    def tensor(self, pe):
        pass

    def vector(self, dve):
        pass

    def scalar(self, act):
        pass

    def pool(self, g):
        pass

    def emit(self, who, eng):
        own, none = {"tensor": (self.tensor, Stage.tensor), "vector": (self.vector, Stage.vector),
                     "scalar": (self.scalar, Stage.scalar), "pool": (self.pool, Stage.pool)}[who]
        takes_part = own.__func__ is not none
        if self.before is not None and takes_part:
            for other in ("tensor", "vector", "scalar", "pool"):
                sem, value = self.before.by(other).at("end")
                if value:
                    eng.wait_ge(sem, value)
        start = self.by(who).steps.count
        if takes_part:
            own(eng)
        s = self.by(who).steps
        s.book.setdefault((s.name, (self.l, "end")), s.count if s.count > start else 0)


class Ring:

    def __init__(self, k):
        self.k, self.loads, self.released = k, [], 0

    def add(self, place, dst, src):
        self.loads.append((place, dst, src, self.k.guard))
        return len(self.loads) - 1

    def arrived(self, eng, n):
        place = self.loads[n][0]
        eng.wait_ge(self.k.slot_loaded[place], 16 * sum(load[0] == place for load in self.loads[:n + 1]))

    def release(self, n, steps):
        self.k.book.setdefault(("release", n), (steps.steps.name, steps.steps.count))

    def fill(self, eng):
        last, guarded = {}, None
        for n, (place, dst, src, guard) in enumerate(self.loads):
            if place in last:
                name, count = self.k.book.get(("release", last[place]), (None, 0))
                if name:
                    eng.wait_ge(self.k.named[name].sem, count)
            if place >= RING_KEPT and guard is not None and guard is not guarded:
                for who in ("tensor", "vector", "scalar", "pool"):
                    sem, value = guard.by(who).at("end")
                    if value:
                        eng.wait_ge(sem, value)
                guarded = guard
            last[place] = n
            eng.dma_start(dst, src).then_inc(self.k.slot_loaded[place], 16)


class Kernel:

    def __init__(self, nc, dram, out, book):
        self.nc, self.book, self.out = nc, book, out
        self.stages, self.named, self.stores, self.page_turn = [], {}, 0, 0
        self.turn, self.guard = 0, None
        size = nc.sbuf_bytes_remaining // 32 * 8
        self.sb = nc.alloc_sbuf_tensor("work", [P, size], F32)
        kept = Arena(self.sb, 0, size)
        self.x, self.h, self.root = kept.take(KC, T), kept.take(KC, T), kept.take(T)
        self.consts, self.vecs, self.small = kept.take(NCONST), kept.take(NVEC), kept.take(NSMALL)
        self.ada, self.scale_a, self.scale_f = kept.take(48, NSEQ), kept.take(8, NSEQ), kept.take(8, NSEQ)
        self.c_in, self.silu_c = kept.take(KC, NSEQ), kept.take(KC, NSEQ)
        self.shift_in, self.conv_in, self.lastrow = kept.take(RW_CH, NB), kept.take(8, NB, 3), kept.take(RW_CH, NSEQ)
        self.one_minus_ka, self.small_a, self.pool_mark, self.gated_s = kept.take(4), kept.take(1), kept.take(1), kept.take(NB)
        self.table = kept.take(64).bitcast(I32)
        self.logits, self.gates, self.top_v, self.top_f = (kept.take(3, 8) for _ in range(4))
        self.top_i = kept.take(3, 8).bitcast(U32)
        self.top_e, self.top_w, self.one_hot = kept.take(3), kept.take(2, 3), kept.take(8)
        self.ring_at = kept.next
        self.work_at, self.work_size = self.ring_at + RING_KEPT * SLOT, (RING - RING_KEPT) * SLOT
        rest = Arena(self.sb, self.work_at + self.work_size, size - self.work_at - self.work_size)
        start = rest.next
        self.rw, self.xbc, self.xbc_s = rest.take(RW_CH, 1 + T), rest.take(8, 3 + SEQ), rest.take(8, NB, 4)
        self.z, self.dt_raw = rest.take(4, T), rest.take(T)
        self.mla_at, self.mla_size = self.work_at, rest.next - self.work_at
        self.qkv, self.kr, self.branches = rest.take(4, T), rest.take(T), rest.take(12, T)
        spare = Arena(self.sb, start, self.mla_at + self.mla_size - start)
        self.merge_mix, self.merge_gated, self.merge_gate = spare.take(KC, T), spare.take(2, T), spare.take(2, T)
        spare = Arena(self.sb, start, size - start)
        self.sq = spare.take(KC, T)
        spare = Arena(self.sb, start, size - start)
        self.hidden, self.moe_out, self.gate_rows, self.silu_up = (spare.take(*n) for n in ((FE // P, T), (KC, T), (NE, T), (2, T)))
        self.bank = [nc.alloc_psum_tensor(f"bank{i}", [P, 512], F32) for i in range(8)]
        self.slot_loaded = [nc.alloc_semaphore(f"slot{i}_loaded") for i in range(RING)]
        (self.const_loaded, self.vec_loaded, self.small_loaded, self.shift_loaded, self.conv_loaded, self.rwkv_w_loaded,
         self.mla_w_loaded, self.wkv_loaded, self.ssm_loaded, self.stored) = (nc.alloc_semaphore(n) for n in (
             "const_loaded", "vec_loaded", "small_loaded", "shift_loaded", "conv_loaded", "rwkv_w_loaded",
             "mla_w_loaded", "wkv_loaded", "ssm_loaded", "stored"))
        self.pages_loaded = [nc.alloc_semaphore(f"pages{i}_loaded") for i in range(2)]
        (self.x_in, self.consts_in, self.table_in, self.c_dram, self.vecs_in, self.small_in, self.shift_dram, self.conv_dram,
         self.rwkv_w, self.mla_w, self.wkv_in, self.ssm_in, self.cache, self.w_ada, self.w_in, self.w_branch, self.w_out,
         self.w1, self.w3, self.w2, self.e1, self.e3, self.e2) = (dram[n] for n in DRAM)
        self.page_regs = [nc.gpsimd.alloc_register(f"page{i}") for i in range(4)]
        self.ring = Ring(self)

    def steps(self, kind, who):
        name = f"{kind}_{who}"
        if name not in self.named:
            self.named[name] = Steps(self.nc, name, self.book)
        return self.named[name]

    def next_place(self):
        self.turn += 1
        return (self.turn - 1) % RING

    def slot(self, place):
        return self.sb[:, self.ring_at + SLOT * place:self.ring_at + SLOT * place + SLOT]

    def c(self, name):
        return self.consts[:, CONST[name][0]:CONST[name][1]]

    def vec(self, layer, name):
        return self.vecs[:, VEC[name][0]:VEC[name][1]]


DRAM = ("x", "consts", "table", "c", "vecs", "small", "shift", "conv", "rwkv_w", "mla_w", "wkv", "ssm", "cache", "w_ada", "w_in",
        "w_branch", "w_out", "ffn_w1", "ffn_w3", "ffn_w2", "moe_w1", "moe_w3", "moe_w2")
OUTS = {"y": (P, KC, T), "ckv": (DEPTH, P, 2, T), "kpe": (DEPTH, ROPE, T), "shift": (DEPTH, P, RW_CH, NSEQ),
        "p_wkv": (DEPTH, P, 4, 64), "s_wkv": (DEPTH, P, 4, NB, 64), "p_conv": (DEPTH, P, 8, 3), "s_conv": (DEPTH, P, 8, NB, 3),
        "p_ssm": (DEPTH, P, 512), "s_ssm": (DEPTH, P, 4, NB, P)}


class Ada(Stage):

    def __init__(self, k, l):
        super().__init__(k, "ada", l)
        self.slots = []
        for n in range(12):
            place = k.next_place()
            dst = k.slot(place).rearrange("p (k n) -> p k n", k=KC)
            self.slots.append(k.ring.add(place, dst, k.w_ada[l].rearrange("(k p) n -> p k n", p=P)[:, :, 512 * n:512 * n + 512]))

    def tensor(self, pe):
        k = self.k
        if self.l == 0:
            pe.wait_ge(*k.setup.a.at("silu_c"))
        for n, slot in enumerate(self.slots):
            k.ring.arrived(pe, slot)
            w = k.ring.loads[slot][1]
            for t in range(4):
                c = 4 * n + t
                for kk in range(KC):
                    mm = pe.matmul(k.bank[0][:, NSEQ * c:NSEQ * c + NSEQ], w[:, kk, P * t:P * t + P], k.silu_c[:, kk, :],
                                   start=kk == 0, stop=kk == KC - 1)
            mm.then_inc(*self.t.did("slot", n))
            k.ring.release(slot, self.t)

    def vector(self, dve):
        k = self.k
        do = self.v.serial(dve)
        dve.wait_ge(k.vec_loaded, 16 * (self.l + 1))
        dve.wait_ge(*self.t.at("slot", 11))
        do(dve.tensor_tensor(k.ada[:, :, :], k.bank[0][:, 0:48 * NSEQ].rearrange("p (c s) -> p c s", s=NSEQ),
                             k.vec(self.l, "b_ada").unsqueeze(2).broadcast_to([P, 48, NSEQ]), ALU.add))
        for part, w, out in ((1, "norm_attn", k.scale_a), (4, "norm_ffn", k.scale_f)):
            do(dve.scalar_tensor_tensor(out=out[:, :, :], in0=k.ada[:, 8 * part:8 * part + 8, :], scalar=1.0,
                                        in1=k.vec(self.l, w).unsqueeze(2).broadcast_to([P, 8, NSEQ]), op0=ALU.add, op1=ALU.mult))


class Norm(Stage):

    def __init__(self, k, l, which):
        super().__init__(k, f"norm_{which}", l)
        self.which = which

    def scalar(self, act):
        k = self.k
        act.activation(k.sq[:, :, :], k.x[:, :, :], ACT.Square).then_inc(*self.a.did("squares"))
        act.wait_ge(*self.t.at("sum"))
        act.activation(k.root[:, :], k.bank[1][:, 0:T], ACT.Sqrt, scale=1.0 / D, bias=k.c("eps")).then_inc(*self.a.did("root"))

    def tensor(self, pe):
        k = self.k
        pe.wait_ge(*self.a.at("squares"))
        for c in range(KC):
            mm = pe.matmul(k.bank[1][:, 0:T], k.c("ones"), k.sq[:, c, :], start=c == 0, stop=c == KC - 1)
        mm.then_inc(*self.t.did("sum"))

    def vector(self, dve):
        k = self.k
        do = self.v.serial(dve)
        dve.wait_ge(*self.a.at("root"))
        do(dve.reciprocal(k.root[:, :], k.root[:, :]))
        do(dve.tensor_tensor(k.h[:, :, :], k.x[:, :, :], bc(k.root[:, :], 1, KC), ALU.mult))
        if self.which == "final":
            do(dve.tensor_tensor(k.h[:, :, :], k.h[:, :, :], k.vec(self.l, "norm_final").unsqueeze(2).broadcast_to([P, KC, T]), ALU.mult))
            return
        part, scale = (0, k.scale_a) if self.which == "attn" else (3, k.scale_f)
        shift = k.ada[:, 8 * part:8 * part + 8, :]
        for c in range(KC):
            dve.tensor_scalar(k.h[:, c, 0:SEQ], k.h[:, c, 0:SEQ], scale[:, c, 0:1], shift[:, c, 0:1], ALU.mult, ALU.add)
        do(dve.tensor_tensor(k.h[:, :, SEQ:T], k.h[:, :, SEQ:T], scale[:, :, 1:NSEQ], ALU.mult))
        do(dve.tensor_tensor(k.h[:, :, SEQ:T], k.h[:, :, SEQ:T], shift[:, :, 1:NSEQ], ALU.add))


class Project(Stage):

    def __init__(self, k, l):
        super().__init__(k, "project", l)
        self.slots = []
        for c0, n in [(0, 512)] + [(544 + 512 * i, min(512, 3872 - 544 - 512 * i)) for i in range(7)]:
            place = k.next_place()
            dst = k.slot(place)[:, 0:KC * n].rearrange("p (k n) -> p k n", k=KC)
            self.slots.append((k.ring.add(place, dst, k.w_in[l].rearrange("(k p) n -> p k n", p=P)[:, :, c0:c0 + n]), n // P))

    def tiles(self):
        out, at = [], 0
        for s, (slot, n) in enumerate(self.slots):
            for t in range(n):
                name = ("qkv", at) if at < 4 else ("rw", at - 4) if at < 18 else ("z", at - 18) if at < 22 else ("xbc", at - 22)
                out.append((slot, t, name, t == n - 1))
                at += 1
        return [(None, "w_kr", ("kr", 0), False), (None, "w_dt", ("dt", 0), False)] + out

    def tensor(self, pe):
        k = self.k
        pe.wait_ge(k.small_loaded, 16 * (self.l + 1))
        for i, (slot, t, name, last) in enumerate(self.tiles()):
            if i >= 4:
                by = self.a if i % 2 else self.v
                pe.wait_ge(*by.at("tile", i - 4))
            m = 8 if name[0] == "dt" else P
            if slot is None:
                w = k.small[:, SMALL[t][0]:SMALL[t][1]].rearrange("p (k n) -> p k n", k=KC)
                cols = slice(0, m)
            else:
                k.ring.arrived(pe, slot)
                w, cols = k.ring.loads[slot][1], slice(P * t, P * t + P)
            for kk in range(KC):
                mm = pe.matmul(k.bank[i % 4][0:m, 0:T], w[:, kk, cols], k.h[:, kk, :], start=kk == 0, stop=kk == KC - 1)
            mm.then_inc(*self.t.did("tile", i))
            if last:
                k.ring.release(slot, self.t)

    def evict(self, eng, steps, odd):
        k = self.k
        tiles = self.tiles()
        for i, (_, _, (name, c), _) in enumerate(tiles):
            if i % 2 != odd:
                continue
            src = k.bank[i % 4]
            eng.wait_ge(*self.t.at("tile", i))
            copy = eng.copy if odd else eng.tensor_copy
            if name == "qkv":
                ins = copy(k.qkv[:, c, :], src[:, 0:T])
            elif name == "kr":
                ins = copy(k.kr[:, :], src[:, 0:T])
            elif name == "rw":
                ins = copy(k.rw[:, c, 1:1 + T], src[:, 0:T])
            elif name == "z":
                ins = copy(k.z[:, c, :], src[:, 0:T])
            elif name == "dt":
                ins = copy(k.dt_raw[0:8, :], src[0:8, 0:T])
            else:
                copy(k.xbc[:, c, 3:3 + SEQ], src[:, 0:SEQ])
                ins = copy(k.xbc_s[:, c, :, 3], src[:, SEQ:T])
            ins.then_inc(*steps.did("tile", i))

    def vector(self, dve):
        k = self.k
        dve.memset(k.rw[:, :, 0:1], 0.0)
        dve.memset(k.xbc[:, :, 0:3], 0.0)
        self.evict(dve, self.v, 0)

    def scalar(self, act):
        self.evict(act, self.a, 1)


class Rwkv(Stage):

    def __init__(self, k, l):
        super().__init__(k, "rwkv", l)
        ar = Arena(k.sb, k.work_at, k.work_size)
        self.w = ar.take(NRWKV)
        self.ep, self.en = ar.take(4, 129), ar.take(4, 129)
        self.ws = ar.take(4, NB)
        self.kk, self.kh, self.bb = ar.take(4, T), ar.take(4, T), ar.take(4, T)
        self.tilde = ar.take(2048)
        self.at, self.rt, self.bt, self.kt = (self.tilde[:, 512 * i:512 * i + 512].rearrange("p (c t) -> p c t", c=4) for i in range(4))
        self.tok = ar.take(3, 512)
        self.vt, self.btt, self.ktt = (self.tok[:, i, :] for i in range(3))
        self.AT, self.BT = ar.take(8, P), ar.take(8, P)
        self.inv = ar.take(4096)
        self.X, self.Y, self.Pm, self.M = (self.inv[:, 1024 * i:1024 * i + 1024].rearrange("p (h t) -> p h t", h=8) for i in range(4))
        self.RB, self.RK, self.W, self.U = self.X, self.Pm, self.M[:, 0:4, :], self.M[:, 4:8, :]
        self.a_steps = self.a
        self.S, self.S0 = ar.take(4, 64), ar.take(4, 64)
        self.sg = ar.take(T)
        self.av = self.inv[:, 0:4 * T].rearrange("p (c t) -> p c t", c=4)
        self.d = self.inv[:, 0:14 * T].rearrange("p (c t) -> p c t", c=14)
        self.tw = self.tok[:, 0, 0:T]
        self.sw = k.branches[:, 8:12, :].rearrange("p c t -> p (c t)")
        self.sws = k.branches[:, 0:4, :].rearrange("p c t -> p (c t)")[:, 0:512]
        self.st, self.t1 = (self.inv[:, 2048 * i:2048 * i + 2048].rearrange("p (c b i) -> p c b i", c=4, b=NB) for i in range(2))
        self.sq = self.tilde[:, 0:4 * T].rearrange("p (c t) -> p c t", c=4)
        self.g_sb = self.tilde[:, 0:4 * T].rearrange("p (c t) -> p c t", c=4)
        self.y = k.branches[:, 4:8, :]

    def pool(self, g):
        k, l = self.k, self.l
        g.dma_start(self.w[:, :], k.rwkv_w[l]).then_inc(k.rwkv_w_loaded, 16)
        g.wait_ge(*self.v.at("lastrow"))
        g.dma_start(k.out["shift"][l], k.lastrow[:, :, :]).then_inc(k.stored, 16)
        g.wait_ge(*self.v.at("state", NT - 1))
        g.dma_start(k.out["p_wkv"][l], self.S[:, :, :]).then_inc(k.stored, 16)
        g.wait_ge(*self.a_steps.at("y", NT - 1))
        g.dma_start(self.st, k.wkv_in[l]).then_inc(k.wkv_loaded, 16)
        g.wait_ge(*self.v.at("s_state"))
        g.dma_start(k.out["s_wkv"][l], self.st).then_inc(k.stored, 16)
        k.stores += 3
        g.wait_ge(k.stored, 16 * k.stores)
        g.memset(k.pool_mark[0:1, 0:1], 0.0).then_inc(*self.g.did("stored"))

    def tensor(self, pe):
        k, t = self.k, self.t
        w, c_ = self.w, k.c
        pe.wait_ge(k.rwkv_w_loaded, 16 * (self.l + 1))
        w2, a2, g2 = (w[:, RWKV_W[n][0]:RWKV_W[n][1]] for n in ("w2", "a2", "g2"))
        pe.wait_ge(*self.a.at("tanh"))
        for i in range(3):
            m = P if i < 2 else NB
            mm = pe.matmul(k.bank[i][0:m, :], self.tw[0:65, P * i:P * i + m], w2[0:65, :], start=True, stop=True)
        mm.then_inc(*t.did("w"))
        for c in range(4):
            if c:
                pe.wait_ge(*self.a.at("a", c - 1))
            mm = pe.matmul(k.bank[3][:, 0:T], a2[64:128, P * c:P * c + P], k.rw[64:128, 12, 1:1 + T], start=True, stop=True)
            mm.then_inc(*t.did("a", c))
        pe.wait_ge(*self.a.at("kk_sq"))
        for c in range(4):
            mm = pe.matmul(k.bank[4 + c][:, 0:T], c_("block_ones"), self.d[:, 4 + c, :], start=True, stop=True)
        mm.then_inc(*t.did("kk_norm"))
        pe.wait_ge(*self.a.at("sw"))
        for c in range(4):
            mm = pe.matmul(k.bank[0][:, NB * c:NB * c + NB], self.sws[0:NB, P * c:P * c + P],
                           c_("decay_id")[0:NB, :], start=True, stop=True)
        mm.then_inc(*t.did("ws"))
        for ti in range(NT):
            cols = slice(1 + P * ti, 1 + P * ti + P)
            if ti == 0:
                pe.wait_ge(*self.a.at("ws"))
            else:
                pe.wait_ge(*self.v.at("state", ti - 1))
                pe.wait_ge(*self.a.at("y", ti - 1))
            for c in range(4):
                mm = pe.matmul(k.bank[c // 2][:, 129 * (c % 2):129 * (c % 2) + 129],
                               self.sw[:, 512 * ti + P * c:512 * ti + P * c + P], c_("decay_tri"), start=True, stop=True)
            mm.then_inc(*t.did("logs", ti))
            for c in range(4):
                mm = pe.transpose(k.bank[2][:, P * c:P * c + P], k.rw[:, 8 + c, cols], c_("ident"))
            mm.then_inc(*t.did("v_tok", ti))
            pe.wait_ge(*self.v.at("tilde", ti))
            for c in range(4):
                pe.transpose(k.bank[3][:, P * c:P * c + P], self.bt[:, c, :], c_("ident"))
            for c in range(4):
                mm = pe.transpose(k.bank[4][:, P * c:P * c + P], self.kt[:, c, :], c_("ident"))
            mm.then_inc(*t.did("bk_tok", ti))
            for q, src in enumerate((self.bt, self.kt)):
                for g in range(2):
                    b = (5, 6, 7, 0)[2 * q + g]
                    if b == 0:
                        pe.wait_ge(*self.a.at("logs", ti))
                    r = slice(64 * g, 64 * g + 64)
                    for c in range(4):
                        mm = pe.matmul(k.bank[b][:, P * c:P * c + P], src[r, c, :], self.at[r, c, :], start=True, stop=True)
                    mm.then_inc(*t.did("AB", ti, q, g))
            for n in range(7):
                for g in range(2):
                    hs = range(4 * g, 4 * g + 4)
                    pe.wait_ge(*self.v.at("M", ti, n, g))
                    if n:
                        pe.wait_ge(*self.v.at("XY", ti, n - 1, g))
                    if n == 0 and g == 0:
                        pe.wait_ge(*self.a.at("bk_tok", ti))
                    for h in hs:
                        mm = pe.matmul(k.bank[1 + g][:, P * (h % 4):P * (h % 4) + P], self.M[:, h, :],
                                       c_("ident") if n == 0 else self.X[:, h, :], start=True, stop=True)
                    mm.then_inc(*t.did("MX", ti, n, g))
                if n == 0:
                    continue
                for g in range(2):
                    hs = range(4 * g, 4 * g + 4)
                    pe.wait_ge(*self.a.at("MX", ti, n, g))
                    if n < 6:
                        for h in hs:
                            pe.matmul(k.bank[3 + g][:, P * (h % 4):P * (h % 4) + P], self.Y[:, h, :], self.Pm[:, h, :],
                                      start=True, stop=True)
                    for h in hs:
                        mm = pe.matmul(k.bank[5 + g][:, P * (h % 4):P * (h % 4) + P], self.Pm[:, h, :], self.Y[:, h, :],
                                       start=True, stop=True)
                    mm.then_inc(*t.did("XMX", ti, n, g))
            pe.wait_ge(*self.v.at("XY", ti, 6, 0))
            pe.wait_ge(*self.v.at("XY", ti, 6, 1))
            for q, src in enumerate((self.bt, self.kt)):
                for g in range(2):
                    b = 3 + 2 * q + g
                    r = slice(64 * g, 64 * g + 64)
                    for c in range(4):
                        mm = pe.matmul(k.bank[b][:, P * c:P * c + P], src[r, c, :], self.rt[r, c, :], start=True, stop=True)
                    mm.then_inc(*t.did("R", ti, q, g))
            pe.wait_ge(*self.a.at("v_tok", ti))
            for n in range(8):
                g, c = n // 4, n % 4
                r, h = slice(64 * g, 64 * g + 64), 2 * c + g
                o = k.bank[(7, 2)[g]][:, 64 * c:64 * c + 64]
                if ti:
                    pe.matmul(o, self.at[r, c, :], self.S0[r, c, :], start=True, stop=False)
                mm = pe.matmul(o, self.BT[:, n, :], self.vt[:, 64 * h:64 * h + 64], start=not ti, stop=True)
            mm.then_inc(*t.did("W", ti))
            pe.wait_ge(*self.a.at("W", ti))
            W, U = self.W.rearrange("p a b -> p (a b)"), self.U.rearrange("p a b -> p (a b)")
            for n in range(8):
                mm = pe.matmul(k.bank[0][:, 64 * n:64 * n + 64], self.Y[:, n, :], W[:, 64 * n:64 * n + 64], start=True, stop=True)
            mm.then_inc(*t.did("U", ti))
            pe.wait_ge(*self.a.at("U", ti))
            pe.wait_ge(*self.v.at("R", ti))
            for n in range(8):
                g, c = n // 4, n % 4
                r, h = slice(64 * g, 64 * g + 64), 2 * c + g
                o = k.bank[1][r, P * c:P * c + P]
                if ti:
                    pe.matmul(o, self.S0[r, c, :], self.rt[r, c, :], start=True, stop=False)
                pe.matmul(o, U[:, 64 * n:64 * n + 64], self.RB[:, n, :], start=not ti, stop=False)
                mm = pe.matmul(o, self.vt[:, 64 * h:64 * h + 64], self.RK[:, n, :], start=False, stop=True)
            mm.then_inc(*t.did("y", ti))
            for n in range(8):
                g, c = n // 4, n % 4
                r, h = slice(64 * g, 64 * g + 64), 2 * c + g
                o = k.bank[2][r, 64 * c:64 * c + 64]
                pe.matmul(o, self.btt[:, 64 * h:64 * h + 64], U[:, 64 * n:64 * n + 64], start=True, stop=False)
                mm = pe.matmul(o, self.ktt[:, 64 * h:64 * h + 64], self.vt[:, 64 * h:64 * h + 64], start=False, stop=True)
            mm.then_inc(*t.did("state", ti))
        for n, key in enumerate(("s_kk", "s_v", "s_r")):
            pe.wait_ge(*self.v.at(key))
            for c in range(4):
                mm = pe.matmul(k.bank[4 * (n % 2) + c][:, :], c_("block_ones"), self.t1[:, c, :, :].rearrange("p b i -> p (b i)"),
                               start=True, stop=True)
            mm.then_inc(*t.did(key))
        pe.wait_ge(*self.v.at("y"))
        for c in range(4):
            mm = pe.matmul(k.bank[4 + c][:, 0:T], c_("block_ones"), self.y[:, c, :], start=True, stop=True)
        mm.then_inc(*t.did("mean"))
        pe.wait_ge(*self.a.at("y_sq"))
        for c in range(4):
            mm = pe.matmul(k.bank[c][:, 0:T], c_("block_ones"), self.sq[:, c, :], start=True, stop=True)
        mm.then_inc(*t.did("var"))
        pe.wait_ge(*self.v.at("bonus_in"))
        for c in range(4):
            mm = pe.matmul(k.bank[4 + c][:, 0:T], c_("block_ones"), self.bb[:, c, :], start=True, stop=True)
        mm.then_inc(*t.did("bonus"))
        pe.wait_ge(*self.v.at("ln"))
        for c in range(4):
            mm = pe.matmul(k.bank[c][:, 0:T], g2[:, P * c:P * c + P], self.sg[:, :], start=True, stop=True)
        mm.then_inc(*t.did("g"))

    def scalar(self, act):
        k, a, t, v = self.k, self.a, self.t, self.v
        act.wait_ge(*v.at("shifted"))
        act.activation(self.tw[0:64, :], k.rw[0:64, 12, 1:1 + T], ACT.Tanh).then_inc(*a.did("tanh_only"))
        act.wait_ge(*v.at("ones_row"))
        act.activation(self.sg[:, :], k.rw[:, 13, 1:1 + T], ACT.Sigmoid).then_inc(*a.did("tanh"))
        act.wait_ge(*t.at("w"))
        act.activation(self.sw[:, 0:512], k.bank[0][:, :], ACT.Sigmoid)
        act.activation(self.sw[:, 512:1024], k.bank[1][:, :], ACT.Sigmoid)
        act.activation(self.sws[0:NB, :], k.bank[2][0:NB, :], ACT.Sigmoid).then_inc(*a.did("sw"))
        for c in range(4):
            act.wait_ge(*t.at("a", c))
            act.activation(self.av[:, c, :], k.bank[3][:, 0:T], ACT.Sigmoid, bias=k.vec(self.l, "a0")[:, c:c + 1]).then_inc(*a.did("a", c))
        act.wait_ge(*v.at("kk_raw"))
        act.activation(self.d[:, 4:8, :], self.kk[:, :, :], ACT.Square).then_inc(*a.did("kk_sq"))
        act.wait_ge(*v.at("kk_max"))
        act.activation(self.d[:, 4:8, :], self.d[:, 4:8, :], ACT.Sqrt).then_inc(*a.did("kk_root"))
        act.wait_ge(*t.at("ws"))
        act.activation(self.ws[:, :, :], k.bank[0][:, 0:4 * NB].rearrange("p (c b) -> p c b", c=4), ACT.Exp).then_inc(*a.did("ws"))
        for ti in range(NT):
            act.wait_ge(*t.at("logs", ti))
            for q in range(2):
                src = k.bank[q][:, 0:258].rearrange("p (c t) -> p c t", c=2)
                act.activation(self.ep[:, 2 * q:2 * q + 2, :], src, ACT.Exp)
                ins = act.activation(self.en[:, 2 * q:2 * q + 2, :], src, ACT.Exp, scale=-1.0)
            ins.then_inc(*a.did("logs", ti))
            act.wait_ge(*t.at("v_tok", ti))
            act.copy(self.vt, k.bank[2][:, :]).then_inc(*a.did("v_tok", ti))
            act.wait_ge(*t.at("bk_tok", ti))
            act.copy(self.btt, k.bank[3][:, :])
            act.copy(self.ktt, k.bank[4][:, :]).then_inc(*a.did("bk_tok", ti))
            for n in range(1, 7):
                for g in range(2):
                    act.wait_ge(*t.at("MX", ti, n, g))
                    act.copy(self.Pm[:, 4 * g:4 * g + 4, :].rearrange("p h t -> p (h t)"), k.bank[1 + g][:, :]).then_inc(*a.did("MX", ti, n, g))
            act.wait_ge(*t.at("W", ti))
            W = self.W.rearrange("p a b -> p (a b)")
            act.copy(W[:, 0:256], k.bank[7][:, 0:256])
            act.copy(W[:, 256:512], k.bank[2][:, 0:256]).then_inc(*a.did("W", ti))
            act.wait_ge(*t.at("U", ti))
            act.mul(self.U.rearrange("p a b -> p (a b)"), k.bank[0][:, :], -1.0).then_inc(*a.did("U", ti))
            act.wait_ge(*t.at("y", ti))
            act.copy(self.y[:, :, P * ti:P * ti + P], k.bank[1][:, :].rearrange("p (c t) -> p c t", c=4)).then_inc(*a.did("y", ti))
        act.wait_ge(*v.at("centred"))
        act.activation(self.sq[:, :, :], self.y, ACT.Square).then_inc(*a.did("y_sq"))
        act.wait_ge(*t.at("var"))
        for c in range(4):
            ins = act.activation(self.sq[:, c, :], k.bank[c][:, 0:T], ACT.Sqrt, scale=1.0 / 64, bias=k.c("ln_eps"))
        ins.then_inc(*a.did("y_root"))

    def vector(self, dve):
        k, a, t, v, l = self.k, self.a, self.t, self.v, self.l
        do = v.serial(dve)
        rw = k.rw
        dve.tensor_copy(k.lastrow[:, :, 0:1], rw[:, :, SEQ:SEQ + 1])
        dve.tensor_copy(k.lastrow[:, :, 1:NSEQ], rw[:, :, 1 + SEQ:1 + T])
        dve.tensor_tensor(self.d[:, :, 0:SEQ], rw[:, :, 0:SEQ], rw[:, :, 1:1 + SEQ], ALU.subtract)
        dve.wait_ge(k.shift_loaded, 16 * (l + 1))
        do(dve.tensor_tensor(self.d[:, :, SEQ:T], k.shift_in[:, :, :], rw[:, :, 1 + SEQ:1 + T], ALU.subtract), "lastrow")
        for c in range(RW_CH):
            ins = dve.scalar_tensor_tensor(out=rw[:, c, 1:1 + T], in0=self.d[:, c, :], scalar=k.vec(l, "mu")[:, c:c + 1],
                                           in1=rw[:, c, 1:1 + T], op0=ALU.mult, op1=ALU.add)
        do(ins, "shifted")
        do(dve.memset(self.tw[64:65, :], 1.0), "ones_row")
        for c in range(4):
            ins = dve.tensor_scalar(self.kk[:, c, :], rw[:, 4 + c, 1:1 + T], k.vec(l, "k_k")[:, c:c + 1], None, ALU.mult)
        do(ins, "kk_raw")
        do(dve.tensor_scalar(k.one_minus_ka[:, :], k.vec(l, "k_a"), -1.0, 1.0, ALU.mult, ALU.add))
        dve.wait_ge(*t.at("kk_norm"))
        for c in range(4):
            ins = dve.tensor_scalar(self.d[:, 4 + c, :], k.bank[4 + c][:, 0:T], 1e-24, None, ALU.max)
        do(ins, "kk_max")
        dve.wait_ge(*a.at("a", 3))
        for c in range(4):
            ins = dve.tensor_scalar(self.kh[:, c, :], self.av[:, c, :], k.vec(l, "k_a")[:, c:c + 1], k.one_minus_ka[:, c:c + 1], ALU.mult, ALU.add)
        do(ins)
        do(dve.tensor_tensor(self.kh[:, :, :], self.kh[:, :, :], rw[:, 4:8, 1:1 + T], ALU.mult))
        dve.wait_ge(*a.at("kk_root"))
        do(dve.reciprocal(self.d[:, 4:8, :], self.d[:, 4:8, :]))
        do(dve.tensor_tensor(self.kk[:, :, :], self.kk[:, :, :], self.d[:, 4:8, :], ALU.mult))
        do(dve.tensor_tensor(self.bb[:, :, :], self.kk[:, :, :], self.av[:, :, :], ALU.mult))
        for ti in range(NT):
            s = slice(P * ti, P * ti + P)
            dve.wait_ge(*a.at("logs", ti))
            if ti:
                do(dve.tensor_tensor(self.S0[:, :, :], self.S[:, :, :], self.en[:, :, 0:1].broadcast_to([P, 4, 64]), ALU.mult))
            dve.tensor_tensor(self.at[:, :, :], self.kk[:, :, s], self.ep[:, :, 0:P], ALU.mult)
            dve.tensor_tensor(self.rt[:, :, :], rw[:, 0:4, 1 + P * ti:1 + P * ti + P], self.ep[:, :, 1:129], ALU.mult)
            dve.tensor_tensor(self.bt[:, :, :], self.bb[:, :, s], self.en[:, :, 1:129], ALU.mult)
            do(dve.tensor_tensor(self.kt[:, :, :], self.kh[:, :, s], self.en[:, :, 1:129], ALU.mult), "tilde", ti)
            for q, (dst, b) in enumerate(((self.AT, (5, 6)), (self.BT, (7, 0)))):
                for g in range(2):
                    dve.wait_ge(*t.at("AB", ti, q, g))
                    do(dve.tensor_tensor(dst[:, 4 * g:4 * g + 4, :], k.bank[b[g]][:, :].rearrange("p (h t) -> p h t", h=4),
                                         bc(k.c("strict"), 1, 4), ALU.mult))
            for n in range(7):
                mask = k.c("levels")[:, P * n:P * n + P]
                for g in range(2):
                    hs = slice(4 * g, 4 * g + 4)
                    if n:
                        dve.wait_ge(*t.at("MX", ti, n - 1, g))
                    do(dve.tensor_tensor(self.M[:, hs, :], self.AT[:, hs, :], bc(mask, 1, 4), ALU.mult), "M", ti, n, g)
                for g in range(2):
                    hs = slice(4 * g, 4 * g + 4)
                    if n == 0:
                        do(dve.tensor_tensor(self.Y[:, hs, :], bc(k.c("ident"), 1, 4), self.M[:, hs, :], ALU.subtract))
                        dve.wait_ge(*t.at("MX", ti, 0, g))
                        do(dve.tensor_tensor(self.X[:, hs, :], bc(k.c("ident"), 1, 4),
                                             k.bank[1 + g][:, :].rearrange("p (h t) -> p h t", h=4), ALU.subtract), "XY", ti, 0, g)
                        continue
                    dve.wait_ge(*t.at("XMX", ti, n, g))
                    if n < 6:
                        dve.tensor_tensor(self.X[:, hs, :], self.X[:, hs, :], k.bank[3 + g][:, :].rearrange("p (h t) -> p h t", h=4), ALU.subtract)
                    do(dve.tensor_tensor(self.Y[:, hs, :], self.Y[:, hs, :], k.bank[5 + g][:, :].rearrange("p (h t) -> p h t", h=4),
                                         ALU.subtract), "XY", ti, n, g)
            for q, dst in enumerate((self.RB, self.RK)):
                for g in range(2):
                    dve.wait_ge(*t.at("R", ti, q, g))
                    ins = dve.tensor_tensor(dst[:, 4 * g:4 * g + 4, :], k.bank[3 + 2 * q + g][:, :].rearrange("p (h t) -> p h t", h=4),
                                            bc(k.c("upto"), 1, 4), ALU.mult)
            do(ins, "R", ti)
            dve.wait_ge(*t.at("state", ti))
            new = k.bank[2][:, 0:256].rearrange("p (c i) -> p c i", c=4)
            if ti:
                do(dve.tensor_tensor(self.S0[:, :, :], self.S0[:, :, :], new, ALU.add))
                new = self.S0[:, :, :]
            do(dve.tensor_tensor(self.S[:, :, :], new, self.ep[:, :, 128:129].broadcast_to([P, 4, 64]), ALU.mult), "state", ti)
        sam = slice(SEQ, T)

        def along(x):
            return x.unsqueeze(3).broadcast_to([P, 4, NB, 64])
        fold = k.c("fold")
        rs = rw[:, 0:4, 1 + SEQ:1 + T]
        vs = rw[:, 8:12, 1 + SEQ:1 + T]
        dve.wait_ge(k.wkv_loaded, 16 * (l + 1))
        for c in range(4):
            ins = dve.tensor_tensor(self.t1[:, c], self.st[:, c], self.kk[:, c, sam].unsqueeze(2).broadcast_to([P, NB, 64]), ALU.mult)
        do(ins, "s_kk")
        for c in range(4):
            ins = dve.tensor_tensor(self.st[:, c], self.st[:, c], self.ws[:, c].unsqueeze(2).broadcast_to([P, NB, 64]), ALU.mult)
        do(ins)
        dve.wait_ge(*t.at("s_kk"))
        for c in range(4):
            ins = dve.tensor_tensor(self.t1[:, c], k.bank[c][:, :].rearrange("p (b i) -> p b i", b=NB),
                                    self.bb[:, c, sam].unsqueeze(2).broadcast_to([P, NB, 64]), ALU.mult)
        do(ins)
        do(dve.tensor_tensor(self.st, self.st, self.t1, ALU.subtract))
        for c in range(4):
            ins = dve.tensor_tensor(self.t1[:, c], bc(fold, 1, NB), vs[:, c, :].unsqueeze(2).broadcast_to([P, NB, 64]), ALU.mult)
        do(ins, "s_v")
        dve.wait_ge(*t.at("s_v"))
        for c in range(4):
            ins = dve.tensor_tensor(self.t1[:, c], k.bank[4 + c][:, :].rearrange("p (b i) -> p b i", b=NB),
                                    self.kh[:, c, sam].unsqueeze(2).broadcast_to([P, NB, 64]), ALU.mult)
        do(ins)
        do(dve.tensor_tensor(self.st, self.st, self.t1, ALU.add), "s_state")
        for c in range(4):
            ins = dve.tensor_tensor(self.t1[:, c], self.st[:, c], rs[:, c, :].unsqueeze(2).broadcast_to([P, NB, 64]), ALU.mult)
        do(ins, "s_r")
        dve.wait_ge(*t.at("s_r"))
        for c in range(4):
            ins = dve.tensor_tensor(self.t1[:, c], k.bank[c][:, :].rearrange("p (b i) -> p b i", b=NB), bc(fold, 1, NB), ALU.mult)
        do(ins)
        dve.wait_ge(*a.at("y", NT - 1))
        for c in range(4):
            ins = dve.tensor_reduce(self.y[:, c, sam], self.t1[:, c], X, ALU.add)
        do(ins, "y")
        dve.wait_ge(*t.at("mean"))
        for c in range(4):
            ins = dve.scalar_tensor_tensor(out=self.y[:, c, :], in0=k.bank[4 + c][:, 0:T], scalar=-1.0 / 64, in1=self.y[:, c, :],
                                           op0=ALU.mult, op1=ALU.add)
        do(ins, "centred")
        for c in range(4):
            ins = dve.scalar_tensor_tensor(out=self.bb[:, c, :], in0=rw[:, c, 1:1 + T], scalar=k.vec(l, "r_k")[:, c:c + 1],
                                           in1=self.kh[:, c, :], op0=ALU.mult, op1=ALU.mult)
        do(ins, "bonus_in")
        dve.wait_ge(*a.at("y_root"))
        do(dve.reciprocal(self.sq[:, :, :], self.sq[:, :, :]))
        do(dve.tensor_tensor(self.y, self.y, self.sq[:, :, :], ALU.mult))
        for c in range(4):
            ins = dve.tensor_scalar(self.y[:, c, :], self.y[:, c, :], k.vec(l, "ln_w")[:, c:c + 1], k.vec(l, "ln_b")[:, c:c + 1], ALU.mult, ALU.add)
        do(ins, "ln")
        dve.wait_ge(*t.at("bonus"))
        for c in range(4):
            ins = dve.tensor_tensor(self.bb[:, c, :], k.bank[4 + c][:, 0:T], rw[:, 8 + c, 1:1 + T], ALU.mult)
        do(ins)
        do(dve.tensor_tensor(self.y, self.y, self.bb[:, :, :], ALU.add))
        dve.wait_ge(*t.at("g"))
        for c in range(4):
            ins = dve.tensor_tensor(self.y[:, c, :], self.y[:, c, :], k.bank[c][:, 0:T], ALU.mult)
        do(ins)


class Ssm(Stage):

    def __init__(self, k, l):
        super().__init__(k, "ssm", l)
        ar = Arena(k.sb, k.work_at, k.work_size)
        self.cv = ar.take(8, T)
        self.rows = ar.take(9, T)
        self.tokens = ar.take(NT, 6, 8)
        self.dtx, self.dax = ar.take(4, NB), ar.take(4, NB)
        self.hs = ar.take(512)
        big = ar.take(8192)
        self.st, self.t1 = (big[:, 4096 * i:4096 * i + 4096].rearrange("p (c b n) -> p c b n", c=4, b=NB) for i in range(2))
        small = Arena(k.sb, ar.next - 8192, 8192)
        self.xt, self.bt = small.take(512), small.take(256)
        self.xd, self.xdd = small.take(512), small.take(512)
        self.gt = small.take(2, P)
        self.seg = small.take(8, P)
        self.ecs = small.take(8, P)
        self.csb = small.take(8, P)
        self.spread = self.st.rearrange("p c b n -> p (c b n)")
        self.y = k.branches[:, 8:12, :]

    def pool(self, g):
        k, l = self.k, self.l
        g.wait_ge(*self.v.at("conv"))
        g.dma_start(k.out["p_conv"][l], k.xbc[:, :, SEQ:SEQ + 3]).then_inc(k.stored, 16)
        for c in range(8):
            g.dma_start(k.out["s_conv"][l, :, c], k.xbc_s[:, c, :, 1:4]).then_inc(k.stored, 16)
        g.wait_ge(*self.v.at("state", NT - 1))
        g.dma_start(k.out["p_ssm"][l], self.hs[:, :]).then_inc(k.stored, 16)
        g.wait_ge(*self.t.at("y", NT - 1))
        g.wait_ge(*self.v.at("y_off"))
        g.dma_start(self.st, k.ssm_in[l]).then_inc(k.ssm_loaded, 16)
        g.wait_ge(*self.v.at("s_state"))
        g.dma_start(k.out["s_ssm"][l], self.st).then_inc(k.stored, 16)
        k.stores += 11
        g.wait_ge(k.stored, 16 * k.stores)
        g.memset(k.pool_mark[0:1, 0:1], 0.0).then_inc(*self.g.did("stored"))

    def scalar(self, act):
        k, a, t, v = self.k, self.a, self.t, self.v
        act.wait_ge(*v.at("dt_abs"))
        act.activation(self.rows[0:8, 1, :], self.rows[0:8, 1, :], ACT.Exp, scale=-1.0)
        act.activation(k.small_a[0:8, 0:1], k.vec(self.l, "a_log")[0:8, :], ACT.Exp).then_inc(*a.did("dt_exp"))
        act.wait_ge(*v.at("conv"))
        act.activation(self.t1.rearrange("p c b n -> p (c b n)")[:, 0:8 * T].rearrange("p (c t) -> p c t", c=8), self.cv[:, :, :],
                       ACT.Sigmoid).then_inc(*a.did("silu"))
        act.wait_ge(*v.at("dt"))
        act.activation(self.rows[0:8, 5, SEQ:T], self.rows[0:8, 4, SEQ:T], ACT.Exp).then_inc(*a.did("da"))
        for ti in range(NT):
            act.wait_ge(*v.at("cs", ti))
            act.activation(self.tokens[:, ti, 4:6, :], self.tokens[:, ti, 4:6, :], ACT.Exp).then_inc(*a.did("ecs", ti))
            act.wait_ge(*t.at("csb", ti))
            for q in range(2):
                ins = act.activation(self.ecs[:, 4 * q:4 * q + 4, :], k.bank[2 + q][:, :].rearrange("p (h t) -> p h t", h=4), ACT.Exp)
            ins.then_inc(*a.did("ecsb", ti))
            act.wait_ge(*v.at("seg", ti))
            act.activation(self.seg[:, :, :], self.seg[:, :, :], ACT.Exp).then_inc(*a.did("seg", ti))
        act.wait_ge(*v.at("skip"))
        act.activation(k.z[:, :, :], k.z[:, :, :], ACT.Silu).then_inc(*a.did("z"))
        act.wait_ge(*v.at("gated"))
        act.activation(self.cv[:, 0:4, :], self.y, ACT.Square).then_inc(*a.did("y_sq"))
        act.wait_ge(*t.at("ms"))
        for g in range(2):
            ins = act.activation(self.cv[:, 4 + g, :], k.bank[g][:, 0:T], ACT.Sqrt, scale=1.0 / 256, bias=k.c("eps"))
        ins.then_inc(*a.did("root"))

    def tensor(self, pe):
        k, t, v, a = self.k, self.t, self.v, self.a
        ident, ones, upto = k.c("ident"), k.c("ones"), k.c("upto")
        pe.wait_ge(*v.at("dt"))
        pe.wait_ge(*a.at("da"))
        for q, row in enumerate((3, 5)):
            for c in range(4):
                mm = pe.matmul(k.bank[0][:, 32 * q + NB * c:32 * q + NB * c + NB], k.c("spread")[0:8, P * c:P * c + P],
                               self.rows[0:8, row, SEQ:T], start=True, stop=True)
        mm.then_inc(*t.did("s_dt"))
        for ti in range(NT):
            s = slice(P * ti, P * ti + P)
            if ti:
                pe.wait_ge(*v.at("state", ti - 1))
                pe.wait_ge(*v.at("y", ti - 1))
            for q, row in enumerate((3, 4)):
                mm = pe.transpose(k.bank[1][:, 8 * q:8 * q + 8], self.rows[0:8, row, s], ident[0:8, 0:8])
            mm.then_inc(*t.did("tok", ti))
            pe.wait_ge(*v.at("tok", ti))
            pe.matmul(k.bank[1][:, 32:40], upto, self.tokens[:, ti, 1, :], start=True, stop=True)
            mm = pe.matmul(k.bank[1][:, 40:48], ones, self.tokens[:, ti, 1, :], start=True, stop=True)
            mm.then_inc(*t.did("cs", ti))
            for h in range(8):
                mm = pe.matmul(k.bank[2 + h // 4][:, P * (h % 4):P * (h % 4) + P],
                               self.tokens[:, ti, 1, h:h + 1].broadcast_to([P, P]), upto, start=True, stop=True)
            mm.then_inc(*t.did("csb", ti))
            if ti == 0:
                pe.wait_ge(*v.at("silu"))
            for g in range(2):
                mm = pe.matmul(k.bank[4][:, P * g:P * g + P], self.cv[:, 4 + g, s], self.cv[:, 6 + g, s], start=True, stop=True)
            mm.then_inc(*t.did("gt", ti))
            for c in range(4):
                pe.transpose(k.bank[5][:, P * c:P * c + P], self.cv[:, c, s], ident)
            for c in range(2):
                mm = pe.transpose(k.bank[6][:, P * c:P * c + P], self.cv[:, 4 + c, s], ident)
            mm.then_inc(*t.did("xb_tok", ti))
            pe.wait_ge(*v.at("mt", ti))
            for h in range(8):
                o = k.bank[7][64 * (h % 2):64 * (h % 2) + 64, P * (h // 2):P * (h // 2) + P]
                mm = pe.matmul(o, self.xd[:, 64 * h:64 * h + 64], self.seg[:, h, :], start=True, stop=not ti)
                if ti:
                    mm = pe.matmul(o, self.hs[:, 64 * h:64 * h + 64], self.ecs[:, h, :], start=False, stop=True)
            mm.then_inc(*t.did("y", ti))
            for g in range(2):
                mm = pe.matmul(k.bank[0][:, 256 * g:256 * g + 256], self.bt[:, P * g:P * g + P], self.xdd[:, 256 * g:256 * g + 256],
                               start=True, stop=True)
            mm.then_inc(*t.did("state", ti))
        for q in range(2):
            pe.wait_ge(*v.at("s_diag", q))
            for g in range(2):
                for n in range(2):
                    mm = pe.matmul(k.bank[4 * q + 2 * g + n][:, :], ones,
                                   self.t1[:, g, 4 * n:4 * n + 4, :].rearrange("p b n -> p (b n)"), start=True, stop=True)
            mm.then_inc(*t.did("s_spread", q))
        pe.wait_ge(*a.at("y_sq"))
        for g in range(2):
            for n in range(2):
                mm = pe.matmul(k.bank[g][:, 0:T], ones, self.cv[:, 2 * g + n, :], start=n == 0, stop=n == 1)
        mm.then_inc(*t.did("ms"))

    def vector(self, dve):
        k, a, t, v, l = self.k, self.a, self.t, self.v, self.l
        do = v.serial(dve)
        r = self.rows[0:8]
        do(dve.tensor_scalar(r[:, 0, :], k.dt_raw[0:8, :], k.vec(l, "dt_bias")[0:8, :], None, ALU.add))
        do(dve.tensor_scalar(r[:, 1, :], r[:, 0, :], -1.0, None, ALU.mult))
        do(dve.tensor_tensor(r[:, 1, :], r[:, 0, :], r[:, 1, :], ALU.max), "dt_abs")
        do(dve.tensor_scalar(r[:, 0, :], r[:, 0, :], 0.0, None, ALU.max))
        dve.wait_ge(k.conv_loaded, 16 * (l + 1))
        dve.tensor_copy(k.xbc_s[:, :, :, 0:3].rearrange("p c b i -> p (c b) i"), k.conv_in[:, :, :, :].rearrange("p c b i -> p (c b) i"))
        cw = k.vec(l, "conv_w")
        for i in range(4):
            for c in range(8):
                wt = cw[:, 8 * i + c:8 * i + c + 1]
                if i == 0:
                    ins = dve.tensor_scalar(self.cv[:, c, 0:SEQ], k.xbc[:, c, 0:SEQ], wt, None, ALU.mult)
                else:
                    ins = dve.scalar_tensor_tensor(out=self.cv[:, c, 0:SEQ], in0=k.xbc[:, c, i:i + SEQ], scalar=wt,
                                                   in1=self.cv[:, c, 0:SEQ], op0=ALU.mult, op1=ALU.add)
            do(ins)
            for c in range(8):
                wt = cw[:, 8 * i + c:8 * i + c + 1]
                if i == 0:
                    ins = dve.tensor_scalar(self.cv[:, c, SEQ:T], k.xbc_s[:, c, :, 0], wt, None, ALU.mult)
                else:
                    ins = dve.scalar_tensor_tensor(out=self.cv[:, c, SEQ:T], in0=k.xbc_s[:, c, :, i], scalar=wt,
                                                   in1=self.cv[:, c, SEQ:T], op0=ALU.mult, op1=ALU.add)
            do(ins)
        do(dve.tensor_tensor(self.cv[:, :, :], self.cv[:, :, :], k.vec(l, "conv_b").unsqueeze(2).broadcast_to([P, 8, T]), ALU.add), "conv")
        dve.wait_ge(*a.at("dt_exp"))
        do(dve.tensor_scalar(r[:, 2, :], r[:, 1, :], 2.0, None, ALU.add))
        do(dve.reciprocal(r[:, 2, :], r[:, 2, :]))
        do(dve.tensor_tensor(r[:, 2, :], r[:, 2, :], r[:, 1, :], ALU.mult))
        do(dve.tensor_tensor(r[:, 3, :], r[:, 2, :], r[:, 2, :], ALU.mult))
        do(dve.tensor_scalar(r[:, 4, :], r[:, 3, :], 1.0 / 17, None, ALU.mult))
        for n in range(15, 1, -2):
            do(dve.scalar_tensor_tensor(out=r[:, 4, :], in0=r[:, 4, :], scalar=1.0 / n, in1=r[:, 3, :], op0=ALU.add, op1=ALU.mult))
        do(dve.scalar_tensor_tensor(out=r[:, 4, :], in0=r[:, 4, :], scalar=1.0, in1=r[:, 2, :], op0=ALU.add, op1=ALU.mult))
        do(dve.scalar_tensor_tensor(out=r[:, 3, :], in0=r[:, 4, :], scalar=2.0, in1=r[:, 0, :], op0=ALU.mult, op1=ALU.add))
        do(dve.tensor_scalar(r[:, 4, :], r[:, 3, :], k.small_a[0:8, 0:1], -1.0, ALU.mult, ALU.mult), "dt")
        dve.wait_ge(*a.at("silu"))
        do(dve.tensor_tensor(self.cv[:, :, :], self.cv[:, :, :], self.t1.rearrange("p c b n -> p (c b n)")[:, 0:8 * T].rearrange("p (c t) -> p c t", c=8), ALU.mult), "silu")
        dve.wait_ge(*t.at("s_dt"))
        dve.tensor_copy(self.dtx[:, :, :], k.bank[0][:, 0:32].rearrange("p (c b) -> p c b", c=4))
        do(dve.tensor_copy(self.dax[:, :, :], k.bank[0][:, 32:64].rearrange("p (c b) -> p c b", c=4)))
        for ti in range(NT):
            s = slice(P * ti, P * ti + P)
            tk = self.tokens[:, ti]
            dve.wait_ge(*t.at("tok", ti))
            do(dve.tensor_copy(tk[:, 0:2, :], k.bank[1][:, 0:16].rearrange("p (q h) -> p q h", q=2)), "tok", ti)
            dve.wait_ge(*t.at("cs", ti))
            do(dve.tensor_copy(tk[:, 2:4, :], k.bank[1][:, 32:48].rearrange("p (q h) -> p q h", q=2)))
            dve.tensor_copy(tk[:, 4, :], tk[:, 3, :])
            do(dve.tensor_tensor(tk[:, 5, :], tk[:, 3, :], tk[:, 2, :], ALU.subtract), "cs", ti)
            dve.wait_ge(*a.at("ecsb", ti))
            for q in range(2):
                ins = dve.tensor_tensor(self.seg[:, 4 * q:4 * q + 4, :], k.bank[2 + q][:, :].rearrange("p (h t) -> p h t", h=4),
                                        tk[:, 2, 4 * q:4 * q + 4].unsqueeze(2).broadcast_to([P, 4, P]), ALU.subtract)
            do(ins)
            do(dve.tensor_scalar(self.seg[:, :, :], self.seg[:, :, :], 0.0, None, ALU.min), "seg", ti)
            dve.wait_ge(*t.at("gt", ti))
            do(dve.tensor_tensor(self.gt[:, :, :], k.bank[4][:, 0:256].rearrange("p (g t) -> p g t", g=2), bc(k.c("upto"), 1, 2), ALU.mult))
            dve.wait_ge(*t.at("xb_tok", ti))
            dve.tensor_copy(self.bt[:, :], k.bank[6][:, 0:256])
            do(dve.tensor_tensor(self.xd[:, :].rearrange("p (h d) -> p h d", h=8), k.bank[5][:, :].rearrange("p (h d) -> p h d", h=8),
                                 tk[:, 0, :].unsqueeze(2).broadcast_to([P, 8, 64]), ALU.mult))
            dve.wait_ge(*a.at("ecs", ti))
            do(dve.tensor_tensor(self.xdd[:, :].rearrange("p (h d) -> p h d", h=8), self.xd[:, :].rearrange("p (h d) -> p h d", h=8),
                                 tk[:, 5, :].unsqueeze(2).broadcast_to([P, 8, 64]), ALU.mult))
            dve.wait_ge(*a.at("ecsb", ti))
            dve.wait_ge(*a.at("seg", ti))
            for g in range(2):
                hs = slice(4 * g, 4 * g + 4)
                dve.tensor_tensor(self.seg[:, hs, :], self.seg[:, hs, :], bc(self.gt[:, g, :], 1, 4), ALU.mult)
                ins = dve.tensor_tensor(self.ecs[:, hs, :], self.ecs[:, hs, :], bc(self.cv[:, 6 + g, s], 1, 4), ALU.mult)
            do(ins, "mt", ti)
            dve.wait_ge(*t.at("y", ti))
            do(dve.tensor_copy(self.y[:, :, s], k.bank[7][:, :].rearrange("p (c t) -> p c t", c=4)), "y", ti)
            dve.wait_ge(*t.at("state", ti))
            if ti:
                do(dve.tensor_tensor(self.hs[:, :].rearrange("p (h d) -> p h d", h=8), self.hs[:, :].rearrange("p (h d) -> p h d", h=8),
                                     tk[:, 4, :].unsqueeze(2).broadcast_to([P, 8, 64]), ALU.mult))
                do(dve.tensor_tensor(self.hs[:, :], self.hs[:, :], k.bank[0][:, :], ALU.add), "state", ti)
            else:
                do(dve.tensor_copy(self.hs[:, :], k.bank[0][:, :]), "state", ti)
        sam = slice(SEQ, T)
        do(dve.tensor_tensor(self.dtx[:, :, :], self.dtx[:, :, :], self.cv[:, 0:4, sam], ALU.mult), "y_off")
        for q, c0 in enumerate((4, 6)):
            for g in range(2):
                ins = dve.tensor_tensor(self.t1[:, g], bc(k.c("ident"), 1, NB), self.cv[:, c0 + g, sam].unsqueeze(2).broadcast_to([P, NB, P]), ALU.mult)
            do(ins, "s_diag", q)
            if q == 0:
                dve.wait_ge(k.ssm_loaded, 16 * (l + 1))
                for c in range(4):
                    ins = dve.tensor_tensor(self.st[:, c], self.st[:, c], self.dax[:, c].unsqueeze(2).broadcast_to([P, NB, P]), ALU.mult)
                do(ins)
            dve.wait_ge(*t.at("s_spread", q))
            for c in range(4):
                for n in range(2):
                    bs = slice(4 * n, 4 * n + 4)
                    src = k.bank[4 * q + 2 * (c // 2) + n][:, :].rearrange("p (b n) -> p b n", b=4)
                    other = self.dtx[:, c, bs].unsqueeze(2).broadcast_to([P, 4, P]) if q == 0 else self.st[:, c, bs, :]
                    ins = dve.tensor_tensor(self.t1[:, c, bs, :], src, other, ALU.mult)
            do(ins)
            if q == 0:
                do(dve.tensor_tensor(self.st, self.st, self.t1, ALU.add), "s_state")
        for c in range(4):
            ins = dve.tensor_reduce(self.y[:, c, sam], self.t1[:, c], X, ALU.add)
        do(ins)
        for c in range(4):
            ins = dve.scalar_tensor_tensor(out=self.y[:, c, :], in0=self.cv[:, c, :], scalar=k.vec(l, "d")[:, c:c + 1], in1=self.y[:, c, :],
                                           op0=ALU.mult, op1=ALU.add)
        do(ins, "skip")
        dve.wait_ge(*a.at("z"))
        do(dve.tensor_tensor(self.y, self.y, k.z[:, :, :], ALU.mult), "gated")
        dve.wait_ge(*a.at("root"))
        do(dve.reciprocal(self.cv[:, 4:6, :], self.cv[:, 4:6, :]))
        for c in range(4):
            ins = dve.tensor_tensor(self.y[:, c, :], self.y[:, c, :], self.cv[:, 4 + c // 2, :], ALU.mult)
        do(ins)
        for c in range(4):
            ins = dve.tensor_scalar(self.y[:, c, :], self.y[:, c, :], k.vec(l, "ssm_norm")[:, c:c + 1], None, ALU.mult)
        do(ins)


class Mla(Stage):
    GROUP = 2

    def __init__(self, k, l):
        super().__init__(k, "mla", l)
        ar = Arena(k.sb, k.mla_at, k.mla_size)
        self.w = ar.take(NMLA)
        self.q = ar.take(8, T)
        tmp_at = ar.next
        self.tmp = ar.take(6, T)
        self.kpe = ar.take(T)
        self.cache = [ar.take(self.GROUP, NPAGE, CACHE) for _ in range(2)]
        early = Arena(k.sb, ar.next - self.GROUP * NPAGE * CACHE, self.GROUP * NPAGE * CACHE)
        self.kn, self.vt = early.take(8, SEQ), early.take(NT, 512)
        late, ar = ar, Arena(k.sb, tmp_at, 6 * T)
        self.qabs = ar.take(2, NB, 8)
        self.qpe = ar.take(NB, 8)
        self.prod, self.prodpe = ar.take(2, NB, 8), ar.take(NB, 8)
        self.snew, self.olat = ar.take(NB, 8), ar.take(2, NB, 8)
        self.m1, self.mrow, self.diag, self.m, self.rsum = ar.take(16), ar.take(1), ar.take(16), ar.take(16), ar.take(16)
        self.ps = ar.take(self.GROUP * 64)
        ar = late
        self.mx, self.sm = ar.take(8), ar.take(8)
        self.s = ar.take(8 * SEQ)
        self.pt = ar.take(2, 8, P)
        self.kT = self.s.rearrange("p (c t) -> p c t", c=2)
        self.kpT = self.pt.rearrange("p a b c -> p (a b c)")[0:32, 0:1024]
        self.root = self.tmp[:, 4:6, :]

    def weights(self, name, n):
        return self.w[:, MLA_W[name][0]:MLA_W[name][1]].rearrange("p (c n) -> p c n", c=n)

    def load_group(self, g, i):
        k, l = self.k, self.l
        for j in range(self.GROUP):
            for p in range(NPAGE):
                reg = k.page_regs[k.page_turn % len(k.page_regs)]
                k.page_turn += 1
                n = (self.GROUP * i + j) * NPAGE + p
                g.reg_load(reg, k.table[0:1, n:n + 1])
                page = g.snap(reg, min_val=0, max_val=k.cache.shape[1] - 1)
                g.dma_start(self.cache[i % 2][:, j, p, :], k.cache[l, bass.ds(page, 1)].rearrange("o s c -> (o s) c")).then_inc(k.pages_loaded[i % 2], 16)

    def pool(self, g):
        k, l = self.k, self.l
        g.dma_start(self.w[:, :], k.mla_w[l]).then_inc(k.mla_w_loaded, 16)
        if l == 0:
            g.wait_ge(k.const_loaded, 48)
        for i in range(NB // self.GROUP):
            if i == 1:
                g.wait_ge(*self.v.at("prompt_out"))
            if i >= 2:
                g.wait_ge(*self.t.at("pv", i - 2))
            self.load_group(g, i)
        g.wait_ge(*self.v.at("ckv"))
        g.dma_start(k.out["ckv"][l], k.qkv[:, 2:4, :]).then_inc(k.stored, 16)
        g.wait_ge(*self.v.at("pe"))
        g.dma_start(k.out["kpe"][l], self.kpe[0:32, :]).then_inc(k.stored, 16)
        k.stores += 2
        g.wait_ge(k.stored, 16 * k.stores)
        g.memset(k.pool_mark[0:1, 0:1], 0.0).then_inc(*self.g.did("stored"))

    def tensor(self, pe):
        k, t, v, a = self.k, self.t, self.v, self.a
        ident, ones = k.c("ident"), k.c("ones")
        w_uq, w_uk, w_uv, w_ukT = (self.weights(n, c) for n, c in (("w_uq", 2), ("w_uk", 2), ("w_uv", 2), ("w_ukT", 8)))
        pe.wait_ge(*a.at("latent_sq"))
        for g in range(2):
            for n in range(2):
                mm = pe.matmul(k.bank[g][:, 0:T], ones, self.tmp[:, 2 * g + n, :], start=n == 0, stop=n == 1)
        mm.then_inc(*t.did("latent_ms"))
        mm = pe.matmul(k.bank[2][:, 0:T], k.c("rotate"), k.kr[:, :], start=True, stop=True)
        mm.then_inc(*t.did("kr_rot"))
        pe.wait_ge(k.mla_w_loaded, 16 * (self.l + 1))
        pe.wait_ge(*v.at("ckv"))
        for h in range(8):
            if h >= 2:
                pe.wait_ge(*a.at("q", h - 2))
            for n in range(2):
                mm = pe.matmul(k.bank[4 + h % 2][0:96, 0:T], w_uq[:, n, 96 * h:96 * h + 96], k.qkv[:, n, :], start=n == 0, stop=n == 1)
            mm.then_inc(*t.did("q", h))
        pe.wait_ge(*v.at("pe_key"))
        for h in range(8):
            pe.wait_ge(*a.at("q", h))
            if h >= 2:
                pe.wait_ge(*v.at("q_rot", h - 2))
            mm = pe.matmul(k.bank[2 + h % 2][64:96, 0:T], k.c("rotate")[64:96, 64:96], self.q[64:96, h, :], start=True, stop=True,
                           tile_position=(64, 64))
            mm.then_inc(*t.did("q_rot", h))
        for h in range(8):
            if h == 4:
                pe.wait_ge(*a.at("q", 7))
            for n in range(2):
                mm = pe.matmul(k.bank[(6, 7, 4, 5)[h // 2]][0:64, SEQ * (h % 2):SEQ * (h % 2) + SEQ], w_uk[:, n, 64 * h:64 * h + 64],
                               k.qkv[:, 2 + n, 0:SEQ], start=n == 0, stop=n == 1)
        mm.then_inc(*t.did("keys"))
        for i in range(NT):
            for n in range(2):
                mm = pe.matmul(k.bank[i][:, :], k.qkv[:, 2 + n, P * i:P * i + P], w_uv[:, n, :], start=n == 0, stop=n == 1)
        mm.then_inc(*t.did("values"))
        pe.wait_ge(*v.at("pe"))
        pe.wait_ge(*a.at("kv"))
        for qi in range(NT):
            nk = P * (qi + 1)
            per = 512 // nk
            if qi:
                pe.wait_ge(*v.at("masked", qi - 1))
            for h in range(8):
                o = k.bank[2 + h // per][:, nk * (h % per):nk * (h % per) + nk]
                mm = pe.matmul(o, self.q[0:96, h, P * qi:P * qi + P], self.kn[0:96, h, 0:nk], start=True, stop=True)
            mm.then_inc(*t.did("scores", qi))
            pe.wait_ge(*v.at("probs", qi))
            s = self.s[:, 0:8 * nk].rearrange("p (h n) -> p h n", h=8)
            for ki in range(qi + 1):
                if ki:
                    pe.wait_ge(*a.at("pt", qi, ki - 1))
                for h in range(8):
                    mm = pe.transpose(k.bank[6 + h // 4][:, P * (h % 4):P * (h % 4) + P], s[:, h, P * ki:P * ki + P], ident)
                mm.then_inc(*t.did("pt", qi, ki))
            pe.wait_ge(*a.at("pt", qi, qi))
            for h in range(8):
                o = k.bank[h // 4][64 * (h % 2):64 * (h % 2) + 64, SEQ * (h // 2 % 2) + P * qi:SEQ * (h // 2 % 2) + P * qi + P]
                for ki in range(qi + 1):
                    mm = pe.matmul(o, self.vt[:, ki, 64 * h:64 * h + 64], self.pt[:, ki, h, :], start=ki == 0, stop=ki == qi)
            mm.then_inc(*t.did("out", qi))
        pe.wait_ge(*v.at("masked", NT - 1))
        for cc in range(2):
            for h in range(8):
                mm = pe.matmul(k.bank[2][:, 64 * cc + NB * h:64 * cc + NB * h + NB], w_ukT[0:64, h, P * cc:P * cc + P],
                               self.q[0:64, h, SEQ:T], start=True, stop=True)
        for h in range(8):
            mm = pe.matmul(k.bank[3][0:32, NB * h:NB * h + NB], ident[64:96, 64:96], self.q[64:96, h, SEQ:T], start=True, stop=True,
                           tile_position=(64, 0))
        mm.then_inc(*t.did("qabs"))
        pe.wait_ge(*v.at("prod"))
        o = k.bank[2][:, 128:192]
        for cc in range(2):
            pe.matmul(o, ones, self.prod[:, cc].rearrange("p b h -> p (b h)"), start=cc == 0, stop=False)
        mm = pe.matmul(o, ones[0:32, :], self.prodpe[0:32].rearrange("p b h -> p (b h)"), start=False, stop=True)
        mm.then_inc(*t.did("s_new"))
        pe.wait_ge(*v.at("prompt_out"))
        for i in range(NB // self.GROUP):
            pe.wait_ge(k.pages_loaded[i % 2], 16 * self.GROUP * NPAGE * (2 * self.l + i // 2 + 1))
            cache = self.cache[i % 2]
            if i:
                pe.wait_ge(*v.at("olat", i - 1))
            for j in range(self.GROUP):
                b = self.GROUP * i + j
                for p in range(NPAGE):
                    if (j or p >= 4) and p % 2 == 0:
                        pe.wait_ge(*a.at("kT", i, j if p >= 4 else j - 1, (p // 2 + 2) % 4))
                    for cc in range(2):
                        mm = pe.transpose(k.bank[4 + p // 2 % 2][:, 256 * cc + P * (p % 2):256 * cc + P * (p % 2) + P],
                                          cache[:, j, p, P * cc:P * cc + P], ident)
                    if p % 2:
                        mm.then_inc(*t.did("kT", i, j, p // 2))
                    if j and p % 4 == 0:
                        pe.wait_ge(*v.at("kpT", i, j - 1, p // 4))
                    mm = pe.transpose(k.bank[6 + p // 4][0:32, P * (p % 4):P * (p % 4) + P], cache[:, j, p, LORA:CACHE], ident)
                    if p % 4 == 3:
                        mm.then_inc(*t.did("kpT", i, j, p // 4))
                pe.wait_ge(*a.at("kT", i, j, 3))
                pe.wait_ge(*v.at("kpT", i, j, 1))
                for p in range(NPAGE):
                    o = k.bank[3][:, 64 * j + 8 * p:64 * j + 8 * p + 8]
                    for cc in range(2):
                        pe.matmul(o, self.kT[:, cc, P * p:P * p + P], self.qabs[:, cc, b, :], start=cc == 0, stop=False)
                    mm = pe.matmul(o, self.kpT[:, P * p:P * p + P], self.qpe[0:32, b, :], start=False, stop=True)
                mm.then_inc(*t.did("s_scores", i, j))
            pe.wait_ge(*v.at("m1", i))
            pe.transpose(k.bank[2][0:16, 192:320], self.m1[:, :], ident).then_inc(*t.did("m1", i))
            pe.wait_ge(*v.at("diag", i))
            pe.matmul(k.bank[2][:, 320:336], ones[0:16, :], self.diag[0:16, :], start=True, stop=True).then_inc(*t.did("max", i))
            pe.wait_ge(*v.at("rsum", i))
            pe.matmul(k.bank[2][:, 336:352], ones, self.rsum[:, :], start=True, stop=True).then_inc(*t.did("total", i))
            pe.wait_ge(*v.at("ps", i))
            ps = self.ps[:, :].rearrange("p (b n h) -> p b n h", b=self.GROUP, n=NPAGE)
            for cc in range(2):
                for j in range(self.GROUP):
                    o = k.bank[0][:, 16 * cc + 8 * j:16 * cc + 8 * j + 8]
                    for p in range(NPAGE):
                        mm = pe.matmul(o, cache[:, j, p, P * cc:P * cc + P], ps[:, j, p, :], start=p == 0, stop=p == NPAGE - 1)
            mm.then_inc(*t.did("pv", i))
        pe.wait_ge(*v.at("olat", NB // self.GROUP - 1))
        for h in range(8):
            o = k.bank[1][64 * (h % 2):64 * (h % 2) + 64, NB * (h // 2):NB * (h // 2) + NB]
            for cc in range(2):
                mm = pe.matmul(o, w_uv[:, cc, 64 * h:64 * h + 64], self.olat[:, cc, :, h], start=cc == 0, stop=cc == 1)
        mm.then_inc(*t.did("s_out"))

    def scalar(self, act):
        k, t, v, a = self.k, self.t, self.v, self.a
        act.activation(self.tmp[:, 0:4, :], k.qkv[:, :, :], ACT.Square).then_inc(*a.did("latent_sq"))
        act.wait_ge(*t.at("latent_ms"))
        for g in range(2):
            ins = act.activation(self.root[:, g, :], k.bank[g][:, 0:T], ACT.Sqrt, scale=1.0 / 256, bias=k.c("eps"))
        ins.then_inc(*a.did("latent_root"))
        for h in range(8):
            act.wait_ge(*t.at("q", h))
            act.copy(self.q[0:96, h, :], k.bank[4 + h % 2][0:96, 0:T]).then_inc(*a.did("q", h))
        act.wait_ge(*t.at("keys"))
        for n in range(4):
            act.copy(self.kn[0:64, 2 * n:2 * n + 2, :], k.bank[(6, 7, 4, 5)[n]][0:64, :].rearrange("p (h t) -> p h t", h=2))
        act.wait_ge(*t.at("values"))
        act.copy(self.vt[:, 0, :], k.bank[0][:, :])
        act.copy(self.vt[:, 1, :], k.bank[1][:, :]).then_inc(*a.did("kv"))
        for qi in range(NT):
            nk = P * (qi + 1)
            act.wait_ge(*v.at("less_max", qi))
            act.activation(self.s[:, 0:8 * nk], self.s[:, 0:8 * nk], ACT.Exp, scale=MLA_SCALE).then_inc(*a.did("exp", qi))
            for ki in range(qi + 1):
                act.wait_ge(*t.at("pt", qi, ki))
                for g in range(2):
                    ins = act.copy(self.pt[:, ki, 4 * g:4 * g + 4, :].rearrange("p h t -> p (h t)"), k.bank[6 + g][:, :])
                ins.then_inc(*a.did("pt", qi, ki))
        act.wait_ge(*t.at("out", NT - 1))
        for i in range(NB // self.GROUP):
            for j in range(self.GROUP):
                if i or j:
                    act.wait_ge(*t.at("s_scores", i if j else i - 1, j - 1 if j else self.GROUP - 1))
                for n in range(4):
                    act.wait_ge(*t.at("kT", i, j, n))
                    act.copy(self.kT[:, :, 256 * n:256 * n + 256], k.bank[4 + n % 2][:, :].rearrange("p (c t) -> p c t", c=2)).then_inc(*a.did("kT", i, j, n))
            act.wait_ge(*v.at("s_less_max", i))
            act.activation(self.ps[:, :], self.ps[:, :], ACT.Exp, scale=MLA_SCALE)
            act.activation(self.m[:, :], self.m[:, :], ACT.Exp, scale=MLA_SCALE).then_inc(*a.did("s_exp", i))

    def vector(self, dve):
        k, a, t, v, l = self.k, self.a, self.t, self.v, self.l
        do = v.serial(dve)
        dve.wait_ge(*a.at("latent_root"))
        do(dve.reciprocal(self.root[:, :, :], self.root[:, :, :]))
        for c in range(4):
            name = "q_norm" if c < 2 else "kv_norm"
            ins = dve.scalar_tensor_tensor(out=k.qkv[:, c, :], in0=k.qkv[:, c, :], scalar=k.vec(l, name)[:, c % 2:c % 2 + 1],
                                           in1=self.root[:, c // 2, :], op0=ALU.mult, op1=ALU.mult)
        do(ins, "ckv")
        cos, sin = k.c("cos"), k.c("sin")
        do(dve.tensor_tensor(self.kpe[:, :], k.kr[:, :], cos, ALU.mult))
        dve.wait_ge(*t.at("kr_rot"))
        do(dve.tensor_tensor(self.tmp[:, 0, :], k.bank[2][:, 0:T], sin, ALU.mult), "pe_key")
        do(dve.tensor_tensor(self.kpe[:, :], self.kpe[:, :], self.tmp[:, 0, :], ALU.add))
        rp = slice(64, 96)
        do(dve.tensor_copy(self.kn[rp, :, :], bc(self.kpe[rp, 0:SEQ], 1, 8)))
        for h in range(8):
            dve.wait_ge(*t.at("q_rot", h))
            dve.tensor_tensor(self.q[rp, h, :], self.q[rp, h, :], cos[rp, :], ALU.mult)
            do(dve.tensor_tensor(self.tmp[rp, h % 2, :], k.bank[2 + h % 2][rp, 0:T], sin[rp, :], ALU.mult), "q_rot", h)
            do(dve.tensor_tensor(self.q[rp, h, :], self.q[rp, h, :], self.tmp[rp, h % 2, :], ALU.add), *(("pe",) if h == 7 else ()))
        for qi in range(NT):
            nk = P * (qi + 1)
            per = 512 // nk
            s = self.s[:, 0:8 * nk].rearrange("p (h n) -> p h n", h=8)
            dve.wait_ge(*t.at("scores", qi))
            if qi:
                dve.wait_ge(*t.at("pt", qi - 1, qi - 1))
            for n in range(8 // per):
                hs = slice(per * n, per * n + per)
                src = k.bank[2 + n][:, :].rearrange("p (h n) -> p h n", h=per)
                if qi:
                    dve.tensor_copy(s[:, hs, 0:P * qi], src[:, :, 0:P * qi])
                ins = dve.tensor_tensor(s[:, hs, P * qi:nk], src[:, :, P * qi:nk], bc(k.c("causal"), 1, per), ALU.add)
            do(ins, "masked", qi)
            do(dve.tensor_reduce(self.mx[:, :], s, X, ALU.max))
            do(dve.tensor_tensor(s, s, self.mx[:, :].unsqueeze(2).broadcast_to([P, 8, nk]), ALU.subtract), "less_max", qi)
            dve.wait_ge(*a.at("exp", qi))
            do(dve.tensor_reduce(self.sm[:, :], s, X, ALU.add))
            do(dve.reciprocal(self.sm[:, :], self.sm[:, :]))
            do(dve.tensor_tensor(s, s, self.sm[:, :].unsqueeze(2).broadcast_to([P, 8, nk]), ALU.mult), "probs", qi)
        dve.wait_ge(*t.at("out", NT - 1))
        for c in range(4):
            ins = dve.tensor_copy(k.branches[:, c, 0:SEQ], k.bank[c // 2][:, SEQ * (c % 2):SEQ * (c % 2) + SEQ])
        do(ins, "prompt_out")
        dve.wait_ge(*t.at("qabs"))
        for cc in range(2):
            dve.tensor_copy(self.qabs[:, cc].rearrange("p b h -> p h b"), k.bank[2][:, 64 * cc:64 * cc + 64].rearrange("p (h b) -> p h b", h=8))
        do(dve.tensor_copy(self.qpe[0:32].rearrange("p b h -> p h b"), k.bank[3][0:32, 0:64].rearrange("p (h b) -> p h b", h=8)))
        sam = slice(SEQ, T)
        for cc in range(2):
            dve.tensor_tensor(self.prod[:, cc], self.qabs[:, cc], k.qkv[:, 2 + cc, sam].unsqueeze(2).broadcast_to([P, NB, 8]), ALU.mult)
        do(dve.tensor_tensor(self.prodpe[0:32], self.qpe[0:32], self.kpe[0:32, sam].unsqueeze(2).broadcast_to([32, NB, 8]), ALU.mult), "prod")
        dve.wait_ge(*t.at("s_new"))
        do(dve.tensor_copy(self.snew[:, :, :], k.bank[2][:, 128:192].rearrange("p (b h) -> p b h", b=NB)))
        for i in range(NB // self.GROUP):
            bs = slice(self.GROUP * i, self.GROUP * i + self.GROUP)
            for j in range(self.GROUP):
                if i or j:
                    dve.wait_ge(*t.at("s_scores", i if j else i - 1, j - 1 if j else self.GROUP - 1))
                for n in range(2):
                    dve.wait_ge(*t.at("kpT", i, j, n))
                    dve.tensor_copy(self.kpT[:, 512 * n:512 * n + 512], k.bank[6 + n][0:32, :]).then_inc(*v.did("kpT", i, j, n))
            dve.wait_ge(*t.at("s_scores", i, self.GROUP - 1))
            scores = k.bank[3][:, 0:128].rearrange("p (b n h) -> p b n h", b=self.GROUP, n=NPAGE)
            m1, m = (x.rearrange("p (b h) -> p b h", b=self.GROUP) for x in (self.m1, self.m))
            do(dve.tensor_reduce(m1, scores.rearrange("p b n h -> p b h n"), X, ALU.max), "m1", i)
            dve.wait_ge(*t.at("m1", i))
            do(dve.tensor_reduce(self.mrow[0:16, :], k.bank[2][0:16, 192:320], X, ALU.max))
            do(dve.tensor_scalar(self.diag[0:16, :], k.c("ident")[0:16, 0:16], self.mrow[0:16, 0:1], None, ALU.mult), "diag", i)
            dve.wait_ge(*t.at("max", i))
            do(dve.tensor_tensor(m, k.bank[2][:, 320:336].rearrange("p (b h) -> p b h", b=self.GROUP), self.snew[:, bs, :], ALU.max))
            ps = self.ps[:, :].rearrange("p (b n h) -> p b n h", b=self.GROUP, n=NPAGE)
            for j in range(self.GROUP):
                ins = dve.tensor_tensor(ps[:, j], scores[:, j], bc(m[:, j, :], 1, NPAGE), ALU.subtract)
            do(ins)
            do(dve.tensor_tensor(m, self.snew[:, bs, :], m, ALU.subtract), "s_less_max", i)
            dve.wait_ge(*a.at("s_exp", i))
            do(dve.tensor_reduce(self.rsum.rearrange("p (b h) -> p b h", b=self.GROUP), ps.rearrange("p b n h -> p b h n"), X, ALU.add), "rsum", i)
            dve.wait_ge(*t.at("total", i))
            do(dve.tensor_tensor(self.rsum[:, :], k.bank[2][:, 336:352], self.m[:, :], ALU.add))
            do(dve.reciprocal(self.rsum[:, :], self.rsum[:, :]))
            rs = self.rsum.rearrange("p (b h) -> p b h", b=self.GROUP)
            dve.tensor_tensor(self.m[:, :], self.m[:, :], self.rsum[:, :], ALU.mult)
            for j in range(self.GROUP):
                ins = dve.tensor_tensor(ps[:, j], ps[:, j], bc(rs[:, j, :], 1, NPAGE), ALU.mult)
            do(ins, "ps", i)
            for cc in range(2):
                ins = dve.tensor_tensor(self.olat[:, cc, bs, :], m, k.qkv[:, 2 + cc, SEQ + self.GROUP * i:SEQ + self.GROUP * (i + 1)].unsqueeze(2).broadcast_to([P, self.GROUP, 8]), ALU.mult)
            do(ins)
            dve.wait_ge(*t.at("pv", i))
            for cc in range(2):
                ins = dve.tensor_tensor(self.olat[:, cc, bs, :], self.olat[:, cc, bs, :],
                                        k.bank[0][:, 16 * cc:16 * cc + 16].rearrange("p (b h) -> p b h", b=self.GROUP), ALU.add)
            do(ins, "olat", i)
        dve.wait_ge(*t.at("s_out"))
        do(dve.tensor_copy(k.branches[:, 0:4, SEQ:T], k.bank[1][:, 0:32].rearrange("p (c b) -> p c b", c=4)))


class Merge(Stage):

    def __init__(self, k, l):
        super().__init__(k, "merge", l)
        self.mix, self.gated, self.gate = k.merge_mix, k.merge_gated, k.merge_gate
        self.slots = []
        for r in range(3):
            place = k.next_place()
            dst = k.slot(place).rearrange("p (c n) -> p c n", c=4)
            wb = k.ring.add(place, dst, k.w_branch[l, r].rearrange("(c p) n -> p c n", p=P))
            gs = []
            for i in range(2):
                place = k.next_place()
                dst = k.slot(place).rearrange("p (k n) -> p k n", k=KC)
                c0 = 3880 + D * r + 512 * i
                gs.append(k.ring.add(place, dst, k.w_in[l].rearrange("(k p) n -> p k n", p=P)[:, :, c0:c0 + 512]))
            self.slots.append((wb, gs))
        self.out_slots = []
        for i in range(2):
            place = k.next_place()
            dst = k.slot(place).rearrange("p (k n) -> p k n", k=KC)
            self.out_slots.append(k.ring.add(place, dst, k.w_out[l].rearrange("(k p) n -> p k n", p=P)[:, :, 512 * i:512 * i + 512]))

    def tensor(self, pe):
        k, t, v = self.k, self.t, self.v
        for r in range(3):
            wb, gs = self.slots[r]
            k.ring.arrived(pe, wb)
            w = k.ring.loads[wb][1]
            for d in range(KC):
                n = KC * r + d
                slot = gs[d // 4]
                k.ring.arrived(pe, slot)
                if n >= 4:
                    pe.wait_ge(*v.at("merged", n - 4))
                g = k.ring.loads[slot][1]
                for kk in range(KC):
                    mm = pe.matmul(k.bank[n % 4][:, 0:T], g[:, kk, P * (d % 4):P * (d % 4) + P], k.h[:, kk, :], start=kk == 0, stop=kk == KC - 1)
                mm.then_inc(*t.did("gate", n))
                if d % 4 == 3:
                    k.ring.release(slot, t)
                for c in range(4):
                    mm = pe.matmul(k.bank[4 + n % 4][:, 0:T], w[:, c, P * d:P * d + P], k.branches[:, 4 * r + c, :], start=c == 0, stop=c == 3)
                mm.then_inc(*t.did("branch", n))
            k.ring.release(wb, t)
        pe.wait_ge(*v.at("merged", 3 * KC - 1))
        for d in range(KC):
            slot = self.out_slots[d // 4]
            k.ring.arrived(pe, slot)
            w = k.ring.loads[slot][1]
            for kk in range(KC):
                mm = pe.matmul(k.bank[d][:, 0:T], w[:, kk, P * (d % 4):P * (d % 4) + P], self.mix[:, kk, :], start=kk == 0, stop=kk == KC - 1)
            mm.then_inc(*t.did("out", d))
            if d % 4 == 3:
                k.ring.release(slot, t)

    def scalar(self, act):
        k = self.k
        for n in range(3 * KC):
            act.wait_ge(*self.t.at("gate", n))
            if n >= 2:
                act.wait_ge(*self.v.at("merged", n - 2))
            act.activation(self.gate[:, n % 2, :], k.bank[n % 4][:, 0:T], ACT.Sigmoid).then_inc(*self.a.did("gate", n))

    def vector(self, dve):
        k, t, a, v = self.k, self.t, self.a, self.v
        do = v.serial(dve)
        for n in range(3 * KC):
            d = n % KC
            dve.wait_ge(*a.at("gate", n))
            dve.wait_ge(*t.at("branch", n))
            src = k.bank[4 + n % 4][:, 0:T]
            if n < KC:
                do(dve.tensor_tensor(self.mix[:, d, :], src, self.gate[:, n % 2, :], ALU.mult), "merged", n)
            else:
                do(dve.tensor_tensor(self.gated[:, n % 2, :], src, self.gate[:, n % 2, :], ALU.mult))
                do(dve.tensor_tensor(self.mix[:, d, :], self.mix[:, d, :], self.gated[:, n % 2, :], ALU.add), "merged", n)
        for d in range(KC):
            dve.wait_ge(*t.at("out", d))
            add_gated(k, dve, do, k.bank[d], d, 2)


def add_gated(k, dve, do, src, d, part):
    gate = k.ada[:, 8 * part + d, :]
    do(dve.tensor_tensor(k.gated_s[:, :], src[:, SEQ:T], gate[:, 1:NSEQ], ALU.mult))
    dve.tensor_tensor(k.x[:, d, SEQ:T], k.x[:, d, SEQ:T], k.gated_s[:, :], ALU.add)
    do(dve.scalar_tensor_tensor(out=k.x[:, d, 0:SEQ], in0=src[:, 0:SEQ], scalar=gate[:, 0:1], in1=k.x[:, d, 0:SEQ],
                                op0=ALU.mult, op1=ALU.add))


class Route(Stage):

    def __init__(self, k, l):
        super().__init__(k, "route", l)

    def tensor(self, pe):
        k, t, v = self.k, self.t, self.v
        router = k.small[:, SMALL["router"][0]:SMALL["router"][1]].rearrange("p (k e) -> p k e", k=KC)
        for i in range(3):
            m = P if i < 2 else NB
            for kk in range(KC):
                mm = pe.matmul(k.bank[0][0:m, 8 * i:8 * i + 8], k.h[:, kk, P * i:P * i + m], router[:, kk, :], start=kk == 0, stop=kk == KC - 1)
        mm.then_inc(*t.did("logits"))
        pe.wait_ge(*v.at("gates"))
        for e in range(NE):
            for i in range(3):
                m = P if i < 2 else NB
                mm = pe.matmul(k.bank[e][:, P * i:P * i + m], k.gates[0:m, i, e:e + 1].broadcast_to([m, P]), k.c("ident")[0:m, 0:m], start=True, stop=True)
        mm.then_inc(*t.did("spread"))

    def scalar(self, act):
        act.wait_ge(*self.v.at("diff"))
        act.activation(self.k.top_e[:, :], self.k.top_e[:, :], ACT.Exp).then_inc(*self.a.did("exp"))

    def vector(self, dve):
        k, t, a, v, l = self.k, self.t, self.a, self.v, self.l
        do = v.serial(dve)
        dve.memset(k.logits[:, :, :], 0.0)
        do(dve.memset(k.gates[:, :, :], 0.0))
        dve.wait_ge(*t.at("logits"))
        for i in range(3):
            m = P if i < 2 else NB
            do(dve.tensor_tensor(k.logits[0:m, i, :], k.bank[0][0:m, 8 * i:8 * i + 8], k.vec(l, "router_b")[0:m, :], ALU.add))
        for i in range(3):
            do(dve.max(k.top_v[:, i, :], k.logits[:, i, :]))
            do(dve.max_index(k.top_i[:, i, :], k.top_v[:, i, :], k.logits[:, i, :]))
        do(dve.tensor_copy(k.top_f[:, :, :], k.top_i[:, :, :]))
        do(dve.tensor_tensor(k.top_e[:, :], k.top_v[:, :, 1], k.top_v[:, :, 0], ALU.subtract), "diff")
        dve.wait_ge(*a.at("exp"))
        do(dve.tensor_scalar(k.top_w[:, 0, :], k.top_e[:, :], 1.0, None, ALU.add))
        do(dve.reciprocal(k.top_w[:, 0, :], k.top_w[:, 0, :]))
        do(dve.tensor_tensor(k.top_w[:, 1, :], k.top_w[:, 0, :], k.top_e[:, :], ALU.mult))
        for i in range(3):
            for n in range(2):
                do(dve.tensor_scalar(k.one_hot[:, :], k.c("expert_ids"), k.top_f[:, i, n:n + 1], k.top_w[:, n, i:i + 1], ALU.is_equal, ALU.mult))
                do(dve.tensor_tensor(k.gates[:, i, :], k.gates[:, i, :], k.one_hot[:, :], ALU.add), *(("gates",) if (i, n) == (2, 1) else ()))
        dve.wait_ge(*t.at("spread"))
        for e in range(NE):
            ins = dve.tensor_copy(k.gate_rows[:, e, :], k.bank[e][:, 0:T])
        do(ins)


class Swiglu(Stage):

    def __init__(self, k, l, w1, w3, w2, width, expert=None):
        super().__init__(k, "swiglu", (l, expert))
        self.expert = expert
        self.nf = width // P
        self.half = self.nf // 2
        self.up, self.down = [], []
        for c0 in range(0, width, 512):
            n = min(512, width - c0)
            pair = []
            for w in (w1, w3):
                place = k.next_place()
                dst = k.slot(place)[:, 0:KC * n].rearrange("p (k n) -> p k n", k=KC)
                pair.append(k.ring.add(place, dst, w.rearrange("(k p) n -> p k n", p=P)[:, :, c0:c0 + n]))
            self.up.append((pair, n // P))
        for d in range(4):
            for i in range(2):
                place = k.next_place()
                dst = k.slot(place)[:, 0:self.half * 256].rearrange("p (f n) -> p f n", n=256)
                src = w2.rearrange("(f p) n -> p f n", p=P)[:, self.half * i:self.half * (i + 1), 256 * d:256 * d + 256]
                self.down.append(k.ring.add(place, dst, src))

    def tensor(self, pe):
        k, t, v, a = self.k, self.t, self.v, self.a
        f = 0
        for pair, n in self.up:
            for i in range(n):
                for q in range(2):
                    k.ring.arrived(pe, pair[q])
                    if f >= 2:
                        pe.wait_ge(*(a, v)[q].at("up", f - 2))
                    w = k.ring.loads[pair[q]][1]
                    for kk in range(KC):
                        mm = pe.matmul(k.bank[2 * (f % 2) + q][:, 0:T], w[:, kk, P * i:P * i + P], k.h[:, kk, :], start=kk == 0, stop=kk == KC - 1)
                    mm.then_inc(*t.did("up", f, q))
                    if i == n - 1:
                        k.ring.release(pair[q], t)
                f += 1
        pe.wait_ge(*v.at("up", self.nf - 1))
        for d in range(4):
            for i in range(2):
                slot = self.down[2 * d + i]
                k.ring.arrived(pe, slot)
                w = k.ring.loads[slot][1]
                if i == 0 and d >= 2:
                    pe.wait_ge(*v.at("down", d - 2))
                for j in range(2):
                    for f in range(self.half):
                        mm = pe.matmul(k.bank[4 + 2 * (d % 2) + j][:, 0:T], w[:, f, P * j:P * j + P], k.hidden[:, self.half * i + f, :],
                                       start=i == 0 and f == 0, stop=i == 1 and f == self.half - 1)
                mm.then_inc(*t.did("down", d, i))
                k.ring.release(slot, t)

    def scalar(self, act):
        k = self.k
        for f in range(self.nf):
            act.wait_ge(*self.t.at("up", f, 0))
            if f >= 2:
                act.wait_ge(*self.v.at("up", f - 2))
            act.activation(k.silu_up[:, f % 2, :], k.bank[2 * (f % 2)][:, 0:T], ACT.Silu).then_inc(*self.a.did("up", f))

    def vector(self, dve):
        k, t, a, v = self.k, self.t, self.a, self.v
        do = v.serial(dve)
        for f in range(self.nf):
            dve.wait_ge(*a.at("up", f))
            dve.wait_ge(*t.at("up", f, 1))
            ins = dve.tensor_tensor(k.hidden[:, f, :], k.bank[2 * (f % 2) + 1][:, 0:T], k.silu_up[:, f % 2, :], ALU.mult)
            if self.expert is not None:
                do(ins)
                ins = dve.tensor_tensor(k.hidden[:, f, :], k.hidden[:, f, :], k.gate_rows[:, self.expert, :], ALU.mult)
            ins.then_inc(*v.did("up", f))
        for d in range(4):
            dve.wait_ge(*t.at("down", d, 1))
            for j in range(2):
                src, c = k.bank[4 + 2 * (d % 2) + j], 2 * d + j
                if self.expert is None:
                    add_gated(k, dve, do, src, c, 5)
                elif self.expert == 0:
                    do(dve.tensor_copy(k.moe_out[:, c, :], src[:, 0:T]))
                else:
                    do(dve.tensor_tensor(k.moe_out[:, c, :], k.moe_out[:, c, :], src[:, 0:T], ALU.add))
                if self.expert == NE - 1:
                    add_gated(k, dve, do, k.moe_out[:, c, :], c, 5)
            v.steps.book.setdefault((v.steps.name, (v.layer, "down", d)), v.steps.count)


class Setup(Stage):

    def __init__(self, k):
        super().__init__(k, "setup", 0)

    def scalar(self, act):
        k = self.k
        act.wait_ge(k.const_loaded, 64)
        act.activation(k.silu_c[:, :, :], k.c_in[:, :, :], ACT.Silu).then_inc(*self.a.did("silu_c"))


class LayerLoads(Stage):

    def __init__(self, k, l):
        super().__init__(k, "loads", l)

    def pool(self, g):
        k, l = self.k, self.l
        if l == 0:
            g.dma_start(k.x[:, :, :], k.x_in).then_inc(k.const_loaded, 16)
            g.dma_start(k.consts[:, :], k.consts_in).then_inc(k.const_loaded, 16)
            g.dma_start(k.table[0:1, :], k.table_in).then_inc(k.const_loaded, 16)
            g.dma_start(k.c_in[:, :, :], k.c_dram).then_inc(k.const_loaded, 16)
        g.dma_start(k.vecs[:, :], k.vecs_in[l]).then_inc(k.vec_loaded, 16)
        g.dma_start(k.small[:, :], k.small_in[l]).then_inc(k.small_loaded, 16)
        g.dma_start(k.shift_in[:, :, :], k.shift_dram[l]).then_inc(k.shift_loaded, 16)
        g.dma_start(k.conv_in[:, :, :, :], k.conv_dram[l]).then_inc(k.conv_loaded, 16)
        g.wait_ge(k.const_loaded, 64)
        for sem in (k.vec_loaded, k.small_loaded, k.shift_loaded, k.conv_loaded):
            g.wait_ge(sem, 16 * (l + 1))
        g.memset(k.pool_mark[0:1, 0:1], 0.0).then_inc(*self.g.did("loaded"))


class Store(Stage):

    def __init__(self, k):
        super().__init__(k, "store", 0)

    def pool(self, g):
        k = self.k
        g.dma_start(k.out["y"], k.h[:, :, :]).then_inc(k.stored, 16)
        k.stores += 1
        g.wait_ge(k.stored, 16 * k.stores)



def build(nc, dram, out, book):
    k = Kernel(nc, dram, out, book)
    for l in range(DEPTH):
        LayerLoads(k, l)
        if l == 0:
            k.setup = Setup(k)
        Ada(k, l)
        Norm(k, l, "attn")
        Project(k, l)
        k.turn = 0
        Rwkv(k, l)
        Ssm(k, l)
        k.guard = Mla(k, l)
        Merge(k, l)
        Norm(k, l, "ffn")
        if l % 2 == 0:
            Swiglu(k, l, k.w1[l // 2], k.w3[l // 2], k.w2[l // 2], FF)
        else:
            Route(k, l)
            for e in range(NE):
                Swiglu(k, l, k.e1[l // 2, e], k.e3[l // 2, e], k.e2[l // 2, e], FE, e)
    Norm(k, DEPTH - 1, "final")
    Store(k)
    with nc.Block() as block:

        @block.sync
        def _(sp):
            k.ring.fill(sp)

        @block.tensor
        def _(pe):
            for stage in k.stages:
                stage.emit("tensor", pe)

        @block.scalar
        def _(act):
            for stage in k.stages:
                stage.emit("scalar", act)

        @block.vector
        def _(dve):
            for stage in k.stages:
                stage.emit("vector", dve)

        @block.gpsimd
        def _(g):
            for stage in k.stages:
                stage.emit("pool", g)
    return k


def constants():
    a = np.zeros((P, NCONST), np.float32)

    def put(name, v):
        a[:v.shape[0], CONST[name][0]:CONST[name][0] + v.shape[1]] = v
    i, j = np.arange(P)[:, None], np.arange(P)[None, :]
    put("ident", np.eye(P))
    put("ones", np.ones((P, P)))
    put("block_ones", (i // 64 == j // 64).astype(float))
    t = np.arange(P + 1)[None, :]
    put("decay_tri", DECAY * ((i < t).astype(float) - (i < P // 2)))
    put("decay_id", DECAY * np.eye(NB))
    put("levels", np.concatenate([((i // (2 * m) == j // (2 * m)) & (i // m % 2 == 0) & (j // m % 2 == 1)).astype(float) for m in LEVELS], 1))
    put("strict", (i < j).astype(float))
    put("upto", (i <= j).astype(float))
    put("causal", np.where(j <= i, 0.0, -1e30))
    put("fold", (i % 64 == np.arange(64)[None, :]).astype(float))
    rot = np.zeros((P, P))
    for m in range(P):
        half = m % ROPE < ROPE // 2
        rot[m + 16 if half else m - 16, m] = -1.0 if half else 1.0
    put("rotate", rot)
    freq = np.float32(10000.0) ** (-np.arange(16, dtype=np.float32) / np.float32(16))
    pos = np.concatenate([np.arange(SEQ), np.full(NB, PAGE * NPAGE)]).astype(np.float32)
    ang = (pos[None, :] * freq[np.arange(P) % 16][:, None]).astype(np.float32)
    put("cos", np.cos(ang.astype(np.float64)))
    put("sin", np.sin(ang.astype(np.float64)))
    put("spread", (np.arange(8)[:, None] == np.arange(512)[None, :] // 64).astype(float))
    put("eps", np.full((P, 1), EPS))
    put("ln_eps", np.full((P, 1), LN_EPS))
    put("expert_ids", np.broadcast_to(np.arange(8.0), (P, 8)))
    return a


def chunks(v):
    return np.swapaxes(v.reshape(v.shape[:-1] + (-1, P)), -1, -2)


def lay_out(i):
    i = {n: np.asarray(v) for n, v in i.items()}
    L = DEPTH
    x = np.concatenate([i["x_prompt"][0], i["x_sample"][:, 0]], 0)
    c = np.concatenate([i["c_prompt"], i["c_sample"]], 0)

    def fm(v):
        return v.T.reshape(-1, P, v.shape[0]).transpose(1, 0, 2)

    def rows8(v):
        out = np.zeros((L, P, 1), np.float32)
        out[:, :8, 0] = v
        return out
    parts = {
        "norm_attn": chunks(i["norm_attn"]), "norm_ffn": chunks(i["norm_ffn"]),
        "norm_final": np.broadcast_to(chunks(i["norm_final"]), (L, P, 8)), "b_ada": chunks(i["b_ada"]),
        "q_norm": chunks(i["mla_q_norm"]), "kv_norm": chunks(i["mla_kv_norm"]), "mu": chunks(i["rwkv_mu"]),
        "a0": chunks(i["rwkv_a0"]), "k_k": chunks(i["rwkv_k_k"]), "k_a": chunks(i["rwkv_k_a"]),
        "r_k": chunks(i["rwkv_r_k"].reshape(L, 512)), "ln_w": chunks(i["rwkv_ln_w"]), "ln_b": chunks(i["rwkv_ln_b"]),
        "conv_w": chunks(i["ssm_conv_w"]).transpose(0, 2, 1, 3).reshape(L, P, 32), "conv_b": chunks(i["ssm_conv_b"]),
        "d": chunks(np.repeat(i["ssm_d"], 64, axis=1)), "ssm_norm": chunks(i["ssm_norm"]),
        "dt_bias": rows8(i["ssm_dt_bias"]), "a_log": rows8(i["ssm_a_log"]),
        "router_b": np.broadcast_to(np.concatenate([np.zeros_like(i["moe_router_b"]), i["moe_router_b"]])[:, None, :], (L, P, 8)),
    }

    def by_k(w):
        return w.reshape(L, -1, P, w.shape[-1]).transpose(0, 2, 1, 3).reshape(L, P, -1)
    w_in = i["w_in"]
    router = np.concatenate([np.zeros_like(i["moe_router"]), i["moe_router"]])
    rwkv_w = np.zeros((L, P, NRWKV), np.float32)
    rwkv_w[:, 0:64, 0:512], rwkv_w[:, 64, 0:512] = i["rwkv_w2"], i["rwkv_w0"]
    rwkv_w[:, 64:128, 512:1024], rwkv_w[:, :, 1024:1536] = i["rwkv_a2"], i["rwkv_g2"]
    uq = i["mla_w_uq"]
    ukT = np.zeros((L, P, 2048), np.float32)
    ukT[:, 0:64] = i["mla_w_uk"].transpose(0, 3, 2, 1).reshape(L, 64, 2048)
    uk, uv = i["mla_w_uk"].reshape(L, LORA, 512), i["mla_w_uv"].reshape(L, LORA, 512)
    arrays = {
        "x": fm(x), "consts": constants(), "table": i["page_table"].reshape(1, 64), "c": fm(c),
        "vecs": np.concatenate([parts[n] for n in VEC], -1),
        "small": np.concatenate([by_k(np.tile(w_in[:, :, 512:544], (1, 1, 4))), by_k(w_in[:, :, 3872:3880]), by_k(router)], -1),
        "shift": chunks(i["state_rwkv_shift"]).transpose(0, 2, 3, 1),
        "conv": chunks(i["state_ssm_conv"]).transpose(0, 3, 4, 1, 2),
        "rwkv_w": rwkv_w, "mla_w": np.concatenate([by_k(uq), by_k(uk), by_k(uv), ukT], -1),
        "wkv": i["state_rwkv_wkv"].reshape(L, NB, 4, 2, 64, 64).transpose(0, 3, 5, 2, 1, 4).reshape(L, P, 4, NB, 64),
        "ssm": i["state_ssm"].reshape(L, NB, 4, 2, 64, P).transpose(0, 3, 4, 2, 1, 5).reshape(L, P, 4, NB, P),
        "cache": np.concatenate([i["cache_ckv"], i["cache_kpe"]], -1),
    }
    for n in DRAM:
        if n not in arrays:
            arrays[n] = i[n]
    return {n: np.ascontiguousarray(arrays[n]) for n in DRAM}


def hand_back(o):
    L = DEPTH

    def rows(v):
        return v.transpose(2, 1, 0).reshape(v.shape[2], -1)
    y = rows(o["y"])
    ckv = np.stack([rows(o["ckv"][l]) for l in range(L)])
    kpe = o["kpe"].transpose(0, 2, 1)
    shift = np.stack([rows(o["shift"][l]) for l in range(L)])
    p_wkv = o["p_wkv"].reshape(L, 2, 64, 4, 64).transpose(0, 3, 1, 4, 2).reshape(L, 1, 8, 64, 64)
    s_wkv = o["s_wkv"].reshape(L, 2, 64, 4, NB, 64).transpose(0, 4, 3, 1, 5, 2).reshape(L, NB, 8, 64, 64)
    p_conv = o["p_conv"].transpose(0, 3, 2, 1).reshape(L, 1, 3, D)
    s_conv = o["s_conv"].transpose(0, 3, 4, 2, 1).reshape(L, NB, 3, D)
    p_ssm = o["p_ssm"].reshape(L, P, 8, 64).transpose(0, 2, 3, 1).reshape(L, 1, 8, 64, P)
    s_ssm = o["s_ssm"].reshape(L, 2, 64, 4, NB, P).transpose(0, 4, 3, 1, 2, 5).reshape(L, NB, 8, 64, P)
    c = np.ascontiguousarray
    return (c(y[:SEQ][None]), c(y[SEQ:][:, None]), c(ckv[:, :SEQ].reshape(L, NT, PAGE, LORA)), c(kpe[:, :SEQ].reshape(L, NT, PAGE, ROPE)),
            c(shift[:, 0:1]), c(p_wkv), c(p_conv), c(p_ssm), c(ckv[:, SEQ:][:, :, None]), c(kpe[:, SEQ:][:, :, None]),
            c(shift[:, 1:]), c(s_wkv), c(s_conv), c(s_ssm))


def declare(nc, arrays):
    dram = {n: nc.dram_tensor(f"in_{n}", a.shape, mybir.dt.from_np(a.dtype), kind="ExternalInput").ap() for n, a in arrays.items()}
    out = {n: nc.dram_tensor(f"out_{n}", shape, F32, kind="ExternalOutput").ap() for n, shape in OUTS.items()}
    return dram, out


def kernel(**inputs):
    import concourse.bacc as bacc
    from concourse.bass_utils import run_bass_kernel_spmd as run

    arrays = lay_out(inputs)
    book = {}
    for _ in range(2):
        nc = bacc.Bacc("TRN2", target_bir_lowering=False, num_devices=1, dynamic_dma_scratch_size=4096)
        build(nc, *declare(nc, arrays), book)
    r = run(nc, [{f"in_{n}": a for n, a in arrays.items()}], core_ids=[0])
    return hand_back({n: np.asarray(r.results[0][f"out_{n}"]) for n in OUTS})
```

```python
import concourse.bass as bass
import numpy as np
from concourse import mybir

F32 = mybir.dt.float32
F32R = mybir.dt.float32r
I32 = mybir.dt.int32
U32 = mybir.dt.uint32
ALU = mybir.AluOpType
ACT = mybir.ActivationFunctionType
X = mybir.AxisListType.X

P = 128
D = 1024
KC = D // P
SEQ = 256
NB = 8
T = SEQ + NB
NT = SEQ // P
DEPTH = 2
PAGE = 128
NPAGE = 8
HEADS = 8
ROPE = 32
LORA = 256
CACHE = LORA + ROPE
MLA_SCALE = 96 ** -0.5
RW_CH = 14
FF = 2816
NE = 8
FE = 3584
SLOT = KC * 512
RING_KEPT = 2
RING = 6
UNIT = 2048
MOE_RING = 7
MOE_SPLIT = 3
MOE_UP = 28
MOE_UNITS = 42
NSEQ = 1 + NB
MAX_TURNS = 2 * T // P + NE
EPS = 1e-6
LN_EPS = 64e-5
DECAY = -float(np.exp(-0.5))
LEVELS = (1, 2, 4, 8, 16, 32, 64)


def columns(widths):
    at, out = 0, {}
    for name, n in widths:
        out[name] = (at, at + n)
        at += n
    return out, at


VEC, NVEC = columns([("norm_attn", 8), ("norm_ffn", 8), ("norm_final", 8), ("b_ada", 48), ("q_norm", 2),
                     ("kv_norm", 2), ("mu", 14), ("a0", 4), ("k_k", 4), ("k_a", 4), ("r_k", 4), ("ln_w", 4),
                     ("ln_b", 4), ("conv_w", 32), ("conv_b", 8), ("d", 4), ("ssm_norm", 4), ("dt_bias", 1),
                     ("a_log", 1), ("router_b", 8)])
SMALL, NSMALL = columns([("w_kr", 1024), ("w_dt", 64), ("router", 64)])
MLA_W, NMLA = columns([("w_uq", 1536), ("w_uk", 1024), ("w_uv", 1024), ("w_ukT", 2048)])
RWKV_W, NRWKV = columns([("w2", 512), ("a2", 512), ("g2", 512)])
CONST, NCONST = columns([("ident", 128), ("ones", 128), ("block_ones", 128), ("decay_tri", 129), ("decay_id", 8),
                         ("levels", 7 * 128), ("strict", 128), ("upto", 128), ("causal", 128), ("fold", 64),
                         ("rotate", 128), ("cos", T), ("sin", T), ("spread", 512), ("eps", 1), ("ln_eps", 1), ("expert_ids", 8), ("slot_ids", 128)])


class Steps:

    def __init__(self, nc, name, book):
        self.sem, self.name, self.book, self.count = nc.alloc_semaphore(name), name, book, 0

    def did(self, *step, by=1):
        self.count += by
        self.book.setdefault((self.name, step), self.count)
        return self.sem, by

    def at(self, *step):
        return self.sem, self.book.get((self.name, step), 1)


class Arena:

    def __init__(self, tensor, at, size):
        self.tensor, self.next, self.end = tensor, at, at + size

    def take(self, *shape):
        n = int(np.prod(shape))
        assert self.next + n <= self.end, (self.next, n, self.end)
        ap = self.tensor[:, self.next:self.next + n]
        self.next += n
        if len(shape) == 2:
            ap = ap.rearrange("p (a b) -> p a b", a=shape[0])
        elif len(shape) == 3:
            ap = ap.rearrange("p (a b c) -> p a b c", a=shape[0], b=shape[1])
        elif len(shape) == 4:
            ap = ap.rearrange("p (a b c d) -> p a b c d", a=shape[0], b=shape[1], c=shape[2])
        return ap


def bc(ap, axis, n):
    v = ap.unsqueeze(axis)
    shape = list(v.shape)
    shape[axis] = n
    return v.broadcast_to(shape)


class LoopSteps:

    def __init__(self, nc, name, book):
        self.sem, self.name, self.book, self.count = nc.alloc_semaphore(name), name, book, 0

    def did(self, *step):
        self.count += 1
        self.book.setdefault((self.name, step), self.count)
        return self.sem, 1

    def ends(self):
        self.book.setdefault((self.name, "per_turn"), self.count)

    def at(self, n, *step):
        return self.sem, n * self.book.get((self.name, "per_turn"), 1) + self.book.get((self.name, step), 1)

    def serial(self, eng, n):
        def do(ins, *step):
            ins.then_inc(*self.did(*(step or ("step", self.count))))
            eng.wait_ge(self.sem, n * self.book.get((self.name, "per_turn"), 1) + self.count)
        return do


class StageSteps:

    def __init__(self, steps, layer):
        self.steps, self.layer = steps, layer

    def did(self, *step):
        return self.steps.did(self.layer, *(step or ("step", self.steps.count)))

    def at(self, *step):
        return self.steps.at(self.layer, *step)

    def serial(self, eng):
        def do(ins, *step):
            ins.then_inc(*self.did(*step))
            eng.wait_ge(self.steps.sem, self.steps.count)
        return do


class Stage:

    def __init__(self, k, kind, layer):
        self.k, self.kind, self.l = k, kind, layer
        k.stages.append(self)
        self.before = k.stages[-2] if len(k.stages) > 1 else None
        self.t, self.v, self.a, self.g = (StageSteps(k.steps(kind, e), layer) for e in ("tensor", "vector", "scalar", "pool"))

    def by(self, who):
        return {"tensor": self.t, "vector": self.v, "scalar": self.a, "pool": self.g}[who]

    def tensor(self, pe):
        pass

    def vector(self, dve):
        pass

    def scalar(self, act):
        pass

    def pool(self, g):
        pass

    def emit(self, who, eng):
        own, none = {"tensor": (self.tensor, Stage.tensor), "vector": (self.vector, Stage.vector),
                     "scalar": (self.scalar, Stage.scalar), "pool": (self.pool, Stage.pool)}[who]
        takes_part = own.__func__ is not none
        if self.before is not None and takes_part:
            for other in ("tensor", "vector", "scalar", "pool"):
                sem, value = self.before.by(other).at("end")
                if value:
                    eng.wait_ge(sem, value)
        start = self.by(who).steps.count
        if takes_part:
            own(eng)
        s = self.by(who).steps
        s.book.setdefault((s.name, (self.l, "end")), s.count if s.count > start else 0)


class Ring:

    def __init__(self, k):
        self.k, self.loads, self.released = k, [], 0

    def add(self, place, dst, src):
        self.loads.append((place, dst, src, self.k.guard))
        return len(self.loads) - 1

    def arrived(self, eng, n):
        place = self.loads[n][0]
        eng.wait_ge(self.k.slot_loaded[place], 16 * sum(load[0] == place for load in self.loads[:n + 1]))

    def release(self, n, steps):
        self.k.book.setdefault(("release", n), (steps.steps.name, steps.steps.count))

    def fill(self, eng):
        last, guarded = {}, None
        for n, (place, dst, src, guard) in enumerate(self.loads):
            if place in last:
                name, count = self.k.book.get(("release", last[place]), (None, 0))
                if name:
                    eng.wait_ge(self.k.named[name].sem, count)
            if place >= RING_KEPT and guard is not None and guard is not guarded:
                guard.load(eng)
                for who in ("tensor", "vector", "scalar", "pool"):
                    sem, value = guard.by(who).at("end")
                    if value:
                        eng.wait_ge(sem, value)
                guarded = guard
            last[place] = n
            eng.dma_start(dst, src).then_inc(self.k.slot_loaded[place], 16)


class Kernel:

    def __init__(self, nc, dram, out, book):
        self.nc, self.book, self.out = nc, book, out
        self.stages, self.named, self.stores, self.page_turn = [], {}, 0, 0
        self.turn, self.guard = 0, None
        size = nc.sbuf_bytes_remaining // 32 * 8
        self.sb = nc.alloc_sbuf_tensor("work", [P, size], F32)
        kept = Arena(self.sb, 0, size)
        self.x, self.h, self.root = kept.take(KC, T), kept.take(KC, T), kept.take(T)
        self.consts, self.vecs, self.small = kept.take(NCONST), kept.take(NVEC), kept.take(NSMALL)
        self.ada, self.scale_a, self.scale_f = kept.take(48, NSEQ), kept.take(8, NSEQ), kept.take(8, NSEQ)
        self.c_in, self.silu_c = kept.take(KC, NSEQ), kept.take(KC, NSEQ)
        self.shift_in, self.conv_in, self.lastrow = kept.take(RW_CH, NB), kept.take(8, NB, 3), kept.take(RW_CH, NSEQ)
        self.one_minus_ka, self.small_a, self.pool_mark, self.act_mark, self.gated_s = kept.take(4), kept.take(1), kept.take(1), kept.take(1), kept.take(NB)
        self.table = kept.take(64).bitcast(I32)
        self.logits, self.top_v, self.top_f = (kept.take(3, 8) for _ in range(3))
        self.top_i = kept.take(3, 8).bitcast(U32)
        self.top_e, self.top_w, self.one_hot = kept.take(3), kept.take(2, 3), kept.take(8)
        self.ring_at = kept.next
        self.work_at, self.work_size = self.ring_at + RING_KEPT * SLOT, (RING - RING_KEPT) * SLOT
        rest = Arena(self.sb, self.work_at + self.work_size, size - self.work_at - self.work_size)
        start = rest.next
        self.rw, self.xbc, self.xbc_s = rest.take(RW_CH, 1 + T), rest.take(8, 3 + SEQ), rest.take(8, NB, 4)
        self.z, self.dt_raw = rest.take(4, T), rest.take(T)
        self.mla_at, self.mla_size = self.work_at, rest.next - self.work_at
        self.qkv, self.kr, self.branches = rest.take(4, T), rest.take(T), rest.take(12, T)
        spare = Arena(self.sb, start, self.mla_at + self.mla_size - start)
        self.merge_mix, self.merge_gated, self.merge_gate = spare.take(KC, T), spare.take(2, T), spare.take(2, T)
        spare = Arena(self.sb, start, size - start)
        self.sq = Arena(self.sb, size - KC * T, KC * T).take(KC, T)
        spare = Arena(self.sb, start, size - start)
        self.hidden, self.silu_up = spare.take(FF // P, T), spare.take(2, T)
        moe = Arena(self.sb, -(-self.ring_at // 8) * 8, size - self.ring_at - 8)

        def named(name, *shape, dtype=F32R):
            at = nc.lookup_mloc(self.sb).addr + 4 * moe.next
            moe.take(int(np.prod(shape)))
            return nc.alloc_sbuf_tensor_at(name, [P, *shape], dtype, offset=at)
        self.units = named("units", MOE_RING, UNIT, dtype=F32)
        self.w_hi, self.w_lo = named("w_hi", MOE_SPLIT, UNIT), named("w_lo", MOE_SPLIT, UNIT)
        self.xg_hi, self.xg_lo = named("xg_hi", KC, P), named("xg_lo", KC, P)
        self.hid_hi, self.hid_lo = named("hid_hi", FE // P, P), named("hid_lo", FE // P, P)
        self.h_tok, self.sel, self.selg = moe.take(3, D), moe.take(3, P), moe.take(3, P)
        self.selT, self.hid, self.silu_g = moe.take(T), moe.take(2, 512), moe.take(2, 512)
        self.y_sb, self.moe_out = moe.take(D), moe.take(KC, T)
        self.mask, self.rank, self.gate_e = moe.take(NE, 3), moe.take(NE, 3), moe.take(NE, 3)
        self.turns, self.turn_expert = moe.take(NE), moe.take(MAX_TURNS)
        self.turns_i, self.turn_expert_i = moe.take(NE).bitcast(I32), moe.take(MAX_TURNS).bitcast(I32)
        self.bank = [nc.alloc_psum_tensor(f"bank{i}", [P, 512], F32) for i in range(8)]
        self.slot_loaded = [nc.alloc_semaphore(f"slot{i}_loaded") for i in range(RING)]
        (self.c_loaded, self.const_loaded, self.vec_loaded, self.small_loaded, self.shift_loaded, self.conv_loaded, self.rwkv_w_loaded,
         self.mla_w_loaded, self.wkv_loaded, self.ssm_loaded, self.stored) = (nc.alloc_semaphore(n) for n in (
             "c_loaded", "const_loaded", "vec_loaded", "small_loaded", "shift_loaded", "conv_loaded", "rwkv_w_loaded",
             "mla_w_loaded", "wkv_loaded", "ssm_loaded", "stored"))
        self.pages_loaded = [nc.alloc_semaphore(f"pages{i}_loaded") for i in range(2)]
        (self.x_in, self.consts_in, self.table_in, self.c_dram, self.vecs_in, self.small_in, self.shift_dram, self.conv_dram,
         self.rwkv_w, self.mla_w, self.wkv_in, self.ssm_in, self.cache, self.w_ada, self.w_in, self.w_branch, self.w_out,
         self.w1, self.w3, self.w2, self.e1, self.e3, self.e2) = (dram[n] for n in DRAM)
        self.page_regs = [nc.sync.alloc_register(f"page{i}") for i in range(4)]
        self.ring = Ring(self)
        self.moe_loaded = [nc.alloc_semaphore(f"unit{i}_loaded") for i in range(MOE_RING)]
        self.unit_split, self.unit_used = nc.alloc_semaphore("unit_split"), nc.alloc_semaphore("unit_used")

    def steps(self, kind, who):
        name = f"{kind}_{who}"
        if name not in self.named:
            self.named[name] = Steps(self.nc, name, self.book)
        return self.named[name]

    def loop_steps(self, name):
        return LoopSteps(self.nc, name, self.book)

    def next_place(self):
        self.turn += 1
        return (self.turn - 1) % RING

    def slot(self, place):
        return self.sb[:, self.ring_at + SLOT * place:self.ring_at + SLOT * place + SLOT]

    def c(self, name):
        return self.consts[:, CONST[name][0]:CONST[name][1]]

    def vec(self, layer, name):
        return self.vecs[:, VEC[name][0]:VEC[name][1]]


DRAM = ("x", "consts", "table", "c", "vecs", "small", "shift", "conv", "rwkv_w", "mla_w", "wkv", "ssm", "cache", "w_ada", "w_in",
        "w_branch", "w_out", "ffn_w1", "ffn_w3", "ffn_w2", "moe_w1", "moe_w3", "moe_w2")
OUTS = {"y": (P, KC, T), "ckv": (DEPTH, P, 2, T), "kpe": (DEPTH, ROPE, T), "shift": (DEPTH, P, RW_CH, NSEQ),
        "p_wkv": (DEPTH, P, 4, 64), "s_wkv": (DEPTH, P, 4, NB, 64), "p_conv": (DEPTH, P, 8, 3), "s_conv": (DEPTH, P, 8, NB, 3),
        "p_ssm": (DEPTH, P, 512), "s_ssm": (DEPTH, P, 4, NB, P)}


class Ada(Stage):

    def __init__(self, k, l):
        super().__init__(k, "ada", l)
        self.rows = k.h.rearrange("p c t -> p (c t)")[:, 0:2048].rearrange("p (i n) -> p i n", i=4)
        self.slots = []
        for n in range(12):
            place = k.next_place()
            dst = k.slot(place).rearrange("p (k n) -> p k n", k=KC)
            self.slots.append(k.ring.add(place, dst, k.w_ada[l].rearrange("(k p) n -> p k n", p=P)[:, :, 512 * n:512 * n + 512]))

    def tensor(self, pe):
        k, t, a = self.k, self.t, self.a
        if self.l == 0:
            pe.wait_ge(*k.loads.a.at("silu_c"))
            pe.wait_ge(k.const_loaded, 48)

        def turn(n):
            pe.wait_ge(*a.at("rows", n))
            for j in range(4):
                c = 4 * n + j
                mm = pe.transpose(k.bank[0][:, NSEQ * c:NSEQ * c + NSEQ], self.rows[0:NSEQ, n % 4, P * j:P * j + P], k.c("ident")[0:NSEQ, 0:NSEQ])
            mm.then_inc(*t.did("turned", n))
        for n, slot in enumerate(self.slots):
            k.ring.arrived(pe, slot)
            w = k.ring.loads[slot][1]
            if n >= 2:
                pe.wait_ge(*a.at("rows", n - 2))
            for kk in range(KC):
                mm = pe.matmul(k.bank[1 + n % 2][0:NSEQ, :], k.silu_c[:, kk, :], w[:, kk, :], start=kk == 0, stop=kk == KC - 1)
            mm.then_inc(*t.did("slot", n))
            k.ring.release(slot, t)
            if n:
                turn(n - 1)
        turn(11)

    def scalar(self, act):
        k = self.k
        for n in range(12):
            act.wait_ge(*self.t.at("slot", n))
            if n >= 4:
                act.wait_ge(*self.t.at("turned", n - 4))
            act.copy(self.rows[0:NSEQ, n % 4, :], k.bank[1 + n % 2][0:NSEQ, :]).then_inc(*self.a.did("rows", n))

    def vector(self, dve):
        k = self.k
        do = self.v.serial(dve)
        dve.wait_ge(k.vec_loaded, 16 * (self.l + 1))
        dve.wait_ge(*self.t.at("turned", 11))
        do(dve.tensor_tensor(k.ada[:, :, :], k.bank[0][:, 0:48 * NSEQ].rearrange("p (c s) -> p c s", s=NSEQ),
                             k.vec(self.l, "b_ada").unsqueeze(2).broadcast_to([P, 48, NSEQ]), ALU.add))
        for part, w, out in ((1, "norm_attn", k.scale_a), (4, "norm_ffn", k.scale_f)):
            do(dve.scalar_tensor_tensor(out=out[:, :, :], in0=k.ada[:, 8 * part:8 * part + 8, :], scalar=1.0,
                                        in1=k.vec(self.l, w).unsqueeze(2).broadcast_to([P, 8, NSEQ]), op0=ALU.add, op1=ALU.mult))


class Norm(Stage):

    def __init__(self, k, l, which):
        super().__init__(k, f"norm_{which}", l)
        self.which = which

    def scalar(self, act):
        k = self.k
        if self.l == 0:
            act.wait_ge(k.const_loaded, 48)
        act.activation(k.sq[:, :, :], k.x[:, :, :], ACT.Square).then_inc(*self.a.did("squares"))
        act.wait_ge(*self.t.at("sum"))
        act.activation(k.root[:, :], k.bank[1][:, 0:T], ACT.Sqrt, scale=1.0 / D, bias=k.c("eps")).then_inc(*self.a.did("root"))

    def tensor(self, pe):
        k = self.k
        pe.wait_ge(*self.a.at("squares"))
        for c in range(KC):
            mm = pe.matmul(k.bank[1][:, 0:T], k.c("ones"), k.sq[:, c, :], start=c == 0, stop=c == KC - 1)
        mm.then_inc(*self.t.did("sum"))

    def vector(self, dve):
        k = self.k
        do = self.v.serial(dve)
        dve.wait_ge(*self.a.at("root"))
        do(dve.reciprocal(k.root[:, :], k.root[:, :]))
        do(dve.tensor_tensor(k.h[:, :, :], k.x[:, :, :], bc(k.root[:, :], 1, KC), ALU.mult))
        if self.which == "final":
            do(dve.tensor_tensor(k.h[:, :, :], k.h[:, :, :], k.vec(self.l, "norm_final").unsqueeze(2).broadcast_to([P, KC, T]), ALU.mult))
            return
        part, scale = (0, k.scale_a) if self.which == "attn" else (3, k.scale_f)
        shift = k.ada[:, 8 * part:8 * part + 8, :]
        for c in range(KC):
            dve.tensor_scalar(k.h[:, c, 0:SEQ], k.h[:, c, 0:SEQ], scale[:, c, 0:1], shift[:, c, 0:1], ALU.mult, ALU.add)
        do(dve.tensor_tensor(k.h[:, :, SEQ:T], k.h[:, :, SEQ:T], scale[:, :, 1:NSEQ], ALU.mult))
        do(dve.tensor_tensor(k.h[:, :, SEQ:T], k.h[:, :, SEQ:T], shift[:, :, 1:NSEQ], ALU.add))


class Project(Stage):

    def __init__(self, k, l):
        super().__init__(k, "project", l)
        self.slots = []
        for c0, n in [(0, 512)] + [(544 + 512 * i, min(512, 3872 - 544 - 512 * i)) for i in range(7)]:
            place = k.next_place()
            dst = k.slot(place)[:, 0:KC * n].rearrange("p (k n) -> p k n", k=KC)
            self.slots.append((k.ring.add(place, dst, k.w_in[l].rearrange("(k p) n -> p k n", p=P)[:, :, c0:c0 + n]), n // P))

    def tiles(self):
        out, at = [], 0
        for s, (slot, n) in enumerate(self.slots):
            for t in range(n):
                name = ("qkv", at) if at < 4 else ("rw", at - 4) if at < 18 else ("z", at - 18) if at < 22 else ("xbc", at - 22)
                out.append((slot, t, name, t == n - 1))
                at += 1
        return [(None, "w_kr", ("kr", 0), False), (None, "w_dt", ("dt", 0), False)] + out

    def tensor(self, pe):
        k = self.k
        pe.wait_ge(k.small_loaded, 16 * (self.l + 1))
        for i, (slot, t, name, last) in enumerate(self.tiles()):
            if i >= 4:
                by = self.a if i % 2 else self.v
                pe.wait_ge(*by.at("tile", i - 4))
            m = 8 if name[0] == "dt" else P
            if slot is None:
                w = k.small[:, SMALL[t][0]:SMALL[t][1]].rearrange("p (k n) -> p k n", k=KC)
                cols = slice(0, m)
            else:
                k.ring.arrived(pe, slot)
                w, cols = k.ring.loads[slot][1], slice(P * t, P * t + P)
            for kk in range(KC):
                mm = pe.matmul(k.bank[i % 4][0:m, 0:T], w[:, kk, cols], k.h[:, kk, :], start=kk == 0, stop=kk == KC - 1)
            mm.then_inc(*self.t.did("tile", i))
            if last:
                k.ring.release(slot, self.t)

    def evict(self, eng, steps, odd):
        k = self.k
        tiles = self.tiles()
        for i, (_, _, (name, c), _) in enumerate(tiles):
            if i % 2 != odd:
                continue
            src = k.bank[i % 4]
            eng.wait_ge(*self.t.at("tile", i))
            copy = eng.copy if odd else eng.tensor_copy
            if name == "qkv":
                ins = copy(k.qkv[:, c, :], src[:, 0:T])
            elif name == "kr":
                ins = copy(k.kr[:, :], src[:, 0:T])
            elif name == "rw":
                ins = copy(k.rw[:, c, 1:1 + T], src[:, 0:T])
            elif name == "z":
                ins = copy(k.z[:, c, :], src[:, 0:T])
            elif name == "dt":
                ins = copy(k.dt_raw[0:8, :], src[0:8, 0:T])
            else:
                copy(k.xbc[:, c, 3:3 + SEQ], src[:, 0:SEQ])
                ins = copy(k.xbc_s[:, c, :, 3], src[:, SEQ:T])
            ins.then_inc(*steps.did("tile", i))

    def vector(self, dve):
        k = self.k
        dve.memset(k.rw[:, :, 0:1], 0.0)
        dve.memset(k.xbc[:, :, 0:3], 0.0)
        self.evict(dve, self.v, 0)

    def scalar(self, act):
        self.evict(act, self.a, 1)


class Rwkv(Stage):

    def __init__(self, k, l):
        super().__init__(k, "rwkv", l)
        ar = Arena(k.sb, k.work_at, k.work_size)
        self.w = ar.take(NRWKV)
        self.ep, self.en = ar.take(4, 129), ar.take(4, 129)
        self.ws = ar.take(4, NB)
        self.kk, self.kh, self.bb = ar.take(4, T), ar.take(4, T), ar.take(4, T)
        self.tilde = ar.take(2048)
        self.at, self.rt, self.bt, self.kt = (self.tilde[:, 512 * i:512 * i + 512].rearrange("p (c t) -> p c t", c=4) for i in range(4))
        self.tok = ar.take(3, 512)
        self.vt, self.btt, self.ktt = (self.tok[:, i, :] for i in range(3))
        self.AT, self.BT = ar.take(8, P), ar.take(8, P)
        self.inv = ar.take(4096)
        self.X, self.Y, self.Pm, self.M = (self.inv[:, 1024 * i:1024 * i + 1024].rearrange("p (h t) -> p h t", h=8) for i in range(4))
        self.RB, self.RK, self.W, self.U = self.X, self.Pm, self.M[:, 0:4, :], self.M[:, 4:8, :]
        self.a_steps = self.a
        self.S, self.S0 = ar.take(4, 64), ar.take(4, 64)
        self.sg = ar.take(T)
        self.av = self.inv[:, 0:4 * T].rearrange("p (c t) -> p c t", c=4)
        self.d = self.inv[:, 0:14 * T].rearrange("p (c t) -> p c t", c=14)
        self.tw = self.tok[:, 0, 0:T]
        self.sw = k.branches[:, 8:12, :].rearrange("p c t -> p (c t)")
        self.sws = k.branches[:, 0:4, :].rearrange("p c t -> p (c t)")[:, 0:512]
        self.st, self.t1 = (self.inv[:, 2048 * i:2048 * i + 2048].rearrange("p (c b i) -> p c b i", c=4, b=NB) for i in range(2))
        self.sq = self.tilde[:, 0:4 * T].rearrange("p (c t) -> p c t", c=4)
        self.g_sb = self.tilde[:, 0:4 * T].rearrange("p (c t) -> p c t", c=4)
        self.y = k.branches[:, 4:8, :]

    def pool(self, g):
        k, l = self.k, self.l
        g.dma_start(self.w[:, :], k.rwkv_w[l]).then_inc(k.rwkv_w_loaded, 16)
        g.wait_ge(*self.v.at("lastrow"))
        g.dma_start(k.out["shift"][l], k.lastrow[:, :, :]).then_inc(k.stored, 16)
        g.wait_ge(*self.v.at("state", NT - 1))
        g.dma_start(k.out["p_wkv"][l], self.S[:, :, :]).then_inc(k.stored, 16)
        g.wait_ge(*self.a_steps.at("y", NT - 1))
        g.dma_start(self.st, k.wkv_in[l]).then_inc(k.wkv_loaded, 16)
        g.wait_ge(*self.v.at("s_state"))
        g.dma_start(k.out["s_wkv"][l], self.st).then_inc(k.stored, 16)
        k.stores += 3
        g.wait_ge(k.stored, 16 * k.stores)
        g.memset(k.pool_mark[0:1, 0:1], 0.0).then_inc(*self.g.did("stored"))

    def tensor(self, pe):
        k, t = self.k, self.t
        w, c_ = self.w, k.c
        pe.wait_ge(k.rwkv_w_loaded, 16 * (self.l + 1))
        w2, a2, g2 = (w[:, RWKV_W[n][0]:RWKV_W[n][1]] for n in ("w2", "a2", "g2"))
        pe.wait_ge(*self.a.at("tanh"))
        for i in range(3):
            m = P if i < 2 else NB
            mm = pe.matmul(k.bank[i][0:m, :], self.tw[0:65, P * i:P * i + m], w2[0:65, :], start=True, stop=True)
        mm.then_inc(*t.did("w"))
        for c in range(4):
            if c:
                pe.wait_ge(*self.a.at("a", c - 1))
            mm = pe.matmul(k.bank[3][:, 0:T], a2[64:128, P * c:P * c + P], k.rw[64:128, 12, 1:1 + T], start=True, stop=True)
            mm.then_inc(*t.did("a", c))
        pe.wait_ge(*self.a.at("kk_sq"))
        for c in range(4):
            mm = pe.matmul(k.bank[4 + c][:, 0:T], c_("block_ones"), self.d[:, 4 + c, :], start=True, stop=True)
        mm.then_inc(*t.did("kk_norm"))
        pe.wait_ge(*self.a.at("sw"))
        for c in range(4):
            mm = pe.matmul(k.bank[0][:, NB * c:NB * c + NB], self.sws[0:NB, P * c:P * c + P],
                           c_("decay_id")[0:NB, :], start=True, stop=True)
        mm.then_inc(*t.did("ws"))
        for ti in range(NT):
            cols = slice(1 + P * ti, 1 + P * ti + P)
            if ti == 0:
                pe.wait_ge(*self.a.at("ws"))
            else:
                pe.wait_ge(*self.v.at("state", ti - 1))
                pe.wait_ge(*self.a.at("y", ti - 1))
            for c in range(4):
                mm = pe.matmul(k.bank[c // 2][:, 129 * (c % 2):129 * (c % 2) + 129],
                               self.sw[:, 512 * ti + P * c:512 * ti + P * c + P], c_("decay_tri"), start=True, stop=True)
            mm.then_inc(*t.did("logs", ti))
            for c in range(4):
                mm = pe.transpose(k.bank[2][:, P * c:P * c + P], k.rw[:, 8 + c, cols], c_("ident"))
            mm.then_inc(*t.did("v_tok", ti))
            pe.wait_ge(*self.v.at("tilde", ti))
            for c in range(4):
                pe.transpose(k.bank[3][:, P * c:P * c + P], self.bt[:, c, :], c_("ident"))
            for c in range(4):
                mm = pe.transpose(k.bank[4][:, P * c:P * c + P], self.kt[:, c, :], c_("ident"))
            mm.then_inc(*t.did("bk_tok", ti))
            for q, src in enumerate((self.bt, self.kt)):
                for g in range(2):
                    b = (5, 6, 7, 0)[2 * q + g]
                    if b == 0:
                        pe.wait_ge(*self.a.at("logs", ti))
                    r = slice(64 * g, 64 * g + 64)
                    for c in range(4):
                        mm = pe.matmul(k.bank[b][:, P * c:P * c + P], src[r, c, :], self.at[r, c, :], start=True, stop=True)
                    mm.then_inc(*t.did("AB", ti, q, g))
            for n in range(7):
                for g in range(2):
                    hs = range(4 * g, 4 * g + 4)
                    pe.wait_ge(*self.v.at("M", ti, n, g))
                    if n:
                        pe.wait_ge(*self.v.at("XY", ti, n - 1, g))
                    if n == 0 and g == 0:
                        pe.wait_ge(*self.a.at("bk_tok", ti))
                    for h in hs:
                        mm = pe.matmul(k.bank[1 + g][:, P * (h % 4):P * (h % 4) + P], self.M[:, h, :],
                                       c_("ident") if n == 0 else self.X[:, h, :], start=True, stop=True)
                    mm.then_inc(*t.did("MX", ti, n, g))
                if n == 0:
                    continue
                for g in range(2):
                    hs = range(4 * g, 4 * g + 4)
                    pe.wait_ge(*self.a.at("MX", ti, n, g))
                    if n < 6:
                        for h in hs:
                            pe.matmul(k.bank[3 + g][:, P * (h % 4):P * (h % 4) + P], self.Y[:, h, :], self.Pm[:, h, :],
                                      start=True, stop=True)
                    for h in hs:
                        mm = pe.matmul(k.bank[5 + g][:, P * (h % 4):P * (h % 4) + P], self.Pm[:, h, :], self.Y[:, h, :],
                                       start=True, stop=True)
                    mm.then_inc(*t.did("XMX", ti, n, g))
            pe.wait_ge(*self.v.at("XY", ti, 6, 0))
            pe.wait_ge(*self.v.at("XY", ti, 6, 1))
            for q, src in enumerate((self.bt, self.kt)):
                for g in range(2):
                    b = 3 + 2 * q + g
                    r = slice(64 * g, 64 * g + 64)
                    for c in range(4):
                        mm = pe.matmul(k.bank[b][:, P * c:P * c + P], src[r, c, :], self.rt[r, c, :], start=True, stop=True)
                    mm.then_inc(*t.did("R", ti, q, g))
            pe.wait_ge(*self.a.at("v_tok", ti))
            for n in range(8):
                g, c = n // 4, n % 4
                r, h = slice(64 * g, 64 * g + 64), 2 * c + g
                o = k.bank[(7, 2)[g]][:, 64 * c:64 * c + 64]
                if ti:
                    pe.matmul(o, self.at[r, c, :], self.S0[r, c, :], start=True, stop=False)
                mm = pe.matmul(o, self.BT[:, n, :], self.vt[:, 64 * h:64 * h + 64], start=not ti, stop=True)
            mm.then_inc(*t.did("W", ti))
            pe.wait_ge(*self.a.at("W", ti))
            W, U = self.W.rearrange("p a b -> p (a b)"), self.U.rearrange("p a b -> p (a b)")
            for n in range(8):
                mm = pe.matmul(k.bank[0][:, 64 * n:64 * n + 64], self.Y[:, n, :], W[:, 64 * n:64 * n + 64], start=True, stop=True)
            mm.then_inc(*t.did("U", ti))
            pe.wait_ge(*self.a.at("U", ti))
            pe.wait_ge(*self.v.at("R", ti))
            for n in range(8):
                g, c = n // 4, n % 4
                r, h = slice(64 * g, 64 * g + 64), 2 * c + g
                o = k.bank[1][r, P * c:P * c + P]
                if ti:
                    pe.matmul(o, self.S0[r, c, :], self.rt[r, c, :], start=True, stop=False)
                pe.matmul(o, U[:, 64 * n:64 * n + 64], self.RB[:, n, :], start=not ti, stop=False)
                mm = pe.matmul(o, self.vt[:, 64 * h:64 * h + 64], self.RK[:, n, :], start=False, stop=True)
            mm.then_inc(*t.did("y", ti))
            for n in range(8):
                g, c = n // 4, n % 4
                r, h = slice(64 * g, 64 * g + 64), 2 * c + g
                o = k.bank[2][r, 64 * c:64 * c + 64]
                pe.matmul(o, self.btt[:, 64 * h:64 * h + 64], U[:, 64 * n:64 * n + 64], start=True, stop=False)
                mm = pe.matmul(o, self.ktt[:, 64 * h:64 * h + 64], self.vt[:, 64 * h:64 * h + 64], start=False, stop=True)
            mm.then_inc(*t.did("state", ti))
        for n, key in enumerate(("s_kk", "s_v", "s_r")):
            pe.wait_ge(*self.v.at(key))
            for c in range(4):
                mm = pe.matmul(k.bank[4 * (n % 2) + c][:, :], c_("block_ones"), self.t1[:, c, :, :].rearrange("p b i -> p (b i)"),
                               start=True, stop=True)
            mm.then_inc(*t.did(key))
        pe.wait_ge(*self.v.at("y"))
        for c in range(4):
            mm = pe.matmul(k.bank[4 + c][:, 0:T], c_("block_ones"), self.y[:, c, :], start=True, stop=True)
        mm.then_inc(*t.did("mean"))
        pe.wait_ge(*self.a.at("y_sq"))
        for c in range(4):
            mm = pe.matmul(k.bank[c][:, 0:T], c_("block_ones"), self.sq[:, c, :], start=True, stop=True)
        mm.then_inc(*t.did("var"))
        pe.wait_ge(*self.v.at("bonus_in"))
        for c in range(4):
            mm = pe.matmul(k.bank[4 + c][:, 0:T], c_("block_ones"), self.bb[:, c, :], start=True, stop=True)
        mm.then_inc(*t.did("bonus"))
        pe.wait_ge(*self.v.at("ln"))
        for c in range(4):
            mm = pe.matmul(k.bank[c][:, 0:T], g2[:, P * c:P * c + P], self.sg[:, :], start=True, stop=True)
        mm.then_inc(*t.did("g"))

    def scalar(self, act):
        k, a, t, v = self.k, self.a, self.t, self.v
        act.wait_ge(*v.at("shifted"))
        act.activation(self.tw[0:64, :], k.rw[0:64, 12, 1:1 + T], ACT.Tanh).then_inc(*a.did("tanh_only"))
        act.wait_ge(*v.at("ones_row"))
        act.activation(self.sg[:, :], k.rw[:, 13, 1:1 + T], ACT.Sigmoid).then_inc(*a.did("tanh"))
        act.wait_ge(*t.at("w"))
        act.activation(self.sw[:, 0:512], k.bank[0][:, :], ACT.Sigmoid)
        act.activation(self.sw[:, 512:1024], k.bank[1][:, :], ACT.Sigmoid)
        act.activation(self.sws[0:NB, :], k.bank[2][0:NB, :], ACT.Sigmoid).then_inc(*a.did("sw"))
        for c in range(4):
            act.wait_ge(*t.at("a", c))
            act.activation(self.av[:, c, :], k.bank[3][:, 0:T], ACT.Sigmoid, bias=k.vec(self.l, "a0")[:, c:c + 1]).then_inc(*a.did("a", c))
        act.wait_ge(*v.at("kk_raw"))
        act.activation(self.d[:, 4:8, :], self.kk[:, :, :], ACT.Square).then_inc(*a.did("kk_sq"))
        act.wait_ge(*v.at("kk_max"))
        act.activation(self.d[:, 4:8, :], self.d[:, 4:8, :], ACT.Sqrt).then_inc(*a.did("kk_root"))
        act.wait_ge(*t.at("ws"))
        act.activation(self.ws[:, :, :], k.bank[0][:, 0:4 * NB].rearrange("p (c b) -> p c b", c=4), ACT.Exp).then_inc(*a.did("ws"))
        for ti in range(NT):
            act.wait_ge(*t.at("logs", ti))
            for q in range(2):
                src = k.bank[q][:, 0:258].rearrange("p (c t) -> p c t", c=2)
                act.activation(self.ep[:, 2 * q:2 * q + 2, :], src, ACT.Exp)
                ins = act.activation(self.en[:, 2 * q:2 * q + 2, :], src, ACT.Exp, scale=-1.0)
            ins.then_inc(*a.did("logs", ti))
            act.wait_ge(*t.at("v_tok", ti))
            act.copy(self.vt, k.bank[2][:, :]).then_inc(*a.did("v_tok", ti))
            act.wait_ge(*t.at("bk_tok", ti))
            act.copy(self.btt, k.bank[3][:, :])
            act.copy(self.ktt, k.bank[4][:, :]).then_inc(*a.did("bk_tok", ti))
            for n in range(1, 7):
                for g in range(2):
                    act.wait_ge(*t.at("MX", ti, n, g))
                    act.copy(self.Pm[:, 4 * g:4 * g + 4, :].rearrange("p h t -> p (h t)"), k.bank[1 + g][:, :]).then_inc(*a.did("MX", ti, n, g))
            act.wait_ge(*t.at("W", ti))
            W = self.W.rearrange("p a b -> p (a b)")
            act.copy(W[:, 0:256], k.bank[7][:, 0:256])
            act.copy(W[:, 256:512], k.bank[2][:, 0:256]).then_inc(*a.did("W", ti))
            act.wait_ge(*t.at("U", ti))
            act.mul(self.U.rearrange("p a b -> p (a b)"), k.bank[0][:, :], -1.0).then_inc(*a.did("U", ti))
            act.wait_ge(*t.at("y", ti))
            act.copy(self.y[:, :, P * ti:P * ti + P], k.bank[1][:, :].rearrange("p (c t) -> p c t", c=4)).then_inc(*a.did("y", ti))
        act.wait_ge(*v.at("centred"))
        act.activation(self.sq[:, :, :], self.y, ACT.Square).then_inc(*a.did("y_sq"))
        act.wait_ge(*t.at("var"))
        for c in range(4):
            ins = act.activation(self.sq[:, c, :], k.bank[c][:, 0:T], ACT.Sqrt, scale=1.0 / 64, bias=k.c("ln_eps"))
        ins.then_inc(*a.did("y_root"))

    def vector(self, dve):
        k, a, t, v, l = self.k, self.a, self.t, self.v, self.l
        do = v.serial(dve)
        rw = k.rw
        dve.tensor_copy(k.lastrow[:, :, 0:1], rw[:, :, SEQ:SEQ + 1])
        dve.tensor_copy(k.lastrow[:, :, 1:NSEQ], rw[:, :, 1 + SEQ:1 + T])
        dve.tensor_tensor(self.d[:, :, 0:SEQ], rw[:, :, 0:SEQ], rw[:, :, 1:1 + SEQ], ALU.subtract)
        dve.wait_ge(k.shift_loaded, 16 * (l + 1))
        do(dve.tensor_tensor(self.d[:, :, SEQ:T], k.shift_in[:, :, :], rw[:, :, 1 + SEQ:1 + T], ALU.subtract), "lastrow")
        for c in range(RW_CH):
            ins = dve.scalar_tensor_tensor(out=rw[:, c, 1:1 + T], in0=self.d[:, c, :], scalar=k.vec(l, "mu")[:, c:c + 1],
                                           in1=rw[:, c, 1:1 + T], op0=ALU.mult, op1=ALU.add)
        do(ins, "shifted")
        do(dve.memset(self.tw[64:65, :], 1.0), "ones_row")
        for c in range(4):
            ins = dve.tensor_scalar(self.kk[:, c, :], rw[:, 4 + c, 1:1 + T], k.vec(l, "k_k")[:, c:c + 1], None, ALU.mult)
        do(ins, "kk_raw")
        do(dve.tensor_scalar(k.one_minus_ka[:, :], k.vec(l, "k_a"), -1.0, 1.0, ALU.mult, ALU.add))
        dve.wait_ge(*t.at("kk_norm"))
        for c in range(4):
            ins = dve.tensor_scalar(self.d[:, 4 + c, :], k.bank[4 + c][:, 0:T], 1e-24, None, ALU.max)
        do(ins, "kk_max")
        dve.wait_ge(*a.at("a", 3))
        for c in range(4):
            ins = dve.tensor_scalar(self.kh[:, c, :], self.av[:, c, :], k.vec(l, "k_a")[:, c:c + 1], k.one_minus_ka[:, c:c + 1], ALU.mult, ALU.add)
        do(ins)
        do(dve.tensor_tensor(self.kh[:, :, :], self.kh[:, :, :], rw[:, 4:8, 1:1 + T], ALU.mult))
        dve.wait_ge(*a.at("kk_root"))
        do(dve.reciprocal(self.d[:, 4:8, :], self.d[:, 4:8, :]))
        do(dve.tensor_tensor(self.kk[:, :, :], self.kk[:, :, :], self.d[:, 4:8, :], ALU.mult))
        do(dve.tensor_tensor(self.bb[:, :, :], self.kk[:, :, :], self.av[:, :, :], ALU.mult))
        for ti in range(NT):
            s = slice(P * ti, P * ti + P)
            dve.wait_ge(*a.at("logs", ti))
            if ti:
                do(dve.tensor_tensor(self.S0[:, :, :], self.S[:, :, :], self.en[:, :, 0:1].broadcast_to([P, 4, 64]), ALU.mult))
            dve.tensor_tensor(self.at[:, :, :], self.kk[:, :, s], self.ep[:, :, 0:P], ALU.mult)
            dve.tensor_tensor(self.rt[:, :, :], rw[:, 0:4, 1 + P * ti:1 + P * ti + P], self.ep[:, :, 1:129], ALU.mult)
            dve.tensor_tensor(self.bt[:, :, :], self.bb[:, :, s], self.en[:, :, 1:129], ALU.mult)
            do(dve.tensor_tensor(self.kt[:, :, :], self.kh[:, :, s], self.en[:, :, 1:129], ALU.mult), "tilde", ti)
            for q, (dst, b) in enumerate(((self.AT, (5, 6)), (self.BT, (7, 0)))):
                for g in range(2):
                    dve.wait_ge(*t.at("AB", ti, q, g))
                    do(dve.tensor_tensor(dst[:, 4 * g:4 * g + 4, :], k.bank[b[g]][:, :].rearrange("p (h t) -> p h t", h=4),
                                         bc(k.c("strict"), 1, 4), ALU.mult))
            for n in range(7):
                mask = k.c("levels")[:, P * n:P * n + P]
                for g in range(2):
                    hs = slice(4 * g, 4 * g + 4)
                    if n:
                        dve.wait_ge(*t.at("MX", ti, n - 1, g))
                    do(dve.tensor_tensor(self.M[:, hs, :], self.AT[:, hs, :], bc(mask, 1, 4), ALU.mult), "M", ti, n, g)
                for g in range(2):
                    hs = slice(4 * g, 4 * g + 4)
                    if n == 0:
                        do(dve.tensor_tensor(self.Y[:, hs, :], bc(k.c("ident"), 1, 4), self.M[:, hs, :], ALU.subtract))
                        dve.wait_ge(*t.at("MX", ti, 0, g))
                        do(dve.tensor_tensor(self.X[:, hs, :], bc(k.c("ident"), 1, 4),
                                             k.bank[1 + g][:, :].rearrange("p (h t) -> p h t", h=4), ALU.subtract), "XY", ti, 0, g)
                        continue
                    dve.wait_ge(*t.at("XMX", ti, n, g))
                    if n < 6:
                        dve.tensor_tensor(self.X[:, hs, :], self.X[:, hs, :], k.bank[3 + g][:, :].rearrange("p (h t) -> p h t", h=4), ALU.subtract)
                    do(dve.tensor_tensor(self.Y[:, hs, :], self.Y[:, hs, :], k.bank[5 + g][:, :].rearrange("p (h t) -> p h t", h=4),
                                         ALU.subtract), "XY", ti, n, g)
            for q, dst in enumerate((self.RB, self.RK)):
                for g in range(2):
                    dve.wait_ge(*t.at("R", ti, q, g))
                    ins = dve.tensor_tensor(dst[:, 4 * g:4 * g + 4, :], k.bank[3 + 2 * q + g][:, :].rearrange("p (h t) -> p h t", h=4),
                                            bc(k.c("upto"), 1, 4), ALU.mult)
            do(ins, "R", ti)
            dve.wait_ge(*t.at("state", ti))
            new = k.bank[2][:, 0:256].rearrange("p (c i) -> p c i", c=4)
            if ti:
                do(dve.tensor_tensor(self.S0[:, :, :], self.S0[:, :, :], new, ALU.add))
                new = self.S0[:, :, :]
            do(dve.tensor_tensor(self.S[:, :, :], new, self.ep[:, :, 128:129].broadcast_to([P, 4, 64]), ALU.mult), "state", ti)
        sam = slice(SEQ, T)

        def along(x):
            return x.unsqueeze(3).broadcast_to([P, 4, NB, 64])
        fold = k.c("fold")
        rs = rw[:, 0:4, 1 + SEQ:1 + T]
        vs = rw[:, 8:12, 1 + SEQ:1 + T]
        dve.wait_ge(k.wkv_loaded, 16 * (l + 1))
        for c in range(4):
            ins = dve.tensor_tensor(self.t1[:, c], self.st[:, c], self.kk[:, c, sam].unsqueeze(2).broadcast_to([P, NB, 64]), ALU.mult)
        do(ins, "s_kk")
        for c in range(4):
            ins = dve.tensor_tensor(self.st[:, c], self.st[:, c], self.ws[:, c].unsqueeze(2).broadcast_to([P, NB, 64]), ALU.mult)
        do(ins)
        dve.wait_ge(*t.at("s_kk"))
        for c in range(4):
            ins = dve.tensor_tensor(self.t1[:, c], k.bank[c][:, :].rearrange("p (b i) -> p b i", b=NB),
                                    self.bb[:, c, sam].unsqueeze(2).broadcast_to([P, NB, 64]), ALU.mult)
        do(ins)
        do(dve.tensor_tensor(self.st, self.st, self.t1, ALU.subtract))
        for c in range(4):
            ins = dve.tensor_tensor(self.t1[:, c], bc(fold, 1, NB), vs[:, c, :].unsqueeze(2).broadcast_to([P, NB, 64]), ALU.mult)
        do(ins, "s_v")
        dve.wait_ge(*t.at("s_v"))
        for c in range(4):
            ins = dve.tensor_tensor(self.t1[:, c], k.bank[4 + c][:, :].rearrange("p (b i) -> p b i", b=NB),
                                    self.kh[:, c, sam].unsqueeze(2).broadcast_to([P, NB, 64]), ALU.mult)
        do(ins)
        do(dve.tensor_tensor(self.st, self.st, self.t1, ALU.add), "s_state")
        for c in range(4):
            ins = dve.tensor_tensor(self.t1[:, c], self.st[:, c], rs[:, c, :].unsqueeze(2).broadcast_to([P, NB, 64]), ALU.mult)
        do(ins, "s_r")
        dve.wait_ge(*t.at("s_r"))
        for c in range(4):
            ins = dve.tensor_tensor(self.t1[:, c], k.bank[c][:, :].rearrange("p (b i) -> p b i", b=NB), bc(fold, 1, NB), ALU.mult)
        do(ins)
        dve.wait_ge(*a.at("y", NT - 1))
        for c in range(4):
            ins = dve.tensor_reduce(self.y[:, c, sam], self.t1[:, c], X, ALU.add)
        do(ins, "y")
        dve.wait_ge(*t.at("mean"))
        for c in range(4):
            ins = dve.scalar_tensor_tensor(out=self.y[:, c, :], in0=k.bank[4 + c][:, 0:T], scalar=-1.0 / 64, in1=self.y[:, c, :],
                                           op0=ALU.mult, op1=ALU.add)
        do(ins, "centred")
        for c in range(4):
            ins = dve.scalar_tensor_tensor(out=self.bb[:, c, :], in0=rw[:, c, 1:1 + T], scalar=k.vec(l, "r_k")[:, c:c + 1],
                                           in1=self.kh[:, c, :], op0=ALU.mult, op1=ALU.mult)
        do(ins, "bonus_in")
        dve.wait_ge(*a.at("y_root"))
        do(dve.reciprocal(self.sq[:, :, :], self.sq[:, :, :]))
        do(dve.tensor_tensor(self.y, self.y, self.sq[:, :, :], ALU.mult))
        for c in range(4):
            ins = dve.tensor_scalar(self.y[:, c, :], self.y[:, c, :], k.vec(l, "ln_w")[:, c:c + 1], k.vec(l, "ln_b")[:, c:c + 1], ALU.mult, ALU.add)
        do(ins, "ln")
        dve.wait_ge(*t.at("bonus"))
        for c in range(4):
            ins = dve.tensor_tensor(self.bb[:, c, :], k.bank[4 + c][:, 0:T], rw[:, 8 + c, 1:1 + T], ALU.mult)
        do(ins)
        do(dve.tensor_tensor(self.y, self.y, self.bb[:, :, :], ALU.add))
        dve.wait_ge(*t.at("g"))
        for c in range(4):
            ins = dve.tensor_tensor(self.y[:, c, :], self.y[:, c, :], k.bank[c][:, 0:T], ALU.mult)
        do(ins)


class Ssm(Stage):

    def __init__(self, k, l):
        super().__init__(k, "ssm", l)
        ar = Arena(k.sb, k.work_at, k.work_size)
        self.cv = ar.take(8, T)
        self.rows = ar.take(9, T)
        self.tokens = ar.take(NT, 6, 8)
        self.dtx, self.dax = ar.take(4, NB), ar.take(4, NB)
        self.hs = ar.take(512)
        big = ar.take(8192)
        self.st, self.t1 = (big[:, 4096 * i:4096 * i + 4096].rearrange("p (c b n) -> p c b n", c=4, b=NB) for i in range(2))
        small = Arena(k.sb, ar.next - 8192, 8192)
        self.xt, self.bt = small.take(512), small.take(256)
        self.xd, self.xdd = small.take(512), small.take(512)
        self.gt = small.take(2, P)
        self.seg = small.take(8, P)
        self.ecs = small.take(8, P)
        self.csb = small.take(8, P)
        self.spread = self.st.rearrange("p c b n -> p (c b n)")
        self.y = k.branches[:, 8:12, :]

    def pool(self, g):
        k, l = self.k, self.l
        g.wait_ge(*self.v.at("conv"))
        g.dma_start(k.out["p_conv"][l], k.xbc[:, :, SEQ:SEQ + 3]).then_inc(k.stored, 16)
        for c in range(8):
            g.dma_start(k.out["s_conv"][l, :, c], k.xbc_s[:, c, :, 1:4]).then_inc(k.stored, 16)
        g.wait_ge(*self.v.at("state", NT - 1))
        g.dma_start(k.out["p_ssm"][l], self.hs[:, :]).then_inc(k.stored, 16)
        g.wait_ge(*self.t.at("y", NT - 1))
        g.wait_ge(*self.v.at("y_off"))
        g.dma_start(self.st, k.ssm_in[l]).then_inc(k.ssm_loaded, 16)
        g.wait_ge(*self.v.at("s_state"))
        g.dma_start(k.out["s_ssm"][l], self.st).then_inc(k.stored, 16)
        k.stores += 11
        g.wait_ge(k.stored, 16 * k.stores)
        g.memset(k.pool_mark[0:1, 0:1], 0.0).then_inc(*self.g.did("stored"))

    def scalar(self, act):
        k, a, t, v = self.k, self.a, self.t, self.v
        act.wait_ge(*v.at("dt_abs"))
        act.activation(self.rows[0:8, 1, :], self.rows[0:8, 1, :], ACT.Exp, scale=-1.0)
        act.activation(k.small_a[0:8, 0:1], k.vec(self.l, "a_log")[0:8, :], ACT.Exp).then_inc(*a.did("dt_exp"))
        act.wait_ge(*v.at("conv"))
        act.activation(self.t1.rearrange("p c b n -> p (c b n)")[:, 0:8 * T].rearrange("p (c t) -> p c t", c=8), self.cv[:, :, :],
                       ACT.Sigmoid).then_inc(*a.did("silu"))
        act.wait_ge(*v.at("dt"))
        act.activation(self.rows[0:8, 5, SEQ:T], self.rows[0:8, 4, SEQ:T], ACT.Exp).then_inc(*a.did("da"))
        for ti in range(NT):
            act.wait_ge(*v.at("cs", ti))
            act.activation(self.tokens[:, ti, 4:6, :], self.tokens[:, ti, 4:6, :], ACT.Exp).then_inc(*a.did("ecs", ti))
            act.wait_ge(*t.at("csb", ti))
            for q in range(2):
                ins = act.activation(self.ecs[:, 4 * q:4 * q + 4, :], k.bank[2 + q][:, :].rearrange("p (h t) -> p h t", h=4), ACT.Exp)
            ins.then_inc(*a.did("ecsb", ti))
            act.wait_ge(*v.at("seg", ti))
            act.activation(self.seg[:, :, :], self.seg[:, :, :], ACT.Exp).then_inc(*a.did("seg", ti))
        act.wait_ge(*v.at("skip"))
        act.activation(k.z[:, :, :], k.z[:, :, :], ACT.Silu).then_inc(*a.did("z"))
        act.wait_ge(*v.at("gated"))
        act.activation(self.cv[:, 0:4, :], self.y, ACT.Square).then_inc(*a.did("y_sq"))
        act.wait_ge(*t.at("ms"))
        for g in range(2):
            ins = act.activation(self.cv[:, 4 + g, :], k.bank[g][:, 0:T], ACT.Sqrt, scale=1.0 / 256, bias=k.c("eps"))
        ins.then_inc(*a.did("root"))

    def tensor(self, pe):
        k, t, v, a = self.k, self.t, self.v, self.a
        ident, ones, upto = k.c("ident"), k.c("ones"), k.c("upto")
        pe.wait_ge(*v.at("dt"))
        pe.wait_ge(*a.at("da"))
        for q, row in enumerate((3, 5)):
            for c in range(4):
                mm = pe.matmul(k.bank[0][:, 32 * q + NB * c:32 * q + NB * c + NB], k.c("spread")[0:8, P * c:P * c + P],
                               self.rows[0:8, row, SEQ:T], start=True, stop=True)
        mm.then_inc(*t.did("s_dt"))
        for ti in range(NT):
            s = slice(P * ti, P * ti + P)
            if ti:
                pe.wait_ge(*v.at("state", ti - 1))
                pe.wait_ge(*v.at("y", ti - 1))
            for q, row in enumerate((3, 4)):
                mm = pe.transpose(k.bank[1][:, 8 * q:8 * q + 8], self.rows[0:8, row, s], ident[0:8, 0:8])
            mm.then_inc(*t.did("tok", ti))
            pe.wait_ge(*v.at("tok", ti))
            pe.matmul(k.bank[1][:, 32:40], upto, self.tokens[:, ti, 1, :], start=True, stop=True)
            mm = pe.matmul(k.bank[1][:, 40:48], ones, self.tokens[:, ti, 1, :], start=True, stop=True)
            mm.then_inc(*t.did("cs", ti))
            for h in range(8):
                mm = pe.matmul(k.bank[2 + h // 4][:, P * (h % 4):P * (h % 4) + P],
                               self.tokens[:, ti, 1, h:h + 1].broadcast_to([P, P]), upto, start=True, stop=True)
            mm.then_inc(*t.did("csb", ti))
            if ti == 0:
                pe.wait_ge(*v.at("silu"))
            for g in range(2):
                mm = pe.matmul(k.bank[4][:, P * g:P * g + P], self.cv[:, 4 + g, s], self.cv[:, 6 + g, s], start=True, stop=True)
            mm.then_inc(*t.did("gt", ti))
            for c in range(4):
                pe.transpose(k.bank[5][:, P * c:P * c + P], self.cv[:, c, s], ident)
            for c in range(2):
                mm = pe.transpose(k.bank[6][:, P * c:P * c + P], self.cv[:, 4 + c, s], ident)
            mm.then_inc(*t.did("xb_tok", ti))
            pe.wait_ge(*v.at("mt", ti))
            for h in range(8):
                o = k.bank[7][64 * (h % 2):64 * (h % 2) + 64, P * (h // 2):P * (h // 2) + P]
                mm = pe.matmul(o, self.xd[:, 64 * h:64 * h + 64], self.seg[:, h, :], start=True, stop=not ti)
                if ti:
                    mm = pe.matmul(o, self.hs[:, 64 * h:64 * h + 64], self.ecs[:, h, :], start=False, stop=True)
            mm.then_inc(*t.did("y", ti))
            for g in range(2):
                mm = pe.matmul(k.bank[0][:, 256 * g:256 * g + 256], self.bt[:, P * g:P * g + P], self.xdd[:, 256 * g:256 * g + 256],
                               start=True, stop=True)
            mm.then_inc(*t.did("state", ti))
        for q in range(2):
            pe.wait_ge(*v.at("s_diag", q))
            for g in range(2):
                for n in range(2):
                    mm = pe.matmul(k.bank[4 * q + 2 * g + n][:, :], ones,
                                   self.t1[:, g, 4 * n:4 * n + 4, :].rearrange("p b n -> p (b n)"), start=True, stop=True)
            mm.then_inc(*t.did("s_spread", q))
        pe.wait_ge(*a.at("y_sq"))
        for g in range(2):
            for n in range(2):
                mm = pe.matmul(k.bank[g][:, 0:T], ones, self.cv[:, 2 * g + n, :], start=n == 0, stop=n == 1)
        mm.then_inc(*t.did("ms"))

    def vector(self, dve):
        k, a, t, v, l = self.k, self.a, self.t, self.v, self.l
        do = v.serial(dve)
        r = self.rows[0:8]
        do(dve.tensor_scalar(r[:, 0, :], k.dt_raw[0:8, :], k.vec(l, "dt_bias")[0:8, :], None, ALU.add))
        do(dve.tensor_scalar(r[:, 1, :], r[:, 0, :], -1.0, None, ALU.mult))
        do(dve.tensor_tensor(r[:, 1, :], r[:, 0, :], r[:, 1, :], ALU.max), "dt_abs")
        do(dve.tensor_scalar(r[:, 0, :], r[:, 0, :], 0.0, None, ALU.max))
        dve.wait_ge(k.conv_loaded, 16 * (l + 1))
        dve.tensor_copy(k.xbc_s[:, :, :, 0:3].rearrange("p c b i -> p (c b) i"), k.conv_in[:, :, :, :].rearrange("p c b i -> p (c b) i"))
        cw = k.vec(l, "conv_w")
        for i in range(4):
            for c in range(8):
                wt = cw[:, 8 * i + c:8 * i + c + 1]
                if i == 0:
                    ins = dve.tensor_scalar(self.cv[:, c, 0:SEQ], k.xbc[:, c, 0:SEQ], wt, None, ALU.mult)
                else:
                    ins = dve.scalar_tensor_tensor(out=self.cv[:, c, 0:SEQ], in0=k.xbc[:, c, i:i + SEQ], scalar=wt,
                                                   in1=self.cv[:, c, 0:SEQ], op0=ALU.mult, op1=ALU.add)
            do(ins)
            for c in range(8):
                wt = cw[:, 8 * i + c:8 * i + c + 1]
                if i == 0:
                    ins = dve.tensor_scalar(self.cv[:, c, SEQ:T], k.xbc_s[:, c, :, 0], wt, None, ALU.mult)
                else:
                    ins = dve.scalar_tensor_tensor(out=self.cv[:, c, SEQ:T], in0=k.xbc_s[:, c, :, i], scalar=wt,
                                                   in1=self.cv[:, c, SEQ:T], op0=ALU.mult, op1=ALU.add)
            do(ins)
        do(dve.tensor_tensor(self.cv[:, :, :], self.cv[:, :, :], k.vec(l, "conv_b").unsqueeze(2).broadcast_to([P, 8, T]), ALU.add), "conv")
        dve.wait_ge(*a.at("dt_exp"))
        do(dve.tensor_scalar(r[:, 2, :], r[:, 1, :], 2.0, None, ALU.add))
        do(dve.reciprocal(r[:, 2, :], r[:, 2, :]))
        do(dve.tensor_tensor(r[:, 2, :], r[:, 2, :], r[:, 1, :], ALU.mult))
        do(dve.tensor_tensor(r[:, 3, :], r[:, 2, :], r[:, 2, :], ALU.mult))
        do(dve.tensor_scalar(r[:, 4, :], r[:, 3, :], 1.0 / 17, None, ALU.mult))
        for n in range(15, 1, -2):
            do(dve.scalar_tensor_tensor(out=r[:, 4, :], in0=r[:, 4, :], scalar=1.0 / n, in1=r[:, 3, :], op0=ALU.add, op1=ALU.mult))
        do(dve.scalar_tensor_tensor(out=r[:, 4, :], in0=r[:, 4, :], scalar=1.0, in1=r[:, 2, :], op0=ALU.add, op1=ALU.mult))
        do(dve.scalar_tensor_tensor(out=r[:, 3, :], in0=r[:, 4, :], scalar=2.0, in1=r[:, 0, :], op0=ALU.mult, op1=ALU.add))
        do(dve.tensor_scalar(r[:, 4, :], r[:, 3, :], k.small_a[0:8, 0:1], -1.0, ALU.mult, ALU.mult), "dt")
        dve.wait_ge(*a.at("silu"))
        do(dve.tensor_tensor(self.cv[:, :, :], self.cv[:, :, :], self.t1.rearrange("p c b n -> p (c b n)")[:, 0:8 * T].rearrange("p (c t) -> p c t", c=8), ALU.mult), "silu")
        dve.wait_ge(*t.at("s_dt"))
        dve.tensor_copy(self.dtx[:, :, :], k.bank[0][:, 0:32].rearrange("p (c b) -> p c b", c=4))
        do(dve.tensor_copy(self.dax[:, :, :], k.bank[0][:, 32:64].rearrange("p (c b) -> p c b", c=4)))
        for ti in range(NT):
            s = slice(P * ti, P * ti + P)
            tk = self.tokens[:, ti]
            dve.wait_ge(*t.at("tok", ti))
            do(dve.tensor_copy(tk[:, 0:2, :], k.bank[1][:, 0:16].rearrange("p (q h) -> p q h", q=2)), "tok", ti)
            dve.wait_ge(*t.at("cs", ti))
            do(dve.tensor_copy(tk[:, 2:4, :], k.bank[1][:, 32:48].rearrange("p (q h) -> p q h", q=2)))
            dve.tensor_copy(tk[:, 4, :], tk[:, 3, :])
            do(dve.tensor_tensor(tk[:, 5, :], tk[:, 3, :], tk[:, 2, :], ALU.subtract), "cs", ti)
            dve.wait_ge(*a.at("ecsb", ti))
            for q in range(2):
                ins = dve.tensor_tensor(self.seg[:, 4 * q:4 * q + 4, :], k.bank[2 + q][:, :].rearrange("p (h t) -> p h t", h=4),
                                        tk[:, 2, 4 * q:4 * q + 4].unsqueeze(2).broadcast_to([P, 4, P]), ALU.subtract)
            do(ins)
            do(dve.tensor_scalar(self.seg[:, :, :], self.seg[:, :, :], 0.0, None, ALU.min), "seg", ti)
            dve.wait_ge(*t.at("gt", ti))
            do(dve.tensor_tensor(self.gt[:, :, :], k.bank[4][:, 0:256].rearrange("p (g t) -> p g t", g=2), bc(k.c("upto"), 1, 2), ALU.mult))
            dve.wait_ge(*t.at("xb_tok", ti))
            dve.tensor_copy(self.bt[:, :], k.bank[6][:, 0:256])
            do(dve.tensor_tensor(self.xd[:, :].rearrange("p (h d) -> p h d", h=8), k.bank[5][:, :].rearrange("p (h d) -> p h d", h=8),
                                 tk[:, 0, :].unsqueeze(2).broadcast_to([P, 8, 64]), ALU.mult))
            dve.wait_ge(*a.at("ecs", ti))
            do(dve.tensor_tensor(self.xdd[:, :].rearrange("p (h d) -> p h d", h=8), self.xd[:, :].rearrange("p (h d) -> p h d", h=8),
                                 tk[:, 5, :].unsqueeze(2).broadcast_to([P, 8, 64]), ALU.mult))
            dve.wait_ge(*a.at("ecsb", ti))
            dve.wait_ge(*a.at("seg", ti))
            for g in range(2):
                hs = slice(4 * g, 4 * g + 4)
                dve.tensor_tensor(self.seg[:, hs, :], self.seg[:, hs, :], bc(self.gt[:, g, :], 1, 4), ALU.mult)
                ins = dve.tensor_tensor(self.ecs[:, hs, :], self.ecs[:, hs, :], bc(self.cv[:, 6 + g, s], 1, 4), ALU.mult)
            do(ins, "mt", ti)
            dve.wait_ge(*t.at("y", ti))
            do(dve.tensor_copy(self.y[:, :, s], k.bank[7][:, :].rearrange("p (c t) -> p c t", c=4)), "y", ti)
            dve.wait_ge(*t.at("state", ti))
            if ti:
                do(dve.tensor_tensor(self.hs[:, :].rearrange("p (h d) -> p h d", h=8), self.hs[:, :].rearrange("p (h d) -> p h d", h=8),
                                     tk[:, 4, :].unsqueeze(2).broadcast_to([P, 8, 64]), ALU.mult))
                do(dve.tensor_tensor(self.hs[:, :], self.hs[:, :], k.bank[0][:, :], ALU.add), "state", ti)
            else:
                do(dve.tensor_copy(self.hs[:, :], k.bank[0][:, :]), "state", ti)
        sam = slice(SEQ, T)
        do(dve.tensor_tensor(self.dtx[:, :, :], self.dtx[:, :, :], self.cv[:, 0:4, sam], ALU.mult), "y_off")
        for q, c0 in enumerate((4, 6)):
            for g in range(2):
                ins = dve.tensor_tensor(self.t1[:, g], bc(k.c("ident"), 1, NB), self.cv[:, c0 + g, sam].unsqueeze(2).broadcast_to([P, NB, P]), ALU.mult)
            do(ins, "s_diag", q)
            if q == 0:
                dve.wait_ge(k.ssm_loaded, 16 * (l + 1))
                for c in range(4):
                    ins = dve.tensor_tensor(self.st[:, c], self.st[:, c], self.dax[:, c].unsqueeze(2).broadcast_to([P, NB, P]), ALU.mult)
                do(ins)
            dve.wait_ge(*t.at("s_spread", q))
            for c in range(4):
                for n in range(2):
                    bs = slice(4 * n, 4 * n + 4)
                    src = k.bank[4 * q + 2 * (c // 2) + n][:, :].rearrange("p (b n) -> p b n", b=4)
                    other = self.dtx[:, c, bs].unsqueeze(2).broadcast_to([P, 4, P]) if q == 0 else self.st[:, c, bs, :]
                    ins = dve.tensor_tensor(self.t1[:, c, bs, :], src, other, ALU.mult)
            do(ins)
            if q == 0:
                do(dve.tensor_tensor(self.st, self.st, self.t1, ALU.add), "s_state")
        for c in range(4):
            ins = dve.tensor_reduce(self.y[:, c, sam], self.t1[:, c], X, ALU.add)
        do(ins)
        for c in range(4):
            ins = dve.scalar_tensor_tensor(out=self.y[:, c, :], in0=self.cv[:, c, :], scalar=k.vec(l, "d")[:, c:c + 1], in1=self.y[:, c, :],
                                           op0=ALU.mult, op1=ALU.add)
        do(ins, "skip")
        dve.wait_ge(*a.at("z"))
        do(dve.tensor_tensor(self.y, self.y, k.z[:, :, :], ALU.mult), "gated")
        dve.wait_ge(*a.at("root"))
        do(dve.reciprocal(self.cv[:, 4:6, :], self.cv[:, 4:6, :]))
        for c in range(4):
            ins = dve.tensor_tensor(self.y[:, c, :], self.y[:, c, :], self.cv[:, 4 + c // 2, :], ALU.mult)
        do(ins)
        for c in range(4):
            ins = dve.tensor_scalar(self.y[:, c, :], self.y[:, c, :], k.vec(l, "ssm_norm")[:, c:c + 1], None, ALU.mult)
        do(ins)


class Mla(Stage):
    GROUP = 2

    def __init__(self, k, l):
        super().__init__(k, "mla", l)
        ar = Arena(k.sb, k.mla_at, k.mla_size)
        self.w = ar.take(NMLA)
        self.q = ar.take(8, T)
        tmp_at = ar.next
        self.tmp = ar.take(6, T)
        self.kpe = ar.take(T)
        self.cache = [ar.take(self.GROUP, NPAGE, CACHE) for _ in range(2)]
        early = Arena(k.sb, ar.next - self.GROUP * NPAGE * CACHE, self.GROUP * NPAGE * CACHE)
        self.kn, self.vt = early.take(8, SEQ), early.take(NT, 512)
        late, ar = ar, Arena(k.sb, tmp_at, 6 * T)
        self.qabs = ar.take(2, NB, 8)
        self.qpe = ar.take(NB, 8)
        self.prod, self.prodpe = ar.take(2, NB, 8), ar.take(NB, 8)
        self.snew, self.olat = ar.take(NB, 8), ar.take(2, NB, 8)
        self.m1, self.mrow, self.diag, self.m, self.rsum = ar.take(16), ar.take(1), ar.take(16), ar.take(16), ar.take(16)
        self.ps = ar.take(self.GROUP * 64)
        ar = late
        self.mx, self.sm = ar.take(8), ar.take(8)
        self.s = ar.take(8 * SEQ)
        self.pt = ar.take(2, 8, P)
        self.kT = self.s.rearrange("p (c t) -> p c t", c=2)
        self.kpT = self.pt.rearrange("p a b c -> p (a b c)")[0:32, 0:1024]
        self.root = self.tmp[:, 4:6, :]

    def weights(self, name, n):
        return self.w[:, MLA_W[name][0]:MLA_W[name][1]].rearrange("p (c n) -> p c n", c=n)

    def load(self, sp):
        k, l = self.k, self.l
        for who in ("tensor", "vector", "scalar", "pool"):
            sp.wait_ge(*self.before.by(who).at("end"))
        sp.dma_start(self.w[:, :], k.mla_w[l]).then_inc(k.mla_w_loaded, 16)
        if l == 0:
            sp.wait_ge(k.const_loaded, 48)
        for i in range(NB // self.GROUP):
            if i == 1:
                sp.wait_ge(*self.v.at("prompt_out"))
            if i >= 2:
                sp.wait_ge(*self.t.at("pv", i - 2))
            for j in range(self.GROUP):
                for p in range(NPAGE):
                    reg = k.page_regs[k.page_turn % len(k.page_regs)]
                    k.page_turn += 1
                    n = (self.GROUP * i + j) * NPAGE + p
                    sp.reg_load(reg, k.table[0:1, n:n + 1])
                    page = sp.snap(reg, min_val=0, max_val=k.cache.shape[1] - 1)
                    sp.dma_start(self.cache[i % 2][:, j, p, :], k.cache[l, bass.ds(page, 1)].rearrange("o s c -> (o s) c")).then_inc(k.pages_loaded[i % 2], 16)

    def pool(self, g):
        k, l = self.k, self.l
        g.wait_ge(*self.v.at("ckv"))
        g.dma_start(k.out["ckv"][l], k.qkv[:, 2:4, :]).then_inc(k.stored, 16)
        g.wait_ge(*self.v.at("pe"))
        g.dma_start(k.out["kpe"][l], self.kpe[0:32, :]).then_inc(k.stored, 16)
        k.stores += 2
        g.wait_ge(k.stored, 16 * k.stores)
        g.memset(k.pool_mark[0:1, 0:1], 0.0).then_inc(*self.g.did("stored"))

    def tensor(self, pe):
        k, t, v, a = self.k, self.t, self.v, self.a
        ident, ones = k.c("ident"), k.c("ones")
        w_uq, w_uk, w_uv, w_ukT = (self.weights(n, c) for n, c in (("w_uq", 2), ("w_uk", 2), ("w_uv", 2), ("w_ukT", 8)))
        pe.wait_ge(*a.at("latent_sq"))
        for g in range(2):
            for n in range(2):
                mm = pe.matmul(k.bank[g][:, 0:T], ones, self.tmp[:, 2 * g + n, :], start=n == 0, stop=n == 1)
        mm.then_inc(*t.did("latent_ms"))
        mm = pe.matmul(k.bank[2][:, 0:T], k.c("rotate"), k.kr[:, :], start=True, stop=True)
        mm.then_inc(*t.did("kr_rot"))
        pe.wait_ge(k.mla_w_loaded, 16 * (self.l + 1))
        pe.wait_ge(*v.at("ckv"))
        for h in range(8):
            if h >= 2:
                pe.wait_ge(*a.at("q", h - 2))
            for n in range(2):
                mm = pe.matmul(k.bank[4 + h % 2][0:96, 0:T], w_uq[:, n, 96 * h:96 * h + 96], k.qkv[:, n, :], start=n == 0, stop=n == 1)
            mm.then_inc(*t.did("q", h))
        pe.wait_ge(*v.at("pe_key"))
        for h in range(8):
            pe.wait_ge(*a.at("q", h))
            if h >= 2:
                pe.wait_ge(*v.at("q_rot", h - 2))
            mm = pe.matmul(k.bank[2 + h % 2][64:96, 0:T], k.c("rotate")[64:96, 64:96], self.q[64:96, h, :], start=True, stop=True,
                           tile_position=(64, 64))
            mm.then_inc(*t.did("q_rot", h))
        for h in range(8):
            if h == 4:
                pe.wait_ge(*a.at("q", 7))
            for n in range(2):
                mm = pe.matmul(k.bank[(6, 7, 4, 5)[h // 2]][0:64, SEQ * (h % 2):SEQ * (h % 2) + SEQ], w_uk[:, n, 64 * h:64 * h + 64],
                               k.qkv[:, 2 + n, 0:SEQ], start=n == 0, stop=n == 1)
        mm.then_inc(*t.did("keys"))
        for i in range(NT):
            for n in range(2):
                mm = pe.matmul(k.bank[i][:, :], k.qkv[:, 2 + n, P * i:P * i + P], w_uv[:, n, :], start=n == 0, stop=n == 1)
        mm.then_inc(*t.did("values"))
        pe.wait_ge(*v.at("pe"))
        pe.wait_ge(*a.at("kv"))
        for qi in range(NT):
            nk = P * (qi + 1)
            per = 512 // nk
            if qi:
                pe.wait_ge(*v.at("masked", qi - 1))
            for h in range(8):
                o = k.bank[2 + h // per][:, nk * (h % per):nk * (h % per) + nk]
                mm = pe.matmul(o, self.q[0:96, h, P * qi:P * qi + P], self.kn[0:96, h, 0:nk], start=True, stop=True)
            mm.then_inc(*t.did("scores", qi))
            pe.wait_ge(*v.at("probs", qi))
            s = self.s[:, 0:8 * nk].rearrange("p (h n) -> p h n", h=8)
            for ki in range(qi + 1):
                if ki:
                    pe.wait_ge(*a.at("pt", qi, ki - 1))
                for h in range(8):
                    mm = pe.transpose(k.bank[6 + h // 4][:, P * (h % 4):P * (h % 4) + P], s[:, h, P * ki:P * ki + P], ident)
                mm.then_inc(*t.did("pt", qi, ki))
            pe.wait_ge(*a.at("pt", qi, qi))
            for h in range(8):
                o = k.bank[h // 4][64 * (h % 2):64 * (h % 2) + 64, SEQ * (h // 2 % 2) + P * qi:SEQ * (h // 2 % 2) + P * qi + P]
                for ki in range(qi + 1):
                    mm = pe.matmul(o, self.vt[:, ki, 64 * h:64 * h + 64], self.pt[:, ki, h, :], start=ki == 0, stop=ki == qi)
            mm.then_inc(*t.did("out", qi))
        pe.wait_ge(*v.at("masked", NT - 1))
        for cc in range(2):
            for h in range(8):
                mm = pe.matmul(k.bank[2][:, 64 * cc + NB * h:64 * cc + NB * h + NB], w_ukT[0:64, h, P * cc:P * cc + P],
                               self.q[0:64, h, SEQ:T], start=True, stop=True)
        for h in range(8):
            mm = pe.matmul(k.bank[3][0:32, NB * h:NB * h + NB], ident[64:96, 64:96], self.q[64:96, h, SEQ:T], start=True, stop=True,
                           tile_position=(64, 0))
        mm.then_inc(*t.did("qabs"))
        pe.wait_ge(*v.at("prod"))
        o = k.bank[2][:, 128:192]
        for cc in range(2):
            pe.matmul(o, ones, self.prod[:, cc].rearrange("p b h -> p (b h)"), start=cc == 0, stop=False)
        mm = pe.matmul(o, ones[0:32, :], self.prodpe[0:32].rearrange("p b h -> p (b h)"), start=False, stop=True)
        mm.then_inc(*t.did("s_new"))
        pe.wait_ge(*v.at("prompt_out"))
        for i in range(NB // self.GROUP):
            pe.wait_ge(k.pages_loaded[i % 2], 16 * self.GROUP * NPAGE * (2 * self.l + i // 2 + 1))
            cache = self.cache[i % 2]
            if i:
                pe.wait_ge(*v.at("olat", i - 1))
            for j in range(self.GROUP):
                b = self.GROUP * i + j
                for p in range(NPAGE):
                    if (j or p >= 4) and p % 2 == 0:
                        pe.wait_ge(*a.at("kT", i, j if p >= 4 else j - 1, (p // 2 + 2) % 4))
                    for cc in range(2):
                        mm = pe.transpose(k.bank[4 + p // 2 % 2][:, 256 * cc + P * (p % 2):256 * cc + P * (p % 2) + P],
                                          cache[:, j, p, P * cc:P * cc + P], ident)
                    if p % 2:
                        mm.then_inc(*t.did("kT", i, j, p // 2))
                    if j and p % 4 == 0:
                        pe.wait_ge(*v.at("kpT", i, j - 1, p // 4))
                    mm = pe.transpose(k.bank[6 + p // 4][0:32, P * (p % 4):P * (p % 4) + P], cache[:, j, p, LORA:CACHE], ident)
                    if p % 4 == 3:
                        mm.then_inc(*t.did("kpT", i, j, p // 4))
                pe.wait_ge(*a.at("kT", i, j, 3))
                pe.wait_ge(*v.at("kpT", i, j, 1))
                for p in range(NPAGE):
                    o = k.bank[3][:, 64 * j + 8 * p:64 * j + 8 * p + 8]
                    for cc in range(2):
                        pe.matmul(o, self.kT[:, cc, P * p:P * p + P], self.qabs[:, cc, b, :], start=cc == 0, stop=False)
                    mm = pe.matmul(o, self.kpT[:, P * p:P * p + P], self.qpe[0:32, b, :], start=False, stop=True)
                mm.then_inc(*t.did("s_scores", i, j))
            pe.wait_ge(*v.at("m1", i))
            pe.transpose(k.bank[2][0:16, 192:320], self.m1[:, :], ident).then_inc(*t.did("m1", i))
            pe.wait_ge(*v.at("diag", i))
            pe.matmul(k.bank[2][:, 320:336], ones[0:16, :], self.diag[0:16, :], start=True, stop=True).then_inc(*t.did("max", i))
            pe.wait_ge(*v.at("rsum", i))
            pe.matmul(k.bank[2][:, 336:352], ones, self.rsum[:, :], start=True, stop=True).then_inc(*t.did("total", i))
            pe.wait_ge(*v.at("ps", i))
            ps = self.ps[:, :].rearrange("p (b n h) -> p b n h", b=self.GROUP, n=NPAGE)
            for cc in range(2):
                for j in range(self.GROUP):
                    o = k.bank[0][:, 16 * cc + 8 * j:16 * cc + 8 * j + 8]
                    for p in range(NPAGE):
                        mm = pe.matmul(o, cache[:, j, p, P * cc:P * cc + P], ps[:, j, p, :], start=p == 0, stop=p == NPAGE - 1)
            mm.then_inc(*t.did("pv", i))
        pe.wait_ge(*v.at("olat", NB // self.GROUP - 1))
        for h in range(8):
            o = k.bank[1][64 * (h % 2):64 * (h % 2) + 64, NB * (h // 2):NB * (h // 2) + NB]
            for cc in range(2):
                mm = pe.matmul(o, w_uv[:, cc, 64 * h:64 * h + 64], self.olat[:, cc, :, h], start=cc == 0, stop=cc == 1)
        mm.then_inc(*t.did("s_out"))

    def scalar(self, act):
        k, t, v, a = self.k, self.t, self.v, self.a
        act.activation(self.tmp[:, 0:4, :], k.qkv[:, :, :], ACT.Square).then_inc(*a.did("latent_sq"))
        act.wait_ge(*t.at("latent_ms"))
        for g in range(2):
            ins = act.activation(self.root[:, g, :], k.bank[g][:, 0:T], ACT.Sqrt, scale=1.0 / 256, bias=k.c("eps"))
        ins.then_inc(*a.did("latent_root"))
        for h in range(8):
            act.wait_ge(*t.at("q", h))
            act.copy(self.q[0:96, h, :], k.bank[4 + h % 2][0:96, 0:T]).then_inc(*a.did("q", h))
        act.wait_ge(*t.at("keys"))
        for n in range(4):
            act.copy(self.kn[0:64, 2 * n:2 * n + 2, :], k.bank[(6, 7, 4, 5)[n]][0:64, :].rearrange("p (h t) -> p h t", h=2))
        act.wait_ge(*t.at("values"))
        act.copy(self.vt[:, 0, :], k.bank[0][:, :])
        act.copy(self.vt[:, 1, :], k.bank[1][:, :]).then_inc(*a.did("kv"))
        for qi in range(NT):
            nk = P * (qi + 1)
            act.wait_ge(*v.at("less_max", qi))
            act.activation(self.s[:, 0:8 * nk], self.s[:, 0:8 * nk], ACT.Exp, scale=MLA_SCALE).then_inc(*a.did("exp", qi))
            for ki in range(qi + 1):
                act.wait_ge(*t.at("pt", qi, ki))
                for g in range(2):
                    ins = act.copy(self.pt[:, ki, 4 * g:4 * g + 4, :].rearrange("p h t -> p (h t)"), k.bank[6 + g][:, :])
                ins.then_inc(*a.did("pt", qi, ki))
        act.wait_ge(*t.at("out", NT - 1))
        for i in range(NB // self.GROUP):
            for j in range(self.GROUP):
                if i or j:
                    act.wait_ge(*t.at("s_scores", i if j else i - 1, j - 1 if j else self.GROUP - 1))
                for n in range(4):
                    act.wait_ge(*t.at("kT", i, j, n))
                    act.copy(self.kT[:, :, 256 * n:256 * n + 256], k.bank[4 + n % 2][:, :].rearrange("p (c t) -> p c t", c=2)).then_inc(*a.did("kT", i, j, n))
            act.wait_ge(*v.at("s_less_max", i))
            act.activation(self.ps[:, :], self.ps[:, :], ACT.Exp, scale=MLA_SCALE)
            act.activation(self.m[:, :], self.m[:, :], ACT.Exp, scale=MLA_SCALE).then_inc(*a.did("s_exp", i))

    def vector(self, dve):
        k, a, t, v, l = self.k, self.a, self.t, self.v, self.l
        do = v.serial(dve)
        dve.wait_ge(*a.at("latent_root"))
        do(dve.reciprocal(self.root[:, :, :], self.root[:, :, :]))
        for c in range(4):
            name = "q_norm" if c < 2 else "kv_norm"
            ins = dve.scalar_tensor_tensor(out=k.qkv[:, c, :], in0=k.qkv[:, c, :], scalar=k.vec(l, name)[:, c % 2:c % 2 + 1],
                                           in1=self.root[:, c // 2, :], op0=ALU.mult, op1=ALU.mult)
        do(ins, "ckv")
        cos, sin = k.c("cos"), k.c("sin")
        do(dve.tensor_tensor(self.kpe[:, :], k.kr[:, :], cos, ALU.mult))
        dve.wait_ge(*t.at("kr_rot"))
        do(dve.tensor_tensor(self.tmp[:, 0, :], k.bank[2][:, 0:T], sin, ALU.mult), "pe_key")
        do(dve.tensor_tensor(self.kpe[:, :], self.kpe[:, :], self.tmp[:, 0, :], ALU.add))
        rp = slice(64, 96)
        do(dve.tensor_copy(self.kn[rp, :, :], bc(self.kpe[rp, 0:SEQ], 1, 8)))
        for h in range(8):
            dve.wait_ge(*t.at("q_rot", h))
            dve.tensor_tensor(self.q[rp, h, :], self.q[rp, h, :], cos[rp, :], ALU.mult)
            do(dve.tensor_tensor(self.tmp[rp, h % 2, :], k.bank[2 + h % 2][rp, 0:T], sin[rp, :], ALU.mult), "q_rot", h)
            do(dve.tensor_tensor(self.q[rp, h, :], self.q[rp, h, :], self.tmp[rp, h % 2, :], ALU.add), *(("pe",) if h == 7 else ()))
        for qi in range(NT):
            nk = P * (qi + 1)
            per = 512 // nk
            s = self.s[:, 0:8 * nk].rearrange("p (h n) -> p h n", h=8)
            dve.wait_ge(*t.at("scores", qi))
            if qi:
                dve.wait_ge(*t.at("pt", qi - 1, qi - 1))
            for n in range(8 // per):
                hs = slice(per * n, per * n + per)
                src = k.bank[2 + n][:, :].rearrange("p (h n) -> p h n", h=per)
                if qi:
                    dve.tensor_copy(s[:, hs, 0:P * qi], src[:, :, 0:P * qi])
                ins = dve.tensor_tensor(s[:, hs, P * qi:nk], src[:, :, P * qi:nk], bc(k.c("causal"), 1, per), ALU.add)
            do(ins, "masked", qi)
            do(dve.tensor_reduce(self.mx[:, :], s, X, ALU.max))
            do(dve.tensor_tensor(s, s, self.mx[:, :].unsqueeze(2).broadcast_to([P, 8, nk]), ALU.subtract), "less_max", qi)
            dve.wait_ge(*a.at("exp", qi))
            do(dve.tensor_reduce(self.sm[:, :], s, X, ALU.add))
            do(dve.reciprocal(self.sm[:, :], self.sm[:, :]))
            do(dve.tensor_tensor(s, s, self.sm[:, :].unsqueeze(2).broadcast_to([P, 8, nk]), ALU.mult), "probs", qi)
        dve.wait_ge(*t.at("out", NT - 1))
        for c in range(4):
            ins = dve.tensor_copy(k.branches[:, c, 0:SEQ], k.bank[c // 2][:, SEQ * (c % 2):SEQ * (c % 2) + SEQ])
        do(ins, "prompt_out")
        dve.wait_ge(*t.at("qabs"))
        for cc in range(2):
            dve.tensor_copy(self.qabs[:, cc].rearrange("p b h -> p h b"), k.bank[2][:, 64 * cc:64 * cc + 64].rearrange("p (h b) -> p h b", h=8))
        do(dve.tensor_copy(self.qpe[0:32].rearrange("p b h -> p h b"), k.bank[3][0:32, 0:64].rearrange("p (h b) -> p h b", h=8)))
        sam = slice(SEQ, T)
        for cc in range(2):
            dve.tensor_tensor(self.prod[:, cc], self.qabs[:, cc], k.qkv[:, 2 + cc, sam].unsqueeze(2).broadcast_to([P, NB, 8]), ALU.mult)
        do(dve.tensor_tensor(self.prodpe[0:32], self.qpe[0:32], self.kpe[0:32, sam].unsqueeze(2).broadcast_to([32, NB, 8]), ALU.mult), "prod")
        dve.wait_ge(*t.at("s_new"))
        do(dve.tensor_copy(self.snew[:, :, :], k.bank[2][:, 128:192].rearrange("p (b h) -> p b h", b=NB)))
        for i in range(NB // self.GROUP):
            bs = slice(self.GROUP * i, self.GROUP * i + self.GROUP)
            for j in range(self.GROUP):
                if i or j:
                    dve.wait_ge(*t.at("s_scores", i if j else i - 1, j - 1 if j else self.GROUP - 1))
                for n in range(2):
                    dve.wait_ge(*t.at("kpT", i, j, n))
                    dve.tensor_copy(self.kpT[:, 512 * n:512 * n + 512], k.bank[6 + n][0:32, :]).then_inc(*v.did("kpT", i, j, n))
            dve.wait_ge(*t.at("s_scores", i, self.GROUP - 1))
            scores = k.bank[3][:, 0:128].rearrange("p (b n h) -> p b n h", b=self.GROUP, n=NPAGE)
            m1, m = (x.rearrange("p (b h) -> p b h", b=self.GROUP) for x in (self.m1, self.m))
            do(dve.tensor_reduce(m1, scores.rearrange("p b n h -> p b h n"), X, ALU.max), "m1", i)
            dve.wait_ge(*t.at("m1", i))
            do(dve.tensor_reduce(self.mrow[0:16, :], k.bank[2][0:16, 192:320], X, ALU.max))
            do(dve.tensor_scalar(self.diag[0:16, :], k.c("ident")[0:16, 0:16], self.mrow[0:16, 0:1], None, ALU.mult), "diag", i)
            dve.wait_ge(*t.at("max", i))
            do(dve.tensor_tensor(m, k.bank[2][:, 320:336].rearrange("p (b h) -> p b h", b=self.GROUP), self.snew[:, bs, :], ALU.max))
            ps = self.ps[:, :].rearrange("p (b n h) -> p b n h", b=self.GROUP, n=NPAGE)
            for j in range(self.GROUP):
                ins = dve.tensor_tensor(ps[:, j], scores[:, j], bc(m[:, j, :], 1, NPAGE), ALU.subtract)
            do(ins)
            do(dve.tensor_tensor(m, self.snew[:, bs, :], m, ALU.subtract), "s_less_max", i)
            dve.wait_ge(*a.at("s_exp", i))
            do(dve.tensor_reduce(self.rsum.rearrange("p (b h) -> p b h", b=self.GROUP), ps.rearrange("p b n h -> p b h n"), X, ALU.add), "rsum", i)
            dve.wait_ge(*t.at("total", i))
            do(dve.tensor_tensor(self.rsum[:, :], k.bank[2][:, 336:352], self.m[:, :], ALU.add))
            do(dve.reciprocal(self.rsum[:, :], self.rsum[:, :]))
            rs = self.rsum.rearrange("p (b h) -> p b h", b=self.GROUP)
            dve.tensor_tensor(self.m[:, :], self.m[:, :], self.rsum[:, :], ALU.mult)
            for j in range(self.GROUP):
                ins = dve.tensor_tensor(ps[:, j], ps[:, j], bc(rs[:, j, :], 1, NPAGE), ALU.mult)
            do(ins, "ps", i)
            for cc in range(2):
                ins = dve.tensor_tensor(self.olat[:, cc, bs, :], m, k.qkv[:, 2 + cc, SEQ + self.GROUP * i:SEQ + self.GROUP * (i + 1)].unsqueeze(2).broadcast_to([P, self.GROUP, 8]), ALU.mult)
            do(ins)
            dve.wait_ge(*t.at("pv", i))
            for cc in range(2):
                ins = dve.tensor_tensor(self.olat[:, cc, bs, :], self.olat[:, cc, bs, :],
                                        k.bank[0][:, 16 * cc:16 * cc + 16].rearrange("p (b h) -> p b h", b=self.GROUP), ALU.add)
            do(ins, "olat", i)
        dve.wait_ge(*t.at("s_out"))
        do(dve.tensor_copy(k.branches[:, 0:4, SEQ:T], k.bank[1][:, 0:32].rearrange("p (c b) -> p c b", c=4)))


class Merge(Stage):

    def __init__(self, k, l):
        super().__init__(k, "merge", l)
        self.mix, self.gated, self.gate = k.merge_mix, k.merge_gated, k.merge_gate
        self.slots = []
        for r in range(3):
            place = k.next_place()
            dst = k.slot(place).rearrange("p (c n) -> p c n", c=4)
            wb = k.ring.add(place, dst, k.w_branch[l, r].rearrange("(c p) n -> p c n", p=P))
            gs = []
            for i in range(2):
                place = k.next_place()
                dst = k.slot(place).rearrange("p (k n) -> p k n", k=KC)
                c0 = 3880 + D * r + 512 * i
                gs.append(k.ring.add(place, dst, k.w_in[l].rearrange("(k p) n -> p k n", p=P)[:, :, c0:c0 + 512]))
            self.slots.append((wb, gs))
        self.out_slots = []
        for i in range(2):
            place = k.next_place()
            dst = k.slot(place).rearrange("p (k n) -> p k n", k=KC)
            self.out_slots.append(k.ring.add(place, dst, k.w_out[l].rearrange("(k p) n -> p k n", p=P)[:, :, 512 * i:512 * i + 512]))

    def tensor(self, pe):
        k, t, v = self.k, self.t, self.v
        for r in range(3):
            wb, gs = self.slots[r]
            k.ring.arrived(pe, wb)
            w = k.ring.loads[wb][1]
            for d in range(KC):
                n = KC * r + d
                slot = gs[d // 4]
                k.ring.arrived(pe, slot)
                if n >= 4:
                    pe.wait_ge(*v.at("merged", n - 4))
                g = k.ring.loads[slot][1]
                for kk in range(KC):
                    mm = pe.matmul(k.bank[n % 4][:, 0:T], g[:, kk, P * (d % 4):P * (d % 4) + P], k.h[:, kk, :], start=kk == 0, stop=kk == KC - 1)
                mm.then_inc(*t.did("gate", n))
                if d % 4 == 3:
                    k.ring.release(slot, t)
                for c in range(4):
                    mm = pe.matmul(k.bank[4 + n % 4][:, 0:T], w[:, c, P * d:P * d + P], k.branches[:, 4 * r + c, :], start=c == 0, stop=c == 3)
                mm.then_inc(*t.did("branch", n))
            k.ring.release(wb, t)
        pe.wait_ge(*v.at("merged", 3 * KC - 1))
        for d in range(KC):
            slot = self.out_slots[d // 4]
            k.ring.arrived(pe, slot)
            w = k.ring.loads[slot][1]
            for kk in range(KC):
                mm = pe.matmul(k.bank[d][:, 0:T], w[:, kk, P * (d % 4):P * (d % 4) + P], self.mix[:, kk, :], start=kk == 0, stop=kk == KC - 1)
            mm.then_inc(*t.did("out", d))
            if d % 4 == 3:
                k.ring.release(slot, t)

    def scalar(self, act):
        k = self.k
        for n in range(3 * KC):
            act.wait_ge(*self.t.at("gate", n))
            if n >= 2:
                act.wait_ge(*self.v.at("merged", n - 2))
            act.activation(self.gate[:, n % 2, :], k.bank[n % 4][:, 0:T], ACT.Sigmoid).then_inc(*self.a.did("gate", n))

    def vector(self, dve):
        k, t, a, v = self.k, self.t, self.a, self.v
        do = v.serial(dve)
        for n in range(3 * KC):
            d = n % KC
            dve.wait_ge(*a.at("gate", n))
            dve.wait_ge(*t.at("branch", n))
            src = k.bank[4 + n % 4][:, 0:T]
            if n < KC:
                do(dve.tensor_tensor(self.mix[:, d, :], src, self.gate[:, n % 2, :], ALU.mult), "merged", n)
            else:
                do(dve.tensor_tensor(self.gated[:, n % 2, :], src, self.gate[:, n % 2, :], ALU.mult))
                do(dve.tensor_tensor(self.mix[:, d, :], self.mix[:, d, :], self.gated[:, n % 2, :], ALU.add), "merged", n)
        for d in range(KC):
            dve.wait_ge(*t.at("out", d))
            add_gated(k, dve, do, k.bank[d], d, 2)


def add_gated(k, dve, do, src, d, part):
    gate = k.ada[:, 8 * part + d, :]
    do(dve.tensor_tensor(k.gated_s[:, :], src[:, SEQ:T], gate[:, 1:NSEQ], ALU.mult))
    dve.tensor_tensor(k.x[:, d, SEQ:T], k.x[:, d, SEQ:T], k.gated_s[:, :], ALU.add)
    do(dve.scalar_tensor_tensor(out=k.x[:, d, 0:SEQ], in0=src[:, 0:SEQ], scalar=gate[:, 0:1], in1=k.x[:, d, 0:SEQ],
                                op0=ALU.mult, op1=ALU.add))


class Experts(Stage):

    def __init__(self, k, l):
        super().__init__(k, "experts", l)
        self.w1, self.w3, self.w2 = k.e1[l // 2], k.e3[l // 2], k.e2[l // 2]
        self.lt, self.lv, self.la = (k.loop_steps(f"experts_loop_{w}") for w in ("tensor", "vector", "scalar"))
        k.experts = self

    def turns(self, eng, body, *before):
        k = self.k
        eng.wait_ge(*self.v.at("turns"))
        turns = eng.value_load(k.turns_i[0:1, NE - 1:NE], min_val=1, max_val=MAX_TURNS)
        for do in before:
            do()
        with eng.Fori(0, turns) as n:
            body(n, eng.value_load(k.turn_expert_i[0:1, bass.ds(n, 1)], min_val=0, max_val=NE - 1))

    def loaded(self, eng, n, s):
        eng.wait_ge(self.k.moe_loaded[s % MOE_RING], (MOE_UNITS // MOE_RING) * 16 * n + 16 * (s // MOE_RING + 1))

    def split(self, n, s):
        return self.k.unit_split, MOE_RING + n * MOE_UNITS + s + 1

    def place_free(self, n, s):
        return self.k.unit_split, n * MOE_UNITS + s + 1

    def used(self, n, s):
        return self.k.unit_used, MOE_SPLIT + n * MOE_UNITS + s + 1

    def split_free(self, n, s):
        return self.k.unit_used, n * MOE_UNITS + s + 1

    def sync(self, sp):
        k = self.k

        def body(n, e):
            w1, w3, w2 = (w[bass.ds(e, 1)].rearrange("o (k p) n -> p (o k) n", p=P) for w in (self.w1, self.w3, self.w2))
            for s in range(MOE_UNITS):
                dst = k.units[:, s % MOE_RING, :]
                if s < MOE_UP:
                    f, q, half = s // 4, s // 2 % 2, s % 2
                    src = (w1, w3)[q][:, 4 * half:4 * half + 4, 512 * f:512 * f + 512]
                    dst = dst.rearrange("p (k n) -> p k n", k=4)
                else:
                    src = w2[:, 2 * (s - MOE_UP):2 * (s - MOE_UP) + 2, :]
                    dst = dst.rearrange("p (k n) -> p k n", k=2)
                sp.wait_ge(*self.place_free(n, s))
                sp.dma_start(dst, src).then_inc(k.moe_loaded[s % MOE_RING], 16)
        self.turns(sp, body)

    def tensor(self, pe):
        k, t, v, a = self.k, self.t, self.v, self.a
        ident, ones = k.c("ident"), k.c("ones")
        router = k.small[:, SMALL["router"][0]:SMALL["router"][1]].rearrange("p (k e) -> p k e", k=KC)
        for i in range(3):
            m = P if i < 2 else NB
            for kk in range(KC):
                mm = pe.matmul(k.bank[0][0:m, 8 * i:8 * i + 8], k.h[:, kk, P * i:P * i + m], router[:, kk, :], start=kk == 0, stop=kk == KC - 1)
        mm.then_inc(*t.did("logits"))
        for i in range(3):
            m = P if i < 2 else NB
            for c in range(KC):
                mm = pe.transpose(k.bank[1 + 2 * i + c // 4][0:m, P * (c % 4):P * (c % 4) + P], k.h[:, c, P * i:P * i + m], ident)
            mm.then_inc(*t.did("h_tok", i))
        pe.wait_ge(*v.at("mask"))
        for i in range(3):
            m = P if i < 2 else NB
            o = k.bank[0][0:m, 32 * i:32 * i + 8]
            for j in range(i + 1):
                mj = P if j < 2 else NB
                w = (k.c("strict") if j == i else ones)[0:mj, 0:m]
                pe.matmul(o, w, k.mask[0:mj, :, j], start=j == 0, stop=j == i)
        for j in range(3):
            mj = P if j < 2 else NB
            mm = pe.matmul(k.bank[0][:, 96:104], ones[0:mj, :], k.mask[0:mj, :, j], start=j == 0, stop=j == 2)
        mm.then_inc(*t.did("rank"))

        def grant():
            pe.nop().then_inc(k.unit_used, MOE_SPLIT)

        def product(out, hi, lo, s, at, start, stop):
            w_hi, w_lo = (w[:, s % MOE_SPLIT, at:at + 512] for w in (k.w_hi, k.w_lo))
            pe.matmul(out, hi, w_hi, start=start, stop=False)
            pe.matmul(out, hi, w_lo, start=False, stop=False)
            return pe.matmul(out, lo, w_hi, start=False, stop=stop)

        def body(n, e):
            lt, lv, la = self.lt, self.lv, self.la
            pe.wait_ge(*lv.at(n, "sel"))
            for c in range(KC):
                for i in range(3):
                    m = P if i < 2 else NB
                    mm = pe.matmul(k.bank[(7, 4)[c // 4]][:, P * (c % 4):P * (c % 4) + P], k.h_tok[0:m, i, P * c:P * c + P], k.sel[0:m, i, :],
                                   start=i == 0, stop=i == 2)
                if c % 4 == 3:
                    mm.then_inc(*lt.did("gather", c // 4))
            for i in range(3):
                m = P if i < 2 else NB
                mm = pe.transpose(k.bank[5][:, P * i:P * i + m], k.selg[0:m, i, :], ident[0:m, 0:m])
            mm.then_inc(*lt.did("selT"))
            pe.wait_ge(*lv.at(n, "gather", 1))
            for f in range(8):
                for u in range(4 * f, 4 * f + 2):
                    pe.wait_ge(*self.split(n, u))
                    self.unit(pe, product, n, u)
                if f:
                    pe.wait_ge(*lv.at(n, "hid", f - 1))
                    if f > 1:
                        pe.wait_ge(*lv.at(n, "hid_split", f - 2))
                    for j in range(4):
                        mm = pe.transpose(k.bank[4][:, P * j:P * j + P], k.hid[:, (f - 1) % 2, P * j:P * j + P], ident)
                    mm.then_inc(*lt.did("hidT", f - 1))
                for u in range(4 * f + 2, 4 * f + 4):
                    pe.wait_ge(*self.split(n, u))
                    self.unit(pe, product, n, u)
            for u in range(32, MOE_UNITS):
                pe.wait_ge(*self.split(n, u))
                self.unit(pe, product, n, u)
            pe.wait_ge(*la.at(n, "y"))
            for c in range(KC):
                if c >= 2:
                    pe.wait_ge(*lv.at(n, "added", c - 2))
                pe.matmul(k.bank[(7, 0)[c % 2]][:, 0:T], k.y_sb[:, P * c:P * c + P], k.selT[:, :], start=True, stop=True).then_inc(*lt.did("back", c))
            pe.wait_ge(*lv.at(n, "added", KC - 1))
            lt.ends()
        self.turns(pe, body, grant)

    def unit(self, pe, product, n, u):
        k, lv = self.k, self.lv
        if u < MOE_UP:
            f, q, half = u // 4, u // 2 % 2, u % 2
            if f >= 2 and half == 0:
                pe.wait_ge(*lv.at(n, "hid", f - 2))
            for j in range(4):
                kk = 4 * half + j
                mm = product(k.bank[2 * q + f % 2][:, :], k.xg_hi[:, kk, :], k.xg_lo[:, kk, :], u, 512 * j, kk == 0, kk == KC - 1)
        else:
            if u == MOE_UP:
                pe.wait_ge(*lv.at(n, "selT"))
            if (u - MOE_UP) % 2 == 0:
                pe.wait_ge(*lv.at(n, "hid_split", (u - MOE_UP) // 2))
            for j in range(2):
                c = 2 * (u - MOE_UP) + j
                for d in range(2):
                    mm = product(k.bank[5 + d][:, :], k.hid_hi[:, c, :], k.hid_lo[:, c, :], u, 1024 * j + 512 * d, c == 0, c == FE // P - 1)
        mm.then_inc(k.unit_used, 1)

    def scalar(self, act):
        k, t, a, v = self.k, self.t, self.a, self.v
        act.wait_ge(*v.at("diff"))
        act.activation(k.top_e[:, :], k.top_e[:, :], ACT.Exp).then_inc(*a.did("exp"))
        for i in range(3):
            m = P if i < 2 else NB
            act.wait_ge(*t.at("h_tok", i))
            for q in range(2):
                ins = act.copy(k.h_tok[0:m, i, 512 * q:512 * q + 512], k.bank[1 + 2 * i + q][0:m, :])
        ins.then_inc(*a.did("h_tok"))

        def body(n, e):
            lt, lv, la = self.lt, self.lv, self.la

            def round_units(*units):
                for u in units:
                    self.loaded(act, n, u)
                    act.wait_ge(*self.split_free(n, u))
                    act.copy(k.w_hi[:, u % MOE_SPLIT, :], k.units[:, u % MOE_RING, :]).then_inc(*la.did("w_hi", u))
            round_units(0, 1)
            for q in range(2):
                act.wait_ge(*lt.at(n, "gather", q))
                act.copy(k.xg_hi[:, 4 * q:4 * q + 4, :].rearrange("p c t -> p (c t)"), k.bank[(7, 4)[q]][:, :]).then_inc(*la.did("gather", q))
            for f in range(8):
                round_units(*range(4 * f + (2 if f == 0 else 0), 4 * f + 4))
                if f < 7:
                    act.wait_ge(*self.used(n, 4 * f + 1))
                    if f >= 2:
                        act.wait_ge(*lv.at(n, "hid", f - 2))
                    act.activation(k.silu_g[:, f % 2, :], k.bank[f % 2][:, :], ACT.Silu).then_inc(*la.did("silu", f))
                if f:
                    act.wait_ge(*lt.at(n, "hidT", f - 1))
                    act.copy(k.hid_hi[:, 4 * f - 4:4 * f, :].rearrange("p c t -> p (c t)"), k.bank[4][:, :]).then_inc(*la.did("hid_hi", f - 1))
            round_units(*range(32, MOE_UNITS))
            act.wait_ge(*self.used(n, MOE_UNITS - 1))
            act.copy(k.y_sb[:, 0:512], k.bank[5][:, :])
            act.copy(k.y_sb[:, 512:1024], k.bank[6][:, :]).then_inc(*la.did("y"))
            la.ends()
        self.turns(act, body)

    def vector(self, dve):
        k, t, a, v, l = self.k, self.t, self.a, self.v, self.l
        do = v.serial(dve)
        for x in (k.logits, k.mask, k.gate_e, k.rank):
            do(dve.memset(x[:, :, :], 0.0))
        dve.wait_ge(*t.at("logits"))
        for i in range(3):
            m = P if i < 2 else NB
            do(dve.tensor_tensor(k.logits[0:m, i, :], k.bank[0][0:m, 8 * i:8 * i + 8], k.vec(l, "router_b")[0:m, :], ALU.add))
        for i in range(3):
            do(dve.max(k.top_v[:, i, :], k.logits[:, i, :]))
            do(dve.max_index(k.top_i[:, i, :], k.top_v[:, i, :], k.logits[:, i, :]))
        do(dve.tensor_copy(k.top_f[:, :, :], k.top_i[:, :, :]))
        do(dve.tensor_tensor(k.top_e[:, :], k.top_v[:, :, 1], k.top_v[:, :, 0], ALU.subtract), "diff")
        for i in range(3):
            m = P if i < 2 else NB
            for c in range(2):
                do(dve.tensor_scalar(k.one_hot[0:m, :], k.c("expert_ids")[0:m, :], k.top_f[0:m, i, c:c + 1], None, ALU.is_equal))
                do(dve.tensor_tensor(k.mask[0:m, :, i], k.mask[0:m, :, i], k.one_hot[0:m, :], ALU.add), *(("mask",) if (i, c) == (2, 1) else ()))
        dve.wait_ge(*a.at("exp"))
        do(dve.tensor_scalar(k.top_w[:, 0, :], k.top_e[:, :], 1.0, None, ALU.add))
        do(dve.reciprocal(k.top_w[:, 0, :], k.top_w[:, 0, :]))
        do(dve.tensor_tensor(k.top_w[:, 1, :], k.top_w[:, 0, :], k.top_e[:, :], ALU.mult))
        for i in range(3):
            m = P if i < 2 else NB
            for c in range(2):
                do(dve.tensor_scalar(k.one_hot[0:m, :], k.c("expert_ids")[0:m, :], k.top_f[0:m, i, c:c + 1], k.top_w[0:m, c, i:i + 1], ALU.is_equal, ALU.mult))
                do(dve.tensor_tensor(k.gate_e[0:m, :, i], k.gate_e[0:m, :, i], k.one_hot[0:m, :], ALU.add))
        dve.wait_ge(*t.at("rank"))
        for i in range(3):
            m = P if i < 2 else NB
            do(dve.tensor_copy(k.rank[0:m, :, i], k.bank[0][0:m, 32 * i:32 * i + 8]))
        do(dve.tensor_scalar(k.turns[:, :], k.bank[0][:, 96:104], 0.0, None, ALU.is_gt))
        for full in (P, 2 * P):
            do(dve.scalar_tensor_tensor(out=k.turns[:, :], in0=k.bank[0][:, 96:104], scalar=float(full), in1=k.turns[:, :], op0=ALU.is_gt, op1=ALU.add))
        for e in range(1, NE):
            do(dve.tensor_tensor(k.turns[:, e:e + 1], k.turns[:, e:e + 1], k.turns[:, e - 1:e], ALU.add))
        do(dve.memset(k.turn_expert[:, :], 0.0))
        for e in range(NE):
            do(dve.scalar_tensor_tensor(out=k.turn_expert[:, :], in0=k.c("slot_ids")[:, 0:MAX_TURNS], scalar=k.turns[:, e:e + 1], in1=k.turn_expert[:, :],
                                        op0=ALU.is_ge, op1=ALU.add))
        do(dve.tensor_copy(k.turn_expert_i[:, :], k.turn_expert[:, :]))
        do(dve.memset(k.moe_out[:, :, :], 0.0))
        dve.wait_ge(*a.at("h_tok"))
        do(dve.tensor_copy(k.turns_i[:, :], k.turns[:, :]), "turns")

        def body(n, e):
            lt, lv, la = self.lt, self.lv, self.la
            do = lv.serial(dve, n)
            col = bass.ds(e, 1)
            for i in range(3):
                dve.tensor_scalar(k.sel[:, i, :], k.c("slot_ids"), k.rank[:, col, i], k.mask[:, col, i], ALU.is_equal, ALU.mult)
                ins = dve.tensor_scalar(k.selg[:, i, :], k.c("slot_ids"), k.rank[:, col, i], k.gate_e[:, col, i], ALU.is_equal, ALU.mult)
            do(ins, "sel")
            do(dve.tensor_scalar(k.rank[:, col, :], k.rank[:, col, :], -float(P), None, ALU.add))

            def split_units(*units):
                for u in units:
                    dve.wait_ge(*la.at(n, "w_hi", u))
                    ins = dve.tensor_tensor(k.w_lo[:, u % MOE_SPLIT, :], k.units[:, u % MOE_RING, :], k.w_hi[:, u % MOE_SPLIT, :].bitcast(F32), ALU.subtract)
                    ins.then_inc(k.unit_split, 1)
            split_units(0, 1)
            for q in range(2):
                dve.wait_ge(*la.at(n, "gather", q))
                hi, lo = (x[:, 4 * q:4 * q + 4, :].rearrange("p c t -> p (c t)") for x in (k.xg_hi, k.xg_lo))
                dve.tensor_tensor(lo, k.bank[(7, 4)[q]][:, :], hi.bitcast(F32), ALU.subtract).then_inc(*lv.did("gather", q))
            dve.wait_ge(*lt.at(n, "selT"))
            do(dve.tensor_copy(k.selT[:, :], k.bank[5][:, 0:T]), "selT")
            for f in range(8):
                if f:
                    split_units(4 * f, 4 * f + 1)
                    dve.wait_ge(*la.at(n, "silu", f - 1))
                    dve.wait_ge(*self.used(n, 4 * f - 1))
                    dve.tensor_tensor(k.hid[:, (f - 1) % 2, :], k.bank[2 + (f - 1) % 2][:, :], k.silu_g[:, (f - 1) % 2, :], ALU.mult).then_inc(*lv.did("hid", f - 1))
                split_units(4 * f + 2, 4 * f + 3)
                if f:
                    dve.wait_ge(*la.at(n, "hid_hi", f - 1))
                    hi, lo = (x[:, 4 * f - 4:4 * f, :].rearrange("p c t -> p (c t)") for x in (k.hid_hi, k.hid_lo))
                    dve.tensor_tensor(lo, k.bank[4][:, :], hi.bitcast(F32), ALU.subtract).then_inc(*lv.did("hid_split", f - 1))
            split_units(*range(32, MOE_UNITS))
            for c in range(KC):
                dve.wait_ge(*lt.at(n, "back", c))
                dve.tensor_tensor(k.moe_out[:, c, :], k.moe_out[:, c, :], k.bank[(7, 0)[c % 2]][:, 0:T], ALU.add).then_inc(*lv.did("added", c))
            dve.wait_ge(*lv.at(n, "added", KC - 1))
            lv.ends()
        def grant():
            dve.nop().then_inc(k.unit_split, MOE_RING)
        self.turns(dve, body, grant)
        for c in range(KC):
            add_gated(k, dve, do, k.moe_out[:, c, :], c, 5)


class Swiglu(Stage):

    def __init__(self, k, l, w1, w3, w2, width):
        super().__init__(k, "swiglu", l)
        self.nf = width // P
        self.half = self.nf // 2
        self.up, self.down = [], []
        for c0 in range(0, width, 512):
            n = min(512, width - c0)
            pair = []
            for w in (w1, w3):
                place = k.next_place()
                dst = k.slot(place)[:, 0:KC * n].rearrange("p (k n) -> p k n", k=KC)
                pair.append(k.ring.add(place, dst, w.rearrange("(k p) n -> p k n", p=P)[:, :, c0:c0 + n]))
            self.up.append((pair, n // P))
        for d in range(4):
            for i in range(2):
                place = k.next_place()
                dst = k.slot(place)[:, 0:self.half * 256].rearrange("p (f n) -> p f n", n=256)
                src = w2.rearrange("(f p) n -> p f n", p=P)[:, self.half * i:self.half * (i + 1), 256 * d:256 * d + 256]
                self.down.append(k.ring.add(place, dst, src))

    def tensor(self, pe):
        k, t, v, a = self.k, self.t, self.v, self.a
        f = 0
        for pair, n in self.up:
            for i in range(n):
                for q in range(2):
                    k.ring.arrived(pe, pair[q])
                    if f >= 2:
                        pe.wait_ge(*(a, v)[q].at("up", f - 2))
                    w = k.ring.loads[pair[q]][1]
                    for kk in range(KC):
                        mm = pe.matmul(k.bank[2 * (f % 2) + q][:, 0:T], w[:, kk, P * i:P * i + P], k.h[:, kk, :], start=kk == 0, stop=kk == KC - 1)
                    mm.then_inc(*t.did("up", f, q))
                    if i == n - 1:
                        k.ring.release(pair[q], t)
                f += 1
        pe.wait_ge(*v.at("up", self.nf - 1))
        for d in range(4):
            for i in range(2):
                slot = self.down[2 * d + i]
                k.ring.arrived(pe, slot)
                w = k.ring.loads[slot][1]
                if i == 0 and d >= 2:
                    pe.wait_ge(*v.at("down", d - 2))
                for j in range(2):
                    for f in range(self.half):
                        mm = pe.matmul(k.bank[4 + 2 * (d % 2) + j][:, 0:T], w[:, f, P * j:P * j + P], k.hidden[:, self.half * i + f, :],
                                       start=i == 0 and f == 0, stop=i == 1 and f == self.half - 1)
                mm.then_inc(*t.did("down", d, i))
                k.ring.release(slot, t)

    def scalar(self, act):
        k = self.k
        for f in range(self.nf):
            act.wait_ge(*self.t.at("up", f, 0))
            if f >= 2:
                act.wait_ge(*self.v.at("up", f - 2))
            act.activation(k.silu_up[:, f % 2, :], k.bank[2 * (f % 2)][:, 0:T], ACT.Silu).then_inc(*self.a.did("up", f))

    def vector(self, dve):
        k, t, a, v = self.k, self.t, self.a, self.v
        do = v.serial(dve)
        for f in range(self.nf):
            dve.wait_ge(*a.at("up", f))
            dve.wait_ge(*t.at("up", f, 1))
            ins = dve.tensor_tensor(k.hidden[:, f, :], k.bank[2 * (f % 2) + 1][:, 0:T], k.silu_up[:, f % 2, :], ALU.mult)
            ins.then_inc(*v.did("up", f))
        for d in range(4):
            dve.wait_ge(*t.at("down", d, 1))
            for j in range(2):
                add_gated(k, dve, do, k.bank[4 + 2 * (d % 2) + j], 2 * d + j, 5)
            v.steps.book.setdefault((v.steps.name, (v.layer, "down", d)), v.steps.count)


class LayerLoads(Stage):

    def __init__(self, k, l):
        super().__init__(k, "loads", l)
        k.loads = self

    def scalar(self, act):
        k, l = self.k, self.l
        if l == 0:
            act.dma_start(k.c_in[:, :, :], k.c_dram).then_inc(k.c_loaded, 16)
            act.dma_start(k.x[:, :, :], k.x_in).then_inc(k.const_loaded, 16)
            act.dma_start(k.consts[:, :], k.consts_in).then_inc(k.const_loaded, 16)
            act.dma_start(k.table[0:1, :], k.table_in).then_inc(k.const_loaded, 16)
        act.dma_start(k.vecs[:, :], k.vecs_in[l]).then_inc(k.vec_loaded, 16)
        act.dma_start(k.small[:, :], k.small_in[l]).then_inc(k.small_loaded, 16)
        act.dma_start(k.shift_in[:, :, :], k.shift_dram[l]).then_inc(k.shift_loaded, 16)
        act.dma_start(k.conv_in[:, :, :, :], k.conv_dram[l]).then_inc(k.conv_loaded, 16)
        if l == 0:
            act.wait_ge(k.c_loaded, 16)
            act.activation(k.silu_c[:, :, :], k.c_in[:, :, :], ACT.Silu).then_inc(*self.a.did("silu_c"))
        else:
            act.copy(k.act_mark[0:1, :], k.c("eps")[0:1, :]).then_inc(*self.a.did("begun"))


class Store(Stage):

    def __init__(self, k):
        super().__init__(k, "store", 0)

    def pool(self, g):
        k = self.k
        g.dma_start(k.out["y"], k.h[:, :, :]).then_inc(k.stored, 16)
        k.stores += 1
        g.wait_ge(k.stored, 16 * k.stores)



def build(nc, dram, out, book):
    k = Kernel(nc, dram, out, book)
    for l in range(DEPTH):
        LayerLoads(k, l)
        Ada(k, l)
        Norm(k, l, "attn")
        Project(k, l)
        k.turn = 0
        Rwkv(k, l)
        Ssm(k, l)
        k.guard = Mla(k, l)
        Merge(k, l)
        Norm(k, l, "ffn")
        if l % 2 == 0:
            Swiglu(k, l, k.w1[l // 2], k.w3[l // 2], k.w2[l // 2], FF)
        else:
            Experts(k, l)
    Norm(k, DEPTH - 1, "final")
    Store(k)
    with nc.Block() as block:

        @block.sync
        def _(sp):
            k.ring.fill(sp)
            k.experts.sync(sp)

        @block.tensor
        def _(pe):
            for stage in k.stages:
                stage.emit("tensor", pe)

        @block.scalar
        def _(act):
            for stage in k.stages:
                stage.emit("scalar", act)

        @block.vector
        def _(dve):
            for stage in k.stages:
                stage.emit("vector", dve)

        @block.gpsimd
        def _(g):
            for stage in k.stages:
                stage.emit("pool", g)
    return k


def constants():
    a = np.zeros((P, NCONST), np.float32)

    def put(name, v):
        a[:v.shape[0], CONST[name][0]:CONST[name][0] + v.shape[1]] = v
    i, j = np.arange(P)[:, None], np.arange(P)[None, :]
    put("ident", np.eye(P))
    put("ones", np.ones((P, P)))
    put("block_ones", (i // 64 == j // 64).astype(float))
    t = np.arange(P + 1)[None, :]
    put("decay_tri", DECAY * ((i < t).astype(float) - (i < P // 2)))
    put("decay_id", DECAY * np.eye(NB))
    put("levels", np.concatenate([((i // (2 * m) == j // (2 * m)) & (i // m % 2 == 0) & (j // m % 2 == 1)).astype(float) for m in LEVELS], 1))
    put("strict", (i < j).astype(float))
    put("upto", (i <= j).astype(float))
    put("causal", np.where(j <= i, 0.0, -1e30))
    put("fold", (i % 64 == np.arange(64)[None, :]).astype(float))
    rot = np.zeros((P, P))
    for m in range(P):
        half = m % ROPE < ROPE // 2
        rot[m + 16 if half else m - 16, m] = -1.0 if half else 1.0
    put("rotate", rot)
    freq = np.float32(10000.0) ** (-np.arange(16, dtype=np.float32) / np.float32(16))
    pos = np.concatenate([np.arange(SEQ), np.full(NB, PAGE * NPAGE)]).astype(np.float32)
    ang = (pos[None, :] * freq[np.arange(P) % 16][:, None]).astype(np.float32)
    put("cos", np.cos(ang.astype(np.float64)))
    put("sin", np.sin(ang.astype(np.float64)))
    put("spread", (np.arange(8)[:, None] == np.arange(512)[None, :] // 64).astype(float))
    put("eps", np.full((P, 1), EPS))
    put("ln_eps", np.full((P, 1), LN_EPS))
    put("slot_ids", np.broadcast_to(np.arange(128.0), (P, P)))
    put("expert_ids", np.broadcast_to(np.arange(8.0), (P, 8)))
    return a


def chunks(v):
    return np.swapaxes(v.reshape(v.shape[:-1] + (-1, P)), -1, -2)


def lay_out(i):
    i = {n: np.asarray(v) for n, v in i.items()}
    L = DEPTH
    x = np.concatenate([i["x_prompt"][0], i["x_sample"][:, 0]], 0)
    c = np.concatenate([i["c_prompt"], i["c_sample"]], 0)

    def fm(v):
        return v.T.reshape(-1, P, v.shape[0]).transpose(1, 0, 2)

    def rows8(v):
        out = np.zeros((L, P, 1), np.float32)
        out[:, :8, 0] = v
        return out
    parts = {
        "norm_attn": chunks(i["norm_attn"]), "norm_ffn": chunks(i["norm_ffn"]),
        "norm_final": np.broadcast_to(chunks(i["norm_final"]), (L, P, 8)), "b_ada": chunks(i["b_ada"]),
        "q_norm": chunks(i["mla_q_norm"]), "kv_norm": chunks(i["mla_kv_norm"]), "mu": chunks(i["rwkv_mu"]),
        "a0": chunks(i["rwkv_a0"]), "k_k": chunks(i["rwkv_k_k"]), "k_a": chunks(i["rwkv_k_a"]),
        "r_k": chunks(i["rwkv_r_k"].reshape(L, 512)), "ln_w": chunks(i["rwkv_ln_w"]), "ln_b": chunks(i["rwkv_ln_b"]),
        "conv_w": chunks(i["ssm_conv_w"]).transpose(0, 2, 1, 3).reshape(L, P, 32), "conv_b": chunks(i["ssm_conv_b"]),
        "d": chunks(np.repeat(i["ssm_d"], 64, axis=1)), "ssm_norm": chunks(i["ssm_norm"]),
        "dt_bias": rows8(i["ssm_dt_bias"]), "a_log": rows8(i["ssm_a_log"]),
        "router_b": np.broadcast_to(np.concatenate([np.zeros_like(i["moe_router_b"]), i["moe_router_b"]])[:, None, :], (L, P, 8)),
    }

    def by_k(w):
        return w.reshape(L, -1, P, w.shape[-1]).transpose(0, 2, 1, 3).reshape(L, P, -1)
    w_in = i["w_in"]
    router = np.concatenate([np.zeros_like(i["moe_router"]), i["moe_router"]])
    rwkv_w = np.zeros((L, P, NRWKV), np.float32)
    rwkv_w[:, 0:64, 0:512], rwkv_w[:, 64, 0:512] = i["rwkv_w2"], i["rwkv_w0"]
    rwkv_w[:, 64:128, 512:1024], rwkv_w[:, :, 1024:1536] = i["rwkv_a2"], i["rwkv_g2"]
    uq = i["mla_w_uq"]
    ukT = np.zeros((L, P, 2048), np.float32)
    ukT[:, 0:64] = i["mla_w_uk"].transpose(0, 3, 2, 1).reshape(L, 64, 2048)
    uk, uv = i["mla_w_uk"].reshape(L, LORA, 512), i["mla_w_uv"].reshape(L, LORA, 512)
    arrays = {
        "x": fm(x), "consts": constants(), "table": i["page_table"].reshape(1, 64), "c": fm(c),
        "vecs": np.concatenate([parts[n] for n in VEC], -1),
        "small": np.concatenate([by_k(np.tile(w_in[:, :, 512:544], (1, 1, 4))), by_k(w_in[:, :, 3872:3880]), by_k(router)], -1),
        "shift": chunks(i["state_rwkv_shift"]).transpose(0, 2, 3, 1),
        "conv": chunks(i["state_ssm_conv"]).transpose(0, 3, 4, 1, 2),
        "rwkv_w": rwkv_w, "mla_w": np.concatenate([by_k(uq), by_k(uk), by_k(uv), ukT], -1),
        "wkv": i["state_rwkv_wkv"].reshape(L, NB, 4, 2, 64, 64).transpose(0, 3, 5, 2, 1, 4).reshape(L, P, 4, NB, 64),
        "ssm": i["state_ssm"].reshape(L, NB, 4, 2, 64, P).transpose(0, 3, 4, 2, 1, 5).reshape(L, P, 4, NB, P),
        "cache": np.concatenate([i["cache_ckv"], i["cache_kpe"]], -1),
    }
    for n in DRAM:
        if n not in arrays:
            arrays[n] = i[n]
    return {n: np.ascontiguousarray(arrays[n]) for n in DRAM}


def hand_back(o):
    L = DEPTH

    def rows(v):
        return v.transpose(2, 1, 0).reshape(v.shape[2], -1)
    y = rows(o["y"])
    ckv = np.stack([rows(o["ckv"][l]) for l in range(L)])
    kpe = o["kpe"].transpose(0, 2, 1)
    shift = np.stack([rows(o["shift"][l]) for l in range(L)])
    p_wkv = o["p_wkv"].reshape(L, 2, 64, 4, 64).transpose(0, 3, 1, 4, 2).reshape(L, 1, 8, 64, 64)
    s_wkv = o["s_wkv"].reshape(L, 2, 64, 4, NB, 64).transpose(0, 4, 3, 1, 5, 2).reshape(L, NB, 8, 64, 64)
    p_conv = o["p_conv"].transpose(0, 3, 2, 1).reshape(L, 1, 3, D)
    s_conv = o["s_conv"].transpose(0, 3, 4, 2, 1).reshape(L, NB, 3, D)
    p_ssm = o["p_ssm"].reshape(L, P, 8, 64).transpose(0, 2, 3, 1).reshape(L, 1, 8, 64, P)
    s_ssm = o["s_ssm"].reshape(L, 2, 64, 4, NB, P).transpose(0, 4, 3, 1, 2, 5).reshape(L, NB, 8, 64, P)
    c = np.ascontiguousarray
    return (c(y[:SEQ][None]), c(y[SEQ:][:, None]), c(ckv[:, :SEQ].reshape(L, NT, PAGE, LORA)), c(kpe[:, :SEQ].reshape(L, NT, PAGE, ROPE)),
            c(shift[:, 0:1]), c(p_wkv), c(p_conv), c(p_ssm), c(ckv[:, SEQ:][:, :, None]), c(kpe[:, SEQ:][:, :, None]),
            c(shift[:, 1:]), c(s_wkv), c(s_conv), c(s_ssm))


def declare(nc, arrays):
    dram = {n: nc.dram_tensor(f"in_{n}", a.shape, mybir.dt.from_np(a.dtype), kind="ExternalInput").ap() for n, a in arrays.items()}
    out = {n: nc.dram_tensor(f"out_{n}", shape, F32, kind="ExternalOutput").ap() for n, shape in OUTS.items()}
    return dram, out


def kernel(**inputs):
    import concourse.bacc as bacc
    from concourse.bass_utils import run_bass_kernel_spmd as run

    arrays = lay_out(inputs)
    book = {}
    for _ in range(2):
        nc = bacc.Bacc("TRN2", target_bir_lowering=False, num_devices=1, dynamic_dma_scratch_size=4096)
        build(nc, *declare(nc, arrays), book)
    r = run(nc, [{f"in_{n}": a for n, a in arrays.items()}], core_ids=[0])
    return hand_back({n: np.asarray(r.results[0][f"out_{n}"]) for n in OUTS})
```

```python
import concourse.bass as bass
import numpy as np
from concourse import mybir

F32 = mybir.dt.float32
F32R = mybir.dt.float32r
I32 = mybir.dt.int32
U32 = mybir.dt.uint32
ALU = mybir.AluOpType
ACT = mybir.ActivationFunctionType
X = mybir.AxisListType.X

P = 128
D = 1024
KC = D // P
SEQ = 256
NB = 8
T = SEQ + NB
NT = SEQ // P
DEPTH = 2
PAGE = 128
NPAGE = 8
HEADS = 8
ROPE = 32
LORA = 256
CACHE = LORA + ROPE
MLA_SCALE = 96 ** -0.5
RW_CH = 14
FF = 2816
ROWS = 32
NE = 8
FE = 3584
SLOT = KC * 512
RING_KEPT = 2
RING = 6
CONV_PARTS = 9
ADA_PARTS = 12
ADA_AHEAD = 8
UNIT = 2048
MOE_RING = 7
MOE_SPLIT = 3
MOE_UP = 28
MOE_UNITS = 42
NEXT_TURN = 38
NSEQ = 1 + NB
KEPT = 10368 + 48 * NSEQ
MAX_TURNS = 2 * T // P + NE
EPS = 1e-6
LN_EPS = 64e-5
DECAY = -float(np.exp(-0.5))
LEVELS = (1, 2, 4, 8, 16, 32, 64)


def columns(widths):
    at, out = 0, {}
    for name, n in widths:
        out[name] = (at, at + n)
        at += n
    return out, at


VEC, NVEC = columns([("norm_attn", 8), ("norm_ffn", 8), ("norm_final", 8), ("b_ada", 48), ("q_norm", 2),
                     ("kv_norm", 2), ("mu", 14), ("a0", 4), ("k_k", 4), ("k_a", 4), ("r_k", 4), ("ln_w", 4),
                     ("ln_b", 4), ("conv_w", 32), ("conv_b", 8), ("d", 4), ("ssm_norm", 4), ("dt_bias", 1),
                     ("a_log", 1), ("router_b", 8)])
SMALL, NSMALL = columns([("w_kr", 1024), ("w_dt", 64), ("router", 64)])
MLA_W, NMLA = columns([("w_uq", 1536), ("w_uk", 1024), ("w_uv", 1024), ("w_ukT", 2048)])
RWKV_W, NRWKV = columns([("w2", 512), ("a2", 512), ("g2", 512)])
CONST, NCONST = columns([("ident", 128), ("ones", 128), ("block_ones", 128), ("decay_tri", 129), ("decay_id", 8),
                         ("levels", 7 * 128), ("strict", 128), ("upto", 128), ("causal", 128), ("fold", 64),
                         ("rotate", 128), ("cos", T), ("sin", T), ("spread", 512), ("eps", 1), ("ln_eps", 1), ("expert_ids", 8), ("slot_ids", 128), ("own", NB // 2 * NB)])


class Steps:

    def __init__(self, nc, name, book):
        self.sem, self.name, self.book, self.count = nc.alloc_semaphore(name), name, book, 0

    def did(self, *step, by=1):
        self.count += by
        self.book.setdefault((self.name, step), self.count)
        return self.sem, by

    def at(self, *step):
        return self.sem, self.book.get((self.name, step), 1)


class Arena:

    def __init__(self, tensor, at, size):
        self.tensor, self.next, self.end = tensor, at, at + size

    def take(self, *shape):
        n = int(np.prod(shape))
        assert self.next + n <= self.end, (self.next, n, self.end)
        ap = self.tensor[:, self.next:self.next + n]
        self.next += n
        if len(shape) == 2:
            ap = ap.rearrange("p (a b) -> p a b", a=shape[0])
        elif len(shape) == 3:
            ap = ap.rearrange("p (a b c) -> p a b c", a=shape[0], b=shape[1])
        elif len(shape) == 4:
            ap = ap.rearrange("p (a b c d) -> p a b c d", a=shape[0], b=shape[1], c=shape[2])
        return ap


def bc(ap, axis, n):
    v = ap.unsqueeze(axis)
    shape = list(v.shape)
    shape[axis] = n
    return v.broadcast_to(shape)


class LoopSteps:

    def __init__(self, nc, name, book):
        self.sem, self.name, self.book, self.count = nc.alloc_semaphore(name), name, book, 0

    def did(self, *step):
        self.count += 1
        self.book.setdefault((self.name, step), self.count)
        return self.sem, 1

    def ends(self):
        self.book.setdefault((self.name, "per_turn"), self.count)

    def at(self, n, *step):
        return self.sem, n * self.book.get((self.name, "per_turn"), 1) + self.book.get((self.name, step), 1)

    def serial(self, eng, n):
        def do(ins, *step):
            ins.then_inc(*self.did(*(step or ("step", self.count))))
            eng.wait_ge(self.sem, n * self.book.get((self.name, "per_turn"), 1) + self.count)
        return do


class StageSteps:

    def __init__(self, steps, layer):
        self.steps, self.layer = steps, layer

    def did(self, *step):
        return self.steps.did(self.layer, *(step or ("step", self.steps.count)))

    def at(self, *step):
        return self.steps.at(self.layer, *step)

    def serial(self, eng):
        def do(ins, *step):
            ins.then_inc(*self.did(*step))
            eng.wait_ge(self.steps.sem, self.steps.count)
        return do


class Stage:

    def __init__(self, k, kind, layer):
        self.k, self.kind, self.l = k, kind, layer
        k.stages.append(self)
        self.before = k.stages[-2] if len(k.stages) > 1 else None
        self.t, self.v, self.a, self.g = (StageSteps(k.steps(kind, e), layer) for e in ("tensor", "vector", "scalar", "pool"))

    def by(self, who):
        return {"tensor": self.t, "vector": self.v, "scalar": self.a, "pool": self.g}[who]

    def tensor(self, pe):
        pass

    def vector(self, dve):
        pass

    def scalar(self, act):
        pass

    def pool(self, g):
        pass

    def emit(self, who, eng):
        own, none = {"tensor": (self.tensor, Stage.tensor), "vector": (self.vector, Stage.vector),
                     "scalar": (self.scalar, Stage.scalar), "pool": (self.pool, Stage.pool)}[who]
        takes_part = own.__func__ is not none
        if self.before is not None and takes_part:
            for other in ("tensor", "vector", "scalar", "pool"):
                sem, value = self.before.by(other).at("end")
                if value:
                    eng.wait_ge(sem, value)
        start = self.by(who).steps.count
        if takes_part:
            own(eng)
        s = self.by(who).steps
        s.book.setdefault((s.name, (self.l, "end")), s.count if s.count > start else 0)


class Ring:

    def __init__(self, k):
        self.k, self.loads, self.released = k, [], 0

    def add(self, place, dst, src):
        self.loads.append((place, dst, src, self.k.guard))
        return len(self.loads) - 1

    def arrived(self, eng, n):
        place = self.loads[n][0]
        eng.wait_ge(self.k.slot_loaded[place], 16 * sum(load[0] == place for load in self.loads[:n + 1]))

    def release(self, n, steps):
        self.k.book.setdefault(("release", n), (steps.steps.name, steps.steps.count))

    def fill(self, eng):
        last, guarded, loaded = {}, None, None
        for n, (place, dst, src, guard) in enumerate(self.loads):
            if guard is not None and guard is not loaded:
                guard.load(eng)
                loaded = guard
            if place in last:
                name, count = self.k.book.get(("release", last[place]), (None, 0))
                if name:
                    eng.wait_ge(self.k.named[name].sem, count)
            if place >= RING_KEPT and guard is not None and guard is not guarded:
                for who in ("tensor", "vector", "scalar", "pool"):
                    sem, value = guard.by(who).at("end")
                    if value:
                        eng.wait_ge(sem, value)
                guarded = guard
            last[place] = n
            eng.dma_start(dst, src).then_inc(self.k.slot_loaded[place], 16)


class Kernel:

    def __init__(self, nc, dram, out, book):
        self.nc, self.book, self.out = nc, book, out
        self.stages, self.named, self.stores = [], {}, 0
        self.turn, self.guard = 0, None
        kept = Arena(nc.alloc_sbuf_tensor("kept", [P, KEPT], F32), 0, KEPT)
        size = nc.sbuf_bytes_remaining // 32 * 8
        self.sb = nc.alloc_sbuf_tensor("room", [P, size], F32)
        self.x, self.h, self.root = kept.take(KC, T), kept.take(KC, T), kept.take(T)
        self.consts, self.vecs, self.small = kept.take(NCONST), kept.take(NVEC), kept.take(NSMALL)
        self.ada, self.scale_a, self.scale_f = kept.take(48, NSEQ), kept.take(8, NSEQ), kept.take(8, NSEQ)
        self.ada_next = kept.take(48, NSEQ)
        self.c_in, self.silu_c = kept.take(KC, NSEQ), kept.take(KC, NSEQ)
        self.shift_in, self.conv_in, self.lastrow = kept.take(RW_CH, NB), kept.take(8, NB, 3), kept.take(RW_CH, NSEQ)
        self.one_minus_ka, self.small_a, self.pool_mark, self.act_mark, self.gated_s = kept.take(4), kept.take(1), kept.take(1), kept.take(1), kept.take(NB)
        self.table = kept.take(64).bitcast(I32)
        self.logits, self.top_v, self.top_f = (kept.take(3, 8) for _ in range(3))
        self.top_i = kept.take(3, 8).bitcast(U32)
        self.top_e, self.top_w, self.one_hot = kept.take(3), kept.take(2, 3), kept.take(8)
        self.ring_at = 0

        def named(name, arena, *shape, dtype=F32R):
            at = nc.lookup_mloc(self.sb).addr + 4 * arena.next
            arena.take(int(np.prod(shape)))
            return nc.alloc_sbuf_tensor_at(name, [P, *shape], dtype, offset=at)
        self.work_at, self.work_size = self.ring_at + RING_KEPT * SLOT, (RING - RING_KEPT) * SLOT
        rest = Arena(self.sb, self.work_at + self.work_size, size - self.work_at - self.work_size)
        start = rest.next
        self.rw, self.xbc, self.xbc_s = rest.take(RW_CH, 1 + T), rest.take(8, 3 + SEQ), rest.take(8, NB, 4)
        self.z, self.dt_raw = rest.take(4, T), rest.take(T)
        self.mla_at, self.mla_size = self.work_at, rest.next - self.work_at
        self.qkv, self.kr, self.branches = rest.take(4, T), rest.take(T), rest.take(12, T)
        self.gates = rest.take(3 * KC, T)
        spare = Arena(self.sb, start, self.mla_at + self.mla_size - start)
        self.merge_mix, self.merge_gated = spare.take(KC, T), spare.take(2, T)
        top = Arena(self.sb, (size - 2 * KC * T - 4 * KC * P) // 8 * 8, 2 * KC * T + 4 * KC * P)
        self.h_hi, self.h_lo = named("h_hi", top, KC, T), named("h_lo", top, KC, T)
        self.tile_hi, self.tile_lo = named("tile_hi", top, 2, KC, P), named("tile_lo", top, 2, KC, P)
        spare = Arena(self.sb, start, size - start)
        self.sq = Arena(self.sb, size - KC * T, KC * T).take(KC, T)
        spare = Arena(self.sb, start, size - start)
        self.hidden, self.silu_up = spare.take(FF // P, T), spare.take(2, T)
        moe = Arena(self.sb, self.ring_at, size - self.ring_at)
        self.units = named("units", moe, MOE_RING, UNIT, dtype=F32)
        self.w_hi, self.w_lo = named("w_hi", moe, MOE_SPLIT, UNIT), named("w_lo", moe, MOE_SPLIT, UNIT)
        self.xg_hi, self.xg_lo = named("xg_hi", moe, KC, P), named("xg_lo", moe, KC, P)
        self.hid_hi, self.hid_lo = named("hid_hi", moe, FE // P, P), named("hid_lo", moe, FE // P, P)
        self.h_tok, self.sel, self.selg = moe.take(3, D), moe.take(3, P), moe.take(3, P)
        self.selT, self.hid, self.silu_g = moe.take(T), moe.take(2, 512), moe.take(2, 512)
        self.y_sb, self.moe_out = moe.take(D), moe.take(KC, T)
        self.mask, self.rank, self.gate_e = moe.take(NE, 3), moe.take(NE, 3), moe.take(NE, 3)
        self.turns, self.turn_expert, self.rank_next = moe.take(NE), moe.take(MAX_TURNS + 1), moe.take(3)
        self.turns_i, self.turn_expert_i = moe.take(NE).bitcast(I32), moe.take(MAX_TURNS + 1).bitcast(I32)
        self.bank = [nc.alloc_psum_tensor(f"bank{i}", [P, 512], F32) for i in range(8)]
        self.slot_loaded = [nc.alloc_semaphore(f"slot{i}_loaded") for i in range(RING)]
        (self.c_loaded, self.const_loaded, self.vec_loaded, self.small_loaded, self.shift_loaded, self.conv_loaded, self.rwkv_w_loaded,
         self.mla_w_loaded, self.wkv_loaded, self.ssm_loaded, self.stored) = (nc.alloc_semaphore(n) for n in (
             "c_loaded", "const_loaded", "vec_loaded", "small_loaded", "shift_loaded", "conv_loaded", "rwkv_w_loaded",
             "mla_w_loaded", "wkv_loaded", "ssm_loaded", "stored"))
        self.pages_loaded = [nc.alloc_semaphore(f"pages{i}_loaded") for i in range(2)]
        (self.x_in, self.consts_in, self.table_in, self.c_dram, self.vecs_in, self.small_in, self.shift_dram, self.conv_dram,
         self.rwkv_w, self.mla_w, self.wkv_in, self.ssm_in, self.cache, self.w_ada, self.w_in, self.w_branch, self.w_out,
         self.w1, self.w3, self.w2, self.e1, self.e3, self.e2) = (dram[n] for n in DRAM)
        self.ada_loaded = [nc.alloc_semaphore(f"ada{i}_loaded") for i in range(RING_KEPT)]
        self.page_regs = [nc.sync.alloc_register(f"page{i}") for i in range(Mla.GROUP * NPAGE)]
        self.ring = Ring(self)
        self.moe_loaded = [nc.alloc_semaphore(f"unit{i}_loaded") for i in range(MOE_RING)]
        self.unit_split, self.unit_used = nc.alloc_semaphore("unit_split"), nc.alloc_semaphore("unit_used")
        self.places_made, self.gathered, self.xg_rounded, self.xg_split = (nc.alloc_semaphore(n) for n in (
            "places_made", "gathered", "xg_rounded", "xg_split"))

    def steps(self, kind, who):
        name = f"{kind}_{who}"
        if name not in self.named:
            self.named[name] = Steps(self.nc, name, self.book)
        return self.named[name]

    def loop_steps(self, name):
        return LoopSteps(self.nc, name, self.book)

    def next_place(self):
        self.turn += 1
        return (self.turn - 1) % RING

    def slot(self, place):
        return self.sb[:, self.ring_at + SLOT * place:self.ring_at + SLOT * place + SLOT]

    def c(self, name):
        return self.consts[:, CONST[name][0]:CONST[name][1]]

    def vec(self, layer, name):
        return self.vecs[:, VEC[name][0]:VEC[name][1]]


DRAM = ("x", "consts", "table", "c", "vecs", "small", "shift", "conv", "rwkv_w", "mla_w", "wkv", "ssm", "cache", "w_ada", "w_in",
        "w_branch", "w_out", "ffn_w1", "ffn_w3", "ffn_w2", "moe_w1", "moe_w3", "moe_w2")
OUTS = {"y": (P, KC, T), "ckv": (DEPTH, P, 2, T), "kpe": (DEPTH, ROPE, T), "shift": (DEPTH, P, RW_CH, NSEQ),
        "p_wkv": (DEPTH, P, 4, 64), "s_wkv": (DEPTH, P, 4, NB, 64), "p_conv": (DEPTH, P, 8, 3), "s_conv": (DEPTH, P, 8, NB, 3),
        "p_ssm": (DEPTH, P, 512), "s_ssm": (DEPTH, P, 4, NB, P)}


class Ada(Stage):

    def __init__(self, k, l):
        super().__init__(k, "ada", l)
        self.rows = k.h.rearrange("p c t -> p (c t)")[:, 0:2048].rearrange("p (i n) -> p i n", i=4)
        self.first = ADA_AHEAD if l else 0
        self.slots = {}
        for n in range(self.first, ADA_PARTS):
            place = k.next_place()
            dst = k.slot(place).rearrange("p (k n) -> p k n", k=KC)
            self.slots[n] = (k.ring.add(place, dst, k.w_ada[l].rearrange("(k p) n -> p k n", p=P)[:, :, 512 * n:512 * n + 512]))

    def tensor(self, pe):
        k, t, a = self.k, self.t, self.a
        if self.l == 0:
            pe.wait_ge(*k.loads.a.at("silu_c"))

        def turn(n):
            pe.wait_ge(*a.at("rows", n))
            if self.l == 0 and n == 0:
                pe.wait_ge(k.const_loaded, 48)
            for j in range(4):
                c = 4 * n + j
                mm = pe.transpose(k.bank[0][:, NSEQ * c:NSEQ * c + NSEQ], self.rows[0:NSEQ, n % 4, P * j:P * j + P], k.c("ident")[0:NSEQ, 0:NSEQ])
            mm.then_inc(*t.did("turned", n))
        for n, slot in self.slots.items():
            k.ring.arrived(pe, slot)
            w = k.ring.loads[slot][1]
            if n >= self.first + 2:
                pe.wait_ge(*a.at("rows", n - 2))
            for kk in range(KC):
                mm = pe.matmul(k.bank[1 + n % 2][0:NSEQ, :], k.silu_c[:, kk, :], w[:, kk, :], start=kk == 0, stop=kk == KC - 1)
            mm.then_inc(*t.did("slot", n))
            k.ring.release(slot, t)
            if n > self.first:
                turn(n - 1)
        turn(ADA_PARTS - 1)

    def scalar(self, act):
        k = self.k
        for n in self.slots:
            act.wait_ge(*self.t.at("slot", n))
            if n >= self.first + 4:
                act.wait_ge(*self.t.at("turned", n - 4))
            act.copy(self.rows[0:NSEQ, n % 4, :], k.bank[1 + n % 2][0:NSEQ, :]).then_inc(*self.a.did("rows", n))

    def vector(self, dve):
        k = self.k
        do = self.v.serial(dve)
        dve.wait_ge(k.vec_loaded, 16 * (self.l + 1))
        b_ada = k.vec(self.l, "b_ada").unsqueeze(2).broadcast_to([P, 4 * ADA_PARTS, NSEQ])
        if self.first:
            do(dve.tensor_tensor(k.ada[:, 0:4 * self.first, :], k.ada_next[:, 0:4 * self.first, :], b_ada[:, 0:4 * self.first, :], ALU.add))
        dve.wait_ge(*self.t.at("turned", ADA_PARTS - 1))
        do(dve.tensor_tensor(k.ada[:, 4 * self.first:, :], k.bank[0][:, 4 * self.first * NSEQ:48 * NSEQ].rearrange("p (c s) -> p c s", s=NSEQ),
                             b_ada[:, 4 * self.first:, :], ALU.add))
        for part, w, out in ((1, "norm_attn", k.scale_a), (4, "norm_ffn", k.scale_f)):
            do(dve.scalar_tensor_tensor(out=out[:, :, :], in0=k.ada[:, 8 * part:8 * part + 8, :], scalar=1.0,
                                        in1=k.vec(self.l, w).unsqueeze(2).broadcast_to([P, 8, NSEQ]), op0=ALU.add, op1=ALU.mult))


class AdaAhead:

    def __init__(self, k, l, gates):
        self.k, self.l, self.gates = k, l, gates
        self.t, self.a = (StageSteps(k.steps("ada_ahead", e), l) for e in ("tensor", "scalar"))
        self.rows = k.h.rearrange("p c t -> p (c t)")[:, 0:2048].rearrange("p (i n) -> p i n", i=4)
        self.computed = self.collected = 0

    def load(self, act, n):
        k = self.k
        if n < ADA_AHEAD:
            dst = k.slot(n % RING_KEPT).rearrange("p (k n) -> p k n", k=KC)
            act.dma_start(dst, k.w_ada[self.l].rearrange("(k p) n -> p k n", p=P)[:, :, 512 * n:512 * n + 512]).then_inc(k.ada_loaded[n % RING_KEPT], 16)

    def turn(self, pe, n, bank):
        k = self.k
        pe.wait_ge(*self.a.at("rows", n))
        for j in range(4):
            mm = pe.transpose(k.bank[bank][:, NSEQ * j:NSEQ * j + NSEQ], self.rows[0:NSEQ, n % 4, P * j:P * j + P], k.c("ident")[0:NSEQ, 0:NSEQ])
        mm.then_inc(*self.t.did("turned", n))
        k.book.setdefault(("ada turned", n), bank)

    def compute(self, pe, bank, turned):
        k, n = self.k, self.computed
        if n:
            self.turn(pe, n - 1, turned)
        pe.wait_ge(k.ada_loaded[n % RING_KEPT], 16 * (n // RING_KEPT + 1))
        w = k.slot(n % RING_KEPT).rearrange("p (k n) -> p k n", k=KC)
        for kk in range(KC):
            mm = pe.matmul(k.bank[bank][0:NSEQ, :], k.silu_c[:, kk, :], w[:, kk, :], start=kk == 0, stop=kk == KC - 1)
        mm.then_inc(*self.t.did("slot", n))
        k.book.setdefault(("ada slot", n), bank)
        if n >= ADA_AHEAD - RING_KEPT:
            k.ring.release(self.gates.slots[4 + n % RING_KEPT], self.t)
        self.computed += 1

    def settle(self, pe):
        pe.wait_ge(*self.a.at("rows", self.computed - 1))

    def collect(self, act):
        k, n = self.k, self.collected
        if n:
            self.keep_columns(act, n - 1)
        act.wait_ge(*self.t.at("slot", n))
        act.copy(self.rows[0:NSEQ, n % 4, :], k.bank[k.book.get(("ada slot", n), 0)][0:NSEQ, :]).then_inc(*self.a.did("rows", n))
        self.load(act, n + RING_KEPT)
        self.collected += 1

    def keep_columns(self, act, n):
        k = self.k
        act.wait_ge(*self.t.at("turned", n))
        src = k.bank[k.book.get(("ada turned", n), 0)][:, 0:4 * NSEQ].rearrange("p (c s) -> p c s", s=NSEQ)
        act.copy(k.ada_next[:, 4 * n:4 * n + 4, :], src).then_inc(*self.a.did("columns", n))


class Norm(Stage):

    def __init__(self, k, l, which):
        super().__init__(k, f"norm_{which}", l)
        self.which = which

    def scalar(self, act):
        k = self.k
        if self.l == 0:
            act.wait_ge(k.const_loaded, 48)
        act.activation(k.sq[:, :, :], k.x[:, :, :], ACT.Square).then_inc(*self.a.did("squares"))
        act.wait_ge(*self.t.at("sum"))
        act.activation(k.root[:, :], k.bank[1][:, 0:T], ACT.Sqrt, scale=1.0 / D, bias=k.c("eps")).then_inc(*self.a.did("root"))

    def tensor(self, pe):
        k = self.k
        pe.wait_ge(*self.a.at("squares"))
        for c in range(KC):
            mm = pe.matmul(k.bank[1][:, 0:T], k.c("ones"), k.sq[:, c, :], start=c == 0, stop=c == KC - 1)
        mm.then_inc(*self.t.did("sum"))

    def vector(self, dve):
        k = self.k
        do = self.v.serial(dve)
        dve.wait_ge(*self.a.at("root"))
        do(dve.reciprocal(k.root[:, :], k.root[:, :]))
        do(dve.tensor_tensor(k.h[:, :, :], k.x[:, :, :], bc(k.root[:, :], 1, KC), ALU.mult))
        if self.which == "final":
            do(dve.tensor_tensor(k.h[:, :, :], k.h[:, :, :], k.vec(self.l, "norm_final").unsqueeze(2).broadcast_to([P, KC, T]), ALU.mult))
            return
        part, scale = (0, k.scale_a) if self.which == "attn" else (3, k.scale_f)
        shift = k.ada[:, 8 * part:8 * part + 8, :]
        for c in range(KC):
            dve.tensor_scalar(k.h[:, c, 0:SEQ], k.h[:, c, 0:SEQ], scale[:, c, 0:1], shift[:, c, 0:1], ALU.mult, ALU.add)
        do(dve.tensor_tensor(k.h[:, :, SEQ:T], k.h[:, :, SEQ:T], scale[:, :, 1:NSEQ], ALU.mult))
        do(dve.tensor_tensor(k.h[:, :, SEQ:T], k.h[:, :, SEQ:T], shift[:, :, 1:NSEQ], ALU.add))


class SplitTiles:

    def __init__(self, k, kind, l, tiles, used):
        self.k, self.tiles, self.used = k, tiles, used
        self.a, self.v = (StageSteps(k.steps(kind + "_split", e), l) for e in ("scalar", "vector"))

    def weights(self, i):
        slot, column, _ = self.tiles[i]
        return self.k.ring.loads[slot][1][:, :, P * column:P * column + P]

    def h_hi(self, act):
        act.copy(self.k.h_hi[:, :, :], self.k.h[:, :, :]).then_inc(*self.a.did("h"))

    def h_lo(self, dve):
        k = self.k
        dve.wait_ge(*self.a.at("h"))
        dve.tensor_tensor(k.h_lo[:, :, :], k.h[:, :, :], k.h_hi[:, :, :].bitcast(F32), ALU.subtract).then_inc(*self.v.did("h"))

    def hi(self, act, i):
        if i < len(self.tiles):
            k = self.k
            k.ring.arrived(act, self.tiles[i][0])
            if i >= 2:
                act.wait_ge(*self.used(i - 2))
            act.copy(k.tile_hi[:, i % 2], self.weights(i)).then_inc(*self.a.did("tile", i))

    def lo(self, dve, i):
        if i < len(self.tiles):
            k = self.k
            dve.wait_ge(*self.a.at("tile", i))
            dve.tensor_tensor(k.tile_lo[:, i % 2], self.weights(i), k.tile_hi[:, i % 2].bitcast(F32), ALU.subtract).then_inc(*self.v.did("tile", i))
            if self.tiles[i][2]:
                k.ring.release(self.tiles[i][0], self.v)

    def product(self, pe, out, i):
        k = self.k
        if i == 0:
            pe.wait_ge(*self.v.at("h"))
        pe.wait_ge(*self.v.at("tile", i))
        for kk in range(KC):
            hi, lo = k.tile_hi[:, i % 2, kk, :], k.tile_lo[:, i % 2, kk, :]
            pe.matmul(out, hi, k.h_hi[:, kk, :], start=kk == 0, stop=False)
            pe.matmul(out, hi, k.h_lo[:, kk, :], start=False, stop=False)
            mm = pe.matmul(out, lo, k.h_hi[:, kk, :], start=False, stop=kk == KC - 1)
        return mm


class Project(Stage):

    def __init__(self, k, l):
        super().__init__(k, "project", l)
        self.slots = []
        for c0, n in [(0, 512)] + [(544 + 512 * i, min(512, 3872 - 544 - 512 * i)) for i in range(7)]:
            place = k.next_place()
            dst = k.slot(place)[:, 0:KC * n].rearrange("p (k n) -> p k n", k=KC)
            self.slots.append((k.ring.add(place, dst, k.w_in[l].rearrange("(k p) n -> p k n", p=P)[:, :, c0:c0 + n]), n // P))
        tiles = [(slot, t, t == n - 1) for slot, n in self.slots for t in range(n)]
        self.split = SplitTiles(k, "project", l, tiles, lambda i: self.t.at("tile", i + 2))

    def tiles(self):
        out, at = [], 0
        for s, (slot, n) in enumerate(self.slots):
            for t in range(n):
                name = ("qkv", at) if at < 4 else ("rw", at - 4) if at < 18 else ("z", at - 18) if at < 22 else ("xbc", at - 22)
                out.append((slot, t, name, t == n - 1))
                at += 1
        return [(None, "w_kr", ("kr", 0), False), (None, "w_dt", ("dt", 0), False)] + out

    def tensor(self, pe):
        k = self.k
        pe.wait_ge(k.small_loaded, 16 * (self.l + 1))
        for i, (slot, t, name, last) in enumerate(self.tiles()):
            if i >= 4:
                by = self.a if i % 2 else self.v
                pe.wait_ge(*by.at("tile", i - 4))
            m = 8 if name[0] == "dt" else P
            if slot is None:
                w = k.small[:, SMALL[t][0]:SMALL[t][1]].rearrange("p (k n) -> p k n", k=KC)
                for kk in range(KC):
                    mm = pe.matmul(k.bank[i % 4][0:m, 0:T], w[:, kk, 0:m], k.h[:, kk, :], start=kk == 0, stop=kk == KC - 1)
            else:
                mm = self.split.product(pe, k.bank[i % 4][:, 0:T], i - 2)
            mm.then_inc(*self.t.did("tile", i))

    def evict(self, eng, steps, odd):
        k = self.k
        tiles = self.tiles()
        part = self.split.hi if odd else self.split.lo
        part(eng, 0)
        part(eng, 1)
        for i, (_, _, (name, c), _) in enumerate(tiles):
            if i >= 2:
                part(eng, i)
            if i % 2 != odd:
                continue
            src = k.bank[i % 4]
            eng.wait_ge(*self.t.at("tile", i))
            copy = eng.copy if odd else eng.tensor_copy
            if name == "qkv":
                ins = copy(k.qkv[:, c, :], src[:, 0:T])
            elif name == "kr":
                ins = copy(k.kr[:, :], src[:, 0:T])
            elif name == "rw":
                ins = copy(k.rw[:, c, 1:1 + T], src[:, 0:T])
            elif name == "z":
                ins = copy(k.z[:, c, :], src[:, 0:T])
            elif name == "dt":
                ins = copy(k.dt_raw[0:8, :], src[0:8, 0:T])
            else:
                copy(k.xbc[:, c, 3:3 + SEQ], src[:, 0:SEQ])
                ins = copy(k.xbc_s[:, c, :, 3], src[:, SEQ:T])
            ins.then_inc(*steps.did("tile", i))

    def vector(self, dve):
        k = self.k
        dve.memset(k.rw[:, :, 0:1], 0.0)
        dve.memset(k.xbc[:, :, 0:3], 0.0)
        self.split.h_lo(dve)
        self.evict(dve, self.v, 0)

    def scalar(self, act):
        self.split.h_hi(act)
        self.evict(act, self.a, 1)


class Gates:

    def __init__(self, k, l):
        self.k = k
        self.t, self.a = (StageSteps(k.steps("gates", e), l) for e in ("tensor", "scalar"))
        self.computed = self.collected = 0
        self.slots = []
        for i in range(6):
            dst = k.slot(i % RING_KEPT).rearrange("p (k n) -> p k n", k=KC)
            c0 = 3880 + 512 * i
            self.slots.append(k.ring.add(i % RING_KEPT, dst, k.w_in[l].rearrange("(k p) n -> p k n", p=P)[:, :, c0:c0 + 512]))
        self.handed_on = l + 1 < DEPTH

    def compute(self, pe, *banks):
        k = self.k
        for i, bank in enumerate(banks):
            n = self.computed
            if bank in banks[:i]:
                pe.wait_ge(*self.a.at("gate", n - banks[:i][::-1].index(bank) - 1))
            slot = self.slots[n // 4]
            k.ring.arrived(pe, slot)
            w = k.ring.loads[slot][1]
            for kk in range(KC):
                mm = pe.matmul(k.bank[bank][:, 0:T], w[:, kk, P * (n % 4):P * (n % 4) + P], k.h[:, kk, :], start=kk == 0, stop=kk == KC - 1)
            mm.then_inc(*self.t.did("gate", n))
            k.book.setdefault(("gate bank", n), bank)
            if n % 4 == 3 and not (self.handed_on and n // 4 >= 4):
                k.ring.release(slot, self.t)
            self.computed += 1

    def settle(self, pe):
        pe.wait_ge(*self.a.at("gate", self.computed - 1))

    def collect(self, act, count):
        k = self.k
        for n in range(self.collected, self.collected + count):
            act.wait_ge(*self.t.at("gate", n))
            act.copy(k.gates[:, n, :], k.bank[k.book.get(("gate bank", n), 0)][:, 0:T]).then_inc(*self.a.did("gate", n))
        self.collected += count


class Rwkv(Stage):

    def __init__(self, k, l):
        super().__init__(k, "rwkv", l)
        self.gates = k.gate_tiles
        ar = Arena(k.sb, k.work_at, k.work_size)
        self.w = ar.take(NRWKV)
        self.ep, self.en = ar.take(4, 129), ar.take(4, 129)
        self.ws = ar.take(4, NB)
        self.kk, self.kh, self.bb = ar.take(4, T), ar.take(4, T), ar.take(4, T)
        self.tilde = ar.take(2048)
        self.at, self.rt, self.bt, self.kt = (self.tilde[:, 512 * i:512 * i + 512].rearrange("p (c t) -> p c t", c=4) for i in range(4))
        self.tok = ar.take(3, 512)
        self.vt, self.btt, self.ktt = (self.tok[:, i, :] for i in range(3))
        self.AT, self.BT = ar.take(8, P), ar.take(8, P)
        self.inv = ar.take(4096)
        self.X, self.Y, self.Pm, self.M = (self.inv[:, 1024 * i:1024 * i + 1024].rearrange("p (h t) -> p h t", h=8) for i in range(4))
        self.RB, self.RK, self.W, self.U = self.X, self.Pm, self.M[:, 0:4, :], self.M[:, 4:8, :]
        self.a_steps = self.a
        self.S, self.S0 = ar.take(4, 64), ar.take(4, 64)
        self.sg = ar.take(T)
        self.av = self.inv[:, 0:4 * T].rearrange("p (c t) -> p c t", c=4)
        self.d = self.inv[:, 0:14 * T].rearrange("p (c t) -> p c t", c=14)
        self.tw = self.tok[:, 0, 0:T]
        self.sw = k.branches[:, 8:12, :].rearrange("p c t -> p (c t)")
        self.sws = k.branches[:, 0:4, :].rearrange("p c t -> p (c t)")[:, 0:512]
        self.st, self.t1 = (self.inv[:, 2048 * i:2048 * i + 2048].rearrange("p (c b i) -> p c b i", c=4, b=NB) for i in range(2))
        self.sq = self.tilde[:, 0:4 * T].rearrange("p (c t) -> p c t", c=4)
        self.g_sb = self.tilde[:, 0:4 * T].rearrange("p (c t) -> p c t", c=4)
        self.y = k.branches[:, 4:8, :]

    def pool(self, g):
        k, l = self.k, self.l
        g.dma_start(self.w[:, :], k.rwkv_w[l]).then_inc(k.rwkv_w_loaded, 16)
        g.wait_ge(*self.v.at("lastrow"))
        g.dma_start(k.out["shift"][l], k.lastrow[:, :, :]).then_inc(k.stored, 16)
        g.wait_ge(*self.v.at("state", NT - 1))
        g.dma_start(k.out["p_wkv"][l], self.S[:, :, :]).then_inc(k.stored, 16)
        g.wait_ge(*self.a_steps.at("y", NT - 1))
        g.dma_start(self.st, k.wkv_in[l]).then_inc(k.wkv_loaded, 16)
        g.wait_ge(*self.v.at("s_state"))
        g.dma_start(k.out["s_wkv"][l], self.st).then_inc(k.stored, 16)
        k.stores += 3
        g.wait_ge(k.stored, 16 * k.stores)
        g.memset(k.pool_mark[0:1, 0:1], 0.0).then_inc(*self.g.did("stored"))

    def tensor(self, pe):
        k, t = self.k, self.t
        w, c_ = self.w, k.c
        pe.wait_ge(k.rwkv_w_loaded, 16 * (self.l + 1))
        w2, a2, g2 = (w[:, RWKV_W[n][0]:RWKV_W[n][1]] for n in ("w2", "a2", "g2"))
        self.gates.compute(pe, 4, 5, 6)
        pe.wait_ge(*self.a.at("tanh"))
        for i in range(3):
            m = P if i < 2 else NB
            mm = pe.matmul(k.bank[i][0:m, :], self.tw[0:65, P * i:P * i + m], w2[0:65, :], start=True, stop=True)
        mm.then_inc(*t.did("w"))
        for c in range(4):
            if c:
                pe.wait_ge(*self.a.at("a", c - 1))
            mm = pe.matmul(k.bank[3][:, 0:T], a2[64:128, P * c:P * c + P], k.rw[64:128, 12, 1:1 + T], start=True, stop=True)
            mm.then_inc(*t.did("a", c))
        pe.wait_ge(*self.a.at("kk_sq"))
        self.gates.settle(pe)
        for c in range(4):
            mm = pe.matmul(k.bank[4 + c][:, 0:T], c_("block_ones"), self.d[:, 4 + c, :], start=True, stop=True)
        mm.then_inc(*t.did("kk_norm"))
        pe.wait_ge(*self.a.at("sw"))
        for c in range(4):
            mm = pe.matmul(k.bank[0][:, NB * c:NB * c + NB], self.sws[0:NB, P * c:P * c + P],
                           c_("decay_id")[0:NB, :], start=True, stop=True)
        mm.then_inc(*t.did("ws"))
        self.gates.compute(pe, 1, 2)
        for ti in range(NT):
            cols = slice(1 + P * ti, 1 + P * ti + P)
            if ti == 0:
                pe.wait_ge(*self.a.at("ws"))
            else:
                pe.wait_ge(*self.v.at("state", ti - 1))
                pe.wait_ge(*self.a.at("y", ti - 1))
            self.gates.settle(pe)
            for c in range(4):
                mm = pe.matmul(k.bank[c // 2][:, 129 * (c % 2):129 * (c % 2) + 129],
                               self.sw[:, 512 * ti + P * c:512 * ti + P * c + P], c_("decay_tri"), start=True, stop=True)
            mm.then_inc(*t.did("logs", ti))
            for c in range(4):
                mm = pe.transpose(k.bank[2][:, P * c:P * c + P], k.rw[:, 8 + c, cols], c_("ident"))
            mm.then_inc(*t.did("v_tok", ti))
            self.gates.compute(pe, 3)
            pe.wait_ge(*self.v.at("tilde", ti))
            self.gates.settle(pe)
            for c in range(4):
                pe.transpose(k.bank[3][:, P * c:P * c + P], self.bt[:, c, :], c_("ident"))
            for c in range(4):
                mm = pe.transpose(k.bank[4][:, P * c:P * c + P], self.kt[:, c, :], c_("ident"))
            mm.then_inc(*t.did("bk_tok", ti))
            for q, src in enumerate((self.bt, self.kt)):
                for g in range(2):
                    b = (5, 6, 7, 0)[2 * q + g]
                    if b == 0:
                        pe.wait_ge(*self.a.at("logs", ti))
                    r = slice(64 * g, 64 * g + 64)
                    for c in range(4):
                        mm = pe.matmul(k.bank[b][:, P * c:P * c + P], src[r, c, :], self.at[r, c, :], start=True, stop=True)
                    mm.then_inc(*t.did("AB", ti, q, g))
            for n in range(7):
                for g in range(2):
                    hs = range(4 * g, 4 * g + 4)
                    pe.wait_ge(*self.v.at("M", ti, n, g))
                    if n:
                        pe.wait_ge(*self.v.at("X", ti, n - 1, g))
                    if n == 0 and g == 0:
                        pe.wait_ge(*self.a.at("bk_tok", ti))
                    for h in hs:
                        mm = pe.matmul(k.bank[1 + g][:, P * (h % 4):P * (h % 4) + P], self.M[:, h, :],
                                       c_("ident") if n == 0 else self.X[:, h, :], start=True, stop=True)
                    mm.then_inc(*t.did("MX", ti, n, g))
                if n == 0:
                    continue
                for g in range(2):
                    hs = range(4 * g, 4 * g + 4)
                    pe.wait_ge(*self.a.at("MX", ti, n, g))
                    pe.wait_ge(*self.v.at("Y", ti, n - 1, g))
                    if n < 6:
                        for h in hs:
                            mm = pe.matmul(k.bank[3 + g][:, P * (h % 4):P * (h % 4) + P], self.Y[:, h, :], self.Pm[:, h, :],
                                           start=True, stop=True)
                        mm.then_inc(*t.did("XMX for X", ti, n, g))
                    for h in hs:
                        mm = pe.matmul(k.bank[5 + g][:, P * (h % 4):P * (h % 4) + P], self.Pm[:, h, :], self.Y[:, h, :],
                                       start=True, stop=True)
                    mm.then_inc(*t.did("XMX for Y", ti, n, g))
            pe.wait_ge(*self.v.at("Y", ti, 6, 0))
            pe.wait_ge(*self.v.at("Y", ti, 6, 1))
            for q, src in enumerate((self.bt, self.kt)):
                for g in range(2):
                    b = 3 + 2 * q + g
                    r = slice(64 * g, 64 * g + 64)
                    for c in range(4):
                        mm = pe.matmul(k.bank[b][:, P * c:P * c + P], src[r, c, :], self.rt[r, c, :], start=True, stop=True)
                    mm.then_inc(*t.did("R", ti, q, g))
            pe.wait_ge(*self.a.at("v_tok", ti))
            for n in range(8):
                g, c = n // 4, n % 4
                r, h = slice(64 * g, 64 * g + 64), 2 * c + g
                o = k.bank[(7, 2)[g]][:, 64 * c:64 * c + 64]
                if ti:
                    pe.matmul(o, self.at[r, c, :], self.S0[r, c, :], start=True, stop=False)
                mm = pe.matmul(o, self.BT[:, n, :], self.vt[:, 64 * h:64 * h + 64], start=not ti, stop=True)
            mm.then_inc(*t.did("W", ti))
            pe.wait_ge(*self.a.at("W", ti))
            W, U = self.W.rearrange("p a b -> p (a b)"), self.U.rearrange("p a b -> p (a b)")
            for n in range(8):
                mm = pe.matmul(k.bank[0][:, 64 * n:64 * n + 64], self.Y[:, n, :], W[:, 64 * n:64 * n + 64], start=True, stop=True)
            mm.then_inc(*t.did("U", ti))
            pe.wait_ge(*self.a.at("U", ti))
            pe.wait_ge(*self.v.at("R", ti))
            for n in range(8):
                g, c = n // 4, n % 4
                r, h = slice(64 * g, 64 * g + 64), 2 * c + g
                o = k.bank[1][r, P * c:P * c + P]
                if ti:
                    pe.matmul(o, self.S0[r, c, :], self.rt[r, c, :], start=True, stop=False)
                pe.matmul(o, U[:, 64 * n:64 * n + 64], self.RB[:, n, :], start=not ti, stop=False)
                mm = pe.matmul(o, self.vt[:, 64 * h:64 * h + 64], self.RK[:, n, :], start=False, stop=True)
            mm.then_inc(*t.did("y", ti))
            for n in range(8):
                g, c = n // 4, n % 4
                r, h = slice(64 * g, 64 * g + 64), 2 * c + g
                o = k.bank[2][r, 64 * c:64 * c + 64]
                pe.matmul(o, self.btt[:, 64 * h:64 * h + 64], U[:, 64 * n:64 * n + 64], start=True, stop=False)
                mm = pe.matmul(o, self.ktt[:, 64 * h:64 * h + 64], self.vt[:, 64 * h:64 * h + 64], start=False, stop=True)
            mm.then_inc(*t.did("state", ti))
        for n, key in enumerate(("s_kk", "s_v", "s_r")):
            self.gates.compute(pe, *((5, 6), (4, 5), (0, 1))[n])
            pe.wait_ge(*self.v.at(key))
            self.gates.settle(pe)
            for c in range(4):
                mm = pe.matmul(k.bank[4 * (n % 2) + c][:, :], c_("block_ones"), self.t1[:, c, :, :].rearrange("p b i -> p (b i)"),
                               start=True, stop=True)
            mm.then_inc(*t.did(key))
        self.gates.compute(pe, 4)
        pe.wait_ge(*self.v.at("y"))
        self.gates.settle(pe)
        for c in range(4):
            mm = pe.matmul(k.bank[4 + c][:, 0:T], c_("block_ones"), self.y[:, c, :], start=True, stop=True)
        mm.then_inc(*t.did("mean"))
        pe.wait_ge(*self.a.at("y_sq"))
        for c in range(4):
            mm = pe.matmul(k.bank[c][:, 0:T], c_("block_ones"), self.sq[:, c, :], start=True, stop=True)
        mm.then_inc(*t.did("var"))
        pe.wait_ge(*self.v.at("bonus_in"))
        for c in range(4):
            mm = pe.matmul(k.bank[4 + c][:, 0:T], c_("block_ones"), self.bb[:, c, :], start=True, stop=True)
        mm.then_inc(*t.did("bonus"))
        pe.wait_ge(*self.a.at("y_root"))
        self.gates.compute(pe, 0, 1)
        pe.wait_ge(*self.v.at("ln"))
        self.gates.settle(pe)
        for c in range(4):
            mm = pe.matmul(k.bank[c][:, 0:T], g2[:, P * c:P * c + P], self.sg[:, :], start=True, stop=True)
        mm.then_inc(*t.did("g"))

    def scalar(self, act):
        k, a, t, v = self.k, self.a, self.t, self.v
        act.wait_ge(*v.at("shifted"))
        act.activation(self.tw[0:64, :], k.rw[0:64, 12, 1:1 + T], ACT.Tanh).then_inc(*a.did("tanh_only"))
        act.wait_ge(*v.at("ones_row"))
        act.activation(self.sg[:, :], k.rw[:, 13, 1:1 + T], ACT.Sigmoid).then_inc(*a.did("tanh"))
        self.gates.collect(act, 3)
        act.wait_ge(*t.at("w"))
        act.activation(self.sw[:, 0:512], k.bank[0][:, :], ACT.Sigmoid)
        act.activation(self.sw[:, 512:1024], k.bank[1][:, :], ACT.Sigmoid)
        act.activation(self.sws[0:NB, :], k.bank[2][0:NB, :], ACT.Sigmoid).then_inc(*a.did("sw"))
        for c in range(4):
            act.wait_ge(*t.at("a", c))
            act.activation(self.av[:, c, :], k.bank[3][:, 0:T], ACT.Sigmoid, bias=k.vec(self.l, "a0")[:, c:c + 1]).then_inc(*a.did("a", c))
        act.wait_ge(*v.at("kk_raw"))
        act.activation(self.d[:, 4:8, :], self.kk[:, :, :], ACT.Square).then_inc(*a.did("kk_sq"))
        act.wait_ge(*v.at("kk_max"))
        act.activation(self.d[:, 4:8, :], self.d[:, 4:8, :], ACT.Sqrt).then_inc(*a.did("kk_root"))
        act.wait_ge(*t.at("ws"))
        act.activation(self.ws[:, :, :], k.bank[0][:, 0:4 * NB].rearrange("p (c b) -> p c b", c=4), ACT.Exp).then_inc(*a.did("ws"))
        self.gates.collect(act, 2)
        for ti in range(NT):
            act.wait_ge(*t.at("logs", ti))
            for q in range(2):
                src = k.bank[q][:, 0:258].rearrange("p (c t) -> p c t", c=2)
                act.activation(self.ep[:, 2 * q:2 * q + 2, :], src, ACT.Exp)
                ins = act.activation(self.en[:, 2 * q:2 * q + 2, :], src, ACT.Exp, scale=-1.0)
            ins.then_inc(*a.did("logs", ti))
            act.wait_ge(*t.at("v_tok", ti))
            act.copy(self.vt, k.bank[2][:, :]).then_inc(*a.did("v_tok", ti))
            self.gates.collect(act, 1)
            act.wait_ge(*t.at("bk_tok", ti))
            act.copy(self.btt, k.bank[3][:, :])
            act.copy(self.ktt, k.bank[4][:, :]).then_inc(*a.did("bk_tok", ti))
            for n in range(1, 7):
                for g in range(2):
                    act.wait_ge(*t.at("MX", ti, n, g))
                    act.copy(self.Pm[:, 4 * g:4 * g + 4, :].rearrange("p h t -> p (h t)"), k.bank[1 + g][:, :]).then_inc(*a.did("MX", ti, n, g))
            act.wait_ge(*t.at("W", ti))
            W = self.W.rearrange("p a b -> p (a b)")
            act.copy(W[:, 0:256], k.bank[7][:, 0:256])
            act.copy(W[:, 256:512], k.bank[2][:, 0:256]).then_inc(*a.did("W", ti))
            act.wait_ge(*t.at("U", ti))
            act.mul(self.U.rearrange("p a b -> p (a b)"), k.bank[0][:, :], -1.0).then_inc(*a.did("U", ti))
            act.wait_ge(*t.at("y", ti))
            act.copy(self.y[:, :, P * ti:P * ti + P], k.bank[1][:, :].rearrange("p (c t) -> p c t", c=4)).then_inc(*a.did("y", ti))
        self.gates.collect(act, 7)
        act.wait_ge(*v.at("centred"))
        act.activation(self.sq[:, :, :], self.y, ACT.Square).then_inc(*a.did("y_sq"))
        act.wait_ge(*t.at("var"))
        for c in range(4):
            ins = act.activation(self.sq[:, c, :], k.bank[c][:, 0:T], ACT.Sqrt, scale=1.0 / 64, bias=k.c("ln_eps"))
        ins.then_inc(*a.did("y_root"))
        self.gates.collect(act, 2)

    def vector(self, dve):
        k, a, t, v, l = self.k, self.a, self.t, self.v, self.l
        do = v.serial(dve)
        rw = k.rw
        dve.tensor_copy(k.lastrow[:, :, 0:1], rw[:, :, SEQ:SEQ + 1])
        dve.tensor_copy(k.lastrow[:, :, 1:NSEQ], rw[:, :, 1 + SEQ:1 + T])
        dve.tensor_tensor(self.d[:, :, 0:SEQ], rw[:, :, 0:SEQ], rw[:, :, 1:1 + SEQ], ALU.subtract)
        dve.wait_ge(k.shift_loaded, 16 * (l + 1))
        do(dve.tensor_tensor(self.d[:, :, SEQ:T], k.shift_in[:, :, :], rw[:, :, 1 + SEQ:1 + T], ALU.subtract), "lastrow")
        for c in range(RW_CH):
            ins = dve.scalar_tensor_tensor(out=rw[:, c, 1:1 + T], in0=self.d[:, c, :], scalar=k.vec(l, "mu")[:, c:c + 1],
                                           in1=rw[:, c, 1:1 + T], op0=ALU.mult, op1=ALU.add)
        do(ins, "shifted")
        do(dve.memset(self.tw[64:65, :], 1.0), "ones_row")
        for c in range(4):
            ins = dve.tensor_scalar(self.kk[:, c, :], rw[:, 4 + c, 1:1 + T], k.vec(l, "k_k")[:, c:c + 1], None, ALU.mult)
        do(ins, "kk_raw")
        do(dve.tensor_scalar(k.one_minus_ka[:, :], k.vec(l, "k_a"), -1.0, 1.0, ALU.mult, ALU.add))
        dve.wait_ge(*t.at("kk_norm"))
        for c in range(4):
            ins = dve.tensor_scalar(self.d[:, 4 + c, :], k.bank[4 + c][:, 0:T], 1e-24, None, ALU.max)
        do(ins, "kk_max")
        dve.wait_ge(*a.at("a", 3))
        for c in range(4):
            ins = dve.tensor_scalar(self.kh[:, c, :], self.av[:, c, :], k.vec(l, "k_a")[:, c:c + 1], k.one_minus_ka[:, c:c + 1], ALU.mult, ALU.add)
        do(ins)
        do(dve.tensor_tensor(self.kh[:, :, :], self.kh[:, :, :], rw[:, 4:8, 1:1 + T], ALU.mult))
        dve.wait_ge(*a.at("kk_root"))
        do(dve.reciprocal(self.d[:, 4:8, :], self.d[:, 4:8, :]))
        do(dve.tensor_tensor(self.kk[:, :, :], self.kk[:, :, :], self.d[:, 4:8, :], ALU.mult))
        do(dve.tensor_tensor(self.bb[:, :, :], self.kk[:, :, :], self.av[:, :, :], ALU.mult))
        for ti in range(NT):
            s = slice(P * ti, P * ti + P)
            dve.wait_ge(*a.at("logs", ti))
            if ti:
                do(dve.tensor_tensor(self.S0[:, :, :], self.S[:, :, :], self.en[:, :, 0:1].broadcast_to([P, 4, 64]), ALU.mult))
            dve.tensor_tensor(self.at[:, :, :], self.kk[:, :, s], self.ep[:, :, 0:P], ALU.mult)
            dve.tensor_tensor(self.rt[:, :, :], rw[:, 0:4, 1 + P * ti:1 + P * ti + P], self.ep[:, :, 1:129], ALU.mult)
            dve.tensor_tensor(self.bt[:, :, :], self.bb[:, :, s], self.en[:, :, 1:129], ALU.mult)
            do(dve.tensor_tensor(self.kt[:, :, :], self.kh[:, :, s], self.en[:, :, 1:129], ALU.mult), "tilde", ti)
            for q, (dst, b) in enumerate(((self.AT, (5, 6)), (self.BT, (7, 0)))):
                for g in range(2):
                    dve.wait_ge(*t.at("AB", ti, q, g))
                    do(dve.tensor_tensor(dst[:, 4 * g:4 * g + 4, :], k.bank[b[g]][:, :].rearrange("p (h t) -> p h t", h=4),
                                         bc(k.c("strict"), 1, 4), ALU.mult))
            def level(n, g):
                mask = k.c("levels")[:, P * n:P * n + P]
                do(dve.tensor_tensor(self.M[:, 4 * g:4 * g + 4, :], self.AT[:, 4 * g:4 * g + 4, :], bc(mask, 1, 4), ALU.mult), "M", ti, n, g)
            level(0, 0)
            level(0, 1)
            for g in range(2):
                hs = slice(4 * g, 4 * g + 4)
                do(dve.tensor_tensor(self.Y[:, hs, :], bc(k.c("ident"), 1, 4), self.M[:, hs, :], ALU.subtract), "Y", ti, 0, g)
                dve.wait_ge(*t.at("MX", ti, 0, g))
                do(dve.tensor_tensor(self.X[:, hs, :], bc(k.c("ident"), 1, 4),
                                     k.bank[1 + g][:, :].rearrange("p (h t) -> p h t", h=4), ALU.subtract), "X", ti, 0, g)
                level(1, g)
            for n in range(1, 7):
                if n < 6:
                    for g in range(2):
                        dve.wait_ge(*t.at("MX", ti, n, g))
                        level(n + 1, g)
                self.ssm.conv_part(dve)
                for g in range(2):
                    hs = slice(4 * g, 4 * g + 4)
                    if n < 6:
                        dve.wait_ge(*t.at("XMX for X", ti, n, g))
                        ins = dve.tensor_tensor(self.X[:, hs, :], self.X[:, hs, :], k.bank[3 + g][:, :].rearrange("p (h t) -> p h t", h=4), ALU.subtract)
                        ins.then_inc(*v.did("X", ti, n, g))
                    dve.wait_ge(*t.at("XMX for Y", ti, n, g))
                    do(dve.tensor_tensor(self.Y[:, hs, :], self.Y[:, hs, :], k.bank[5 + g][:, :].rearrange("p (h t) -> p h t", h=4),
                                         ALU.subtract), "Y", ti, n, g)
            for q, dst in enumerate((self.RB, self.RK)):
                for g in range(2):
                    dve.wait_ge(*t.at("R", ti, q, g))
                    ins = dve.tensor_tensor(dst[:, 4 * g:4 * g + 4, :], k.bank[3 + 2 * q + g][:, :].rearrange("p (h t) -> p h t", h=4),
                                            bc(k.c("upto"), 1, 4), ALU.mult)
            do(ins, "R", ti)
            dve.wait_ge(*t.at("state", ti))
            new = k.bank[2][:, 0:256].rearrange("p (c i) -> p c i", c=4)
            if ti:
                do(dve.tensor_tensor(self.S0[:, :, :], self.S0[:, :, :], new, ALU.add))
                new = self.S0[:, :, :]
            do(dve.tensor_tensor(self.S[:, :, :], new, self.ep[:, :, 128:129].broadcast_to([P, 4, 64]), ALU.mult), "state", ti)
        sam = slice(SEQ, T)

        def along(x):
            return x.unsqueeze(3).broadcast_to([P, 4, NB, 64])
        fold = k.c("fold")
        rs = rw[:, 0:4, 1 + SEQ:1 + T]
        vs = rw[:, 8:12, 1 + SEQ:1 + T]
        dve.wait_ge(k.wkv_loaded, 16 * (l + 1))
        for c in range(4):
            ins = dve.tensor_tensor(self.t1[:, c], self.st[:, c], self.kk[:, c, sam].unsqueeze(2).broadcast_to([P, NB, 64]), ALU.mult)
        do(ins, "s_kk")
        for c in range(4):
            ins = dve.tensor_tensor(self.st[:, c], self.st[:, c], self.ws[:, c].unsqueeze(2).broadcast_to([P, NB, 64]), ALU.mult)
        do(ins)
        dve.wait_ge(*t.at("s_kk"))
        for c in range(4):
            ins = dve.tensor_tensor(self.t1[:, c], k.bank[c][:, :].rearrange("p (b i) -> p b i", b=NB),
                                    self.bb[:, c, sam].unsqueeze(2).broadcast_to([P, NB, 64]), ALU.mult)
        do(ins)
        do(dve.tensor_tensor(self.st, self.st, self.t1, ALU.subtract))
        for c in range(4):
            ins = dve.tensor_tensor(self.t1[:, c], bc(fold, 1, NB), vs[:, c, :].unsqueeze(2).broadcast_to([P, NB, 64]), ALU.mult)
        do(ins, "s_v")
        dve.wait_ge(*t.at("s_v"))
        for c in range(4):
            ins = dve.tensor_tensor(self.t1[:, c], k.bank[4 + c][:, :].rearrange("p (b i) -> p b i", b=NB),
                                    self.kh[:, c, sam].unsqueeze(2).broadcast_to([P, NB, 64]), ALU.mult)
        do(ins)
        do(dve.tensor_tensor(self.st, self.st, self.t1, ALU.add), "s_state")
        for c in range(4):
            ins = dve.tensor_tensor(self.t1[:, c], self.st[:, c], rs[:, c, :].unsqueeze(2).broadcast_to([P, NB, 64]), ALU.mult)
        do(ins, "s_r")
        dve.wait_ge(*t.at("s_r"))
        for c in range(4):
            ins = dve.tensor_tensor(self.t1[:, c], k.bank[c][:, :].rearrange("p (b i) -> p b i", b=NB), bc(fold, 1, NB), ALU.mult)
        do(ins)
        dve.wait_ge(*a.at("y", NT - 1))
        for c in range(4):
            ins = dve.tensor_reduce(self.y[:, c, sam], self.t1[:, c], X, ALU.add)
        do(ins, "y")
        dve.wait_ge(*t.at("mean"))
        for c in range(4):
            ins = dve.scalar_tensor_tensor(out=self.y[:, c, :], in0=k.bank[4 + c][:, 0:T], scalar=-1.0 / 64, in1=self.y[:, c, :],
                                           op0=ALU.mult, op1=ALU.add)
        do(ins, "centred")
        for c in range(4):
            ins = dve.scalar_tensor_tensor(out=self.bb[:, c, :], in0=rw[:, c, 1:1 + T], scalar=k.vec(l, "r_k")[:, c:c + 1],
                                           in1=self.kh[:, c, :], op0=ALU.mult, op1=ALU.mult)
        do(ins, "bonus_in")
        dve.wait_ge(*a.at("y_root"))
        do(dve.reciprocal(self.sq[:, :, :], self.sq[:, :, :]))
        do(dve.tensor_tensor(self.y, self.y, self.sq[:, :, :], ALU.mult))
        for c in range(4):
            ins = dve.tensor_scalar(self.y[:, c, :], self.y[:, c, :], k.vec(l, "ln_w")[:, c:c + 1], k.vec(l, "ln_b")[:, c:c + 1], ALU.mult, ALU.add)
        do(ins, "ln")
        dve.wait_ge(*t.at("bonus"))
        for c in range(4):
            ins = dve.tensor_tensor(self.bb[:, c, :], k.bank[4 + c][:, 0:T], rw[:, 8 + c, 1:1 + T], ALU.mult)
        do(ins)
        do(dve.tensor_tensor(self.y, self.y, self.bb[:, :, :], ALU.add))
        dve.wait_ge(*t.at("g"))
        for c in range(4):
            ins = dve.tensor_tensor(self.y[:, c, :], self.y[:, c, :], k.bank[c][:, 0:T], ALU.mult)
        do(ins)


class Ssm(Stage):

    def __init__(self, k, l):
        super().__init__(k, "ssm", l)
        self.conv_parts = 0
        self.ahead = k.ahead
        self.gates = k.gate_tiles
        ar = Arena(k.sb, k.work_at, k.work_size)
        self.cv = k.sq
        self.rows = ar.take(9, T)
        self.tokens = ar.take(NT, 6, 8)
        self.dtx, self.dax = ar.take(4, NB), ar.take(4, NB)
        self.hs = ar.take(512)
        big = ar.take(8192)
        self.st, self.t1 = (big[:, 4096 * i:4096 * i + 4096].rearrange("p (c b n) -> p c b n", c=4, b=NB) for i in range(2))
        small = Arena(k.sb, ar.next - 8192, 8192)
        self.xt, self.bt = small.take(512), small.take(256)
        self.xd, self.xdd = small.take(512), small.take(512)
        self.gt = small.take(2, P)
        self.seg = small.take(8, P)
        self.ecs = small.take(8, P)
        self.csb = small.take(8, P)
        self.spread = self.st.rearrange("p c b n -> p (c b n)")
        self.y = k.branches[:, 8:12, :]

    def conv_part(self, dve):
        k, l, n = self.k, self.l, self.conv_parts
        if n == CONV_PARTS:
            return
        self.conv_parts += 1
        do = self.v.serial(dve)
        if n == 0:
            dve.wait_ge(k.conv_loaded, 16 * (l + 1))
            dve.tensor_copy(k.xbc_s[:, :, :, 0:3].rearrange("p c b i -> p (c b) i"), k.conv_in[:, :, :, :].rearrange("p c b i -> p (c b) i"))
        if n == CONV_PARTS - 1:
            do(dve.tensor_tensor(self.cv[:, :, :], self.cv[:, :, :], k.vec(l, "conv_b").unsqueeze(2).broadcast_to([P, 8, T]), ALU.add), "conv")
            return
        i, samples = n // 2, n % 2
        for c in range(8):
            wt = k.vec(l, "conv_w")[:, 8 * i + c:8 * i + c + 1]
            out = self.cv[:, c, SEQ:T] if samples else self.cv[:, c, 0:SEQ]
            src = k.xbc_s[:, c, :, i] if samples else k.xbc[:, c, i:i + SEQ]
            if i == 0:
                ins = dve.tensor_scalar(out, src, wt, None, ALU.mult)
            else:
                ins = dve.scalar_tensor_tensor(out=out, in0=src, scalar=wt, in1=out, op0=ALU.mult, op1=ALU.add)
        do(ins)

    def pool(self, g):
        k, l = self.k, self.l
        g.wait_ge(*self.v.at("conv"))
        g.dma_start(k.out["p_conv"][l], k.xbc[:, :, SEQ:SEQ + 3]).then_inc(k.stored, 16)
        for c in range(8):
            g.dma_start(k.out["s_conv"][l, :, c], k.xbc_s[:, c, :, 1:4]).then_inc(k.stored, 16)
        g.wait_ge(*self.v.at("state", NT - 1))
        g.dma_start(k.out["p_ssm"][l], self.hs[:, :]).then_inc(k.stored, 16)
        g.wait_ge(*self.t.at("y", NT - 1))
        g.wait_ge(*self.v.at("y_off"))
        g.dma_start(self.st, k.ssm_in[l]).then_inc(k.ssm_loaded, 16)
        g.wait_ge(*self.v.at("s_state"))
        g.dma_start(k.out["s_ssm"][l], self.st).then_inc(k.stored, 16)
        k.stores += 11
        g.wait_ge(k.stored, 16 * k.stores)
        g.memset(k.pool_mark[0:1, 0:1], 0.0).then_inc(*self.g.did("stored"))

    def scalar(self, act):
        k, a, t, v = self.k, self.a, self.t, self.v
        act.wait_ge(*v.at("dt_abs"))
        act.activation(self.rows[0:8, 1, :], self.rows[0:8, 1, :], ACT.Exp, scale=-1.0)
        act.activation(k.small_a[0:8, 0:1], k.vec(self.l, "a_log")[0:8, :], ACT.Exp).then_inc(*a.did("dt_exp"))
        self.gates.collect(act, 2)
        act.wait_ge(*v.at("conv"))
        act.activation(self.t1.rearrange("p c b n -> p (c b n)")[:, 0:8 * T].rearrange("p (c t) -> p c t", c=8), self.cv[:, :, :],
                       ACT.Sigmoid).then_inc(*a.did("silu"))
        act.wait_ge(*v.at("dt"))
        act.activation(self.rows[0:8, 5, SEQ:T], self.rows[0:8, 4, SEQ:T], ACT.Exp).then_inc(*a.did("da"))
        for ti in range(NT):
            act.wait_ge(*v.at("cs", ti))
            act.activation(self.tokens[:, ti, 4:6, :], self.tokens[:, ti, 4:6, :], ACT.Exp).then_inc(*a.did("ecs", ti))
            act.wait_ge(*t.at("csb", ti))
            for q in range(2):
                ins = act.activation(self.ecs[:, 4 * q:4 * q + 4, :], k.bank[2 + q][:, :].rearrange("p (h t) -> p h t", h=4), ACT.Exp)
            ins.then_inc(*a.did("ecsb", ti))
            act.wait_ge(*v.at("seg", ti))
            act.activation(self.seg[:, :, :], self.seg[:, :, :], ACT.Exp).then_inc(*a.did("seg", ti))
            self.gates.collect(act, 2)
            if self.ahead and ti == 0:
                self.ahead.load(act, 0)
        self.gates.collect(act, 2)
        if self.ahead:
            self.ahead.load(act, 1)
            for _ in range(3):
                self.ahead.collect(act)
        act.wait_ge(*v.at("skip"))
        act.activation(k.z[:, :, :], k.z[:, :, :], ACT.Silu).then_inc(*a.did("z"))
        act.wait_ge(*v.at("gated"))
        act.activation(self.cv[:, 0:4, :], self.y, ACT.Square).then_inc(*a.did("y_sq"))
        act.wait_ge(*t.at("ms"))
        for g in range(2):
            ins = act.activation(self.cv[:, 4 + g, :], k.bank[g][:, 0:T], ACT.Sqrt, scale=1.0 / 256, bias=k.c("eps"))
        ins.then_inc(*a.did("root"))

    def tensor(self, pe):
        k, t, v, a = self.k, self.t, self.v, self.a
        ident, ones, upto = k.c("ident"), k.c("ones"), k.c("upto")
        self.gates.compute(pe, 4, 5)
        pe.wait_ge(*v.at("dt"))
        pe.wait_ge(*a.at("da"))
        for q, row in enumerate((3, 5)):
            for c in range(4):
                mm = pe.matmul(k.bank[0][:, 32 * q + NB * c:32 * q + NB * c + NB], k.c("spread")[0:8, P * c:P * c + P],
                               self.rows[0:8, row, SEQ:T], start=True, stop=True)
        mm.then_inc(*t.did("s_dt"))
        for ti in range(NT):
            s = slice(P * ti, P * ti + P)
            if ti:
                pe.wait_ge(*v.at("state", ti - 1))
                pe.wait_ge(*v.at("y", ti - 1))
            for q, row in enumerate((3, 4)):
                mm = pe.transpose(k.bank[1][:, 8 * q:8 * q + 8], self.rows[0:8, row, s], ident[0:8, 0:8])
            mm.then_inc(*t.did("tok", ti))
            pe.wait_ge(*v.at("tok", ti))
            pe.matmul(k.bank[1][:, 32:40], upto, self.tokens[:, ti, 1, :], start=True, stop=True)
            mm = pe.matmul(k.bank[1][:, 40:48], ones, self.tokens[:, ti, 1, :], start=True, stop=True)
            mm.then_inc(*t.did("cs", ti))
            for h in range(8):
                mm = pe.matmul(k.bank[2 + h // 4][:, P * (h % 4):P * (h % 4) + P],
                               self.tokens[:, ti, 1, h:h + 1].broadcast_to([P, P]), upto, start=True, stop=True)
            mm.then_inc(*t.did("csb", ti))
            if ti == 0:
                pe.wait_ge(*v.at("silu"))
            self.gates.settle(pe)
            for g in range(2):
                mm = pe.matmul(k.bank[4][:, P * g:P * g + P], self.cv[:, 4 + g, s], self.cv[:, 6 + g, s], start=True, stop=True)
            mm.then_inc(*t.did("gt", ti))
            for c in range(4):
                pe.transpose(k.bank[5][:, P * c:P * c + P], self.cv[:, c, s], ident)
            for c in range(2):
                mm = pe.transpose(k.bank[6][:, P * c:P * c + P], self.cv[:, 4 + c, s], ident)
            mm.then_inc(*t.did("xb_tok", ti))
            self.gates.compute(pe, 7, 0)
            pe.wait_ge(*v.at("mt", ti))
            self.gates.settle(pe)
            for h in range(8):
                o = k.bank[7][64 * (h % 2):64 * (h % 2) + 64, P * (h // 2):P * (h // 2) + P]
                mm = pe.matmul(o, self.xd[:, 64 * h:64 * h + 64], self.seg[:, h, :], start=True, stop=not ti)
                if ti:
                    mm = pe.matmul(o, self.hs[:, 64 * h:64 * h + 64], self.ecs[:, h, :], start=False, stop=True)
            mm.then_inc(*t.did("y", ti))
            for g in range(2):
                mm = pe.matmul(k.bank[0][:, 256 * g:256 * g + 256], self.bt[:, P * g:P * g + P], self.xdd[:, 256 * g:256 * g + 256],
                               start=True, stop=True)
            mm.then_inc(*t.did("state", ti))
        for q in range(2):
            if q:
                self.gates.compute(pe, 5, 6)
                if self.ahead:
                    self.ahead.compute(pe, 4, 7)
                    self.ahead.settle(pe)
            pe.wait_ge(*v.at("s_diag", q))
            self.gates.settle(pe)
            for g in range(2):
                for n in range(2):
                    mm = pe.matmul(k.bank[4 * q + 2 * g + n][:, :], ones,
                                   self.t1[:, g, 4 * n:4 * n + 4, :].rearrange("p b n -> p (b n)"), start=True, stop=True)
            mm.then_inc(*t.did("s_spread", q))
        if self.ahead:
            self.ahead.compute(pe, 2, 3)
            self.ahead.compute(pe, 3, 2)
        pe.wait_ge(*a.at("y_sq"))
        for g in range(2):
            for n in range(2):
                mm = pe.matmul(k.bank[g][:, 0:T], ones, self.cv[:, 2 * g + n, :], start=n == 0, stop=n == 1)
        mm.then_inc(*t.did("ms"))

    def vector(self, dve):
        k, a, t, v, l = self.k, self.a, self.t, self.v, self.l
        do = v.serial(dve)
        r = self.rows[0:8]
        assert self.conv_parts == CONV_PARTS
        do(dve.tensor_scalar(r[:, 0, :], k.dt_raw[0:8, :], k.vec(l, "dt_bias")[0:8, :], None, ALU.add))
        do(dve.tensor_scalar(r[:, 1, :], r[:, 0, :], -1.0, None, ALU.mult))
        do(dve.tensor_tensor(r[:, 1, :], r[:, 0, :], r[:, 1, :], ALU.max), "dt_abs")
        do(dve.tensor_scalar(r[:, 0, :], r[:, 0, :], 0.0, None, ALU.max))
        dve.wait_ge(*a.at("dt_exp"))
        do(dve.tensor_scalar(r[:, 2, :], r[:, 1, :], 2.0, None, ALU.add))
        do(dve.reciprocal(r[:, 2, :], r[:, 2, :]))
        do(dve.tensor_tensor(r[:, 2, :], r[:, 2, :], r[:, 1, :], ALU.mult))
        do(dve.tensor_tensor(r[:, 3, :], r[:, 2, :], r[:, 2, :], ALU.mult))
        do(dve.tensor_scalar(r[:, 4, :], r[:, 3, :], 1.0 / 17, None, ALU.mult))
        for n in range(15, 1, -2):
            do(dve.scalar_tensor_tensor(out=r[:, 4, :], in0=r[:, 4, :], scalar=1.0 / n, in1=r[:, 3, :], op0=ALU.add, op1=ALU.mult))
        do(dve.scalar_tensor_tensor(out=r[:, 4, :], in0=r[:, 4, :], scalar=1.0, in1=r[:, 2, :], op0=ALU.add, op1=ALU.mult))
        do(dve.scalar_tensor_tensor(out=r[:, 3, :], in0=r[:, 4, :], scalar=2.0, in1=r[:, 0, :], op0=ALU.mult, op1=ALU.add))
        do(dve.tensor_scalar(r[:, 4, :], r[:, 3, :], k.small_a[0:8, 0:1], -1.0, ALU.mult, ALU.mult), "dt")
        dve.wait_ge(*a.at("silu"))
        do(dve.tensor_tensor(self.cv[:, :, :], self.cv[:, :, :], self.t1.rearrange("p c b n -> p (c b n)")[:, 0:8 * T].rearrange("p (c t) -> p c t", c=8), ALU.mult), "silu")
        dve.wait_ge(*t.at("s_dt"))
        dve.tensor_copy(self.dtx[:, :, :], k.bank[0][:, 0:32].rearrange("p (c b) -> p c b", c=4))
        do(dve.tensor_copy(self.dax[:, :, :], k.bank[0][:, 32:64].rearrange("p (c b) -> p c b", c=4)))
        for ti in range(NT):
            s = slice(P * ti, P * ti + P)
            tk = self.tokens[:, ti]
            dve.wait_ge(*t.at("tok", ti))
            do(dve.tensor_copy(tk[:, 0:2, :], k.bank[1][:, 0:16].rearrange("p (q h) -> p q h", q=2)), "tok", ti)
            dve.wait_ge(*t.at("cs", ti))
            do(dve.tensor_copy(tk[:, 2:4, :], k.bank[1][:, 32:48].rearrange("p (q h) -> p q h", q=2)))
            dve.tensor_copy(tk[:, 4, :], tk[:, 3, :])
            do(dve.tensor_tensor(tk[:, 5, :], tk[:, 3, :], tk[:, 2, :], ALU.subtract), "cs", ti)
            dve.wait_ge(*a.at("ecsb", ti))
            for q in range(2):
                ins = dve.tensor_tensor(self.seg[:, 4 * q:4 * q + 4, :], k.bank[2 + q][:, :].rearrange("p (h t) -> p h t", h=4),
                                        tk[:, 2, 4 * q:4 * q + 4].unsqueeze(2).broadcast_to([P, 4, P]), ALU.subtract)
            do(ins)
            do(dve.tensor_scalar(self.seg[:, :, :], self.seg[:, :, :], 0.0, None, ALU.min), "seg", ti)
            dve.wait_ge(*t.at("gt", ti))
            do(dve.tensor_tensor(self.gt[:, :, :], k.bank[4][:, 0:256].rearrange("p (g t) -> p g t", g=2), bc(k.c("upto"), 1, 2), ALU.mult))
            dve.wait_ge(*t.at("xb_tok", ti))
            dve.tensor_copy(self.bt[:, :], k.bank[6][:, 0:256])
            do(dve.tensor_tensor(self.xd[:, :].rearrange("p (h d) -> p h d", h=8), k.bank[5][:, :].rearrange("p (h d) -> p h d", h=8),
                                 tk[:, 0, :].unsqueeze(2).broadcast_to([P, 8, 64]), ALU.mult))
            dve.wait_ge(*a.at("ecs", ti))
            do(dve.tensor_tensor(self.xdd[:, :].rearrange("p (h d) -> p h d", h=8), self.xd[:, :].rearrange("p (h d) -> p h d", h=8),
                                 tk[:, 5, :].unsqueeze(2).broadcast_to([P, 8, 64]), ALU.mult))
            dve.wait_ge(*a.at("ecsb", ti))
            dve.wait_ge(*a.at("seg", ti))
            for g in range(2):
                hs = slice(4 * g, 4 * g + 4)
                dve.tensor_tensor(self.seg[:, hs, :], self.seg[:, hs, :], bc(self.gt[:, g, :], 1, 4), ALU.mult)
                ins = dve.tensor_tensor(self.ecs[:, hs, :], self.ecs[:, hs, :], bc(self.cv[:, 6 + g, s], 1, 4), ALU.mult)
            do(ins, "mt", ti)
            dve.wait_ge(*t.at("y", ti))
            do(dve.tensor_copy(self.y[:, :, s], k.bank[7][:, :].rearrange("p (c t) -> p c t", c=4)), "y", ti)
            dve.wait_ge(*t.at("state", ti))
            if ti:
                do(dve.tensor_tensor(self.hs[:, :].rearrange("p (h d) -> p h d", h=8), self.hs[:, :].rearrange("p (h d) -> p h d", h=8),
                                     tk[:, 4, :].unsqueeze(2).broadcast_to([P, 8, 64]), ALU.mult))
                do(dve.tensor_tensor(self.hs[:, :], self.hs[:, :], k.bank[0][:, :], ALU.add), "state", ti)
            else:
                do(dve.tensor_copy(self.hs[:, :], k.bank[0][:, :]), "state", ti)
        sam = slice(SEQ, T)
        do(dve.tensor_tensor(self.dtx[:, :, :], self.dtx[:, :, :], self.cv[:, 0:4, sam], ALU.mult), "y_off")
        for q, c0 in enumerate((4, 6)):
            for g in range(2):
                ins = dve.tensor_tensor(self.t1[:, g], bc(k.c("ident"), 1, NB), self.cv[:, c0 + g, sam].unsqueeze(2).broadcast_to([P, NB, P]), ALU.mult)
            do(ins, "s_diag", q)
            if q == 0:
                dve.wait_ge(k.ssm_loaded, 16 * (l + 1))
                for c in range(4):
                    ins = dve.tensor_tensor(self.st[:, c], self.st[:, c], self.dax[:, c].unsqueeze(2).broadcast_to([P, NB, P]), ALU.mult)
                do(ins)
            dve.wait_ge(*t.at("s_spread", q))
            for c in range(4):
                for n in range(2):
                    bs = slice(4 * n, 4 * n + 4)
                    src = k.bank[4 * q + 2 * (c // 2) + n][:, :].rearrange("p (b n) -> p b n", b=4)
                    other = self.dtx[:, c, bs].unsqueeze(2).broadcast_to([P, 4, P]) if q == 0 else self.st[:, c, bs, :]
                    ins = dve.tensor_tensor(self.t1[:, c, bs, :], src, other, ALU.mult)
            do(ins)
            if q == 0:
                do(dve.tensor_tensor(self.st, self.st, self.t1, ALU.add), "s_state")
        for c in range(4):
            ins = dve.tensor_reduce(self.y[:, c, sam], self.t1[:, c], X, ALU.add)
        do(ins)
        for c in range(4):
            ins = dve.scalar_tensor_tensor(out=self.y[:, c, :], in0=self.cv[:, c, :], scalar=k.vec(l, "d")[:, c:c + 1], in1=self.y[:, c, :],
                                           op0=ALU.mult, op1=ALU.add)
        do(ins, "skip")
        dve.wait_ge(*a.at("z"))
        do(dve.tensor_tensor(self.y, self.y, k.z[:, :, :], ALU.mult), "gated")
        dve.wait_ge(*a.at("root"))
        do(dve.reciprocal(self.cv[:, 4:6, :], self.cv[:, 4:6, :]))
        for c in range(4):
            ins = dve.tensor_tensor(self.y[:, c, :], self.y[:, c, :], self.cv[:, 4 + c // 2, :], ALU.mult)
        do(ins)
        for c in range(4):
            ins = dve.tensor_scalar(self.y[:, c, :], self.y[:, c, :], k.vec(l, "ssm_norm")[:, c:c + 1], None, ALU.mult)
        do(ins)


class Mla(Stage):
    GROUP = 2

    def __init__(self, k, l):
        super().__init__(k, "mla", l)
        self.ahead = k.ahead
        ar = Arena(k.sb, k.mla_at, k.mla_size)
        self.w = ar.take(NMLA)
        self.q = ar.take(8, T)
        tmp_at = ar.next
        self.tmp = ar.take(6, T)
        self.kpe = ar.take(T)
        self.cache = [ar.take(self.GROUP, NPAGE, CACHE) for _ in range(2)]
        early = Arena(k.sb, ar.next - self.GROUP * NPAGE * CACHE, self.GROUP * NPAGE * CACHE)
        self.kn, self.vt = early.take(8, SEQ), early.take(NT, 512)
        late, ar = ar, Arena(k.sb, tmp_at, 6 * T)
        self.qabs, self.qpe = ar.take(2, NB, ROWS), ar.take(NB, ROWS)
        self.ckv_new, self.probsT = ar.take(LORA), ar.take(NPAGE, self.GROUP * ROWS)
        self.s_own, self.p_own = ar.take(NB), ar.take(NB)
        self.m, self.less_m, self.psum = ar.take(4), ar.take(1), ar.take(2)
        ar = late
        self.olat_rows, self.olat, self.p_ownT = ar.take(LORA), ar.take(2, NB, 8), ar.take(self.GROUP * ROWS)
        self.mx, self.sm = ar.take(8), ar.take(8)
        self.s = ar.take(8 * SEQ)
        self.pt = ar.take(2, 8, P)
        self.kT = self.s.rearrange("p (c t) -> p c t", c=2)
        self.kpT = self.pt.rearrange("p a b c -> p (a b c)")[0:32, 0:1024]
        self.probs = self.pt.rearrange("p a b c -> p (a b c)")[0:self.GROUP * ROWS, 1024:2048]
        self.root = self.tmp[:, 4:6, :]

    def weights(self, name, n):
        return self.w[:, MLA_W[name][0]:MLA_W[name][1]].rearrange("p (c n) -> p c n", c=n)

    def load(self, sp):
        k, l = self.k, self.l
        for who in ("tensor", "vector", "scalar", "pool"):
            sp.wait_ge(*self.before.by(who).at("end"))
        sp.dma_start(self.w[:, :], k.mla_w[l]).then_inc(k.mla_w_loaded, 16)
        if l == 0:
            sp.wait_ge(k.const_loaded, 48)
        for i in range(NB // self.GROUP):
            pages = []
            for n in range(self.GROUP * NPAGE):
                reg = k.page_regs[n]
                at = self.GROUP * NPAGE * i + n
                sp.reg_load(reg, k.table[0:1, at:at + 1])
                pages.append(sp.snap(reg, min_val=0, max_val=k.cache.shape[1] - 1))
            if i == 1:
                sp.wait_ge(*self.v.at("prompt_out"))
            if i >= 2:
                sp.wait_ge(*self.t.at("pv", i - 2))
            for n, page in enumerate(pages):
                dst = self.cache[i % 2][:, n // NPAGE, n % NPAGE, :]
                sp.dma_start(dst, k.cache[l, bass.ds(page, 1)].rearrange("o s c -> (o s) c")).then_inc(k.pages_loaded[i % 2], 16)

    def pool(self, g):
        k, l = self.k, self.l
        g.wait_ge(*self.v.at("ckv"))
        g.dma_start(k.out["ckv"][l], k.qkv[:, 2:4, :]).then_inc(k.stored, 16)
        g.wait_ge(*self.v.at("pe"))
        g.dma_start(k.out["kpe"][l], self.kpe[0:32, :]).then_inc(k.stored, 16)
        k.stores += 2
        g.wait_ge(k.stored, 16 * k.stores)
        g.memset(k.pool_mark[0:1, 0:1], 0.0).then_inc(*self.g.did("stored"))

    def tensor(self, pe):
        k, t, v, a = self.k, self.t, self.v, self.a
        ident, ones = k.c("ident"), k.c("ones")
        w_uq, w_uk, w_uv, w_ukT = (self.weights(n, c) for n, c in (("w_uq", 2), ("w_uk", 2), ("w_uv", 2), ("w_ukT", 8)))
        if self.ahead:
            self.ahead.compute(pe, 6, 7)
        pe.wait_ge(*a.at("latent_sq"))
        for g in range(2):
            for n in range(2):
                mm = pe.matmul(k.bank[g][:, 0:T], ones, self.tmp[:, 2 * g + n, :], start=n == 0, stop=n == 1)
        mm.then_inc(*t.did("latent_ms"))
        mm = pe.matmul(k.bank[2][:, 0:T], k.c("rotate"), k.kr[:, :], start=True, stop=True)
        mm.then_inc(*t.did("kr_rot"))
        if self.ahead:
            self.ahead.compute(pe, 6, 7)
        pe.wait_ge(k.mla_w_loaded, 16 * (self.l + 1))
        pe.wait_ge(*v.at("ckv"))
        for h in range(8):
            if h >= 2:
                pe.wait_ge(*a.at("q", h - 2))
            for n in range(2):
                mm = pe.matmul(k.bank[4 + h % 2][0:96, 0:T], w_uq[:, n, 96 * h:96 * h + 96], k.qkv[:, n, :], start=n == 0, stop=n == 1)
            mm.then_inc(*t.did("q", h))
        pe.wait_ge(*v.at("pe_key"))
        for h in range(8):
            pe.wait_ge(*a.at("q", h))
            if h >= 2:
                pe.wait_ge(*v.at("q_rot", h - 2))
            mm = pe.matmul(k.bank[2 + h % 2][64:96, 0:T], k.c("rotate")[64:96, 64:96], self.q[64:96, h, :], start=True, stop=True,
                           tile_position=(64, 64))
            mm.then_inc(*t.did("q_rot", h))
        if self.ahead:
            self.ahead.settle(pe)
        for h in range(8):
            if h == 4:
                pe.wait_ge(*a.at("q", 7))
            for n in range(2):
                mm = pe.matmul(k.bank[(6, 7, 4, 5)[h // 2]][0:64, SEQ * (h % 2):SEQ * (h % 2) + SEQ], w_uk[:, n, 64 * h:64 * h + 64],
                               k.qkv[:, 2 + n, 0:SEQ], start=n == 0, stop=n == 1)
        mm.then_inc(*t.did("keys"))
        for i in range(NT):
            for n in range(2):
                mm = pe.matmul(k.bank[i][:, :], k.qkv[:, 2 + n, P * i:P * i + P], w_uv[:, n, :], start=n == 0, stop=n == 1)
        mm.then_inc(*t.did("values"))
        pe.wait_ge(*v.at("pe"))
        pe.wait_ge(*a.at("kv"))
        for qi in range(NT):
            nk = P * (qi + 1)
            per = 512 // nk
            if qi:
                pe.wait_ge(*v.at("masked", qi - 1))
            for h in range(8):
                o = k.bank[2 + h // per][:, nk * (h % per):nk * (h % per) + nk]
                mm = pe.matmul(o, self.q[0:96, h, P * qi:P * qi + P], self.kn[0:96, h, 0:nk], start=True, stop=True)
            mm.then_inc(*t.did("scores", qi))
            if self.ahead:
                for _ in range(qi + 1):
                    self.ahead.compute(pe, 4 + 2 * qi, 5 + 2 * qi)
                self.ahead.settle(pe)
            pe.wait_ge(*v.at("probs", qi))
            s = self.s[:, 0:8 * nk].rearrange("p (h n) -> p h n", h=8)
            for ki in range(qi + 1):
                if ki:
                    pe.wait_ge(*a.at("pt", qi, ki - 1))
                for h in range(8):
                    mm = pe.transpose(k.bank[6 + h // 4][:, P * (h % 4):P * (h % 4) + P], s[:, h, P * ki:P * ki + P], ident)
                mm.then_inc(*t.did("pt", qi, ki))
            pe.wait_ge(*a.at("pt", qi, qi))
            for h in range(8):
                o = k.bank[h // 4][64 * (h % 2):64 * (h % 2) + 64, SEQ * (h // 2 % 2) + P * qi:SEQ * (h // 2 % 2) + P * qi + P]
                for ki in range(qi + 1):
                    mm = pe.matmul(o, self.vt[:, ki, 64 * h:64 * h + 64], self.pt[:, ki, h, :], start=ki == 0, stop=ki == qi)
            mm.then_inc(*t.did("out", qi))
        if self.ahead:
            self.ahead.turn(pe, ADA_AHEAD - 1, 7)
        pe.wait_ge(*v.at("masked", NT - 1))
        for cc in range(2):
            for h in range(8):
                mm = pe.matmul(k.bank[2][:, 64 * cc + NB * h:64 * cc + NB * h + NB], w_ukT[0:64, h, P * cc:P * cc + P],
                               self.q[0:64, h, SEQ:T], start=True, stop=True)
        for h in range(8):
            mm = pe.matmul(k.bank[3][0:32, NB * h:NB * h + NB], ident[64:96, 64:96], self.q[64:96, h, SEQ:T], start=True, stop=True,
                           tile_position=(64, 0))
        for cc in range(2):
            mm = pe.transpose(k.bank[3][0:NB, 128 + P * cc:256 + P * cc], k.qkv[:, 2 + cc, SEQ:T], ident)
        mm.then_inc(*t.did("queries"))
        if self.ahead:
            pe.wait_ge(*self.ahead.a.at("columns", ADA_AHEAD - 1))
        pe.wait_ge(*v.at("queries"))
        pe.wait_ge(*v.at("prompt_out"))
        G, R = self.GROUP, self.GROUP * ROWS
        groups = NB // G

        def turn_pages(i, j):
            if j == 0:
                pe.wait_ge(k.pages_loaded[i % 2], 16 * G * NPAGE * (2 * self.l + i // 2 + 1))
            cache = self.cache[i % 2]
            i0, j0 = (i, j - 1) if j else (i - 1, G - 1)
            for p in range(NPAGE):
                if p % 2 == 0 and (i or j or p >= 4):
                    pe.wait_ge(*(a.at("kT", i, j, p // 2 - 2) if p >= 4 else a.at("kT", i0, j0, p // 2 + 2)))
                for cc in range(2):
                    mm = pe.transpose(k.bank[4 + p // 2 % 2][:, 256 * cc + P * (p % 2):256 * cc + P * (p % 2) + P], cache[:, j, p, P * cc:P * cc + P], ident)
                if p % 2:
                    mm.then_inc(*t.did("kT", i, j, p // 2))
                if p % 4 == 0 and (i or j):
                    pe.wait_ge(*v.at("kpT", i0, j0, p // 4))
                mm = pe.transpose(k.bank[6 + p // 4][0:32, P * (p % 4):P * (p % 4) + P], cache[:, j, p, LORA:CACHE], ident)
                if p % 4 == 3:
                    mm.then_inc(*t.did("kpT", i, j, p // 4))

        def scores(i, j):
            b = G * i + j
            if i and j == 0:
                pe.wait_ge(*a.at("s_exp", i - 1))
            pe.wait_ge(*a.at("kT", i, j, 3))
            pe.wait_ge(*v.at("kpT", i, j, 1))
            rows = slice(ROWS * j, ROWS * j + ROWS)
            for q in range(2):
                cols = slice(512 * q, 512 * q + 512)
                for cc in range(2):
                    pe.matmul(k.bank[q][rows, :], self.qabs[:, cc, b, :], self.kT[:, cc, cols], start=cc == 0, stop=False)
                pe.matmul(k.bank[q][rows, :], self.qpe[0:32, b, :], self.kpT[:, cols], start=False, stop=True)
            for cc in range(2):
                pe.matmul(k.bank[3][rows, 0:NB], self.qabs[:, cc, b, :], k.qkv[:, 2 + cc, SEQ:T], start=cc == 0, stop=False)
            pe.matmul(k.bank[3][rows, 0:NB], self.qpe[0:32, b, :], self.kpe[0:32, SEQ:T], start=False, stop=True).then_inc(*t.did("s_scores", i, j))

        def turn_olat(i):
            pe.wait_ge(*v.at("olat_rows", i))
            for cc in range(2):
                mm = pe.transpose(k.bank[2][:, 384 + R * cc:384 + R * cc + R], self.olat_rows[0:R, P * cc:P * cc + P], ident[0:R, 0:R])
            mm.then_inc(*t.did("olatT", i))
        for i in range(groups):
            if i == 0:
                turn_pages(0, 0)
            scores(i, 0)
            turn_pages(i, 1)
            if i:
                turn_olat(i - 1)
            scores(i, 1)
            if i + 1 < groups:
                turn_pages(i + 1, 0)
            pe.wait_ge(*a.at("s_exp", i))
            if i:
                pe.wait_ge(*v.at("olat", i - 1))
            for p in range(NPAGE):
                pe.transpose(k.bank[3][:, R * p:R * p + R], self.probs[:, P * p:P * p + P], ident[0:R, 0:R])
            pe.transpose(k.bank[2][0:NB, 64:64 + R], self.p_own[0:R, :], ident[0:R, 0:R]).then_inc(*t.did("probsT", i))
            pe.wait_ge(*a.at("probsT", i))
            cache = self.cache[i % 2]
            for j in range(G):
                rows = slice(ROWS * j, ROWS * j + ROWS)
                for p in range(NPAGE):
                    pe.matmul(k.bank[2][rows, 128:384], self.probsT[:, p, rows], cache[:, j, p, 0:LORA], start=p == 0, stop=False)
                mm = pe.matmul(k.bank[2][rows, 128:384], self.p_ownT[0:NB, rows], self.ckv_new[0:NB, :], start=False, stop=True)
            mm.then_inc(*t.did("pv", i))
        turn_olat(groups - 1)
        pe.wait_ge(*v.at("olat", groups - 1))
        for h in range(8):
            o = k.bank[1][64 * (h % 2):64 * (h % 2) + 64, NB * (h // 2):NB * (h // 2) + NB]
            for cc in range(2):
                mm = pe.matmul(o, w_uv[:, cc, 64 * h:64 * h + 64], self.olat[:, cc, :, h], start=cc == 0, stop=cc == 1)
        mm.then_inc(*t.did("s_out"))

    def scalar(self, act):
        k, t, v, a = self.k, self.t, self.v, self.a
        act.activation(self.tmp[:, 0:4, :], k.qkv[:, :, :], ACT.Square).then_inc(*a.did("latent_sq"))
        if self.ahead:
            self.ahead.collect(act)
        act.wait_ge(*t.at("latent_ms"))
        for g in range(2):
            ins = act.activation(self.root[:, g, :], k.bank[g][:, 0:T], ACT.Sqrt, scale=1.0 / 256, bias=k.c("eps"))
        ins.then_inc(*a.did("latent_root"))
        if self.ahead:
            self.ahead.collect(act)
        for h in range(8):
            act.wait_ge(*t.at("q", h))
            act.copy(self.q[0:96, h, :], k.bank[4 + h % 2][0:96, 0:T]).then_inc(*a.did("q", h))
        act.wait_ge(*t.at("keys"))
        for n in range(4):
            act.copy(self.kn[0:64, 2 * n:2 * n + 2, :], k.bank[(6, 7, 4, 5)[n]][0:64, :].rearrange("p (h t) -> p h t", h=2))
        act.wait_ge(*t.at("values"))
        act.copy(self.vt[:, 0, :], k.bank[0][:, :])
        act.copy(self.vt[:, 1, :], k.bank[1][:, :]).then_inc(*a.did("kv"))
        for qi in range(NT):
            nk = P * (qi + 1)
            act.wait_ge(*v.at("less_max", qi))
            act.activation(self.s[:, 0:8 * nk], self.s[:, 0:8 * nk], ACT.Exp, scale=MLA_SCALE).then_inc(*a.did("exp", qi))
            if self.ahead:
                for _ in range(qi + 1):
                    self.ahead.collect(act)
            for ki in range(qi + 1):
                act.wait_ge(*t.at("pt", qi, ki))
                for g in range(2):
                    ins = act.copy(self.pt[:, ki, 4 * g:4 * g + 4, :].rearrange("p h t -> p (h t)"), k.bank[6 + g][:, :])
                ins.then_inc(*a.did("pt", qi, ki))
        if self.ahead:
            self.ahead.keep_columns(act, ADA_AHEAD - 1)
        act.wait_ge(*v.at("queries"))
        act.wait_ge(*t.at("out", NT - 1))
        G = self.GROUP
        groups = NB // G

        def keep_pages(i, j, *parts):
            if i or j:
                act.wait_ge(*t.at("s_scores", *((i, j - 1) if j else (i - 1, G - 1))))
            for n in parts:
                act.wait_ge(*t.at("kT", i, j, n))
                act.copy(self.kT[:, :, 256 * n:256 * n + 256], k.bank[4 + n % 2][:, :].rearrange("p (c t) -> p c t", c=2)).then_inc(*a.did("kT", i, j, n))
        keep_pages(0, 0, 0, 1, 2, 3)
        for i in range(groups):
            keep_pages(i, 1, 0, 1, 2, 3)
            if i + 1 < groups:
                keep_pages(i + 1, 0, 0, 1)
            act.wait_ge(*v.at("s_max", i))
            bias = self.less_m[0:G * ROWS, :]
            for q in range(2):
                act.activation(self.probs[:, 512 * q:512 * q + 512], k.bank[q][0:G * ROWS, :], ACT.Exp, scale=MLA_SCALE, bias=bias)
            act.activation(self.p_own[0:G * ROWS, :], self.s_own[0:G * ROWS, :], ACT.Exp, scale=MLA_SCALE, bias=bias).then_inc(*a.did("s_exp", i))
            if i + 1 < groups:
                keep_pages(i + 1, 0, 2, 3)
            act.wait_ge(*t.at("probsT", i))
            act.copy(self.probsT[:, :, :].rearrange("p n r -> p (n r)"), k.bank[3][:, :])
            act.copy(self.p_ownT[0:NB, :], k.bank[2][0:NB, 64:64 + G * ROWS]).then_inc(*a.did("probsT", i))

    def vector(self, dve):
        k, a, t, v, l = self.k, self.a, self.t, self.v, self.l
        do = v.serial(dve)
        dve.wait_ge(*a.at("latent_root"))
        do(dve.reciprocal(self.root[:, :, :], self.root[:, :, :]))
        for c in range(4):
            name = "q_norm" if c < 2 else "kv_norm"
            ins = dve.scalar_tensor_tensor(out=k.qkv[:, c, :], in0=k.qkv[:, c, :], scalar=k.vec(l, name)[:, c % 2:c % 2 + 1],
                                           in1=self.root[:, c // 2, :], op0=ALU.mult, op1=ALU.mult)
        do(ins, "ckv")
        cos, sin = k.c("cos"), k.c("sin")
        do(dve.tensor_tensor(self.kpe[:, :], k.kr[:, :], cos, ALU.mult))
        dve.wait_ge(*t.at("kr_rot"))
        do(dve.tensor_tensor(self.tmp[:, 0, :], k.bank[2][:, 0:T], sin, ALU.mult), "pe_key")
        do(dve.tensor_tensor(self.kpe[:, :], self.kpe[:, :], self.tmp[:, 0, :], ALU.add))
        rp = slice(64, 96)
        do(dve.tensor_copy(self.kn[rp, :, :], bc(self.kpe[rp, 0:SEQ], 1, 8)))
        for h in range(8):
            dve.wait_ge(*t.at("q_rot", h))
            dve.tensor_tensor(self.q[rp, h, :], self.q[rp, h, :], cos[rp, :], ALU.mult)
            do(dve.tensor_tensor(self.tmp[rp, h % 2, :], k.bank[2 + h % 2][rp, 0:T], sin[rp, :], ALU.mult), "q_rot", h)
            do(dve.tensor_tensor(self.q[rp, h, :], self.q[rp, h, :], self.tmp[rp, h % 2, :], ALU.add), *(("pe",) if h == 7 else ()))
        for qi in range(NT):
            nk = P * (qi + 1)
            per = 512 // nk
            s = self.s[:, 0:8 * nk].rearrange("p (h n) -> p h n", h=8)
            dve.wait_ge(*t.at("scores", qi))
            if qi:
                dve.wait_ge(*t.at("pt", qi - 1, qi - 1))
            for n in range(8 // per):
                hs = slice(per * n, per * n + per)
                src = k.bank[2 + n][:, :].rearrange("p (h n) -> p h n", h=per)
                if qi:
                    dve.tensor_copy(s[:, hs, 0:P * qi], src[:, :, 0:P * qi])
                ins = dve.tensor_tensor(s[:, hs, P * qi:nk], src[:, :, P * qi:nk], bc(k.c("causal"), 1, per), ALU.add)
            do(ins, "masked", qi)
            do(dve.tensor_reduce(self.mx[:, :], s, X, ALU.max))
            do(dve.tensor_tensor(s, s, self.mx[:, :].unsqueeze(2).broadcast_to([P, 8, nk]), ALU.subtract), "less_max", qi)
            dve.wait_ge(*a.at("exp", qi))
            do(dve.tensor_reduce(self.sm[:, :], s, X, ALU.add))
            do(dve.reciprocal(self.sm[:, :], self.sm[:, :]))
            do(dve.tensor_tensor(s, s, self.sm[:, :].unsqueeze(2).broadcast_to([P, 8, nk]), ALU.mult), "probs", qi)
        dve.wait_ge(*t.at("out", NT - 1))
        for c in range(4):
            ins = dve.tensor_copy(k.branches[:, c, 0:SEQ], k.bank[c // 2][:, SEQ * (c % 2):SEQ * (c % 2) + SEQ])
        do(ins, "prompt_out")
        do(dve.memset(self.qabs[:, :, :, :], 0.0))
        do(dve.memset(self.qpe[0:32], 0.0))
        dve.wait_ge(*t.at("queries"))
        for cc in range(2):
            dve.tensor_copy(self.qabs[:, cc, :, 0:8].rearrange("p b h -> p h b"), k.bank[2][:, 64 * cc:64 * cc + 64].rearrange("p (h b) -> p h b", h=8))
        do(dve.tensor_copy(self.qpe[0:32, :, 0:8].rearrange("p b h -> p h b"), k.bank[3][0:32, 0:64].rearrange("p (h b) -> p h b", h=8)))
        do(dve.tensor_copy(self.ckv_new[0:NB, :], k.bank[3][0:NB, 128:128 + LORA]), "queries")
        G, R = self.GROUP, self.GROUP * ROWS
        groups = NB // G

        def keep_rotary(i, j):
            if i or j:
                dve.wait_ge(*t.at("s_scores", *((i, j - 1) if j else (i - 1, G - 1))))
            for n in range(2):
                dve.wait_ge(*t.at("kpT", i, j, n))
                dve.tensor_copy(self.kpT[:, 512 * n:512 * n + 512], k.bank[6 + n][0:32, :]).then_inc(*v.did("kpT", i, j, n))

        def keep_olat(i):
            dve.wait_ge(*t.at("olatT", i))
            src = k.bank[2][:, 384:384 + 2 * R].rearrange("p (c b h) -> p c b h", c=2, b=G)
            for cc in range(2):
                ins = dve.tensor_copy(self.olat[:, cc, G * i:G * i + G, :], src[:, cc, :, 0:8])
            do(ins, "olat", i)
        keep_rotary(0, 0)
        for i in range(groups):
            keep_rotary(i, 1)
            if i:
                keep_olat(i - 1)
            dve.wait_ge(*t.at("s_scores", i, G - 1))
            do(dve.tensor_tensor(self.s_own[0:R, :], k.bank[3][0:R, 0:NB], k.c("own")[0:R, NB * i:NB * i + NB], ALU.add))
            for q in range(2):
                do(dve.tensor_reduce(self.m[0:R, q:q + 1], k.bank[q][0:R, :], X, ALU.max))
            do(dve.tensor_reduce(self.m[0:R, 2:3], self.s_own[0:R, :], X, ALU.max))
            do(dve.tensor_reduce(self.m[0:R, 3:4], self.m[0:R, 0:3], X, ALU.max))
            do(dve.tensor_scalar(self.less_m[0:R, :], self.m[0:R, 3:4], -MLA_SCALE, None, ALU.mult), "s_max", i)
            if i + 1 < groups:
                keep_rotary(i + 1, 0)
            dve.wait_ge(*a.at("s_exp", i))
            do(dve.tensor_reduce(self.psum[0:R, 0:1], self.probs[:, :], X, ALU.add))
            do(dve.tensor_reduce(self.psum[0:R, 1:2], self.p_own[0:R, :], X, ALU.add))
            do(dve.tensor_tensor(self.psum[0:R, 0:1], self.psum[0:R, 0:1], self.psum[0:R, 1:2], ALU.add))
            do(dve.reciprocal(self.psum[0:R, 0:1], self.psum[0:R, 0:1]))
            dve.wait_ge(*t.at("pv", i))
            do(dve.tensor_scalar(self.olat_rows[0:R, :], k.bank[2][0:R, 128:384], self.psum[0:R, 0:1], None, ALU.mult), "olat_rows", i)
        keep_olat(groups - 1)
        dve.wait_ge(*t.at("s_out"))
        do(dve.tensor_copy(k.branches[:, 0:4, SEQ:T], k.bank[1][:, 0:32].rearrange("p (c b) -> p c b", c=4)))


class Merge(Stage):

    def __init__(self, k, l):
        super().__init__(k, "merge", l)
        self.mix, self.gated = k.merge_mix, k.merge_gated
        self.slots = []
        for r in range(3):
            place = k.next_place()
            dst = k.slot(place).rearrange("p (c n) -> p c n", c=4)
            wb = k.ring.add(place, dst, k.w_branch[l, r].rearrange("(c p) n -> p c n", p=P))
            self.slots.append(wb)
        self.out_slots = []
        for i in range(2):
            place = k.next_place()
            dst = k.slot(place).rearrange("p (k n) -> p k n", k=KC)
            self.out_slots.append(k.ring.add(place, dst, k.w_out[l].rearrange("(k p) n -> p k n", p=P)[:, :, 512 * i:512 * i + 512]))

    def tensor(self, pe):
        k, t, v = self.k, self.t, self.v
        for r, slot in enumerate(self.slots):
            k.ring.arrived(pe, slot)
            w = k.ring.loads[slot][1]
            for d in range(KC):
                n = KC * r + d
                if n >= 8:
                    pe.wait_ge(*v.at("merged", n - 8))
                for c in range(4):
                    mm = pe.matmul(k.bank[n % 8][:, 0:T], w[:, c, P * d:P * d + P], k.branches[:, 4 * r + c, :], start=c == 0, stop=c == 3)
                mm.then_inc(*t.did("branch", n))
            k.ring.release(slot, t)
        pe.wait_ge(*v.at("merged", 3 * KC - 1))
        for d in range(KC):
            slot = self.out_slots[d // 4]
            k.ring.arrived(pe, slot)
            w = k.ring.loads[slot][1]
            for kk in range(KC):
                mm = pe.matmul(k.bank[d][:, 0:T], w[:, kk, P * (d % 4):P * (d % 4) + P], self.mix[:, kk, :], start=kk == 0, stop=kk == KC - 1)
            mm.then_inc(*t.did("out", d))
            if d % 4 == 3:
                k.ring.release(slot, t)

    def scalar(self, act):
        k = self.k
        for n in range(3 * KC):
            act.activation(k.gates[:, n, :], k.gates[:, n, :], ACT.Sigmoid).then_inc(*self.a.did("gate", n))

    def vector(self, dve):
        k, t, a, v = self.k, self.t, self.a, self.v
        do = v.serial(dve)
        for n in range(3 * KC):
            d = n % KC
            dve.wait_ge(*a.at("gate", n))
            dve.wait_ge(*t.at("branch", n))
            src = k.bank[n % 8][:, 0:T]
            if n < KC:
                do(dve.tensor_tensor(self.mix[:, d, :], src, k.gates[:, n, :], ALU.mult), "merged", n)
            else:
                do(dve.tensor_tensor(self.gated[:, n % 2, :], src, k.gates[:, n, :], ALU.mult))
                do(dve.tensor_tensor(self.mix[:, d, :], self.mix[:, d, :], self.gated[:, n % 2, :], ALU.add), "merged", n)
        for d in range(KC):
            dve.wait_ge(*t.at("out", d))
            add_gated(k, dve, do, k.bank[d], d, 2)


def add_gated(k, dve, do, src, d, part):
    gate = k.ada[:, 8 * part + d, :]
    do(dve.tensor_tensor(k.gated_s[:, :], src[:, SEQ:T], gate[:, 1:NSEQ], ALU.mult))
    dve.tensor_tensor(k.x[:, d, SEQ:T], k.x[:, d, SEQ:T], k.gated_s[:, :], ALU.add)
    do(dve.scalar_tensor_tensor(out=k.x[:, d, 0:SEQ], in0=src[:, 0:SEQ], scalar=gate[:, 0:1], in1=k.x[:, d, 0:SEQ],
                                op0=ALU.mult, op1=ALU.add))


class Experts(Stage):

    def __init__(self, k, l):
        super().__init__(k, "experts", l)
        self.w1, self.w3, self.w2 = k.e1[l // 2], k.e3[l // 2], k.e2[l // 2]
        self.lt, self.lv, self.la = (k.loop_steps(f"experts_loop_{w}") for w in ("tensor", "vector", "scalar"))
        k.experts = self

    def turns(self, eng, body, *before):
        k = self.k
        eng.wait_ge(*self.v.at("turns"))
        turns = eng.value_load(k.turns_i[0:1, NE - 1:NE], min_val=1, max_val=MAX_TURNS)
        for do in before:
            do()
        with eng.Fori(0, turns) as n:
            body(n)
        return turns

    def expert(self, eng, turn):
        return eng.value_load(self.k.turn_expert_i[0:1, turn], min_val=0, max_val=NE - 1)

    def loaded(self, eng, n, s):
        eng.wait_ge(self.k.moe_loaded[s % MOE_RING], (MOE_UNITS // MOE_RING) * 16 * n + 16 * (s // MOE_RING + 1))

    def split(self, n, s):
        return self.k.unit_split, MOE_RING + n * MOE_UNITS + s + 1

    def place_free(self, n, s):
        return self.k.unit_split, n * MOE_UNITS + s + 1

    def used(self, n, s):
        return self.k.unit_used, MOE_SPLIT + n * MOE_UNITS + s + 1

    def split_free(self, n, s):
        return self.k.unit_used, n * MOE_UNITS + s + 1

    def sync(self, sp):
        k = self.k

        def body(n):
            e = self.expert(sp, bass.ds(n, 1))
            w1, w3, w2 = (w[bass.ds(e, 1)].rearrange("o (k p) n -> p (o k) n", p=P) for w in (self.w1, self.w3, self.w2))
            for s in range(MOE_UNITS):
                dst = k.units[:, s % MOE_RING, :]
                if s < MOE_UP:
                    f, q, half = s // 4, s // 2 % 2, s % 2
                    src = (w1, w3)[q][:, 4 * half:4 * half + 4, 512 * f:512 * f + 512]
                    dst = dst.rearrange("p (k n) -> p k n", k=4)
                else:
                    src = w2[:, 2 * (s - MOE_UP):2 * (s - MOE_UP) + 2, :]
                    dst = dst.rearrange("p (k n) -> p k n", k=2)
                sp.wait_ge(*self.place_free(n, s))
                sp.dma_start(dst, src).then_inc(k.moe_loaded[s % MOE_RING], 16)
        self.turns(sp, body)

    def tensor(self, pe):
        k, t, v, a = self.k, self.t, self.v, self.a
        ident, ones = k.c("ident"), k.c("ones")
        router = k.small[:, SMALL["router"][0]:SMALL["router"][1]].rearrange("p (k e) -> p k e", k=KC)
        for i in range(3):
            m = P if i < 2 else NB
            for kk in range(KC):
                mm = pe.matmul(k.bank[0][0:m, 8 * i:8 * i + 8], k.h[:, kk, P * i:P * i + m], router[:, kk, :], start=kk == 0, stop=kk == KC - 1)
        mm.then_inc(*t.did("logits"))
        for i in range(3):
            m = P if i < 2 else NB
            for c in range(KC):
                mm = pe.transpose(k.bank[1 + 2 * i + c // 4][0:m, P * (c % 4):P * (c % 4) + P], k.h[:, c, P * i:P * i + m], ident)
            mm.then_inc(*t.did("h_tok", i))
        pe.wait_ge(*v.at("mask"))
        for i in range(3):
            m = P if i < 2 else NB
            o = k.bank[0][0:m, 32 * i:32 * i + 8]
            for j in range(i + 1):
                mj = P if j < 2 else NB
                w = (k.c("strict") if j == i else ones)[0:mj, 0:m]
                pe.matmul(o, w, k.mask[0:mj, :, j], start=j == 0, stop=j == i)
        for j in range(3):
            mj = P if j < 2 else NB
            mm = pe.matmul(k.bank[0][:, 96:104], ones[0:mj, :], k.mask[0:mj, :, j], start=j == 0, stop=j == 2)
        mm.then_inc(*t.did("rank"))

        def gather(turn):
            pe.wait_ge(k.places_made, turn + 1)
            for c in range(KC):
                for i in range(3):
                    m = P if i < 2 else NB
                    mm = pe.matmul(k.bank[(3, 4)[c // 4]][:, P * (c % 4):P * (c % 4) + P], k.h_tok[0:m, i, P * c:P * c + P], k.sel[0:m, i, :],
                                   start=i == 0, stop=i == 2)
                if c % 4 == 3:
                    mm.then_inc(k.gathered, 1)

        def first():
            for bank in (5, 6):
                mm = pe.matmul(k.bank[bank][:, :], k.moe_out[:, 0, 0:P], k.moe_out.rearrange("p c t -> p (c t)")[:, 0:512], start=True, stop=True)
            mm.then_inc(k.unit_used, MOE_SPLIT)
            gather(0)

        def product(out, hi, lo, s, at, start, stop):
            w_hi, w_lo = (w[:, s % MOE_SPLIT, at:at + 512] for w in (k.w_hi, k.w_lo))
            pe.matmul(out, hi, w_hi, start=start, stop=False)
            pe.matmul(out, hi, w_lo, start=False, stop=False)
            return pe.matmul(out, lo, w_hi, start=False, stop=stop)

        def body(n):
            lt, lv, la = self.lt, self.lv, self.la

            def units(*which):
                for u in which:
                    pe.wait_ge(*self.split(n, u))
                    self.unit(pe, product, n, u)
            pe.wait_ge(k.xg_split, 2 * n + 2)
            units(0, 1, 2, 3)
            pe.wait_ge(*la.at(n, "y"))
            for c in range(KC):
                if c >= 2:
                    pe.wait_ge(*lv.at(n, "added", c - 2))
                pe.matmul(k.bank[(7, 6)[c % 2]][:, 0:T], k.y_sb[:, P * c:P * c + P], k.selT[:, :], start=True, stop=True).then_inc(*lt.did("back", c))
            for i in range(3):
                m = P if i < 2 else NB
                mm = pe.transpose(k.bank[5][:, P * i:P * i + m], k.selg[0:m, i, :], ident[0:m, 0:m])
            mm.then_inc(*lt.did("selT"))
            for f in range(1, 8):
                units(4 * f, 4 * f + 1)
                pe.wait_ge(*lv.at(n, "hid", f - 1))
                if f > 1:
                    pe.wait_ge(*lv.at(n, "hid_split", f - 2))
                for j in range(4):
                    mm = pe.transpose(k.bank[4][:, P * j:P * j + P], k.hid[:, (f - 1) % 2, P * j:P * j + P], ident)
                mm.then_inc(*lt.did("hidT", f - 1))
                units(4 * f + 2, 4 * f + 3)
            units(*range(32, NEXT_TURN))
            pe.wait_ge(*lv.at(n, "hid_split", 6))
            gather(n + 1)
            units(*range(NEXT_TURN, MOE_UNITS))
            lt.ends()
        self.turns(pe, body, first)
        pe.wait_ge(*a.at("last y"))
        for c in range(KC):
            if c >= 2:
                pe.wait_ge(*v.at("last added", c - 2))
            pe.matmul(k.bank[(7, 6)[c % 2]][:, 0:T], k.y_sb[:, P * c:P * c + P], k.selT[:, :], start=True, stop=True).then_inc(*t.did("last back", c))

    def unit(self, pe, product, n, u):
        k, lv = self.k, self.lv
        if u < MOE_UP:
            f, q, half = u // 4, u // 2 % 2, u % 2
            if f >= 2 and half == 0:
                pe.wait_ge(*lv.at(n, "hid", f - 2))
            for j in range(4):
                kk = 4 * half + j
                mm = product(k.bank[2 * q + f % 2][:, :], k.xg_hi[:, kk, :], k.xg_lo[:, kk, :], u, 512 * j, kk == 0, kk == KC - 1)
        else:
            if u == MOE_UP:
                pe.wait_ge(*lv.at(n, "selT"))
            if (u - MOE_UP) % 2 == 0:
                pe.wait_ge(*lv.at(n, "hid_split", (u - MOE_UP) // 2))
            for j in range(2):
                c = 2 * (u - MOE_UP) + j
                for d in range(2):
                    mm = product(k.bank[5 + d][:, :], k.hid_hi[:, c, :], k.hid_lo[:, c, :], u, 1024 * j + 512 * d, c == 0, c == FE // P - 1)
        mm.then_inc(k.unit_used, 1)

    def scalar(self, act):
        k, t, a, v = self.k, self.t, self.a, self.v
        act.wait_ge(*v.at("diff"))
        act.activation(k.top_e[:, :], k.top_e[:, :], ACT.Exp).then_inc(*a.did("exp"))
        for i in range(3):
            m = P if i < 2 else NB
            act.wait_ge(*t.at("h_tok", i))
            for q in range(2):
                ins = act.copy(k.h_tok[0:m, i, 512 * q:512 * q + 512], k.bank[1 + 2 * i + q][0:m, :])
        ins.then_inc(*a.did("h_tok"))

        def keep_outputs(turn):
            act.wait_ge(*self.used(turn, -1))
            act.copy(k.y_sb[:, 0:512], k.bank[5][:, :])
            return act.copy(k.y_sb[:, 512:1024], k.bank[6][:, :])

        def keep_gathered(turn):
            for q in range(2):
                act.wait_ge(k.gathered, 2 * turn + q + 1)
                act.copy(k.xg_hi[:, 4 * q:4 * q + 4, :].rearrange("p c t -> p (c t)"), k.bank[(3, 4)[q]][:, :]).then_inc(k.xg_rounded, 1)

        def body(n):
            lt, lv, la = self.lt, self.lv, self.la

            def round_units(*units):
                for u in units:
                    self.loaded(act, n, u)
                    act.wait_ge(*self.split_free(n, u))
                    act.copy(k.w_hi[:, u % MOE_SPLIT, :], k.units[:, u % MOE_RING, :]).then_inc(*la.did("w_hi", u))
            round_units(0, 1)
            keep_outputs(n).then_inc(*la.did("y"))
            for f in range(8):
                round_units(*range(4 * f + (2 if f == 0 else 0), 4 * f + 4))
                if f < 7:
                    act.wait_ge(*self.used(n, 4 * f + 1))
                    if f >= 2:
                        act.wait_ge(*lv.at(n, "hid", f - 2))
                    act.activation(k.silu_g[:, f % 2, :], k.bank[f % 2][:, :], ACT.Silu).then_inc(*la.did("silu", f))
                if f:
                    act.wait_ge(*lt.at(n, "hidT", f - 1))
                    act.copy(k.hid_hi[:, 4 * f - 4:4 * f, :].rearrange("p c t -> p (c t)"), k.bank[4][:, :]).then_inc(*la.did("hid_hi", f - 1))
            round_units(*range(32, NEXT_TURN + 1))
            keep_gathered(n + 1)
            round_units(*range(NEXT_TURN + 1, MOE_UNITS))
            la.ends()
        turns = self.turns(act, body, lambda: keep_gathered(0))
        keep_outputs(turns).then_inc(*a.did("last y"))

    def vector(self, dve):
        k, t, a, v, l = self.k, self.t, self.a, self.v, self.l
        do = v.serial(dve)
        for x in (k.logits, k.mask, k.gate_e, k.rank):
            do(dve.memset(x[:, :, :], 0.0))
        dve.wait_ge(*t.at("logits"))
        for i in range(3):
            m = P if i < 2 else NB
            do(dve.tensor_tensor(k.logits[0:m, i, :], k.bank[0][0:m, 8 * i:8 * i + 8], k.vec(l, "router_b")[0:m, :], ALU.add))
        for i in range(3):
            do(dve.max(k.top_v[:, i, :], k.logits[:, i, :]))
            do(dve.max_index(k.top_i[:, i, :], k.top_v[:, i, :], k.logits[:, i, :]))
        do(dve.tensor_copy(k.top_f[:, :, :], k.top_i[:, :, :]))
        do(dve.tensor_tensor(k.top_e[:, :], k.top_v[:, :, 1], k.top_v[:, :, 0], ALU.subtract), "diff")
        for i in range(3):
            m = P if i < 2 else NB
            for c in range(2):
                do(dve.tensor_scalar(k.one_hot[0:m, :], k.c("expert_ids")[0:m, :], k.top_f[0:m, i, c:c + 1], None, ALU.is_equal))
                do(dve.tensor_tensor(k.mask[0:m, :, i], k.mask[0:m, :, i], k.one_hot[0:m, :], ALU.add), *(("mask",) if (i, c) == (2, 1) else ()))
        dve.wait_ge(*a.at("exp"))
        do(dve.tensor_scalar(k.top_w[:, 0, :], k.top_e[:, :], 1.0, None, ALU.add))
        do(dve.reciprocal(k.top_w[:, 0, :], k.top_w[:, 0, :]))
        do(dve.tensor_tensor(k.top_w[:, 1, :], k.top_w[:, 0, :], k.top_e[:, :], ALU.mult))
        for i in range(3):
            m = P if i < 2 else NB
            for c in range(2):
                do(dve.tensor_scalar(k.one_hot[0:m, :], k.c("expert_ids")[0:m, :], k.top_f[0:m, i, c:c + 1], k.top_w[0:m, c, i:i + 1], ALU.is_equal, ALU.mult))
                do(dve.tensor_tensor(k.gate_e[0:m, :, i], k.gate_e[0:m, :, i], k.one_hot[0:m, :], ALU.add))
        dve.wait_ge(*t.at("rank"))
        for i in range(3):
            m = P if i < 2 else NB
            do(dve.tensor_copy(k.rank[0:m, :, i], k.bank[0][0:m, 32 * i:32 * i + 8]))
        do(dve.tensor_scalar(k.turns[:, :], k.bank[0][:, 96:104], 0.0, None, ALU.is_gt))
        for full in (P, 2 * P):
            do(dve.scalar_tensor_tensor(out=k.turns[:, :], in0=k.bank[0][:, 96:104], scalar=float(full), in1=k.turns[:, :], op0=ALU.is_gt, op1=ALU.add))
        for e in range(1, NE):
            do(dve.tensor_tensor(k.turns[:, e:e + 1], k.turns[:, e:e + 1], k.turns[:, e - 1:e], ALU.add))
        do(dve.memset(k.turn_expert[:, :], 0.0))
        for e in range(NE):
            do(dve.scalar_tensor_tensor(out=k.turn_expert[:, :], in0=k.c("slot_ids")[:, 0:MAX_TURNS + 1], scalar=k.turns[:, e:e + 1], in1=k.turn_expert[:, :],
                                        op0=ALU.is_ge, op1=ALU.add))
        do(dve.tensor_scalar(k.turn_expert[:, :], k.turn_expert[:, :], float(NE - 1), None, ALU.min))
        do(dve.tensor_copy(k.turn_expert_i[:, :], k.turn_expert[:, :]))
        do(dve.memset(k.moe_out[:, :, :], 0.0))
        dve.wait_ge(*a.at("h_tok"))
        do(dve.tensor_copy(k.turns_i[:, :], k.turns[:, :]), "turns")

        def places(turn, do):
            col = bass.ds(self.expert(dve, turn), 1)
            for i in range(3):
                dve.tensor_scalar(k.sel[:, i, :], k.c("slot_ids"), k.rank[:, col, i], k.mask[:, col, i], ALU.is_equal, ALU.mult)
                ins = dve.tensor_scalar(k.selg[:, i, :], k.c("slot_ids"), k.rank[:, col, i], k.gate_e[:, col, i], ALU.is_equal, ALU.mult)
            ins.then_inc(k.places_made, 1)
            do(dve.tensor_copy(k.rank_next[:, :], k.rank[:, col, :].rearrange("p o i -> p (o i)")))
            do(dve.tensor_scalar(k.rank[:, col, :], k.rank_next[:, :].unsqueeze(1), -float(P), None, ALU.add))

        def split_gathered(turn):
            for q in range(2):
                dve.wait_ge(k.xg_rounded, 2 * turn + q + 1)
                hi, lo = (x[:, 4 * q:4 * q + 4, :].rearrange("p c t -> p (c t)") for x in (k.xg_hi, k.xg_lo))
                dve.tensor_tensor(lo, k.bank[(3, 4)[q]][:, :], hi.bitcast(F32), ALU.subtract).then_inc(k.xg_split, 1)

        def first():
            do(dve.memset(k.selT[:, :], 0.0))
            dve.nop().then_inc(k.unit_split, MOE_RING)
            places(slice(0, 1), do)
            split_gathered(0)

        def body(n):
            lt, lv, la = self.lt, self.lv, self.la
            do = lv.serial(dve, n)

            def split_units(*units):
                for u in units:
                    dve.wait_ge(*la.at(n, "w_hi", u))
                    ins = dve.tensor_tensor(k.w_lo[:, u % MOE_SPLIT, :], k.units[:, u % MOE_RING, :], k.w_hi[:, u % MOE_SPLIT, :].bitcast(F32), ALU.subtract)
                    ins.then_inc(k.unit_split, 1)
            split_units(0, 1, 2, 3, 4, 5)
            for c in range(KC):
                dve.wait_ge(*lt.at(n, "back", c))
                dve.tensor_tensor(k.moe_out[:, c, :], k.moe_out[:, c, :], k.bank[(7, 6)[c % 2]][:, 0:T], ALU.add).then_inc(*lv.did("added", c))
            dve.wait_ge(*lt.at(n, "selT"))
            do(dve.tensor_copy(k.selT[:, :], k.bank[5][:, 0:T]), "selT")
            for f in range(1, 8):
                if f > 1:
                    split_units(4 * f, 4 * f + 1)
                dve.wait_ge(*la.at(n, "silu", f - 1))
                dve.wait_ge(*self.used(n, 4 * f - 1))
                dve.tensor_tensor(k.hid[:, (f - 1) % 2, :], k.bank[2 + (f - 1) % 2][:, :], k.silu_g[:, (f - 1) % 2, :], ALU.mult).then_inc(*lv.did("hid", f - 1))
                split_units(4 * f + 2, 4 * f + 3)
                dve.wait_ge(*la.at(n, "hid_hi", f - 1))
                hi, lo = (x[:, 4 * f - 4:4 * f, :].rearrange("p c t -> p (c t)") for x in (k.hid_hi, k.hid_lo))
                dve.tensor_tensor(lo, k.bank[4][:, :], hi.bitcast(F32), ALU.subtract).then_inc(*lv.did("hid_split", f - 1))
            split_units(*range(32, NEXT_TURN - 1))
            places(bass.ds(n + 1, 1), do)
            split_units(NEXT_TURN - 1, NEXT_TURN)
            split_gathered(n + 1)
            split_units(*range(NEXT_TURN + 1, MOE_UNITS))
            lv.ends()
        self.turns(dve, body, first)
        for c in range(KC):
            dve.wait_ge(*t.at("last back", c))
            do(dve.tensor_tensor(k.moe_out[:, c, :], k.moe_out[:, c, :], k.bank[(7, 6)[c % 2]][:, 0:T], ALU.add), "last added", c)
        for c in range(KC):
            add_gated(k, dve, do, k.moe_out[:, c, :], c, 5)


class Swiglu(Stage):

    def __init__(self, k, l, w1, w3, w2, width):
        super().__init__(k, "swiglu", l)
        self.nf = width // P
        self.half = self.nf // 2
        self.up, self.down = [], []
        for c0 in range(0, width, 512):
            n = min(512, width - c0)
            pair = []
            for w in (w1, w3):
                place = k.next_place()
                dst = k.slot(place)[:, 0:KC * n].rearrange("p (k n) -> p k n", k=KC)
                pair.append(k.ring.add(place, dst, w.rearrange("(k p) n -> p k n", p=P)[:, :, c0:c0 + n]))
            self.up.append((pair, n // P))
        tiles = [(pair[q], i, i == n - 1) for pair, n in self.up for i in range(n) for q in range(2)]
        self.split = SplitTiles(k, "swiglu", l, tiles, lambda i: self.t.at("up", i // 2, i % 2))
        for d in range(4):
            for i in range(2):
                place = k.next_place()
                dst = k.slot(place)[:, 0:self.half * 256].rearrange("p (f n) -> p f n", n=256)
                src = w2.rearrange("(f p) n -> p f n", p=P)[:, self.half * i:self.half * (i + 1), 256 * d:256 * d + 256]
                self.down.append(k.ring.add(place, dst, src))

    def tensor(self, pe):
        k, t, v, a = self.k, self.t, self.v, self.a
        for f in range(self.nf):
            for q in range(2):
                if f >= 2:
                    pe.wait_ge(*(a, v)[q].at("up", f - 2))
                self.split.product(pe, k.bank[2 * (f % 2) + q][:, 0:T], 2 * f + q).then_inc(*t.did("up", f, q))
        pe.wait_ge(*v.at("up", self.nf - 1))
        for d in range(4):
            for i in range(2):
                slot = self.down[2 * d + i]
                k.ring.arrived(pe, slot)
                w = k.ring.loads[slot][1]
                if i == 0 and d >= 2:
                    pe.wait_ge(*v.at("down", d - 2))
                for j in range(2):
                    for f in range(self.half):
                        mm = pe.matmul(k.bank[4 + 2 * (d % 2) + j][:, 0:T], w[:, f, P * j:P * j + P], k.hidden[:, self.half * i + f, :],
                                       start=i == 0 and f == 0, stop=i == 1 and f == self.half - 1)
                mm.then_inc(*t.did("down", d, i))
                k.ring.release(slot, t)

    def scalar(self, act):
        k = self.k
        self.split.h_hi(act)
        self.split.hi(act, 0)
        self.split.hi(act, 1)
        for f in range(self.nf):
            self.split.hi(act, 2 * f + 2)
            act.wait_ge(*self.t.at("up", f, 0))
            if f >= 2:
                act.wait_ge(*self.v.at("up", f - 2))
            act.activation(k.silu_up[:, f % 2, :], k.bank[2 * (f % 2)][:, 0:T], ACT.Silu).then_inc(*self.a.did("up", f))
            self.split.hi(act, 2 * f + 3)

    def vector(self, dve):
        k, t, a, v = self.k, self.t, self.a, self.v
        do = v.serial(dve)
        self.split.h_lo(dve)
        self.split.lo(dve, 0)
        self.split.lo(dve, 1)
        for f in range(self.nf):
            self.split.lo(dve, 2 * f + 2)
            dve.wait_ge(*a.at("up", f))
            dve.wait_ge(*t.at("up", f, 1))
            ins = dve.tensor_tensor(k.hidden[:, f, :], k.bank[2 * (f % 2) + 1][:, 0:T], k.silu_up[:, f % 2, :], ALU.mult)
            ins.then_inc(*v.did("up", f))
            self.split.lo(dve, 2 * f + 3)
        for d in range(4):
            dve.wait_ge(*t.at("down", d, 1))
            for j in range(2):
                add_gated(k, dve, do, k.bank[4 + 2 * (d % 2) + j], 2 * d + j, 5)
            v.steps.book.setdefault((v.steps.name, (v.layer, "down", d)), v.steps.count)


class LayerLoads(Stage):

    def __init__(self, k, l):
        super().__init__(k, "loads", l)
        k.loads = self

    def scalar(self, act):
        k, l = self.k, self.l
        if l == 0:
            act.dma_start(k.c_in[:, :, :], k.c_dram).then_inc(k.c_loaded, 16)
            act.dma_start(k.x[:, :, :], k.x_in).then_inc(k.const_loaded, 16)
            act.dma_start(k.consts[:, :], k.consts_in).then_inc(k.const_loaded, 16)
            act.dma_start(k.table[0:1, :], k.table_in).then_inc(k.const_loaded, 16)
        act.dma_start(k.vecs[:, :], k.vecs_in[l]).then_inc(k.vec_loaded, 16)
        act.dma_start(k.small[:, :], k.small_in[l]).then_inc(k.small_loaded, 16)
        act.dma_start(k.shift_in[:, :, :], k.shift_dram[l]).then_inc(k.shift_loaded, 16)
        act.dma_start(k.conv_in[:, :, :, :], k.conv_dram[l]).then_inc(k.conv_loaded, 16)
        if l == 0:
            act.wait_ge(k.c_loaded, 16)
            act.activation(k.silu_c[:, :, :], k.c_in[:, :, :], ACT.Silu).then_inc(*self.a.did("silu_c"))
        else:
            act.copy(k.act_mark[0:1, :], k.c("eps")[0:1, :]).then_inc(*self.a.did("begun"))


class Store(Stage):

    def __init__(self, k):
        super().__init__(k, "store", 0)

    def pool(self, g):
        k = self.k
        g.dma_start(k.out["y"], k.h[:, :, :]).then_inc(k.stored, 16)
        k.stores += 1
        g.wait_ge(k.stored, 16 * k.stores)



def build(nc, dram, out, book):
    k = Kernel(nc, dram, out, book)
    for l in range(DEPTH):
        LayerLoads(k, l)
        Ada(k, l)
        Norm(k, l, "attn")
        Project(k, l)
        k.turn = 0
        k.gate_tiles = Gates(k, l)
        k.ahead = AdaAhead(k, l + 1, k.gate_tiles) if l + 1 < DEPTH else None
        rwkv = Rwkv(k, l)
        rwkv.ssm = Ssm(k, l)
        k.guard = Mla(k, l)
        Merge(k, l)
        Norm(k, l, "ffn")
        if l % 2 == 0:
            Swiglu(k, l, k.w1[l // 2], k.w3[l // 2], k.w2[l // 2], FF)
        else:
            Experts(k, l)
    Norm(k, DEPTH - 1, "final")
    Store(k)
    with nc.Block() as block:

        @block.sync
        def _(sp):
            k.ring.fill(sp)
            k.experts.sync(sp)

        @block.tensor
        def _(pe):
            for stage in k.stages:
                stage.emit("tensor", pe)

        @block.scalar
        def _(act):
            for stage in k.stages:
                stage.emit("scalar", act)

        @block.vector
        def _(dve):
            for stage in k.stages:
                stage.emit("vector", dve)

        @block.gpsimd
        def _(g):
            for stage in k.stages:
                stage.emit("pool", g)
    return k


def constants():
    a = np.zeros((P, NCONST), np.float32)

    def put(name, v):
        a[:v.shape[0], CONST[name][0]:CONST[name][0] + v.shape[1]] = v
    i, j = np.arange(P)[:, None], np.arange(P)[None, :]
    put("ident", np.eye(P))
    put("ones", np.ones((P, P)))
    put("block_ones", (i // 64 == j // 64).astype(float))
    t = np.arange(P + 1)[None, :]
    put("decay_tri", DECAY * ((i < t).astype(float) - (i < P // 2)))
    put("decay_id", DECAY * np.eye(NB))
    put("levels", np.concatenate([((i // (2 * m) == j // (2 * m)) & (i // m % 2 == 0) & (j // m % 2 == 1)).astype(float) for m in LEVELS], 1))
    put("strict", (i < j).astype(float))
    put("upto", (i <= j).astype(float))
    put("causal", np.where(j <= i, 0.0, -1e30))
    put("fold", (i % 64 == np.arange(64)[None, :]).astype(float))
    rot = np.zeros((P, P))
    for m in range(P):
        half = m % ROPE < ROPE // 2
        rot[m + 16 if half else m - 16, m] = -1.0 if half else 1.0
    put("rotate", rot)
    freq = np.float32(10000.0) ** (-np.arange(16, dtype=np.float32) / np.float32(16))
    pos = np.concatenate([np.arange(SEQ), np.full(NB, PAGE * NPAGE)]).astype(np.float32)
    ang = (pos[None, :] * freq[np.arange(P) % 16][:, None]).astype(np.float32)
    put("cos", np.cos(ang.astype(np.float64)))
    put("sin", np.sin(ang.astype(np.float64)))
    put("spread", (np.arange(8)[:, None] == np.arange(512)[None, :] // 64).astype(float))
    put("eps", np.full((P, 1), EPS))
    put("ln_eps", np.full((P, 1), LN_EPS))
    put("slot_ids", np.broadcast_to(np.arange(128.0), (P, P)))
    for g in range(NB // 2):
        own = np.where(2 * g + i // ROWS == np.arange(NB)[None, :], 0.0, -1e30)
        a[:, CONST["own"][0] + NB * g:CONST["own"][0] + NB * g + NB] = own
    put("expert_ids", np.broadcast_to(np.arange(8.0), (P, 8)))
    return a


def chunks(v):
    return np.swapaxes(v.reshape(v.shape[:-1] + (-1, P)), -1, -2)


def lay_out(i):
    i = {n: np.asarray(v) for n, v in i.items()}
    L = DEPTH
    x = np.concatenate([i["x_prompt"][0], i["x_sample"][:, 0]], 0)
    c = np.concatenate([i["c_prompt"], i["c_sample"]], 0)

    def fm(v):
        return v.T.reshape(-1, P, v.shape[0]).transpose(1, 0, 2)

    def rows8(v):
        out = np.zeros((L, P, 1), np.float32)
        out[:, :8, 0] = v
        return out
    parts = {
        "norm_attn": chunks(i["norm_attn"]), "norm_ffn": chunks(i["norm_ffn"]),
        "norm_final": np.broadcast_to(chunks(i["norm_final"]), (L, P, 8)), "b_ada": chunks(i["b_ada"]),
        "q_norm": chunks(i["mla_q_norm"]), "kv_norm": chunks(i["mla_kv_norm"]), "mu": chunks(i["rwkv_mu"]),
        "a0": chunks(i["rwkv_a0"]), "k_k": chunks(i["rwkv_k_k"]), "k_a": chunks(i["rwkv_k_a"]),
        "r_k": chunks(i["rwkv_r_k"].reshape(L, 512)), "ln_w": chunks(i["rwkv_ln_w"]), "ln_b": chunks(i["rwkv_ln_b"]),
        "conv_w": chunks(i["ssm_conv_w"]).transpose(0, 2, 1, 3).reshape(L, P, 32), "conv_b": chunks(i["ssm_conv_b"]),
        "d": chunks(np.repeat(i["ssm_d"], 64, axis=1)), "ssm_norm": chunks(i["ssm_norm"]),
        "dt_bias": rows8(i["ssm_dt_bias"]), "a_log": rows8(i["ssm_a_log"]),
        "router_b": np.broadcast_to(np.concatenate([np.zeros_like(i["moe_router_b"]), i["moe_router_b"]])[:, None, :], (L, P, 8)),
    }

    def by_k(w):
        return w.reshape(L, -1, P, w.shape[-1]).transpose(0, 2, 1, 3).reshape(L, P, -1)
    w_in = i["w_in"]
    router = np.concatenate([np.zeros_like(i["moe_router"]), i["moe_router"]])
    rwkv_w = np.zeros((L, P, NRWKV), np.float32)
    rwkv_w[:, 0:64, 0:512], rwkv_w[:, 64, 0:512] = i["rwkv_w2"], i["rwkv_w0"]
    rwkv_w[:, 64:128, 512:1024], rwkv_w[:, :, 1024:1536] = i["rwkv_a2"], i["rwkv_g2"]
    uq = i["mla_w_uq"]
    ukT = np.zeros((L, P, 2048), np.float32)
    ukT[:, 0:64] = i["mla_w_uk"].transpose(0, 3, 2, 1).reshape(L, 64, 2048)
    uk, uv = i["mla_w_uk"].reshape(L, LORA, 512), i["mla_w_uv"].reshape(L, LORA, 512)
    arrays = {
        "x": fm(x), "consts": constants(), "table": i["page_table"].reshape(1, 64), "c": fm(c),
        "vecs": np.concatenate([parts[n] for n in VEC], -1),
        "small": np.concatenate([by_k(np.tile(w_in[:, :, 512:544], (1, 1, 4))), by_k(w_in[:, :, 3872:3880]), by_k(router)], -1),
        "shift": chunks(i["state_rwkv_shift"]).transpose(0, 2, 3, 1),
        "conv": chunks(i["state_ssm_conv"]).transpose(0, 3, 4, 1, 2),
        "rwkv_w": rwkv_w, "mla_w": np.concatenate([by_k(uq), by_k(uk), by_k(uv), ukT], -1),
        "wkv": i["state_rwkv_wkv"].reshape(L, NB, 4, 2, 64, 64).transpose(0, 3, 5, 2, 1, 4).reshape(L, P, 4, NB, 64),
        "ssm": i["state_ssm"].reshape(L, NB, 4, 2, 64, P).transpose(0, 3, 4, 2, 1, 5).reshape(L, P, 4, NB, P),
        "cache": np.concatenate([i["cache_ckv"], i["cache_kpe"]], -1),
    }
    for n in DRAM:
        if n not in arrays:
            arrays[n] = i[n]
    return {n: np.ascontiguousarray(arrays[n]) for n in DRAM}


def hand_back(o):
    L = DEPTH

    def rows(v):
        return v.transpose(2, 1, 0).reshape(v.shape[2], -1)
    y = rows(o["y"])
    ckv = np.stack([rows(o["ckv"][l]) for l in range(L)])
    kpe = o["kpe"].transpose(0, 2, 1)
    shift = np.stack([rows(o["shift"][l]) for l in range(L)])
    p_wkv = o["p_wkv"].reshape(L, 2, 64, 4, 64).transpose(0, 3, 1, 4, 2).reshape(L, 1, 8, 64, 64)
    s_wkv = o["s_wkv"].reshape(L, 2, 64, 4, NB, 64).transpose(0, 4, 3, 1, 5, 2).reshape(L, NB, 8, 64, 64)
    p_conv = o["p_conv"].transpose(0, 3, 2, 1).reshape(L, 1, 3, D)
    s_conv = o["s_conv"].transpose(0, 3, 4, 2, 1).reshape(L, NB, 3, D)
    p_ssm = o["p_ssm"].reshape(L, P, 8, 64).transpose(0, 2, 3, 1).reshape(L, 1, 8, 64, P)
    s_ssm = o["s_ssm"].reshape(L, 2, 64, 4, NB, P).transpose(0, 4, 3, 1, 2, 5).reshape(L, NB, 8, 64, P)
    c = np.ascontiguousarray
    return (c(y[:SEQ][None]), c(y[SEQ:][:, None]), c(ckv[:, :SEQ].reshape(L, NT, PAGE, LORA)), c(kpe[:, :SEQ].reshape(L, NT, PAGE, ROPE)),
            c(shift[:, 0:1]), c(p_wkv), c(p_conv), c(p_ssm), c(ckv[:, SEQ:][:, :, None]), c(kpe[:, SEQ:][:, :, None]),
            c(shift[:, 1:]), c(s_wkv), c(s_conv), c(s_ssm))


def declare(nc, arrays):
    dram = {n: nc.dram_tensor(f"in_{n}", a.shape, mybir.dt.from_np(a.dtype), kind="ExternalInput").ap() for n, a in arrays.items()}
    out = {n: nc.dram_tensor(f"out_{n}", shape, F32, kind="ExternalOutput").ap() for n, shape in OUTS.items()}
    return dram, out


def kernel(**inputs):
    import concourse.bacc as bacc
    from concourse.bass_utils import run_bass_kernel_spmd as run

    arrays = lay_out(inputs)
    book = {}
    for _ in range(2):
        nc = bacc.Bacc("TRN2", target_bir_lowering=False, num_devices=1, dynamic_dma_scratch_size=4096)
        build(nc, *declare(nc, arrays), book)
    r = run(nc, [{f"in_{n}": a for n, a in arrays.items()}], core_ids=[0])
    return hand_back({n: np.asarray(r.results[0][f"out_{n}"]) for n in OUTS})
```
